# Optimizing a Trainium2 kernel written in Bass

```python
import functools
import jax
import jax.numpy as jnp
from jax import lax
import numpy as np
import jax, jax.numpy as jnp

D_MODEL = 1024
BATCH = 1
SEQ = 256
DEPTH = 4

GRID_W = 64
CTX_LEN = 256
N_MIXERS = 3
EPS = 1e-6
NEG_INF = -1e30
ROPE_BASE = 10000.0
ADA_STD = 0.02

A_HEADS = 16
A_KV_HEADS = 4
A_HEAD_DIM = 64
A_WINDOW = 128
A_BLOCK = 128
A_WIDTH = A_HEADS * A_HEAD_DIM
A_KV_WIDTH = A_KV_HEADS * A_HEAD_DIM
A_IN = 2 * A_WIDTH + 2 * A_KV_WIDTH

B_HEADS = 8
B_NOPE = 128
B_ROPE = 64
B_VDIM = 128
B_Q_RANK = 256
B_KV_RANK = 128
B_BLOCK = 128
B_WIDTH = B_HEADS * B_VDIM
B_IN = B_Q_RANK + B_KV_RANK + B_ROPE + B_WIDTH

C_HEADS = 4
C_QK_DIM = 128
C_V_DIM = 256
C_QK_WIDTH = C_HEADS * C_QK_DIM
C_WIDTH = C_HEADS * C_V_DIM
C_CONV = 5
C_CHUNK = 128
C_IN = 2 * C_QK_WIDTH + 3 * C_WIDTH + 4 * C_HEADS
F_BIAS = 3.0


def rmsnorm(x, g):
    xf = x.astype(jnp.float32)
    y = xf * lax.rsqrt(jnp.mean(xf * xf, axis=-1, keepdims=True) + EPS)
    return (y * g.astype(jnp.float32)).astype(x.dtype)

def axial_rope(n_tok, rot_dim, dtype):
    rows = n_tok // GRID_W
    r, cidx = jnp.meshgrid(jnp.arange(rows), jnp.arange(GRID_W), indexing='ij')
    r = r.reshape(-1).astype(jnp.float32)
    cc = cidx.reshape(-1).astype(jnp.float32)
    n_freq = rot_dim // 4
    inv = ROPE_BASE ** (-jnp.arange(n_freq, dtype=jnp.float32) / n_freq)
    ang = jnp.concatenate([r[:, None] * inv, cc[:, None] * inv], axis=-1)
    return jnp.cos(ang).astype(dtype), jnp.sin(ang).astype(dtype)

def apply_rope(x, cos, sin):
    x1, x2 = x[..., 0::2], x[..., 1::2]
    cos, sin = cos[:, None, :], sin[:, None, :]
    return jnp.stack([x1 * cos - x2 * sin, x1 * sin + x2 * cos], axis=-1).reshape(x.shape)

def sink_softmax(logits, sink):
    m = jnp.maximum(jnp.max(logits, axis=-1, keepdims=True), sink)
    e = jnp.exp(logits - m)
    return e / (jnp.sum(e, axis=-1, keepdims=True) + jnp.exp(sink - m))

def centred_dwconv(x, w):
    k = w.shape[0]
    return lax.conv_general_dilated(x, w[:, None, :].astype(x.dtype), window_strides=(1,),
                                    padding=[(k // 2, k // 2)],
                                    dimension_numbers=('NWC', 'WIO', 'NWC'),
                                    feature_group_count=x.shape[-1])

def window_gqa_mixer(h_lat, h_ctx, need_ctx, w_in, sink, w_out):
    bsz, n_lat, _ = h_lat.shape
    n_ctx = h_ctx.shape[1]
    grp = A_HEADS // A_KV_HEADS
    scale = A_HEAD_DIM ** -0.5
    cuts = [A_WIDTH, A_WIDTH + A_KV_WIDTH, A_WIDTH + 2 * A_KV_WIDTH]
    sink_l = sink.astype(jnp.float32).reshape(A_KV_HEADS, grp, 1, 1)

    q_l, k_l, v_l, z_l = jnp.split(h_lat @ w_in, cuts, axis=-1)
    if need_ctx:
        q_c, k_c, v_c, z_c = jnp.split(h_ctx @ w_in, cuts, axis=-1)
    else:
        k_c, v_c = jnp.split(h_ctx @ w_in[:, A_WIDTH:A_WIDTH + 2 * A_KV_WIDTH], 2, axis=-1)
    k_c = k_c.reshape(bsz, n_ctx, A_KV_HEADS, A_HEAD_DIM)
    v_c = v_c.reshape(bsz, n_ctx, A_KV_HEADS, A_HEAD_DIM)

    cos, sin = axial_rope(n_lat, A_HEAD_DIM, h_lat.dtype)
    q_l = apply_rope(q_l.reshape(bsz, n_lat, A_HEADS, A_HEAD_DIM), cos, sin)
    q_l = q_l.reshape(bsz, n_lat, A_KV_HEADS, grp, A_HEAD_DIM)
    k_l = apply_rope(k_l.reshape(bsz, n_lat, A_KV_HEADS, A_HEAD_DIM), cos, sin)
    v_l = v_l.reshape(bsz, n_lat, A_KV_HEADS, A_HEAD_DIM)

    pad = ((0, 0), (A_BLOCK, A_BLOCK), (0, 0), (0, 0))
    k_pad, v_pad = jnp.pad(k_l, pad), jnp.pad(v_l, pad)
    band = 3 * A_BLOCK
    k_off = jnp.arange(band) - A_BLOCK
    in_window = jnp.abs(k_off[None, :] - jnp.arange(A_BLOCK)[:, None]) <= A_WINDOW
    ctx_ok = jnp.ones((A_BLOCK, n_ctx), dtype=bool)

    def block(n):
        start = n * A_BLOCK
        q_b = lax.dynamic_slice_in_dim(q_l, start, A_BLOCK, axis=1)
        k_b = jnp.concatenate([lax.dynamic_slice_in_dim(k_pad, start, band, axis=1), k_c], axis=1)
        v_b = jnp.concatenate([lax.dynamic_slice_in_dim(v_pad, start, band, axis=1), v_c], axis=1)
        kpos = start + k_off
        valid = in_window & ((kpos >= 0) & (kpos < n_lat))[None, :]
        mask = jnp.concatenate([valid, ctx_ok], axis=1)
        logits = jnp.einsum('bqkgd,bjkd->bkgqj', q_b, k_b).astype(jnp.float32) * scale
        p = sink_softmax(jnp.where(mask, logits, NEG_INF), sink_l)
        return jnp.einsum('bkgqj,bjkd->bqkgd', p.astype(v_b.dtype), v_b)

    o = lax.map(block, jnp.arange(n_lat // A_BLOCK))
    o_l = jnp.moveaxis(o, 0, 1).reshape(bsz, n_lat, A_WIDTH)
    y_l = (o_l * jax.nn.silu(z_l)) @ w_out

    y_c = None
    if need_ctx:
        q_c = q_c.reshape(bsz, n_ctx, A_KV_HEADS, grp, A_HEAD_DIM)
        logits = jnp.einsum('bqkgd,bjkd->bkgqj', q_c, k_c).astype(jnp.float32) * scale
        p = sink_softmax(logits, sink_l)
        o_c = jnp.einsum('bkgqj,bjkd->bqkgd', p.astype(v_c.dtype), v_c).reshape(bsz, n_ctx, A_WIDTH)
        y_c = (o_c * jax.nn.silu(z_c)) @ w_out
    return y_l, y_c

def mla_mixer(h_lat, h_ctx, need_ctx, w_in, g_qa, g_kva, w_uq, w_ukv, w_out):
    bsz, n_lat, _ = h_lat.shape
    n_ctx = h_ctx.shape[1]
    dqk = B_NOPE + B_ROPE
    scale = dqk ** -0.5
    cuts = [B_Q_RANK, B_Q_RANK + B_KV_RANK, B_Q_RANK + B_KV_RANK + B_ROPE]

    def queries(q_a):
        b, n, _ = q_a.shape
        return (rmsnorm(q_a, g_qa) @ w_uq).reshape(b, n, B_HEADS, dqk)

    def keys_values(kv_a, k_pe):
        b, n, _ = kv_a.shape
        kv = (rmsnorm(kv_a, g_kva) @ w_ukv).reshape(b, n, B_HEADS, B_NOPE + B_VDIM)
        k_nope, v = jnp.split(kv, [B_NOPE], axis=-1)
        k_pe = jnp.broadcast_to(k_pe[:, :, None, :], (b, n, B_HEADS, B_ROPE))
        return jnp.concatenate([k_nope, k_pe], axis=-1), v

    q_a_l, kv_a_l, kpe_l, z_l = jnp.split(h_lat @ w_in, cuts, axis=-1)
    if need_ctx:
        q_a_c, kv_a_c, kpe_c, z_c = jnp.split(h_ctx @ w_in, cuts, axis=-1)
    else:
        kv_a_c, kpe_c = jnp.split(h_ctx @ w_in[:, B_Q_RANK:cuts[2]], [B_KV_RANK], axis=-1)

    cos, sin = axial_rope(n_lat, B_ROPE, h_lat.dtype)
    q_l = queries(q_a_l)
    q_l = jnp.concatenate([q_l[..., :B_NOPE], apply_rope(q_l[..., B_NOPE:], cos, sin)], axis=-1)
    kpe_l = apply_rope(kpe_l[:, :, None, :], cos, sin)[:, :, 0]
    k_l, v_l = keys_values(kv_a_l, kpe_l)
    k_c, v_c = keys_values(kv_a_c, kpe_c)

    k_all = jnp.concatenate([k_c, k_l], axis=1)
    v_all = jnp.concatenate([v_c, v_l], axis=1)

    def block(q_b):
        logits = jnp.einsum('bqhd,bkhd->bhqk', q_b, k_all).astype(jnp.float32) * scale
        p = jax.nn.softmax(logits, axis=-1)
        return jnp.einsum('bhqk,bkhd->bqhd', p.astype(v_all.dtype), v_all)

    nb = n_lat // B_BLOCK
    q_blocks = jnp.moveaxis(q_l.reshape(bsz, nb, B_BLOCK, B_HEADS, dqk), 1, 0)
    o = lax.map(block, q_blocks)
    o_l = jnp.moveaxis(o, 0, 1).reshape(bsz, n_lat, B_WIDTH)
    y_l = (o_l * jax.nn.silu(z_l)) @ w_out

    y_c = None
    if need_ctx:
        q_c = queries(q_a_c)
        logits = jnp.einsum('bqhd,bkhd->bhqk', q_c, k_c).astype(jnp.float32) * scale
        p = jax.nn.softmax(logits, axis=-1)
        o_c = jnp.einsum('bhqk,bkhd->bqhd', p.astype(v_c.dtype), v_c).reshape(bsz, n_ctx, B_WIDTH)
        y_c = (o_c * jax.nn.silu(z_c)) @ w_out
    return y_l, y_c

def mlstm_chunkwise(q, k, v, i_pre, f_pre, state, need_out):
    b, h, t, dk = q.shape
    dv = v.shape[-1]
    nc = t // C_CHUNK
    q = q.reshape(b, h, nc, C_CHUNK, dk)
    k = k.reshape(b, h, nc, C_CHUNK, dk)
    v = v.reshape(b, h, nc, C_CHUNK, dv)
    ig = i_pre.reshape(b, h, nc, C_CHUNK)
    cum = jnp.cumsum(jax.nn.log_sigmoid(f_pre).reshape(b, h, nc, C_CHUNK), axis=-1)
    tot = cum[..., -1]

    w_end = tot[..., None] - cum + ig
    m_loc = jnp.max(w_end, axis=-1)
    e_end = jnp.exp(w_end - m_loc[..., None])
    c_loc = jnp.einsum('bhcs,bhcsv,bhcsk->bhcvk', e_end, v, k)
    n_loc = jnp.einsum('bhcs,bhcsk->bhck', e_end, k)

    def step(carry, inp):
        c_prev, n_prev, m_prev = carry
        tot_c, m_l, c_l, n_l = inp
        m_new = jnp.maximum(tot_c + m_prev, m_l)
        a = jnp.exp(tot_c + m_prev - m_new)
        bb = jnp.exp(m_l - m_new)
        new = (a[..., None, None] * c_prev + bb[..., None, None] * c_l,
               a[..., None] * n_prev + bb[..., None] * n_l, m_new)
        return new, carry

    to_front = lambda a: jnp.moveaxis(a, 2, 0)
    final, starts = lax.scan(step, state, (to_front(tot), to_front(m_loc), to_front(c_loc), to_front(n_loc)))
    if not need_out:
        return None, final
    c_st, n_st, m_st = (jnp.moveaxis(s, 0, 2) for s in starts)

    tri = jnp.tril(jnp.ones((C_CHUNK, C_CHUNK), dtype=bool))
    log_d = jnp.where(tri, cum[..., :, None] - cum[..., None, :] + ig[..., None, :], NEG_INF)
    inter = cum + m_st[..., None]
    m_t = jnp.maximum(inter, jnp.max(log_d, axis=-1))
    s_qk = jnp.einsum('bhctd,bhcsd->bhcts', q, k) * jnp.exp(log_d - m_t[..., None])
    a_t = jnp.exp(inter - m_t)
    num = (jnp.einsum('bhcts,bhcsv->bhctv', s_qk, v)
           + a_t[..., None] * jnp.einsum('bhcvk,bhctk->bhctv', c_st, q))
    den = jnp.sum(s_qk, axis=-1) + a_t * jnp.einsum('bhck,bhctk->bhct', n_st, q)
    out = num / jnp.maximum(jnp.abs(den), jnp.exp(-m_t))[..., None]
    return out.reshape(b, h, t, dv), final

def mlstm_mixer(h_lat, h_ctx, need_ctx, w_in, conv, b_gate, g_head, w_out):
    bsz = h_lat.shape[0]
    cuts = [2 * C_QK_WIDTH, 2 * C_QK_WIDTH + C_WIDTH, 2 * C_QK_WIDTH + 2 * C_WIDTH, 2 * C_QK_WIDTH + 3 * C_WIDTH]

    def prepare(h):
        b, n, _ = h.shape
        qk, v, o, z, gates = jnp.split(h @ w_in, cuts, axis=-1)
        qk = jax.nn.silu(centred_dwconv(qk, conv))
        q, k = jnp.split(qk, 2, axis=-1)
        heads = lambda a, d: jnp.moveaxis(a.reshape(b, n, C_HEADS, d), 2, 1).astype(jnp.float32)
        q = heads(q, C_QK_DIM)
        k = heads(k, C_QK_DIM) * (C_QK_DIM ** -0.5)
        v = heads(v, C_V_DIM)
        gates = jnp.moveaxis((gates + b_gate).astype(jnp.float32).reshape(b, n, 4, C_HEADS), 1, -1)
        return q, k, v, o, z, gates

    def finish(hsum, o, z):
        b, n, _ = o.shape
        hh = jnp.moveaxis(hsum, 1, 2).astype(o.dtype)
        hh = hh * jax.nn.sigmoid(o).reshape(b, n, C_HEADS, C_V_DIM)
        hh = rmsnorm(hh, g_head.reshape(C_HEADS, C_V_DIM)).reshape(b, n, C_WIDTH)
        return (hh * jax.nn.silu(z)) @ w_out

    q_c, k_c, v_c, o_c, z_c, g_c = prepare(h_ctx)
    q_l, k_l, v_l, o_l, z_l, g_l = prepare(h_lat)
    zero_state = (jnp.zeros((bsz, C_HEADS, C_V_DIM, C_QK_DIM), jnp.float32),
                  jnp.zeros((bsz, C_HEADS, C_QK_DIM), jnp.float32),
                  jnp.full((bsz, C_HEADS), NEG_INF, jnp.float32))
    flip = lambda a: jnp.flip(a, axis=2)

    hc_f, st_f = mlstm_chunkwise(q_c, k_c, v_c, g_c[:, 0], g_c[:, 1], zero_state, need_ctx)
    hl_f, _ = mlstm_chunkwise(q_l, k_l, v_l, g_l[:, 0], g_l[:, 1], st_f, True)
    hc_b, st_b = mlstm_chunkwise(flip(q_c), flip(k_c), flip(v_c), flip(g_c[:, 2]), flip(g_c[:, 3]), zero_state, need_ctx)
    hl_b, _ = mlstm_chunkwise(flip(q_l), flip(k_l), flip(v_l), flip(g_l[:, 2]), flip(g_l[:, 3]), st_b, True)

    y_l = finish(hl_f + flip(hl_b), o_l, z_l)
    y_c = finish(hc_f + flip(hc_b), o_c, z_c) if need_ctx else None
    return y_l, y_c

def _normal(key, shape, std):
    return std * jax.random.normal(key, shape, jnp.float32)

def _gain(key, n):
    return 1.0 + 0.1 * jax.random.normal(key, (n,), jnp.float32)

def _layer_params(key, kind):
    ks = jax.random.split(key, 10)
    p = {
        'w_ada': _normal(ks[0], (D_MODEL, 3 * D_MODEL), ADA_STD),
        'b_ada': _normal(ks[1], (3 * D_MODEL,), 0.02),
        'g_pre': _gain(ks[2], D_MODEL),
        'g_post': _gain(ks[3], D_MODEL),
    }
    if kind == 0:
        p['w_in'] = _normal(ks[4], (D_MODEL, A_IN), D_MODEL ** -0.5)
        p['sink'] = _normal(ks[5], (A_HEADS,), 0.5)
        p['w_out'] = _normal(ks[6], (A_WIDTH, D_MODEL), A_WIDTH ** -0.5)
    elif kind == 1:
        p['w_in'] = _normal(ks[4], (D_MODEL, B_IN), D_MODEL ** -0.5)
        p['g_qa'] = _gain(ks[5], B_Q_RANK)
        p['g_kva'] = _gain(ks[6], B_KV_RANK)
        p['w_uq'] = _normal(ks[7], (B_Q_RANK, B_HEADS * (B_NOPE + B_ROPE)), B_Q_RANK ** -0.5)
        p['w_ukv'] = _normal(ks[8], (B_KV_RANK, B_HEADS * (B_NOPE + B_VDIM)), B_KV_RANK ** -0.5)
        p['w_out'] = _normal(ks[9], (B_WIDTH, D_MODEL), B_WIDTH ** -0.5)
    else:
        offset = jnp.repeat(jnp.array([0.0, F_BIAS, 0.0, F_BIAS], jnp.float32), C_HEADS)
        p['w_in'] = _normal(ks[4], (D_MODEL, C_IN), D_MODEL ** -0.5)
        p['conv'] = _normal(ks[5], (C_CONV, 2 * C_QK_WIDTH), C_CONV ** -0.5)
        p['b_gate'] = offset + _normal(ks[6], (4 * C_HEADS,), 0.3)
        p['g_head'] = _gain(ks[7], C_WIDTH)
        p['w_out'] = _normal(ks[8], (C_WIDTH, D_MODEL), C_WIDTH ** -0.5)
    return p

def first_inputs(seed: int = 0) -> dict:
    key = jax.random.key(seed)
    k_x, k_c, k_ctx, k_cc, k_layers = jax.random.split(key, 5)
    inputs = {
        'x': jax.random.normal(k_x, (BATCH, SEQ, D_MODEL), jnp.float32),
        'c': jax.random.normal(k_c, (BATCH, D_MODEL), jnp.float32),
        'ctx': jax.random.normal(k_ctx, (BATCH, CTX_LEN, D_MODEL), jnp.float32),
        'c_ctx': jax.random.normal(k_cc, (D_MODEL,), jnp.float32),
    }
    for i, lk in enumerate(jax.random.split(k_layers, DEPTH)):
        for name, val in _layer_params(lk, i % N_MIXERS).items():
            inputs[f'l{i}_{name}'] = val
    return inputs

def modulation(cvec, w_ada, b_ada):
    return jnp.split(jax.nn.silu(cvec) @ w_ada + b_ada, 3, axis=-1)

def first_block(x, c, ctx, c_ctx,
              l0_w_ada, l0_b_ada, l0_g_pre, l0_g_post, l0_w_in, l0_sink, l0_w_out,
              l1_w_ada, l1_b_ada, l1_g_pre, l1_g_post, l1_w_in, l1_g_qa, l1_g_kva, l1_w_uq, l1_w_ukv, l1_w_out,
              l2_w_ada, l2_b_ada, l2_g_pre, l2_g_post, l2_w_in, l2_conv, l2_b_gate, l2_g_head, l2_w_out,
              l3_w_ada, l3_b_ada, l3_g_pre, l3_g_post, l3_w_in, l3_sink, l3_w_out):
    layers = [
        (l0_w_ada, l0_b_ada, l0_g_pre, l0_g_post,
         functools.partial(window_gqa_mixer, w_in=l0_w_in, sink=l0_sink, w_out=l0_w_out)),
        (l1_w_ada, l1_b_ada, l1_g_pre, l1_g_post,
         functools.partial(mla_mixer, w_in=l1_w_in, g_qa=l1_g_qa, g_kva=l1_g_kva,
                           w_uq=l1_w_uq, w_ukv=l1_w_ukv, w_out=l1_w_out)),
        (l2_w_ada, l2_b_ada, l2_g_pre, l2_g_post,
         functools.partial(mlstm_mixer, w_in=l2_w_in, conv=l2_conv, b_gate=l2_b_gate,
                           g_head=l2_g_head, w_out=l2_w_out)),
        (l3_w_ada, l3_b_ada, l3_g_pre, l3_g_post,
         functools.partial(window_gqa_mixer, w_in=l3_w_in, sink=l3_sink, w_out=l3_w_out)),
    ]
    x_lat, x_ctx = x, ctx
    for i in range(DEPTH):
        w_ada, b_ada, g_pre, g_post, mixer = layers[i]
        need_ctx = i < DEPTH - 1
        sh_l, sc_l, gt_l = modulation(c, w_ada, b_ada)
        sh_c, sc_c, gt_c = modulation(c_ctx, w_ada, b_ada)
        h_l = rmsnorm(x_lat, g_pre) * (1.0 + sc_l[:, None, :]) + sh_l[:, None, :]
        h_c = rmsnorm(x_ctx, g_pre) * (1.0 + sc_c) + sh_c
        y_l, y_c = mixer(h_l, h_c, need_ctx=need_ctx)
        x_lat = x_lat + gt_l[:, None, :] * rmsnorm(y_l, g_post)
        if need_ctx:
            x_ctx = x_ctx + gt_c * rmsnorm(y_c, g_post)
    return x_lat


DEPTH_2 = 1

ATTN_HEADS = 8
ATTN_HD = 64
ATTN_WIDTH = ATTN_HEADS * ATTN_HD
DILATED_PATTERNS = ((128, 1), (512, 4), (2048, 16))
ATTN_BLOCK = 128
DN_HEADS = 4
DN_KD = 128
DN_VD = 128
DN_QK_WIDTH = DN_HEADS * DN_KD
DN_V_WIDTH = DN_HEADS * DN_VD
DN_CONV_DIM = 2 * DN_QK_WIDTH + DN_V_WIDTH
CONV_K = 4
DN_CHUNK = 64
D_MIX = ATTN_WIDTH + DN_V_WIDTH
IN_SPLITS = (ATTN_WIDTH, 2 * ATTN_WIDTH, 3 * ATTN_WIDTH,
             3 * ATTN_WIDTH + DN_CONV_DIM,
             3 * ATTN_WIDTH + DN_CONV_DIM + DN_V_WIDTH,
             3 * ATTN_WIDTH + DN_CONV_DIM + DN_V_WIDTH + DN_HEADS)
IN_COLS = 3 * ATTN_WIDTH + DN_CONV_DIM + DN_V_WIDTH + 2 * DN_HEADS
N_EXPERTS = 32
TOP_K = 4
D_EXPERT = 1024
SWIGLU_LIMIT = 7.0
SWIGLU_ALPHA = 1.702
MOE_BLOCK = 128
NORM_EPS = 1e-6


def rms_norm(x, w):
    xf = x.astype(jnp.float32)
    y = xf * lax.rsqrt(jnp.mean(xf * xf, axis=-1, keepdims=True) + NORM_EPS)
    return (y * w.astype(jnp.float32)).astype(x.dtype)

def l2_norm(x):
    return x * lax.rsqrt(jnp.sum(x * x, axis=-1, keepdims=True) + NORM_EPS)

def modulate(x, w, shift, scale):
    return rms_norm(x, w) * (1 + scale[:, None, :]) + shift[:, None, :]

def dilated_branch(q, k, v, window, dilation):
    B, S, H, Dh = q.shape
    L = S // dilation
    span = window // dilation
    nb = -(-L // ATTN_BLOCK)
    Lp = nb * ATTN_BLOCK

    def to_sub(t):
        t = t.astype(jnp.float32).reshape(B, L, dilation, H, Dh).transpose(0, 2, 3, 1, 4)
        return jnp.pad(t, ((0, 0), (0, 0), (0, 0), (0, Lp - L), (0, 0)))

    def window_blocks(t):
        t = jnp.pad(t, ((0, 0), (0, 0), (0, 0), (ATTN_BLOCK, 0), (0, 0)))
        t = t.reshape(B, dilation, H, nb + 1, ATTN_BLOCK, Dh)
        return jnp.concatenate([t[:, :, :, :-1], t[:, :, :, 1:]], axis=-2)

    qb = to_sub(q).reshape(B, dilation, H, nb, ATTN_BLOCK, Dh)
    kw = window_blocks(to_sub(k))
    vw = window_blocks(to_sub(v))
    s = jnp.einsum('bdhnqe,bdhnke->bdhnqk', qb, kw) * (ATTN_HD ** -0.5)
    dist = (jnp.arange(ATTN_BLOCK)[:, None] + ATTN_BLOCK) - jnp.arange(2 * ATTN_BLOCK)[None, :]
    band = (dist >= 0) & (dist <= span)
    kpos = jnp.arange(nb)[:, None] * ATTN_BLOCK - ATTN_BLOCK + jnp.arange(2 * ATTN_BLOCK)[None, :]
    mask = band[None, :, :] & (kpos >= 0)[:, None, :]
    s = jnp.where(mask, s, -jnp.inf)
    m = jnp.max(s, axis=-1, keepdims=True)
    p = jnp.exp(s - m)
    den = jnp.sum(p, axis=-1)
    o = jnp.einsum('bdhnqk,bdhnke->bdhnqe', p, vw) / den[..., None]
    lse = m[..., 0] + jnp.log(den)
    o = o.reshape(B, dilation, H, Lp, Dh)[:, :, :, :L].transpose(0, 3, 1, 2, 4).reshape(B, S, H, Dh)
    lse = lse.reshape(B, dilation, H, Lp)[:, :, :, :L].transpose(0, 3, 1, 2).reshape(B, S, H)
    return o, lse

def dilated_attention(q, k, v):
    outs, lses = [], []
    for window, dilation in DILATED_PATTERNS:
        o, lse = dilated_branch(q, k, v, window, dilation)
        outs.append(o)
        lses.append(lse)
    wts = jax.nn.softmax(jnp.stack(lses, axis=0), axis=0)
    return jnp.einsum('gbsh,gbshe->bshe', wts, jnp.stack(outs, axis=0))

def causal_short_conv(x, w):
    S = x.shape[1]
    xp = jnp.pad(x, ((0, 0), (CONV_K - 1, 0), (0, 0)))
    y = w[CONV_K - 1] * x
    for j in range(CONV_K - 1):
        y = y + w[j] * xp[:, j:j + S]
    return y

def gated_delta_rule(q, k, v, g, beta):
    B, S, H, Dk = q.shape
    Dv = v.shape[-1]
    C = DN_CHUNK
    N = S // C
    q = l2_norm(q) * (Dk ** -0.5)
    k = l2_norm(k)

    def chunk(t):
        return jnp.swapaxes(t.reshape((B, N, C, H) + t.shape[3:]), 2, 3)

    qc, kc, vc, gc, bc = chunk(q), chunk(k), chunk(v), chunk(g), chunk(beta)
    gc = jnp.cumsum(gc, axis=-1)
    tril = jnp.tril(jnp.ones((C, C), dtype=bool))
    strict = jnp.tril(jnp.ones((C, C), dtype=bool), -1)
    decay = jnp.exp(jnp.where(tril, gc[..., :, None] - gc[..., None, :], -jnp.inf))
    kb = kc * bc[..., None]
    vb = vc * bc[..., None]
    a_low = jnp.where(strict, jnp.einsum('bnhie,bnhje->bnhij', kb, kc) * decay, 0.0)
    lhs = a_low + jnp.eye(C, dtype=jnp.float32)
    u = lax.linalg.triangular_solve(lhs, vb, left_side=True, lower=True)
    w = lax.linalg.triangular_solve(lhs, kb * jnp.exp(gc)[..., None], left_side=True, lower=True)
    intra = jnp.einsum('bnhie,bnhje->bnhij', qc, kc) * decay
    q_dec = qc * jnp.exp(gc)[..., None]
    k_dec = kc * jnp.exp(gc[..., -1:] - gc)[..., None]
    g_last = jnp.exp(gc[..., -1])

    def step(state, xs):
        qd, kd, u_i, w_i, intra_i, gl = xs
        v_new = u_i - jnp.einsum('bhce,bhef->bhcf', w_i, state)
        o = jnp.einsum('bhce,bhef->bhcf', qd, state) + jnp.einsum('bhij,bhjf->bhif', intra_i, v_new)
        state = state * gl[..., None, None] + jnp.einsum('bhce,bhcf->bhef', kd, v_new)
        return state, o

    xs = tuple(jnp.moveaxis(t, 1, 0) for t in (q_dec, k_dec, u, w, intra, g_last))
    state0 = jnp.zeros((B, H, Dk, Dv), jnp.float32)
    _, o = lax.scan(step, state0, xs)
    return o.transpose(1, 0, 3, 2, 4).reshape(B, S, H, Dv)

def hybrid_mixer(h, w_in, conv_w, A_log, dt_bias, dn_norm_w, w_out):
    B, S, _ = h.shape
    proj = h @ w_in
    aq, ak, av, dqkv, dz, db, da = jnp.split(proj, IN_SPLITS, axis=-1)
    shp_a = (B, S, ATTN_HEADS, ATTN_HD)
    attn_out = dilated_attention(aq.reshape(shp_a), ak.reshape(shp_a), av.reshape(shp_a))
    attn_out = attn_out.reshape(B, S, ATTN_WIDTH).astype(h.dtype)
    dqkv = jax.nn.silu(causal_short_conv(dqkv, conv_w)).astype(jnp.float32)
    dq, dk, dv = jnp.split(dqkv, (DN_QK_WIDTH, 2 * DN_QK_WIDTH), axis=-1)
    g = -jnp.exp(A_log.astype(jnp.float32)) * jax.nn.softplus(da.astype(jnp.float32) + dt_bias.astype(jnp.float32))
    beta = jax.nn.sigmoid(db.astype(jnp.float32))
    o = gated_delta_rule(dq.reshape(B, S, DN_HEADS, DN_KD), dk.reshape(B, S, DN_HEADS, DN_KD),
                         dv.reshape(B, S, DN_HEADS, DN_VD), g, beta)
    o = rms_norm(o, dn_norm_w) * jax.nn.silu(dz.astype(jnp.float32).reshape(B, S, DN_HEADS, DN_VD))
    dn_out = o.reshape(B, S, DN_V_WIDTH).astype(h.dtype)
    return jnp.concatenate([attn_out, dn_out], axis=-1) @ w_out

def clamped_swiglu(hgu):
    gate, up = jnp.split(hgu, 2, axis=-1)
    gate = jnp.minimum(gate, SWIGLU_LIMIT)
    up = jnp.clip(up, -SWIGLU_LIMIT, SWIGLU_LIMIT)
    return gate * jax.nn.sigmoid(SWIGLU_ALPHA * gate) * (up + 1)

def routed_moe(h, w_router, b_router, w1, b1, w2, b2):
    B, S, D = h.shape
    T = B * S
    xt = h.reshape(T, D)
    logits = (xt @ w_router + b_router).astype(jnp.float32)
    top_v, top_e = lax.top_k(logits, TOP_K)
    gates = jax.nn.softmax(top_v, axis=-1)
    A = T * TOP_K
    e_flat = top_e.reshape(A)
    tok_flat = jnp.repeat(jnp.arange(T, dtype=jnp.int32), TOP_K)
    g_flat = gates.reshape(A)
    order = jnp.argsort(e_flat)
    se, stok, sg = e_flat[order], tok_flat[order], g_flat[order]
    counts = jnp.zeros((N_EXPERTS,), jnp.int32).at[e_flat].add(1)
    padded = (counts + MOE_BLOCK - 1) // MOE_BLOCK * MOE_BLOCK
    pend = jnp.cumsum(padded)
    pstart = pend - padded
    cstart = jnp.cumsum(counts) - counts
    dest = pstart[se] + (jnp.arange(A, dtype=jnp.int32) - cstart[se])
    P = A + N_EXPERTS * MOE_BLOCK
    NB = P // MOE_BLOCK
    row_tok = jnp.zeros((P,), jnp.int32).at[dest].set(stok)
    row_gate = jnp.zeros((P,), jnp.float32).at[dest].set(sg)
    block_exp = jnp.minimum(jnp.searchsorted(pend, jnp.arange(NB) * MOE_BLOCK, side='right'),
                            N_EXPERTS - 1).astype(jnp.int32)
    xs = xt[row_tok].reshape(NB, MOE_BLOCK, D)

    def expert_block(args):
        xb, e = args
        return clamped_swiglu(xb @ w1[e] + b1[e]) @ w2[e] + b2[e]

    yb = lax.map(expert_block, (xs, block_exp)).reshape(P, D)
    y = jnp.zeros((T, D), h.dtype).at[row_tok].add(yb * row_gate[:, None].astype(yb.dtype))
    return y.reshape(B, S, D)

def second_inputs(seed: int = 0) -> dict:
    key = jax.random.key(seed)
    ks = jax.random.split(key, 20)
    D, L, E, F = D_MODEL, DEPTH_2, N_EXPERTS, D_EXPERT
    nrm = jax.random.normal
    return {
        'x': nrm(ks[0], (BATCH, SEQ, D), jnp.float32),
        'c': nrm(ks[1], (BATCH, D), jnp.float32),
        'w_ada': nrm(ks[2], (L, D, 6 * D), jnp.float32) * (0.5 * D ** -0.5),
        'b_ada': nrm(ks[3], (L, 6 * D), jnp.float32) * 0.02,
        'norm1_w': 1.0 + 0.05 * nrm(ks[4], (L, D), jnp.float32),
        'w_in': nrm(ks[5], (L, D, IN_COLS), jnp.float32) * (D ** -0.5),
        'conv_w': nrm(ks[6], (L, CONV_K, DN_CONV_DIM), jnp.float32) * 0.5,
        'A_log': jnp.log(jax.random.uniform(ks[7], (L, DN_HEADS), jnp.float32, 1.0, 16.0)),
        'dt_bias': jax.random.uniform(ks[8], (L, DN_HEADS), jnp.float32, -4.5, -2.5),
        'dn_norm_w': 1.0 + 0.05 * nrm(ks[9], (L, DN_VD), jnp.float32),
        'w_out': nrm(ks[10], (L, D_MIX, D), jnp.float32) * (D_MIX ** -0.5),
        'norm2_w': 1.0 + 0.05 * nrm(ks[11], (L, D), jnp.float32),
        'w_router': nrm(ks[12], (L, D, E), jnp.float32) * (D ** -0.5),
        'b_router': nrm(ks[13], (L, E), jnp.float32) * 0.01,
        'w1': nrm(ks[14], (L, E, D, 2 * F), jnp.float32) * (D ** -0.5),
        'b1': nrm(ks[15], (L, E, 2 * F), jnp.float32) * 0.01,
        'w2': nrm(ks[16], (L, E, F, D), jnp.float32) * (F ** -0.5),
        'b2': nrm(ks[17], (L, E, D), jnp.float32) * 0.01,
        'final_norm_w': 1.0 + 0.05 * nrm(ks[18], (D,), jnp.float32),
    }

def second_block(x, c, w_ada, b_ada, norm1_w, w_in, conv_w, A_log, dt_bias, dn_norm_w, w_out,
              norm2_w, w_router, b_router, w1, b1, w2, b2, final_norm_w):
    cond = jax.nn.silu(c)
    for l in range(DEPTH_2):
        mod = cond @ w_ada[l] + b_ada[l]
        shift1, scale1, gate1, shift2, scale2, gate2 = jnp.split(mod, 6, axis=-1)
        h = modulate(x, norm1_w[l], shift1, scale1)
        x = x + gate1[:, None, :] * hybrid_mixer(h, w_in[l], conv_w[l], A_log[l], dt_bias[l],
                                                 dn_norm_w[l], w_out[l])
        h = modulate(x, norm2_w[l], shift2, scale2)
        x = x + gate2[:, None, :] * routed_moe(h, w_router[l], b_router[l], w1[l], b1[l], w2[l], b2[l])
    return rms_norm(x, final_norm_w)


def setup_inputs(seed=0):
    out = dict(first_inputs(seed))
    for name, value in second_inputs(seed + 1).items():
        if name != "x":
            out[name + "_2"] = value
    return out


def reference(
    x, c, ctx, c_ctx, l0_w_ada, l0_b_ada, l0_g_pre, l0_g_post, l0_w_in, l0_sink, l0_w_out,
    l1_w_ada, l1_b_ada, l1_g_pre, l1_g_post, l1_w_in, l1_g_qa, l1_g_kva, l1_w_uq, l1_w_ukv,
    l1_w_out, l2_w_ada, l2_b_ada, l2_g_pre, l2_g_post, l2_w_in, l2_conv, l2_b_gate, l2_g_head,
    l2_w_out, l3_w_ada, l3_b_ada, l3_g_pre, l3_g_post, l3_w_in, l3_sink, l3_w_out, c_2, w_ada_2,
    b_ada_2, norm1_w_2, w_in_2, conv_w_2, A_log_2, dt_bias_2, dn_norm_w_2, w_out_2, norm2_w_2,
    w_router_2, b_router_2, w1_2, b1_2, w2_2, b2_2, final_norm_w_2,
):
    x = first_block(
        x, c, ctx, c_ctx, l0_w_ada, l0_b_ada, l0_g_pre, l0_g_post, l0_w_in, l0_sink, l0_w_out,
        l1_w_ada, l1_b_ada, l1_g_pre, l1_g_post, l1_w_in, l1_g_qa, l1_g_kva, l1_w_uq, l1_w_ukv,
        l1_w_out, l2_w_ada, l2_b_ada, l2_g_pre, l2_g_post, l2_w_in, l2_conv, l2_b_gate,
        l2_g_head, l2_w_out, l3_w_ada, l3_b_ada, l3_g_pre, l3_g_post, l3_w_in, l3_sink,
        l3_w_out,
    )
    return second_block(
        x, c_2, w_ada_2, b_ada_2, norm1_w_2, w_in_2, conv_w_2, A_log_2, dt_bias_2, dn_norm_w_2,
        w_out_2, norm2_w_2, w_router_2, b_router_2, w1_2, b1_2, w2_2, b2_2, final_norm_w_2,
    )


_drawn_inputs = setup_inputs


def setup_inputs(seed=0):
    import zlib

    import numpy as np

    out = dict(_drawn_inputs(seed))
    spreads = {}
    factors = {'l0_sink': 8.0,
     'l1_g_qa': 3.266,
     'l3_sink': 8.0,
     'norm1_w_2': 4.444,
     'dt_bias_2': 4.01,
     'dn_norm_w_2': 7.798,
     'b_router_2': 64.0,
     'b1_2': 64.0,
     'b2_2': 64.0,
     'norm2_w_2': 8.0}
    for name, (base, spread) in spreads.items():
        noise = np.random.default_rng([zlib.crc32(name.encode()), seed]).standard_normal(out[name].shape)
        drawn = base * np.exp(spread * noise) if base else spread * noise
        out[name] = jnp.asarray(drawn.astype(out[name].dtype))
    for name, factor in factors.items():
        out[name] = (out[name] * factor).astype(out[name].dtype)
    return out
```

```python
from contextlib import ExitStack

import concourse.bass as bass
from concourse import mybir

F32 = mybir.dt.float32
I32 = mybir.dt.int32
U32 = mybir.dt.uint32
ALU = mybir.AluOpType
ACT = mybir.ActivationFunctionType
AX = mybir.AxisListType.X

P = 128
D = 1024
KT = D // P
LAT = 256
CTX = 256
TOK = LAT + CTX
TT = TOK // P
CH = 512
SLOTS = 3
EPS = 1e-6
NEG = -1e30


class Signal:

    def __init__(self, sem):
        self.sem, self.base = sem, 0

    def at(self, n):
        return self.base + n

    def passed(self, n):
        self.base += n


class Chain:

    def __init__(self, sem):
        self.sem, self.n = sem, 0

    def add(self, ins):
        self.n += 1
        return ins.then_inc(self.sem, 1)

    def link(self, eng, ins):
        self.add(ins)
        eng.wait_ge(self.sem, self.n)


class WeightStream:

    def __init__(self, slots, landed, used):
        self.slots, self.landed, self.used = slots, landed, used
        self.chunks, self.first, self.issued = [], {}, 0

    def add(self, name, w, cuts=None):
        self.first[name] = len(self.chunks)
        rows, cols = w.shape
        kt = rows // P
        cuts = cuts or [*range(0, cols, CH * KT // kt), cols]
        for a, b in zip(cuts, cuts[1:]):
            self.chunks.append((w[:, a:b].rearrange("(k p) n -> p k n", p=P), kt))

    def view(self, n):
        src, kt = self.chunks[n]
        cols = src.shape[2]
        return self.slots[:, n % SLOTS, 0:kt * cols].rearrange("p (k n) -> p k n", k=kt)

    def load_until(self, sp, end):
        while self.issued < min(len(self.chunks), end + SLOTS):
            n = self.issued
            if n >= SLOTS:
                sp.wait_ge(self.used.sem, n - SLOTS + 1)
            sp.dma_start(self.view(n), self.chunks[n][0]).then_inc(self.landed[n % SLOTS].sem, 16)
            self.issued += 1

    def wait(self, pe, n):
        pe.wait_ge(self.landed[n % SLOTS].sem, 16 * (n // SLOTS + 1))


def constant_tables():
    import numpy as np
    p = np.arange(P)
    t = np.arange(LAT)
    tabs = {}
    tabs["ident"] = np.eye(P)
    tabs["ones"] = np.ones((P, P))
    swap = np.zeros((P, P))
    swap[p[1::2], p[0::2]] = -1.0
    swap[p[0::2], p[1::2]] = 1.0
    tabs["swap"] = swap
    inv = np.float32(10000.0) ** (-np.arange(16, dtype=np.float32) / np.float32(16))
    ang = np.concatenate([(t // 64).astype(np.float32)[:, None] * inv, (t % 64).astype(np.float32)[:, None] * inv], -1)
    tabs["cos"] = np.cos(ang).T[(p % 64) // 2]
    tabs["sin"] = np.sin(ang).T[(p % 64) // 2]
    q = np.arange(LAT).reshape(2, P)
    dist = (q[:, :, None] - t[None, None, :]).transpose(1, 0, 2)
    tabs["window"] = np.where(np.abs(dist) <= 128, 0.0, NEG).reshape(P, -1)
    n = ((dist >= 0) & (dist <= 128)).astype(int)
    for w, d in ((512, 4), (2048, 16)):
        n = n + ((dist >= 0) & (dist <= w) & (dist % d == 0))
    tabs["dilated"] = np.where(n > 0, 8.0 * np.log(np.maximum(n, 1)), NEG).reshape(P, -1)
    r, c = p[:, None], p[None, :]
    tabs["upto"] = r <= c
    tabs["from"] = r >= c
    tabs["before"] = r < c
    tabs["causal"] = np.where(c <= r, 0.0, NEG)
    tabs["anticausal"] = np.where(c >= r, 0.0, NEG)
    tabs["strict"] = c < r
    for b in (1, 2, 4, 8, 16, 32, 64):
        low = ((r // b) % 2 == 1) & (c // b == r // b - 1)
        tabs[f"low{b}T"] = low.T
        if b == 1:
            tabs["low1"] = low
    tabs["slot_row"] = np.broadcast_to(np.arange(64), (P, 64))
    tabs["slot_col"] = (p % 64)[:, None]
    tabs["expert_row"] = np.broadcast_to(np.arange(32), (P, 32))
    tabs["block_row"] = np.broadcast_to(np.arange(48), (P, 48))
    at, n = {}, 0
    for k, v in tabs.items():
        at[k] = (n, n + v.shape[1])
        n += v.shape[1]
    return np.concatenate([np.asarray(v, np.float32) for v in tabs.values()], 1), at


VECTOR_ROWS = [
    [("l0_b_ada", 24), ("l1_b_ada", 24), ("l2_b_ada", 24), ("l3_b_ada", 24), ("c", 8), ("c_ctx", 8), ("c_2", 8),
     ("l0_g_pre", 8)],
    [("b_ada_2", 48), ("l1_g_pre", 8), ("l2_g_pre", 8), ("l3_g_pre", 8), ("l0_g_post", 8), ("l1_g_post", 8),
     ("l2_g_post", 8), ("l3_g_post", 8), ("norm1_w_2", 8), ("norm2_w_2", 8)],
    [("l2_conv", 40), ("conv_w_2", 48), ("final_norm_w_2", 8), ("l2_g_head", 8), ("l1_g_qa", 2), ("l1_g_kva", 1),
     ("dn_norm_w_2", 1)],
]
BROADCAST = [("l0_sink", 16), ("l3_sink", 16), ("l2_b_gate", 16), ("A_log_2", 4), ("dt_bias_2", 4), ("b_router_2", 32)]


def layers_and_experts_kernel(nc, t, consts_at, out):
    ctx = ExitStack()
    with ctx:
        def sb(name, shape, dt=F32):
            return ctx.enter_context(nc.sbuf_tensor(name, shape, dt))

        def sem(name):
            return Signal(ctx.enter_context(nc.semaphore(name)))

        XT = sb("XT", [P, KT, TOK])
        HT = sb("HT", [P, KT, TOK])
        RING_N = SLOTS * KT * CH
        ARENA_N = 22656
        BIG = sb("BIG", [P, RING_N + ARENA_N])
        PW = sb("PW", [P, 4096])
        n_const = consts_at["block_row"][1]
        CONST = sb("CONST", [P, n_const])
        ROWS = sb("ROWS", [P, 3, P])
        COLS = sb("COLS", [P, 3, P])
        BC = sb("BC", [P, sum(n for _, n in BROADCAST)])
        COND = sb("COND", [P, KT, 2])
        COND2 = sb("COND2", [P, KT])
        MOD = sb("MOD", [P, 48, 2])
        GAIN = sb("GAIN", [P, KT, 2])
        GATE = sb("GATE", [P, KT, 2])
        RSTD, RINV = PW[:, 0:TOK], PW[:, TOK:2 * TOK]
        SM = sb("SM", [P, 720])
        ST = sb("ST", [P, 64])

        ring = BIG[:, 0:RING_N].rearrange("p (s n) -> p s n", s=SLOTS)

        class Arena:

            def __init__(self, at=0):
                self.at = at

            def take(self, *shape):
                n = 1
                for s in shape:
                    n *= s
                v = BIG[:, RING_N + self.at:RING_N + self.at + n]
                self.at += n
                assert self.at <= ARENA_N, self.at
                names = "abcd"[:len(shape)]
                return v.rearrange(f"p ({' '.join(names)}) -> p {' '.join(names)}",
                                   **dict(zip(names, shape))) if len(shape) > 1 else v

        PS = ctx.enter_context(nc.psum_tensor("PS", [P, 8, 512], F32))

        def const(name):
            a, b = consts_at[name]
            return CONST[:, a:b]

        ident, ones = const("ident"), const("ones")
        window = const("window").rearrange("p (t k) -> p t k", t=2)
        dilated = const("dilated").rearrange("p (t k) -> p t k", t=2)

        col_at = {}
        for r, rows in enumerate(VECTOR_ROWS):
            n = 0
            for name, k in rows:
                col_at[name] = (r, n, n + k)
                n += k

        def col(name):
            r, a, b = col_at[name]
            return COLS[:, r, a:b]

        bc_at, n = {}, 0
        for name, k in BROADCAST:
            bc_at[name] = (n, n + k)
            n += k

        def bcast(name):
            return BC[:, bc_at[name][0]:bc_at[name][1]]

        landed = [sem(f"chunk_landed{i}") for i in range(SLOTS)]
        chunk_used = sem("chunk_used")
        ws = WeightStream(ring, landed, chunk_used)
        for i in range(4):
            ws.add(f"l{i}_w_ada", t[f"l{i}_w_ada"])
            ws.add(f"l{i}_w_in", t[f"l{i}_w_in"], [0, 448, 960, 1472] if i == 1 else None)
            if i == 1:
                ws.add("l1_w_uq", t["l1_w_uq"])
                ws.add("l1_w_ukv", t["l1_w_ukv"])
            ws.add(f"l{i}_w_out", t[f"l{i}_w_out"])
        ws.add("w_ada_2", t["w_ada_2"])
        ws.add("w_in_2", t["w_in_2"])
        ws.add("w_out_2", t["w_out_2"])
        ws.first["end"] = len(ws.chunks)

        dve_chain = Chain(ctx.enter_context(nc.semaphore("dve_chain")))
        act_chain = Chain(ctx.enter_context(nc.semaphore("act_chain")))
        pool_chain = Chain(ctx.enter_context(nc.semaphore("pool_chain")))
        names = ("vectors_loaded tokens_loaded consts_loaded transposed transposed_taken cond_ready squares_ready "
                 "square_sum_ready inverse_ready rstd_ready scaled_ready tile_ready tile_taken rope_mixed rope_taken "
                 "scores_ready max_ready exp_ready scores_used probs_ready probs_turned turned_copied heads_ready "
                 "heads_taken stored a_ready b_ready c_ready d_ready e_ready f_ready g_ready h_ready i_ready j_ready").split()
        S = {n: sem(n) for n in names}

        def at(name, n):
            return S[name].sem, S[name].at(n)

        tok0 = Arena().take(TT, D)
        with nc.Block() as block:
            n_vec = sum(len(r) for r in VECTOR_ROWS) + len(BROADCAST)

            @block.sync
            def _(sp):
                sp.dma_start(CONST[:], t["consts"]).then_inc(S["consts_loaded"].sem, 16)
                sp.dma_start(tok0[:, 0:2, :], t["x"].rearrange("o (a p) d -> p (o a) d", p=P)).then_inc(S["tokens_loaded"].sem, 16)
                sp.dma_start(tok0[:, 2:4, :], t["ctx"].rearrange("o (a p) d -> p (o a) d", p=P)).then_inc(S["tokens_loaded"].sem, 16)
                ws.load_until(sp, 0)

            @block.gpsimd
            def _(pool):
                for r, rows in enumerate(VECTOR_ROWS):
                    for name, k in rows:
                        _, a, b = col_at[name]
                        pool.dma_start(ROWS[a:b, r, :], t[name]).then_inc(S["vectors_loaded"].sem, 16)
                for name, k in BROADCAST:
                    pool.dma_start(bcast(name), t[name].partition_broadcast(P)).then_inc(S["vectors_loaded"].sem, 16)

            @block.tensor
            def _(pe):
                pe.wait_ge(*at("consts_loaded", 16))
                pe.wait_ge(*at("tokens_loaded", 32))
                for k in range(KT):
                    for a in range(TT):
                        ins = nc.tensor.transpose(PS[:, k, a * P:(a + 1) * P], tok0[:, a, k * P:(k + 1) * P], ident)
                    ins.then_inc(S["transposed"].sem, 1)
                pe.wait_ge(*at("vectors_loaded", 16 * n_vec))
                pe.wait_ge(*at("transposed_taken", 1))
                for r, rows in enumerate(VECTOR_ROWS):
                    n = sum(k for _, k in rows)
                    ins = nc.tensor.transpose(PS[:, 0, r * P:r * P + n], ROWS[0:n, r, :], ident[0:n, 0:n])
                ins.then_inc(S["transposed"].sem, 1)

            @block.scalar
            def _(act):
                for k in range(KT):
                    act.wait_ge(*at("transposed", k + 1))
                    ins = nc.scalar.copy(XT[:, k, :], PS[:, k, :]).then_inc(S["transposed_taken"].sem, 1)
                act.wait_ge(*at("transposed", KT + 1))
                for r, rows in enumerate(VECTOR_ROWS):
                    n = sum(k for _, k in rows)
                    act_chain.add(nc.scalar.copy(COLS[:, r, 0:n], PS[:, 0, r * P:r * P + n]))
                act.wait_ge(act_chain.sem, act_chain.n)
                nc.scalar.activation(COND[:, :, 0], col("c"), ACT.Silu)
                nc.scalar.activation(COND[:, :, 1], col("c_ctx"), ACT.Silu)
                nc.scalar.activation(COND2[:], col("c_2"), ACT.Silu)

        S["consts_loaded"].passed(16)
        S["tokens_loaded"].passed(32)
        S["vectors_loaded"].passed(16 * n_vec)
        S["transposed"].passed(KT + 1)
        S["transposed_taken"].passed(KT)

        def tile_signals(ends):
            said, n = [], 0
            for chunk in ends:
                n += chunk is None
                said.append(at("tile_ready", n) if chunk is None else (chunk_used.sem, chunk + 1))
            return said, n

        def norm_modulate(w_ada, b_ada, g_pre, g_post, cond, parts, tok):
            first, end = ws.first[w_ada], ws.first[w_ada] + parts * D // CH
            n_tiles = parts * KT
            n_str = tok // LAT
            sq = Arena().take(KT, TOK)
            with nc.Block() as block:

                @block.sync
                def _(sp):
                    ws.load_until(sp, end)

                @block.tensor
                def _(pe):
                    mod = PS[:, 0, 0:n_tiles * n_str].rearrange("p (t s) -> p t s", s=n_str)
                    for c in range(first, end):
                        ws.wait(pe, c)
                        w = ws.view(c)
                        for m in range(CH // P):
                            for k in range(KT):
                                ins = nc.tensor.matmul(mod[:, (c - first) * (CH // P) + m, :], w[:, k, m * P:(m + 1) * P],
                                                       cond[:, k, :], start=(k == 0), stop=(k == KT - 1))
                        ins.then_inc(chunk_used.sem, 1)
                    for k in range(KT):
                        pe.wait_ge(*at("squares_ready", k + 1))
                        ins = nc.tensor.matmul(PS[:, 1, 0:tok], ones, sq[:, k, 0:tok], start=(k == 0), stop=(k == KT - 1))
                    ins.then_inc(S["square_sum_ready"].sem, 1)

                @block.scalar
                def _(act):
                    for k in range(KT):
                        nc.scalar.activation(sq[:, k, 0:tok], XT[:, k, 0:tok], ACT.Square).then_inc(S["squares_ready"].sem, 1)
                    act.wait_ge(*at("inverse_ready", 1))
                    nc.scalar.activation(RSTD[:, 0:tok], RINV[:, 0:tok], ACT.Sqrt).then_inc(S["rstd_ready"].sem, 1)
                    for k in range(KT):
                        act.wait_ge(*at("scaled_ready", k + 1))
                        for s in range(n_str):
                            sl = HT[:, k, s * LAT:(s + 1) * LAT]
                            nc.scalar.activation(sl, sl, ACT.Identity, bias=MOD[:, k, s:s + 1], scale=GAIN[:, k, s:s + 1])

                @block.vector
                def _(dve):
                    dve.wait_ge(chunk_used.sem, end)
                    mod = PS[:, 0, 0:n_tiles * n_str].rearrange("p (t s) -> p t s", s=n_str)
                    dve_chain.link(dve, nc.vector.tensor_tensor(MOD[:, 0:n_tiles, 0:n_str], mod, col(b_ada).unsqueeze(2).to_broadcast(
                        [P, n_tiles, n_str]), ALU.add))
                    dve_chain.add(nc.vector.scalar_tensor_tensor(
                        GAIN[:, :, 0:n_str], MOD[:, KT:2 * KT, 0:n_str], 1.0,
                        col(g_pre).unsqueeze(2).to_broadcast([P, KT, n_str]), ALU.add, ALU.mult))
                    if g_post:
                        dve_chain.add(nc.vector.tensor_tensor(
                            GATE[:, :, 0:n_str], MOD[:, 2 * KT:3 * KT, 0:n_str],
                            col(g_post).unsqueeze(2).to_broadcast([P, KT, n_str]), ALU.mult))
                    dve.wait_ge(*at("square_sum_ready", 1))
                    dve_chain.link(dve, nc.vector.tensor_scalar(RINV[:, 0:tok], PS[:, 1, 0:tok], 1.0 / D, EPS, ALU.mult, ALU.add))
                    nc.vector.reciprocal(RINV[:, 0:tok], RINV[:, 0:tok]).then_inc(S["inverse_ready"].sem, 1)
                    dve.wait_ge(*at("rstd_ready", 1))
                    for k in range(KT):
                        nc.vector.tensor_tensor(HT[:, k, 0:tok], XT[:, k, 0:tok], RSTD[:, 0:tok], ALU.mult).then_inc(
                            S["scaled_ready"].sem, 1)

            S["squares_ready"].passed(KT)
            for n in ("square_sum_ready", "inverse_ready", "rstd_ready"):
                S[n].passed(1)
            S["scaled_ready"].passed(KT)

        def project_out(w_out, ot, tok):
            first = ws.first[w_out]
            a = Arena()
            yt, sq = a.take(KT, TOK), a.take(KT, TOK)
            n_str = tok // LAT
            done, n_plain = tile_signals([None, None, None, first, None, None, None, first + 1])
            with nc.Block() as block:

                @block.sync
                def _(sp):
                    ws.load_until(sp, first + 2)

                @block.tensor
                def _(pe):
                    for m in range(KT):
                        if m % 4 == 0:
                            ws.wait(pe, first + m // 4)
                        w = ws.view(first + m // 4)
                        if m >= 4:
                            pe.wait_ge(*at("tile_taken", m - 3))
                        for k in range(KT):
                            ins = nc.tensor.matmul(PS[:, m % 4, 0:tok], w[:, k, (m % 4) * P:(m % 4 + 1) * P], ot[:, k, 0:tok],
                                                   start=(k == 0), stop=(k == KT - 1))
                        ins.then_inc(done[m][0], 1)
                    for k in range(KT):
                        pe.wait_ge(*at("tile_taken", k + 1))
                        ins = nc.tensor.matmul(PS[:, 4, 0:tok], ones, sq[:, k, 0:tok], start=(k == 0), stop=(k == KT - 1))
                    ins.then_inc(S["square_sum_ready"].sem, 1)

                @block.scalar
                def _(act):
                    for m in range(KT):
                        act.wait_ge(*done[m])
                        nc.scalar.copy(yt[:, m, 0:tok], PS[:, m % 4, 0:tok]).then_inc(S["a_ready"].sem, 1)
                        nc.scalar.activation(sq[:, m, 0:tok], PS[:, m % 4, 0:tok], ACT.Square).then_inc(S["tile_taken"].sem, 1)
                    act.wait_ge(*at("inverse_ready", 1))
                    nc.scalar.activation(RSTD[:, 0:tok], RINV[:, 0:tok], ACT.Sqrt).then_inc(S["rstd_ready"].sem, 1)

                @block.vector
                def _(dve):
                    dve.wait_ge(*at("square_sum_ready", 1))
                    dve_chain.link(dve, nc.vector.tensor_scalar(RINV[:, 0:tok], PS[:, 4, 0:tok], 1.0 / D, EPS, ALU.mult, ALU.add))
                    nc.vector.reciprocal(RINV[:, 0:tok], RINV[:, 0:tok]).then_inc(S["inverse_ready"].sem, 1)
                    dve.wait_ge(*at("rstd_ready", 1))
                    dve.wait_ge(*at("a_ready", KT))
                    for k in range(KT):
                        dve_chain.link(dve, nc.vector.tensor_tensor(yt[:, k, 0:tok], yt[:, k, 0:tok], RSTD[:, 0:tok], ALU.mult))
                        for s in range(n_str):
                            sl = slice(s * LAT, (s + 1) * LAT)
                            dve_chain.add(nc.vector.scalar_tensor_tensor(
                                XT[:, k, sl], yt[:, k, sl], GATE[:, k, s:s + 1], XT[:, k, sl], ALU.mult, ALU.add))

            S["tile_ready"].passed(n_plain)
            S["tile_taken"].passed(KT)
            S["a_ready"].passed(KT)
            for n in ("square_sum_ready", "inverse_ready", "rstd_ready"):
                S[n].passed(1)

        def rope_mix(x, n):
            nc.tensor.matmul(PS[:, 4 + n % 2, 0:LAT], const("swap"), x[:, 0:LAT], start=True, stop=True).then_inc(
                S["rope_mixed"].sem, 1)

        def rope_turn(dve, x, n, tmp):
            dve.wait_ge(*at("rope_mixed", n + 1))
            nc.vector.tensor_tensor(tmp, PS[:, 4 + n % 2, 0:LAT], const("sin"), ALU.mult).then_inc(S["rope_taken"].sem, 1)
            dve_chain.link(dve, nc.vector.tensor_tensor(x[:, 0:LAT], x[:, 0:LAT], const("cos"), ALU.mult))
            dve.wait_ge(*at("rope_taken", n + 1))
            dve_chain.link(dve, nc.vector.tensor_tensor(x[:, 0:LAT], x[:, 0:LAT], tmp, ALU.add))

        def attention(units, scale, score, value, mask_of, sink, gate, together=True):
            probs = PW[:, 0:2048].rearrange("p (b h k) -> p b h k", b=2, h=2)
            turned = PW[:, 2048:4096].rearrange("p (b h k) -> p b h k", b=2, h=2)
            mx = ST[:, 0:8].rearrange("p (b s) -> p b s", b=2)
            nm = ST[:, 8:16].rearrange("p (b s) -> p b s", b=2)
            den = ST[:, 16:24].rearrange("p (b s) -> p b s", b=2)
            es = ST[:, 24:32].rearrange("p (b s) -> p b s", b=2)
            rd = ST[:, 32:40].rearrange("p (b s) -> p b s", b=2)
            N = len(units)

            def cols(u):
                return u[2][0] * P, (u[2][-1] + 1) * P

            with nc.Block() as block:

                @block.sync
                def _(sp):
                    ws.load_until(sp, ws.done)

                @block.tensor
                def _(pe):
                    def scores(i):
                        a, b = cols(units[i])
                        if i >= 2:
                            pe.wait_ge(*at("scores_used", 2 * (i - 1)))
                        for h in range(2):
                            ins = score(h, units[i], slice(a, b), PS[:, 2 * (i % 2) + h, a:b])
                        ins.then_inc(S["scores_ready"].sem, 1)

                    def turn(i):
                        for h in range(2):
                            pe.wait_ge(*at("probs_ready", 2 * i + h + 1))
                            if i >= 1:
                                pe.wait_ge(*at("turned_copied", 2 * i + h - 1))
                            for j, kt in enumerate(units[i][2]):
                                ins = nc.tensor.transpose(PS[:, 4 + h, j * P:(j + 1) * P],
                                                          probs[:, i % 2, h, kt * P:(kt + 1) * P], ident)
                            ins.then_inc(S["probs_turned"].sem, 1)

                    def mix(i):
                        pe.wait_ge(*at("turned_copied", 2 * i + 2))
                        if i >= 2:
                            pe.wait_ge(*at("heads_taken", i - 1))
                        kts = units[i][2]
                        order = [(j, h) for j in range(len(kts)) for h in range(2)]
                        if not together:
                            order.sort(key=lambda x: x[1])
                        for j, h in order:
                            lhs, place = value(units[i], h, kts[j])
                            ins = nc.tensor.matmul(place(PS[:, 6 + i % 2, :]), lhs, turned[:, i % 2, h, j * P:(j + 1) * P],
                                                   start=(j == 0), stop=(j == len(kts) - 1))
                        ins.then_inc(S["heads_ready"].sem, 1)

                    scores(0)
                    for i in range(N):
                        if i + 1 < N:
                            scores(i + 1)
                        turn(i)
                        if i >= 1:
                            mix(i - 1)
                    mix(N - 1)

                @block.scalar
                def _(act):
                    def exps(i):
                        a, b = cols(units[i])
                        act.wait_ge(*at("max_ready", i + 1))
                        if i >= 2:
                            act.wait_ge(*at("probs_turned", 2 * (i - 1)))
                        for h in range(2):
                            nc.scalar.activation(probs[:, i % 2, h, a:b], PS[:, 2 * (i % 2) + h, a:b], ACT.Exp,
                                                 bias=nm[:, i % 2, h:h + 1], scale=scale,
                                                 accum_out=den[:, i % 2, h:h + 1]).then_inc(S["scores_used"].sem, 1)
                            if sink is not None:
                                head = 2 * units[i][0] + h
                                nc.scalar.activation(es[:, i % 2, h:h + 1], sink[:, head:head + 1], ACT.Exp,
                                                     bias=nm[:, i % 2, h:h + 1]).then_inc(S["exp_ready"].sem, 1)

                    def copies(i):
                        n = len(units[i][2]) * P
                        if i >= 2:
                            act.wait_ge(*at("heads_ready", i - 1))
                        for h in range(2):
                            act.wait_ge(*at("probs_turned", 2 * i + h + 1))
                            nc.scalar.copy(turned[:, i % 2, h, 0:n], PS[:, 4 + h, 0:n]).then_inc(S["turned_copied"].sem, 1)

                    exps(0)
                    for i in range(N):
                        if i + 1 < N:
                            exps(i + 1)
                        copies(i)

                @block.vector
                def _(dve):
                    def maxima(i):
                        a, b = cols(units[i])
                        s = PS[:, 2 * (i % 2):2 * (i % 2) + 2, :]
                        dve.wait_ge(*at("scores_ready", i + 1))
                        mask = mask_of(units[i])
                        if mask is not None:
                            w = mask.shape[1]
                            dve_chain.link(dve, nc.vector.tensor_tensor(s[:, :, a:a + w], s[:, :, a:a + w],
                                                                        mask.unsqueeze(1).to_broadcast([P, 2, w]), ALU.add))
                        dve_chain.link(dve, nc.vector.tensor_reduce(mx[:, i % 2, 0:2], s[:, :, a:b], AX, ALU.max))
                        if sink is not None:
                            h = 2 * units[i][0]
                            dve_chain.link(dve, nc.vector.scalar_tensor_tensor(
                                mx[:, i % 2, 2:4], mx[:, i % 2, 0:2], scale, sink[:, h:h + 2], ALU.mult, ALU.max))
                            nc.vector.tensor_scalar(nm[:, i % 2, 0:2], mx[:, i % 2, 2:4], -1.0, None, ALU.mult).then_inc(
                                S["max_ready"].sem, 1)
                        else:
                            nc.vector.tensor_scalar(nm[:, i % 2, 0:2], mx[:, i % 2, 0:2], -scale, None, ALU.mult).then_inc(
                                S["max_ready"].sem, 1)

                    def normalise(i):
                        a, b = cols(units[i])
                        dve.wait_ge(*at("scores_used", 2 * i + 2))
                        if sink is not None:
                            dve.wait_ge(*at("exp_ready", 2 * i + 2))
                            dve_chain.link(dve, nc.vector.tensor_tensor(den[:, i % 2, 0:2], den[:, i % 2, 0:2], es[:, i % 2, 0:2],
                                                                        ALU.add))
                        dve_chain.link(dve, nc.vector.reciprocal(rd[:, i % 2, 0:2], den[:, i % 2, 0:2]))
                        for h in range(2):
                            pr = probs[:, i % 2, h, a:b]
                            nc.vector.tensor_scalar(pr, pr, rd[:, i % 2, h:h + 1], None, ALU.mult).then_inc(
                                S["probs_ready"].sem, 1)

                    def gates(i):
                        dve.wait_ge(*at("heads_ready", i + 1))
                        o, z, src = gate(units[i], PS[:, 6 + i % 2, :])
                        if z is None:
                            nc.vector.tensor_copy(o, src).then_inc(S["heads_taken"].sem, 1)
                        else:
                            nc.vector.tensor_tensor(o, src, z, ALU.mult).then_inc(S["heads_taken"].sem, 1)

                    maxima(0)
                    for i in range(N):
                        if i + 1 < N:
                            maxima(i + 1)
                        normalise(i)
                        if i >= 1:
                            gates(i - 1)
                    gates(N - 1)

            for n, k in (("scores_ready", 1), ("max_ready", 1), ("scores_used", 2), ("exp_ready", 2 if sink is not None else 0),
                         ("probs_ready", 2), ("probs_turned", 2), ("turned_copied", 2), ("heads_ready", 1), ("heads_taken", 1)):
                S[n].passed(k * N)

        def window_layer(i, need_ctx):
            w_in = f"l{i}_w_in"
            first = ws.first[w_in]
            norm_modulate(f"l{i}_w_ada", f"l{i}_b_ada", f"l{i}_g_pre", f"l{i}_g_post", COND, 3, TOK)
            a = Arena()
            qt, kt_, zt = a.take(8, TOK), a.take(2, TOK), a.take(8, TOK)
            keys = a.take(4, TOK)
            v = a.take(TT, 256)
            tmp = a.take(LAT)
            qtok = TOK if need_ctx else LAT
            tiles = [("q", m, m // 4, m % 4 * P, qtok) for m in range(8)]
            tiles += [("k", m, 2, m * P, TOK) for m in range(2)] + [("v", m, 2, 256, 256) for m in range(TT)]
            tiles += [("z", m, 3 + m // 4, m % 4 * P, qtok) for m in range(8)]
            last = [j + 1 == len(tiles) or tiles[j + 1][2] != x[2] for j, x in enumerate(tiles)]
            done, n_plain = tile_signals([first + x[2] if e else None for x, e in zip(tiles, last)])
            roped = [j for j, x in enumerate(tiles) if x[0] in "qk"]
            with nc.Block() as block:

                @block.sync
                def _(sp):
                    ws.load_until(sp, first + 5)

                @block.tensor
                def _(pe):
                    def rope(n):
                        kind, m, _, _, _ = tiles[roped[n]]
                        pe.wait_ge(*at("tile_taken", roped[n] + 1))
                        if n >= 2:
                            pe.wait_ge(*at("rope_taken", n - 1))
                        rope_mix((qt if kind == "q" else kt_)[:, m, :], n)

                    for j, (kind, m, c, x, tok) in enumerate(tiles):
                        if j == 0 or tiles[j - 1][2] != c:
                            ws.wait(pe, first + c)
                        w = ws.view(first + c)
                        if j >= 4:
                            pe.wait_ge(*at("tile_taken", j - 3))
                        for k in range(KT):
                            if kind == "v":
                                ops = HT[:, k, m * P:(m + 1) * P], w[:, k, x:x + tok]
                            else:
                                ops = w[:, k, x:x + P], HT[:, k, 0:tok]
                            ins = nc.tensor.matmul(PS[:, j % 4, 0:tok], *ops, start=(k == 0), stop=(k == KT - 1))
                        ins.then_inc(done[j][0], 1)
                        if 1 <= j <= len(roped):
                            rope(j - 1)

                @block.scalar
                def _(act):
                    for j, (kind, m, c, x, tok) in enumerate(tiles):
                        act.wait_ge(*done[j])
                        dst = {"q": qt, "k": kt_, "v": v, "z": zt}[kind][:, m, 0:tok]
                        nc.scalar.activation(dst, PS[:, j % 4, 0:tok], ACT.Silu if kind == "z" else ACT.Copy).then_inc(
                            S["tile_taken"].sem, 1)

                @block.vector
                def _(dve):
                    for n, j in enumerate(roped):
                        kind, m, _, _, _ = tiles[j]
                        dve.wait_ge(*at("tile_taken", j + 1))
                        rope_turn(dve, (qt if kind == "q" else kt_)[:, m, :], n, tmp)
                    for h in range(4):
                        src = kt_[64 * (h % 2):64 * (h % 2) + 64, h // 2, :]
                        dve_chain.add(nc.vector.tensor_copy(keys[0:64, h, :], src))
                        dve_chain.add(nc.vector.tensor_copy(keys[64:128, h, :], src))

            S["tile_ready"].passed(n_plain)
            S["tile_taken"].passed(len(tiles))
            S["rope_mixed"].passed(len(roped))
            S["rope_taken"].passed(len(roped))
            ws.done = first + 5

            def score(h, u, k, out):
                half = slice(64 * h, 64 * h + 64)
                return nc.tensor.matmul(out, qt[half, u[0], u[1] * P:(u[1] + 1) * P], keys[half, u[0] // 2, k], start=True, stop=True)

            def value(u, h, kt):
                j = u[0] // 2
                return v[:, kt, j * 64:(j + 1) * 64], lambda bank: bank[64 * h:64 * h + 64, 0:P]

            def gate(u, bank):
                q = slice(u[1] * P, (u[1] + 1) * P)
                return HT[:, u[0], q], zt[:, u[0], q], bank[:, 0:P]

            units = [(m, q, [0, 1, 2, 3]) for m in range(8) for q in range(2)]
            if need_ctx:
                units += [(m, q, [2, 3]) for m in range(8) for q in (2, 3)]
            attention(units, 64 ** -0.5, score, value, lambda u: window[:, u[1], :] if u[1] < 2 else None,
                      bcast(f"l{i}_sink"), gate)
            project_out(f"l{i}_w_out", HT, qtok)

        window_layer(0, True)

        def latent_layer():
            heads, nope, rot, rank_q, rank_kv = 8, 128, 64, 256, 128
            norm_modulate("l1_w_ada", "l1_b_ada", "l1_g_pre", "l1_g_post", COND, 3, TOK)
            a = Arena()
            qn, qr, kn = a.take(heads, TOK), a.take(heads // 2, TOK), a.take(heads, TOK)
            kpe, v, zt = a.take(TOK), a.take(TT, heads * P), a.take(8, TOK)
            lowrank, sq, tmp = a.take(3, TOK), a.take(3, TOK), a.take(LAT)
            rstd = [PW[:, 0:TOK], PW[:, TOK:2 * TOK]]
            rinv = [PW[:, 2 * TOK:3 * TOK], PW[:, 3 * TOK:4 * TOK]]
            c_in, c_uq, c_ukv = ws.first["l1_w_in"], ws.first["l1_w_uq"], ws.first["l1_w_ukv"]
            tiles = [("low", m, c_in) for m in range(3)] + [("kpe", 0, c_in)]
            tiles += [("z", m, c_in + 1 + m // 4) for m in range(8)]
            tiles += [("qr", m, c_uq) for m in range(4)] + [("qn", m, c_uq) for m in range(8)]
            tiles += [("kn", m, c_ukv) for m in range(8)] + [("v", m, c_ukv) for m in range(8)]
            last = [j + 1 == len(tiles) or tiles[j + 1][2] != x[2] for j, x in enumerate(tiles)]
            done, n_plain = tile_signals([x[2] if e else None for x, e in zip(tiles, last)])
            roped = [j for j, x in enumerate(tiles) if x[0] in ("kpe", "qr")]
            with nc.Block() as block:

                @block.sync
                def _(sp):
                    ws.load_until(sp, c_ukv + 1)

                @block.tensor
                def _(pe):
                    def rope(n):
                        kind, m, _ = tiles[roped[n]]
                        pe.wait_ge(*at("tile_taken", roped[n] + 1))
                        if n >= 2:
                            pe.wait_ge(*at("rope_taken", n - 1))
                        rope_mix(kpe if kind == "kpe" else qr[:, m, :], n)

                    def square_sums():
                        for n, (x, y) in enumerate(((0, 2), (2, 3))):
                            for m in range(x, y):
                                pe.wait_ge(*at("squares_ready", m + 1))
                                ins = nc.tensor.matmul(PS[:, 6 + n, :], ones, sq[:, m, :], start=(m == x), stop=(m == y - 1))
                            ins.then_inc(S["square_sum_ready"].sem, 1)

                    for j, (kind, m, c) in enumerate(tiles):
                        if j == 0 or tiles[j - 1][2] != c:
                            ws.wait(pe, c)
                        w = ws.view(c)
                        if j >= 4:
                            pe.wait_ge(*at("tile_taken", j - 3))
                        o = PS[:, j % 4, :]
                        if kind in ("low", "z", "kpe"):
                            for k in range(KT):
                                x = 384 if kind == "kpe" else m % 4 * P if kind == "z" else m * P
                                n = rot if kind == "kpe" else P
                                for half in range(P // n):
                                    ins = nc.tensor.matmul(o[n * half:n * half + n, :], w[:, k, x:x + n], HT[:, k, :],
                                                           start=(k == 0), stop=(k == KT - 1))
                        elif kind == "qr":
                            pe.wait_ge(*at("scaled_ready", 2))
                            for h in range(2):
                                x = (2 * m + h) * (nope + rot) + nope
                                for k in range(2):
                                    ins = nc.tensor.matmul(o[64 * h:64 * h + 64, :], w[:, k, x:x + rot], lowrank[:, k, :],
                                                           start=(k == 0), stop=(k == 1))
                        elif kind == "qn":
                            x = m * (nope + rot)
                            for k in range(2):
                                ins = nc.tensor.matmul(o, w[:, k, x:x + nope], lowrank[:, k, :], start=(k == 0), stop=(k == 1))
                        elif kind == "kn":
                            pe.wait_ge(*at("scaled_ready", 3))
                            ins = nc.tensor.matmul(o, w[:, 0, m * 256:m * 256 + 128], lowrank[:, 2, :], start=True, stop=True)
                        else:
                            wv = w[:, 0, :].rearrange("p (h n) -> p h n", n=256)[:, m % 2 * 4:m % 2 * 4 + 4, 128:256]
                            ins = nc.tensor.matmul(o, lowrank[:, 2, m // 2 * P:(m // 2 + 1) * P], wv, start=True, stop=True)
                        ins.then_inc(done[j][0], 1)
                        if kind == "z" and m == 0:
                            square_sums()
                            rope(0)
                        if j - 1 in roped[1:]:
                            rope(roped.index(j - 1))

                @block.scalar
                def _(act):
                    for j, (kind, m, c) in enumerate(tiles):
                        act.wait_ge(*done[j])
                        o = PS[:, j % 4, :]
                        dst = {"low": lowrank[:, m % 3, :], "kpe": kpe, "z": zt[:, m, :], "qr": qr[:, m % 4, :], "qn": qn[:, m, :],
                               "kn": kn[:, m, :], "v": v[:, m // 2, m % 2 * 512:m % 2 * 512 + 512]}[kind]
                        if kind == "low":
                            nc.scalar.activation(sq[:, m, :], o, ACT.Square).then_inc(S["squares_ready"].sem, 1)
                        if kind == "z" and m == 2:
                            for n in range(2):
                                act.wait_ge(*at("inverse_ready", n + 1))
                                nc.scalar.activation(rstd[n], rinv[n], ACT.Sqrt).then_inc(S["rstd_ready"].sem, 1)
                        nc.scalar.activation(dst, o, ACT.Silu if kind == "z" else ACT.Copy).then_inc(S["tile_taken"].sem, 1)

                @block.vector
                def _(dve):
                    for n, width in enumerate((rank_q, rank_kv)):
                        dve.wait_ge(*at("square_sum_ready", n + 1))
                        dve_chain.link(dve, nc.vector.tensor_scalar(rinv[n], PS[:, 6 + n, :], 1.0 / width, EPS, ALU.mult, ALU.add))
                        nc.vector.reciprocal(rinv[n], rinv[n]).then_inc(S["inverse_ready"].sem, 1)
                    dve.wait_ge(*at("tile_taken", 3))
                    for m in range(3):
                        dve.wait_ge(*at("rstd_ready", 1 + m // 2))
                        g = col("l1_g_kva") if m == 2 else col("l1_g_qa")[:, m:m + 1]
                        nc.vector.scalar_tensor_tensor(lowrank[:, m, :], lowrank[:, m, :], g, rstd[m // 2], ALU.mult,
                                                       ALU.mult).then_inc(S["scaled_ready"].sem, 1)
                    for n, j in enumerate(roped):
                        kind, m, _ = tiles[j]
                        dve.wait_ge(*at("tile_taken", j + 1))
                        rope_turn(dve, kpe if kind == "kpe" else qr[:, m, :], n, tmp)

            S["tile_ready"].passed(n_plain)
            S["tile_taken"].passed(len(tiles))
            for n, k in (("squares_ready", 3), ("square_sum_ready", 2), ("inverse_ready", 2), ("rstd_ready", 2),
                         ("scaled_ready", 3), ("rope_mixed", len(roped)), ("rope_taken", len(roped))):
                S[n].passed(k)
            ws.done = c_ukv + 1

            def score(h, u, k, out):
                head, q, half = 2 * u[0] + h, slice(u[1] * P, (u[1] + 1) * P), slice(64 * h, 64 * h + 64)
                nc.tensor.matmul(out, qn[:, head, q], kn[:, head, k], start=True, stop=False)
                return nc.tensor.matmul(out, qr[half, u[0], q], kpe[half, k], start=False, stop=True)

            def value(u, h, kt):
                head = 2 * u[0] + h
                return v[:, kt, head * P:(head + 1) * P], lambda bank: bank[:, h * P:(h + 1) * P]

            def gate(u, bank):
                q, pair = slice(u[1] * P, (u[1] + 1) * P), slice(2 * u[0], 2 * u[0] + 2)
                return HT[:, pair, q], zt[:, pair, q], bank[:, 0:2 * P].rearrange("p (h q) -> p h q", h=2)

            units = [(m, q, [0, 1, 2, 3]) for m in range(4) for q in range(2)]
            units += [(m, q, [2, 3]) for m in range(4) for q in (2, 3)]
            attention(units, (nope + rot) ** -0.5, score, value, lambda u: None, None, gate, together=False)
            project_out("l1_w_out", HT, TOK)

        latent_layer()

        def exact_log1p(dve, r, e, x, y):
            dve_chain.link(dve, nc.vector.tensor_scalar(x, e, 1.0 / 3, -0.5, ALU.mult, ALU.add))
            dve_chain.link(dve, nc.vector.tensor_tensor(x, x, e, ALU.mult))
            dve_chain.link(dve, nc.vector.scalar_tensor_tensor(x, x, 1.0, e, ALU.add, ALU.mult))
            dve_chain.link(dve, nc.vector.tensor_tensor(x, x, r, ALU.subtract))
            dve_chain.link(dve, nc.vector.tensor_scalar(y, e, 1e-3, None, ALU.is_lt))
            dve_chain.link(dve, nc.vector.tensor_tensor(x, x, y, ALU.mult))
            dve_chain.link(dve, nc.vector.tensor_tensor(r, r, x, ALU.add))

        def memory_layer():
            H, DV = 4, 256
            norm_modulate("l2_w_ada", "l2_b_ada", "l2_g_pre", "l2_g_post", COND, 3, TOK)
            order = [[2, 3, 0, 1], [3, 2, 1, 0]]
            a = Arena()
            va = a.take(TT, H, DV + 1)
            qk = a.take(8, TOK)
            ktok = a.take(TT, H, P)
            og = a.take(TT, D)
            raw_at = a.at
            raw = a.take(8, 2, LAT + 4)
            logd = a.take(32, P)
            a2 = Arena(raw_at)
            zt = a2.take(8, TOK)
            hs = HT[:].rearrange("p k t -> p (k t)").rearrange("p (a h v) -> p a h v", a=TT, h=H)
            c_in = ws.first["l2_w_in"]
            taps = col("l2_conv").rearrange("p (j k) -> p j k", j=5)

            small = [0]

            def take(*shape):
                n = 1
                for x in shape:
                    n *= x
                v = SM[:, small[0]:small[0] + n]
                small[0] += n
                names = "abcd"[:len(shape)]
                return v if len(shape) == 1 else v.rearrange(f"p ({' '.join(names)}) -> p {' '.join(names)}",
                                                             **dict(zip(names, shape)))

            gates = take(2, 4, 2, 4)
            logf, ex, t1, t2 = take(2, 4, 4), take(2, 4, 4), take(2, 4, 4), take(2, 4, 4)
            small_cum = small[0]
            cum, tot, u, rowmax, umax = (take(2, 4, 4) for _ in range(5))
            mloc, am, mst = take(2, 4, 4), take(2, 4, 4), take(2, 5, 4)
            keep, gain, at_, nmt, emt, eend, rs, rden = (take(2, 4, 4) for _ in range(8))

            def flat(x):
                return x.rearrange("p a b c -> p (a b c)")

            tiles = [("qk", m, m // 4) for m in range(8)] + [("v", (c, m), 2 + c) for c in range(2) for m in range(TT)]
            tiles += [("o", (c, m), 4 + c) for c in range(2) for m in range(TT)]
            tiles += [("z", m, 6 + m // 4) for m in range(8)] + [("g", 0, 8)]
            last = [j + 1 == len(tiles) or tiles[j + 1][2] != x[2] for j, x in enumerate(tiles)]
            done, n_plain = tile_signals([c_in + x[2] if e else None for x, e in zip(tiles, last)])
            with nc.Block() as block:

                @block.sync
                def _(sp):
                    ws.load_until(sp, c_in + 9)

                @block.gpsimd
                def _(pool):
                    nc.gpsimd.memset(raw[:, :, :, 0:2], 0.0)
                    nc.gpsimd.memset(raw[:, :, :, LAT + 2:LAT + 4], 0.0).then_inc(S["a_ready"].sem, 1)
                    nc.gpsimd.memset(va[:, :, :, DV:DV + 1], 1.0)

                @block.tensor
                def _(pe):
                    for j, (kind, m, c) in enumerate(tiles):
                        if j == 0 or tiles[j - 1][2] != c:
                            ws.wait(pe, c_in + c)
                        w = ws.view(c_in + c)
                        if j >= 4:
                            pe.wait_ge(*at("tile_taken", j - 3))
                        o = PS[:, j % 4, :]
                        for k in range(KT):
                            if kind in ("qk", "z"):
                                ins = nc.tensor.matmul(o, w[:, k, m % 4 * P:m % 4 * P + P], HT[:, k, :], start=(k == 0), stop=(k == KT - 1))
                            elif kind != "g":
                                ins = nc.tensor.matmul(o, HT[:, k, m[1] * P:(m[1] + 1) * P], w[:, k, :], start=(k == 0), stop=(k == KT - 1))
                        if kind == "g":
                            for n in range(TT):
                                for k in range(KT):
                                    ins = nc.tensor.matmul(o[:, n * 16:n * 16 + 16], HT[:, k, n * P:(n + 1) * P], w[:, k, :],
                                                           start=(k == 0), stop=(k == KT - 1))
                        ins.then_inc(done[j][0], 1)
                        if kind == "o" and m == (1, 3):
                            pe.wait_ge(*at("c_ready", 4))
                            for n in range(TT):
                                for h in range(H):
                                    ins = nc.tensor.transpose(PS[:, 4 + n, h * P:(h + 1) * P], qk[:, 4 + h, n * P:(n + 1) * P], ident)
                                ins.then_inc(S["transposed"].sem, 1)

                @block.scalar
                def _(act):
                    for j, (kind, m, c) in enumerate(tiles):
                        act.wait_ge(*done[j])
                        o = PS[:, j % 4, :]
                        if kind == "g":
                            break
                        if kind == "qk":
                            dst, o = raw[:, m, :, 2:LAT + 2], o.rearrange("p (s t) -> p s t", s=2)
                        elif kind == "v":
                            dst, o = va[:, m[1], 2 * m[0]:2 * m[0] + 2, 0:DV], o.rearrange("p (h v) -> p h v", h=2)
                        elif kind == "o":
                            dst = og[:, m[1], m[0] * CH:(m[0] + 1) * CH]
                        else:
                            dst = zt[:, m, :]
                            if m == 0:
                                act.wait_ge(*at("b_ready", 8))
                        f = {"o": ACT.Sigmoid, "z": ACT.Silu}.get(kind, ACT.Copy)
                        nc.scalar.activation(dst, o, f).then_inc(S["tile_taken"].sem, 1)
                        if kind == "v" and m[0] == 1:
                            for n in range(2 * m[1], 2 * m[1] + 2):
                                act.wait_ge(*at("b_ready", n + 1))
                                nc.scalar.activation(qk[:, n, :], qk[:, n, :], ACT.Silu).then_inc(S["squares_ready"].sem, 1)
                        if kind == "z" and m < TT:
                            act.wait_ge(*at("transposed", m + 1))
                            nc.scalar.copy(ktok[:, m, :, :], PS[:, 4 + m, :].rearrange("p (h d) -> p h d", h=H)).then_inc(
                                S["d_ready"].sem, 1)

                @block.vector
                def _(dve):
                    dve.wait_ge(*at("a_ready", 1))
                    for m in range(8):
                        dve.wait_ge(*at("tile_taken", m + 1))
                        o = qk[:, m, :].rearrange("p (s t) -> p s t", s=2)
                        dve_chain.link(dve, nc.vector.tensor_scalar(o, raw[:, m, :, 0:LAT], taps[:, 0, m:m + 1], None, ALU.mult))
                        for j in range(1, 5):
                            ins = nc.vector.scalar_tensor_tensor(o, raw[:, m, :, j:j + LAT], taps[:, j, m:m + 1], o, ALU.mult, ALU.add)
                            if j < 4:
                                dve_chain.link(dve, ins)
                        ins.then_inc(S["b_ready"].sem, 1)
                    for m in range(4, 8):
                        dve.wait_ge(*at("squares_ready", m + 1))
                        nc.vector.tensor_scalar(qk[:, m, :], qk[:, m, :], P ** -0.5, None, ALU.mult).then_inc(S["c_ready"].sem, 1)
                    dve.wait_ge(*done[-1])
                    for d in range(2):
                        for j in range(4):
                            n = order[d][j]
                            x = PS[:, (len(tiles) - 1) % 4, n * 16 + d * 8:n * 16 + d * 8 + 8]
                            dve_chain.add(nc.vector.tensor_tensor(gates[:, d, j, :, :], x.rearrange("p (a h) -> p a h", a=2),
                                                                  bcast("l2_b_gate")[:, d * 8:d * 8 + 8].rearrange("p (a h) -> p a h", a=2), ALU.add))

            S["tile_ready"].passed(n_plain)
            S["tile_taken"].passed(len(tiles) - 1)
            for n, k in (("a_ready", 1), ("b_ready", 8), ("c_ready", 4), ("d_ready", TT), ("squares_ready", 8), ("transposed", TT)):
                S[n].passed(k)
            ws.done = c_in + 9

            with nc.Block() as block:

                @block.tensor
                def _(pe):
                    pe.wait_ge(*at("b_ready", 1))
                    f = flat(logf)
                    nc.tensor.matmul(PS[:, 0, 0:16], const("upto"), f[:, 0:16], start=True, stop=True)
                    nc.tensor.matmul(PS[:, 0, 16:32], const("from"), f[:, 16:32], start=True, stop=True)
                    nc.tensor.matmul(PS[:, 0, 32:64], ones, f, start=True, stop=True).then_inc(S["c_ready"].sem, 1)
                    pe.wait_ge(*at("d_ready", 1))
                    for g in range(8):
                        if g >= 2:
                            pe.wait_ge(*at("f_ready", g - 1))
                        for i in range(4):
                            c = 4 * g + i
                            ins = nc.tensor.matmul(PS[:, 1 + g % 2, i * P:(i + 1) * P], flat(u)[:, c:c + 1].to_broadcast([P, P]), ident,
                                                   start=True, stop=True)
                        ins.then_inc(S["e_ready"].sem, 1)

                @block.scalar
                def _(act):
                    act.wait_ge(*at("a_ready", 1))
                    act_chain.add(nc.scalar.activation(flat(ex), flat(t1), ACT.Exp, scale=-1.0))
                    act.wait_ge(act_chain.sem, act_chain.n)
                    nc.scalar.activation(flat(logf), flat(ex), ACT.Ln, bias=1.0).then_inc(S["g_ready"].sem, 1)
                    act.wait_ge(*at("h_ready", 1))
                    nc.scalar.activation(flat(keep), flat(am), ACT.Exp)
                    nc.scalar.activation(flat(gain), flat(mloc), ACT.Exp)
                    nc.scalar.activation(flat(at_), flat(t1), ACT.Exp)
                    nc.scalar.activation(flat(emt), flat(nmt), ACT.Exp)
                    nc.scalar.activation(flat(eend), flat(t2), ACT.Exp)

                @block.vector
                def _(dve):
                    ig, fg = gates[:, :, :, 0, :], gates[:, :, :, 1, :]
                    tt, ts = nc.vector.tensor_tensor, nc.vector.tensor_scalar
                    nc.vector.scalar_tensor_tensor(t1, fg, -1.0, fg, ALU.mult, ALU.max).then_inc(S["a_ready"].sem, 1)
                    dve.wait_ge(*at("g_ready", 1))
                    exact_log1p(dve, flat(logf), flat(ex), flat(t2), flat(u))
                    nc.vector.scalar_tensor_tensor(logf, fg, 0.0, logf, ALU.min, ALU.subtract).then_inc(S["b_ready"].sem, 1)
                    dve.wait_ge(*at("c_ready", 1))
                    dve_chain.link(dve, nc.vector.tensor_copy(SM[:, small_cum:small_cum + 64], PS[:, 0, 0:64]))
                    tt(u, ig, cum, ALU.subtract).then_inc(S["d_ready"].sem, 1)
                    for g in range(8):
                        dve.wait_ge(*at("e_ready", g + 1))
                        bank = PS[:, 1 + g % 2, :].rearrange("p (c s) -> p c s", c=4)
                        mask = const("causal" if g < 4 else "anticausal")
                        for i in range(4):
                            c = 4 * g + i
                            ins = dve_chain.add(nc.vector.scalar_tensor_tensor(logd[:, c, :], bank[:, i, :], flat(cum)[:, c:c + 1], mask,
                                                                               ALU.add, ALU.add))
                        nc.vector.tensor_reduce(flat(umax)[:, 4 * g:4 * g + 4], bank, AX, ALU.max).then_inc(S["f_ready"].sem, 1)
                        dve.wait_ge(dve_chain.sem, dve_chain.n)
                        dve_chain.add(nc.vector.tensor_reduce(flat(rowmax)[:, 4 * g:4 * g + 4], logd[:, 4 * g:4 * g + 4, :], AX, ALU.max))
                    dve.wait_ge(*at("f_ready", 8))
                    dve.wait_ge(dve_chain.sem, dve_chain.n)
                    dve_chain.add(tt(mloc, tot, umax, ALU.add))
                    dve_chain.link(dve, nc.vector.memset(mst[:, :, 0, :], NEG))
                    for j in range(4):
                        dve_chain.link(dve, tt(am[:, :, j, :], tot[:, :, j, :], mst[:, :, j, :], ALU.add))
                        dve_chain.link(dve, tt(mst[:, :, j + 1, :], am[:, :, j, :], mloc[:, :, j, :], ALU.max))
                    dve_chain.add(tt(am, am, mst[:, :, 1:5, :], ALU.subtract))
                    dve_chain.add(tt(mloc, mloc, mst[:, :, 1:5, :], ALU.subtract))
                    dve_chain.link(dve, tt(t1, cum, mst[:, :, 0:4, :], ALU.add))
                    dve_chain.link(dve, tt(nmt, t1, rowmax, ALU.max))
                    dve_chain.link(dve, tt(t1, t1, nmt, ALU.subtract))
                    dve_chain.add(ts(nmt, nmt, -1.0, None, ALU.mult))
                    tt(t2, u, umax, ALU.subtract).then_inc(S["h_ready"].sem, 1)

            for n, k in (("a_ready", 1), ("b_ready", 1), ("c_ready", 1), ("d_ready", 1), ("e_ready", 8), ("f_ready", 8),
                         ("g_ready", 1), ("h_ready", 1)):
                S[n].passed(k)

            pw = [0]

            def take_pw(*shape):
                n = 1
                for x in shape:
                    n *= x
                v = PW[:, pw[0]:pw[0] + n]
                pw[0] += n
                names = "abcd"[:len(shape)]
                return v.rearrange(f"p ({' '.join(names)}) -> p {' '.join(names)}", **dict(zip(names, shape)))

            state = take_pw(8, DV + 1)
            dm, sq, sqt, ke = (take_pw(2, P) for _ in range(4))
            inter = take_pw(2, DV + 1)
            added = take_pw(1, DV + 1)[:, 0, :]
            units = [(j, d, h) for j in range(4) for d in range(2) for h in range(H)]
            N = len(units)
            first_at = {}
            for i, (j, d, h) in enumerate(units):
                first_at.setdefault((order[d][j], h), i)
            n_state = sum(j < 3 for j, _, _ in units)
            n_inter = sum(j > 0 for j, _, _ in units)

            def upto(i, which):
                return sum((u[0] < 3) if which == "state" else (u[0] > 0) for u in units[:i])

            with nc.Block() as block:

                @block.tensor
                def _(pe):
                    def logits(i):
                        j, d, h = units[i]
                        t_ = slice(order[d][j] * P, (order[d][j] + 1) * P)
                        if i >= 2:
                            pe.wait_ge(*at("a_ready", i - 1))
                        nc.tensor.matmul(PS[:, i % 2, 0:P], qk[:, h, t_], qk[:, 4 + h, t_], start=True, stop=True).then_inc(
                            S["scores_ready"].sem, 1)

                    def mix(i):
                        j, d, h = units[i]
                        pe.wait_ge(*at("turned_copied", i + 1))
                        if i >= 1:
                            pe.wait_ge(*at("heads_taken", i))
                        nc.tensor.matmul(PS[:, 7, 0:DV], sqt[:, i % 2, :], va[:, order[d][j], h, 0:DV], start=True, stop=True).then_inc(
                            S["heads_ready"].sem, 1)

                    logits(0)
                    for i, (j, d, h) in enumerate(units):
                        n = order[d][j]
                        if i + 1 < N:
                            logits(i + 1)
                        if j < 3:
                            s = upto(i, "state")
                            pe.wait_ge(*at("b_ready", s + 1))
                            if s >= 2:
                                pe.wait_ge(*at("c_ready", s - 1))
                            nc.tensor.matmul(PS[:, 2 + s % 2, 0:DV + 1], ke[:, s % 2, :], va[:, n, h, :], start=True, stop=True).then_inc(
                                S["d_ready"].sem, 1)
                        if j > 0:
                            s = upto(i, "inter")
                            pe.wait_ge(*at("e_ready", s + 1))
                            if s >= 2:
                                pe.wait_ge(*at("f_ready", s - 1))
                            nc.tensor.matmul(PS[:, 4 + s % 2, 0:DV + 1], qk[:, h, n * P:(n + 1) * P], state[:, 4 * d + h, :],
                                             start=True, stop=True).then_inc(S["g_ready"].sem, 1)
                        pe.wait_ge(*at("a_ready", i + 1))
                        if i >= 1:
                            pe.wait_ge(*at("turned_copied", i))
                        nc.tensor.transpose(PS[:, 6, 0:P], sq[:, i % 2, :], ident).then_inc(S["probs_turned"].sem, 1)
                        if i >= 1:
                            mix(i - 1)
                    mix(N - 1)

                @block.scalar
                def _(act):
                    def decays(i):
                        j, d, h = units[i]
                        c = 16 * d + 4 * j + h
                        if i >= 2:
                            act.wait_ge(*at("a_ready", i - 1))
                        nc.scalar.activation(dm[:, i % 2, :], logd[:, c, :], ACT.Exp, bias=flat(nmt)[:, c:c + 1]).then_inc(
                            S["exp_ready"].sem, 1)

                    decays(0)
                    for i, (j, d, h) in enumerate(units):
                        c = 16 * d + 4 * j + h
                        if i + 1 < N:
                            decays(i + 1)
                        if j < 3:
                            s = upto(i, "state")
                            act.wait_ge(*at("d_ready", s + 1))
                            if s >= 1:
                                act.wait_ge(*at("e_ready", s))
                            nc.scalar.activation(added, PS[:, 2 + s % 2, 0:DV + 1], ACT.Copy, scale=flat(gain)[:, c:c + 1]).then_inc(
                                S["c_ready"].sem, 1)
                        if j > 0:
                            s = upto(i, "inter")
                            act.wait_ge(*at("g_ready", s + 1))
                            if i >= 2:
                                act.wait_ge(*at("heads_taken", i - 1))
                            nc.scalar.activation(inter[:, i % 2, :], PS[:, 4 + s % 2, 0:DV + 1], ACT.Copy,
                                                 scale=flat(at_)[:, c:c + 1]).then_inc(S["f_ready"].sem, 1)
                        act.wait_ge(*at("probs_turned", i + 1))
                        if i >= 2:
                            act.wait_ge(*at("heads_ready", i - 1))
                        nc.scalar.copy(sqt[:, i % 2, :], PS[:, 6, 0:P]).then_inc(S["turned_copied"].sem, 1)

                @block.vector
                def _(dve):
                    def end_keys(i):
                        j, d, h = units[i]
                        if j < 3:
                            s = upto(i, "state")
                            if s >= 2:
                                dve.wait_ge(*at("d_ready", s - 1))
                            c = 16 * d + 4 * j + h
                            nc.vector.tensor_scalar(ke[:, s % 2, :], ktok[:, order[d][j], h, :], flat(eend)[:, c:c + 1], None,
                                                    ALU.mult).then_inc(S["b_ready"].sem, 1)

                    def combine(i):
                        j, d, h = units[i]
                        c, n = 16 * d + 4 * j + h, order[d][j]
                        r, w = flat(rden)[:, c:c + 1], hs[:, n, h, :]
                        dve.wait_ge(*at("heads_ready", i + 1))
                        src = PS[:, 7, 0:DV]
                        fresh = first_at[(n, h)] == i
                        if j > 0:
                            x = inter[:, i % 2, 0:DV]
                            dve_chain.link(dve, nc.vector.tensor_tensor(x, src, x, ALU.add))
                            src = x
                        if fresh:
                            nc.vector.tensor_scalar(w, src, r, None, ALU.mult).then_inc(S["heads_taken"].sem, 1)
                        else:
                            nc.vector.scalar_tensor_tensor(w, src, r, w, ALU.mult, ALU.add).then_inc(S["heads_taken"].sem, 1)

                    end_keys(0)
                    for i, (j, d, h) in enumerate(units):
                        c = 16 * d + 4 * j + h
                        if i + 1 < N:
                            end_keys(i + 1)
                        dve.wait_ge(*at("scores_ready", i + 1))
                        dve.wait_ge(*at("exp_ready", i + 1))
                        if i >= 2:
                            dve.wait_ge(*at("probs_turned", i - 1))
                        nc.vector.scalar_tensor_tensor(sq[:, i % 2, :], PS[:, i % 2, 0:P], 1.0, dm[:, i % 2, :], ALU.mult, ALU.mult,
                                                       accum_out=flat(rs)[:, c:c + 1]).then_inc(S["a_ready"].sem, 1)
                        if j < 3:
                            s = upto(i, "state")
                            st = state[:, 4 * d + h, :]
                            dve.wait_ge(*at("c_ready", s + 1))
                            if j == 0:
                                nc.vector.tensor_copy(st, added).then_inc(S["e_ready"].sem, 1)
                            else:
                                dve.wait_ge(*at("g_ready", upto(i, "inter") + 1))
                                nc.vector.scalar_tensor_tensor(st, st, flat(keep)[:, c:c + 1], added, ALU.mult, ALU.add).then_inc(
                                    S["e_ready"].sem, 1)
                        dve.wait_ge(*at("a_ready", i + 1))
                        r, den = flat(rden)[:, c:c + 1], flat(rs)[:, c:c + 1]
                        x = flat(t2)[:, c:c + 1]
                        if j > 0:
                            dve.wait_ge(*at("f_ready", upto(i, "inter") + 1))
                            dve_chain.link(dve, nc.vector.tensor_tensor(den, inter[:, i % 2, DV:DV + 1], den, ALU.add))
                        dve_chain.link(dve, nc.vector.scalar_tensor_tensor(x, den, -1.0, flat(emt)[:, c:c + 1], ALU.mult, ALU.max))
                        dve_chain.link(dve, nc.vector.tensor_tensor(r, den, x, ALU.max))
                        dve_chain.link(dve, nc.vector.reciprocal(r, r))
                        if i >= 1:
                            combine(i - 1)
                    combine(N - 1)

            for n, k in (("scores_ready", N), ("exp_ready", N), ("a_ready", N), ("b_ready", n_state), ("c_ready", n_state),
                         ("d_ready", n_state), ("e_ready", n_state), ("f_ready", n_inter), ("g_ready", n_inter),
                         ("probs_turned", N), ("turned_copied", N), ("heads_ready", N), ("heads_taken", N)):
                S[n].passed(k)

            ot = logd.rearrange("p c s -> p (c s)").rearrange("p (k t) -> p k t", k=KT)
            ss, rr = SM[:, 0:16], SM[:, 16:32]
            with nc.Block() as block:

                @block.sync
                def _(sp):
                    ws.load_until(sp, ws.done)

                @block.vector
                def _(dve):
                    for n in range(TT):
                        x = hs[:, n, :, :].rearrange("p h v -> p (h v)")
                        nc.vector.tensor_tensor(x, x, og[:, n, :], ALU.mult).then_inc(S["a_ready"].sem, 1)
                    dve.wait_ge(*at("squares_ready", 16))
                    dve_chain.link(dve, nc.vector.tensor_scalar(ss, ss, 1.0 / DV, EPS, ALU.mult, ALU.add))
                    nc.vector.reciprocal(ss, ss).then_inc(S["inverse_ready"].sem, 1)
                    dve.wait_ge(*at("rstd_ready", 1))
                    for n in range(TT):
                        for h in range(H):
                            c = n * H + h
                            ins = nc.vector.tensor_scalar(hs[:, n, h, :], hs[:, n, h, :], rr[:, c:c + 1], None, ALU.mult)
                            ins.then_inc(S["b_ready"].sem, 1)
                    for k in range(KT):
                        dve.wait_ge(*at("transposed", k + 1))
                        nc.vector.scalar_tensor_tensor(ot[:, k, :], PS[:, k % 4, :], col("l2_g_head")[:, k:k + 1], zt[:, k, :],
                                                       ALU.mult, ALU.mult).then_inc(S["transposed_taken"].sem, 1)

                @block.scalar
                def _(act):
                    for n in range(TT):
                        act.wait_ge(*at("a_ready", n + 1))
                        for h in range(H):
                            c = n * H + h
                            nc.scalar.activation(PW[:, 0:DV], hs[:, n, h, :], ACT.Square, accum_out=ss[:, c:c + 1]).then_inc(
                                S["squares_ready"].sem, 1)
                            act.wait_ge(*at("squares_ready", c + 1))
                    act.wait_ge(*at("inverse_ready", 1))
                    nc.scalar.activation(rr, ss, ACT.Sqrt).then_inc(S["rstd_ready"].sem, 1)

                @block.tensor
                def _(pe):
                    pe.wait_ge(*at("b_ready", 16))
                    for k in range(KT):
                        if k >= 4:
                            pe.wait_ge(*at("transposed_taken", k - 3))
                        for n in range(TT):
                            ins = nc.tensor.transpose(PS[:, k % 4, n * P:(n + 1) * P], hs[:, n, k // 2, k % 2 * P:k % 2 * P + P], ident)
                        ins.then_inc(S["transposed"].sem, 1)

            for n, k in (("a_ready", TT), ("b_ready", 16), ("squares_ready", 16), ("inverse_ready", 1), ("rstd_ready", 1),
                         ("transposed", KT), ("transposed_taken", KT)):
                S[n].passed(k)
            project_out("l2_w_out", ot, TOK)

        memory_layer()
        window_layer(3, False)

        norm_modulate("w_ada_2", "b_ada_2", "norm1_w_2", None, COND2[:].unsqueeze(2), 6, LAT)

        def hybrid_mixer():
            H = 4
            a = Arena()
            aq, ak, av = a.take(4, LAT), a.take(4, LAT), a.take(2, CH)
            raw = a.take(12, LAT + 3)
            qkv = a.take(12, LAT)
            dz = a.take(2, CH)
            mixed = HT[:, :, 0:LAT]
            c_in = ws.first["w_in_2"]
            taps = col("conv_w_2").rearrange("p (j k) -> p j k", j=4)
            small = [0]

            def take(*shape):
                n = 1
                for x in shape:
                    n *= x
                v = SM[:, small[0]:small[0] + n]
                small[0] += n
                names = "abcd"[:len(shape)]
                return v if len(shape) == 1 else v.rearrange(f"p ({' '.join(names)}) -> p {' '.join(names)}",
                                                             **dict(zip(names, shape)))

            ba = take(2, 8)
            beta, ex, g, t1, t2, x1 = (take(2, 4) for _ in range(6))
            gc, gtot, egc, edec, egl, bg = (take(2, 4) for _ in range(6))

            tiles = [("aq", m, 0) for m in range(4)] + [("ak", m, 1) for m in range(4)] + [("av", m, 2) for m in range(2)]
            tiles += [("qkv", m, 3 + m // 4) for m in range(12)] + [("dz", m, 6) for m in range(2)] + [("ba", 0, 7)]
            last = [j + 1 == len(tiles) or tiles[j + 1][2] != x[2] for j, x in enumerate(tiles)]
            done, n_plain = tile_signals([c_in + x[2] if e else None for x, e in zip(tiles, last)])
            with nc.Block() as block:

                @block.sync
                def _(sp):
                    ws.load_until(sp, c_in + 8)

                @block.gpsimd
                def _(pool):
                    nc.gpsimd.memset(raw[:, :, 0:3], 0.0).then_inc(S["a_ready"].sem, 1)

                @block.tensor
                def _(pe):
                    for j, (kind, m, c) in enumerate(tiles):
                        if j == 0 or tiles[j - 1][2] != c:
                            ws.wait(pe, c_in + c)
                        w = ws.view(c_in + c)
                        if j >= 4:
                            pe.wait_ge(*at("tile_taken", j - 3))
                        o = PS[:, j % 4, :]
                        if kind == "ba":
                            for n in range(2):
                                for k in range(KT):
                                    ins = nc.tensor.matmul(o[:, n * 8:n * 8 + 8], HT[:, k, n * P:(n + 1) * P], w[:, k, :],
                                                           start=(k == 0), stop=(k == KT - 1))
                        else:
                            for k in range(KT):
                                if kind in ("av", "dz"):
                                    ins = nc.tensor.matmul(o, HT[:, k, m * P:(m + 1) * P], w[:, k, :], start=(k == 0), stop=(k == KT - 1))
                                else:
                                    ins = nc.tensor.matmul(o[:, 0:LAT], w[:, k, m % 4 * P:m % 4 * P + P], HT[:, k, 0:LAT],
                                                           start=(k == 0), stop=(k == KT - 1))
                        ins.then_inc(done[j][0], 1)

                @block.scalar
                def _(act):
                    act.wait_ge(*at("a_ready", 1))
                    for j, (kind, m, c) in enumerate(tiles[:-1]):
                        act.wait_ge(*done[j])
                        o = PS[:, j % 4, :]
                        dst, o = {"aq": (aq[:, m % 4, :], o[:, 0:LAT]), "ak": (ak[:, m % 4, :], o[:, 0:LAT]), "av": (av[:, m % 2, :], o),
                                  "qkv": (raw[:, m, 3:LAT + 3], o[:, 0:LAT]), "dz": (dz[:, m % 2, :], o)}[kind]
                        nc.scalar.activation(dst, o, ACT.Silu if kind == "dz" else ACT.Copy).then_inc(S["tile_taken"].sem, 1)
                    for m in range(12):
                        act.wait_ge(*at("b_ready", m + 1))
                        act_chain.add(nc.scalar.activation(qkv[:, m, :], qkv[:, m, :], ACT.Silu))

                @block.vector
                def _(dve):
                    for m in range(12):
                        dve.wait_ge(*at("tile_taken", 11 + m))
                        o = qkv[:, m, :]
                        dve_chain.link(dve, nc.vector.tensor_scalar(o, raw[:, m, 0:LAT], taps[:, 0, m:m + 1], None, ALU.mult))
                        for j in range(1, 4):
                            ins = nc.vector.scalar_tensor_tensor(o, raw[:, m, j:j + LAT], taps[:, j, m:m + 1], o, ALU.mult, ALU.add)
                            if j < 3:
                                dve_chain.link(dve, ins)
                        ins.then_inc(S["b_ready"].sem, 1)
                    dve.wait_ge(*done[-1])
                    dve_chain.add(nc.vector.tensor_copy(ba, PS[:, (len(tiles) - 1) % 4, 0:16].rearrange("p (a n) -> p a n", a=2)))

            S["tile_ready"].passed(n_plain)
            S["tile_taken"].passed(len(tiles) - 1)
            S["a_ready"].passed(1)
            S["b_ready"].passed(12)
            ws.done = c_in + 8

            def score(h, u, k, out):
                half = slice(64 * h, 64 * h + 64)
                return nc.tensor.matmul(out, aq[half, u[0], u[1] * P:(u[1] + 1) * P], ak[half, u[0], k], start=True, stop=True)

            def value(u, h, kt):
                head = 2 * u[0] + h
                return av[:, kt, head * 64:head * 64 + 64], lambda bank: bank[64 * h:64 * h + 64, 0:P]

            def gate(u, bank):
                return mixed[:, u[0], u[1] * P:(u[1] + 1) * P], None, bank[:, 0:P]

            units = [(m, q, list(range(q + 1))) for m in range(4) for q in range(2)]
            attention(units, 0.125, score, value, lambda u: dilated[:, u[1], 0:(u[1] + 1) * P], None, gate)

            b = Arena()
            vb, kbg, kd = (b.take(8, P) for _ in range(3))
            b = Arena(a.at)
            kt_, vt, e, amat, amat_t, intra, intra_t = (b.take(8, P) for _ in range(7))
            u_, w_t, o_ = (b.take(8, P) for _ in range(3))
            x = PW[:, 0:1024].rearrange("p (n c) -> p n c", n=8)
            x_t = PW[:, 1024:2048].rearrange("p (n c) -> p n c", n=8)
            y = PW[:, 2048:3072].rearrange("p (n c) -> p n c", n=8)
            lo = PW[:, 3072:4096].rearrange("p (n c) -> p n c", n=8)
            s_ = raw.rearrange("p k t -> p (k t)")[:, 0:512].rearrange("p (h v) -> p h v", h=H)
            norms = raw.rearrange("p k t -> p (k t)")[:, 0:2048].rearrange("p (k t) -> p k t", k=8)
            sq8 = PW[:, 0:2048].rearrange("p (k t) -> p k t", k=8)

            def flat(v):
                return v.rearrange("p a b -> p (a b)")

            def bank4(n):
                return PS[:, n, :].rearrange("p (c s) -> p c s", c=4)

            with nc.Block() as block:

                @block.scalar
                def _(act):
                    for k in range(8):
                        nc.scalar.activation(sq8[:, k, :], qkv[:, k, :], ACT.Square).then_inc(S["squares_ready"].sem, 1)
                    for k in range(8):
                        act.wait_ge(*at("inverse_ready", k + 1))
                        nc.scalar.activation(norms[:, k, :], norms[:, k, :], ACT.Sqrt).then_inc(S["rstd_ready"].sem, 1)
                    act.wait_ge(*at("a_ready", 1))
                    act_chain.link(act, nc.scalar.activation(ex, t1, ACT.Exp, scale=-1.0))
                    nc.scalar.activation(g, ex, ACT.Ln, bias=1.0).then_inc(S["b_ready"].sem, 1)
                    nc.scalar.activation(t2[:, 0, :], bcast("A_log_2"), ACT.Exp).then_inc(S["b_ready"].sem, 1)
                    nc.scalar.activation(beta, ba[:, :, 0:4], ACT.Sigmoid).then_inc(S["b_ready"].sem, 1)
                    for n in range(2):
                        act.wait_ge(*at("transposed", 2 * n + 1))
                        nc.scalar.copy(kt_[:, 4 * n:4 * n + 4, :], bank4(4 + n)).then_inc(S["transposed_taken"].sem, 1)
                        act.wait_ge(*at("transposed", 2 * n + 2))
                        nc.scalar.copy(vt[:, 4 * n:4 * n + 4, :], bank4(6 + n)).then_inc(S["transposed_taken"].sem, 1)

                @block.tensor
                def _(pe):
                    for k in range(8):
                        pe.wait_ge(*at("squares_ready", k + 1))
                        if k >= 4:
                            pe.wait_ge(*at("inverse_ready", k - 3))
                        nc.tensor.matmul(PS[:, k % 4, 0:LAT], ones, sq8[:, k, :], start=True, stop=True).then_inc(
                            S["square_sum_ready"].sem, 1)
                    pe.wait_ge(*at("scaled_ready", 8))
                    for n in range(2):
                        for first, bank in ((4, 4), (8, 6)):
                            for h in range(H):
                                ins = nc.tensor.transpose(PS[:, bank + n, h * P:(h + 1) * P], qkv[:, first + h, n * P:(n + 1) * P], ident)
                            ins.then_inc(S["transposed"].sem, 1)

                @block.vector
                def _(dve):
                    for k in range(8):
                        dve.wait_ge(*at("square_sum_ready", k + 1))
                        dve_chain.link(dve, nc.vector.tensor_scalar(norms[:, k, :], PS[:, k % 4, 0:LAT], EPS, None, ALU.add))
                        nc.vector.reciprocal(norms[:, k, :], norms[:, k, :]).then_inc(S["inverse_ready"].sem, 1)
                    for k in range(8):
                        dve.wait_ge(*at("rstd_ready", k + 1))
                        nc.vector.scalar_tensor_tensor(qkv[:, k, :], qkv[:, k, :], P ** -0.5 if k < 4 else 1.0, norms[:, k, :], ALU.mult,
                                                       ALU.mult).then_inc(S["scaled_ready"].sem, 1)
                    dve_chain.link(dve, nc.vector.tensor_tensor(x1, ba[:, :, 4:8], bcast("dt_bias_2").unsqueeze(1).to_broadcast([P, 2, 4]),
                                                                ALU.add))
                    nc.vector.scalar_tensor_tensor(t1, x1, -1.0, x1, ALU.mult, ALU.max).then_inc(S["a_ready"].sem, 1)
                    dve.wait_ge(*at("b_ready", 1))
                    exact_log1p(dve, flat(g), flat(ex), flat(gc), flat(gtot))
                    dve_chain.link(dve, nc.vector.scalar_tensor_tensor(g, x1, 0.0, g, ALU.max, ALU.add))
                    dve.wait_ge(*at("b_ready", 2))
                    dve_chain.add(nc.vector.scalar_tensor_tensor(g, g, -1.0, t2[:, 0:1, :].to_broadcast([P, 2, 4]), ALU.mult, ALU.mult))

            for n, k in (("squares_ready", 8), ("square_sum_ready", 8), ("inverse_ready", 8), ("rstd_ready", 8), ("scaled_ready", 8),
                         ("transposed", 4), ("transposed_taken", 4), ("a_ready", 1), ("b_ready", 3)):
                S[n].passed(k)

            with nc.Block() as block:

                @block.tensor
                def _(pe):
                    nc.tensor.matmul(PS[:, 0, 0:8], const("upto"), flat(g), start=True, stop=True)
                    nc.tensor.matmul(PS[:, 0, 8:16], ones, flat(g), start=True, stop=True).then_inc(S["a_ready"].sem, 1)
                    for p in range(8):
                        n, h = divmod(p, 4)
                        t_ = slice(n * P, (n + 1) * P)
                        nc.tensor.matmul(PS[:, 1 + n, h * P:(h + 1) * P], qkv[:, 4 + h, t_], qkv[:, 4 + h, t_], start=True, stop=True)
                        ins = nc.tensor.matmul(PS[:, 3 + n, h * P:(h + 1) * P], qkv[:, h, t_], qkv[:, 4 + h, t_], start=True, stop=True)
                    ins.then_inc(S["scores_ready"].sem, 1)
                    pe.wait_ge(*at("b_ready", 1))
                    for p in range(8):
                        ins = nc.tensor.matmul(PS[:, 5 + p // 4, p % 4 * P:(p % 4 + 1) * P], flat(gc)[:, p:p + 1].to_broadcast([P, P]), ident,
                                               start=True, stop=True)
                    ins.then_inc(S["c_ready"].sem, 1)
                    pe.wait_ge(*at("f_ready", 1))
                    pe.wait_ge(*at("d_ready", 2))
                    for p in range(8):
                        ins = nc.tensor.transpose(PS[:, 5 + p // 4, p % 4 * P:(p % 4 + 1) * P], amat[:, p, :], ident)
                    ins.then_inc(S["transposed"].sem, 1)
                    pe.wait_ge(*at("g_ready", 2))
                    for p in range(8):
                        ins = nc.tensor.transpose(PS[:, 3 + p // 4, p % 4 * P:(p % 4 + 1) * P], intra[:, p, :], ident)
                    ins.then_inc(S["transposed"].sem, 1)

                @block.scalar
                def _(act):
                    act.wait_ge(*at("b_ready", 3))
                    nc.scalar.activation(egc, gc, ACT.Exp).then_inc(S["exp_ready"].sem, 1)
                    nc.scalar.activation(edec, edec, ACT.Exp).then_inc(S["exp_ready"].sem, 1)
                    nc.scalar.activation(egl, gtot, ACT.Exp).then_inc(S["exp_ready"].sem, 1)
                    for p in range(8):
                        act.wait_ge(*at("d_ready", 1 + p // 4))
                        nc.scalar.activation(e[:, p, :], e[:, p, :], ACT.Exp, bias=flat(gc)[:, p:p + 1]).then_inc(S["e_ready"].sem, 1)
                    act.wait_ge(*at("transposed", 2))
                    for n in range(2):
                        nc.scalar.copy(intra_t[:, 4 * n:4 * n + 4, :], bank4(3 + n))

                @block.vector
                def _(dve):
                    dve.wait_ge(*at("a_ready", 1))
                    nc.vector.tensor_copy(flat(gc), PS[:, 0, 0:8]).then_inc(S["b_ready"].sem, 1)
                    nc.vector.tensor_copy(flat(gtot), PS[:, 0, 8:16]).then_inc(S["b_ready"].sem, 1)
                    dve.wait_ge(*at("b_ready", 2))
                    nc.vector.tensor_tensor(edec, gtot, gc, ALU.subtract).then_inc(S["b_ready"].sem, 1)
                    dve.wait_ge(*at("c_ready", 1))
                    for n in range(2):
                        nc.vector.scalar_tensor_tensor(e[:, 4 * n:4 * n + 4, :], bank4(5 + n), -1.0,
                                                       const("causal").unsqueeze(1).to_broadcast([P, 4, P]), ALU.mult, ALU.add).then_inc(
                            S["d_ready"].sem, 1)
                    dve.wait_ge(*at("scores_ready", 1))
                    for p in range(8):
                        dve.wait_ge(*at("e_ready", p + 1))
                        dve_chain.add(nc.vector.scalar_tensor_tensor(amat[:, p, :], bank4(1 + p // 4)[:, p % 4, :], flat(beta)[:, p:p + 1],
                                                                     e[:, p, :], ALU.mult, ALU.mult))
                    dve.wait_ge(dve_chain.sem, dve_chain.n)
                    nc.vector.tensor_tensor(amat, amat, const("strict").unsqueeze(1).to_broadcast([P, 8, P]), ALU.mult).then_inc(
                        S["f_ready"].sem, 1)
                    for n in range(2):
                        nc.vector.tensor_tensor(intra[:, 4 * n:4 * n + 4, :], bank4(3 + n), e[:, 4 * n:4 * n + 4, :], ALU.mult).then_inc(
                            S["g_ready"].sem, 1)
                    dve.wait_ge(*at("exp_ready", 3))
                    dve_chain.link(dve, nc.vector.tensor_tensor(bg, beta, egc, ALU.mult))
                    for dst, src, f in ((vb, vt, beta), (kbg, kt_, bg), (kd, kt_, edec)):
                        dve_chain.add(nc.vector.tensor_tensor(dst, src, flat(f).unsqueeze(2).to_broadcast([P, 8, P]), ALU.mult))
                    dve.wait_ge(*at("f_ready", 1))
                    idb = ident.unsqueeze(1).to_broadcast([P, 8, P])
                    dve_chain.link(dve, nc.vector.tensor_tensor(x, amat, const("low1").unsqueeze(1).to_broadcast([P, 8, P]), ALU.mult))
                    dve_chain.link(dve, nc.vector.scalar_tensor_tensor(x, x, -1.0, idb, ALU.mult, ALU.add))
                    dve.wait_ge(*at("transposed", 1))
                    for n in range(2):
                        dve_chain.add(nc.vector.tensor_copy(amat_t[:, 4 * n:4 * n + 4, :], bank4(5 + n)))
                    dve.wait_ge(dve_chain.sem, dve_chain.n)
                    dve_chain.link(dve, nc.vector.tensor_tensor(x_t, amat_t, const("low1T").unsqueeze(1).to_broadcast([P, 8, P]), ALU.mult))
                    dve_chain.link(dve, nc.vector.scalar_tensor_tensor(x_t, x_t, -1.0, idb, ALU.mult, ALU.add))

            for n, k in (("a_ready", 1), ("b_ready", 3), ("c_ready", 1), ("d_ready", 2), ("e_ready", 8), ("f_ready", 1), ("g_ready", 2),
                         ("exp_ready", 3), ("scores_ready", 1), ("transposed", 2)):
                S[n].passed(k)

            levels = (2, 4, 8, 16, 32, 64)
            with nc.Block() as block:

                @block.gpsimd
                def _(pool):
                    for l, bsize in enumerate(levels):
                        if l >= 1:
                            pool.wait_ge(*at("b_ready", l))
                        nc.gpsimd.tensor_tensor(lo, amat_t, const(f"low{bsize}T").unsqueeze(1).to_broadcast([P, 8, P]),
                                                ALU.mult).then_inc(S["a_ready"].sem, 1)

                @block.tensor
                def _(pe):
                    for l in range(len(levels)):
                        pe.wait_ge(*at("a_ready", l + 1))
                        if l >= 1:
                            pe.wait_ge(*at("e_ready", 2 * l))
                            pe.wait_ge(*at("f_ready", 2 * l))
                        for p in range(8):
                            ins = nc.tensor.matmul(PS[:, p // 4, p % 4 * P:(p % 4 + 1) * P], lo[:, p, :], x[:, p, :], start=True, stop=True)
                        ins.then_inc(S["b_ready"].sem, 1)
                        pe.wait_ge(*at("c_ready", 2 * l + 2))
                        for p in range(8):
                            ins = nc.tensor.matmul(PS[:, 2 + p // 4, p % 4 * P:(p % 4 + 1) * P], x_t[:, p, :], y[:, p, :], start=True, stop=True)
                        ins.then_inc(S["d_ready"].sem, 1)
                        for p in range(8):
                            ins = nc.tensor.matmul(PS[:, 4 + p // 4, p % 4 * P:(p % 4 + 1) * P], y[:, p, :], x_t[:, p, :], start=True, stop=True)
                        ins.then_inc(S["g_ready"].sem, 1)
                    pe.wait_ge(*at("f_ready", 2 * len(levels)))
                    for p in range(8):
                        n, h = p // 4, p % 4
                        nc.tensor.matmul(PS[:, n, h * P:(h + 1) * P], x_t[:, p, :], vb[:, p, :], start=True, stop=True)
                        ins = nc.tensor.matmul(PS[:, 2 + n, h * P:(h + 1) * P], kbg[:, p, :], x_t[:, p, :], start=True, stop=True)
                    ins.then_inc(S["scores_ready"].sem, 1)

                @block.scalar
                def _(act):
                    for l in range(len(levels)):
                        act.wait_ge(*at("b_ready", l + 1))
                        if l >= 1:
                            act.wait_ge(*at("g_ready", l))
                        for n in range(2):
                            nc.scalar.copy(y[:, 4 * n:4 * n + 4, :], bank4(n)).then_inc(S["c_ready"].sem, 1)
                    act.wait_ge(*at("scores_ready", 1))
                    for n in range(2):
                        nc.scalar.copy(u_[:, 4 * n:4 * n + 4, :], bank4(n))
                        nc.scalar.copy(w_t[:, 4 * n:4 * n + 4, :], bank4(2 + n))

                @block.vector
                def _(dve):
                    for l in range(len(levels)):
                        dve.wait_ge(*at("d_ready", l + 1))
                        for n in range(2):
                            v = x[:, 4 * n:4 * n + 4, :]
                            nc.vector.tensor_tensor(v, v, bank4(2 + n), ALU.subtract).then_inc(S["e_ready"].sem, 1)
                        dve.wait_ge(*at("g_ready", l + 1))
                        for n in range(2):
                            v = x_t[:, 4 * n:4 * n + 4, :]
                            nc.vector.tensor_tensor(v, v, bank4(4 + n), ALU.subtract).then_inc(S["f_ready"].sem, 1)

            L = len(levels)
            for n, k in (("a_ready", L), ("b_ready", L), ("c_ready", 2 * L), ("d_ready", L), ("e_ready", 2 * L), ("f_ready", 2 * L),
                         ("g_ready", L), ("scores_ready", 1)):
                S[n].passed(k)

            rs, rr = SM[:, 300:308], SM[:, 308:316]
            with nc.Block() as block:

                @block.tensor
                def _(pe):
                    for h in range(H):
                        ins = nc.tensor.matmul(PS[:, 0, h * P:(h + 1) * P], kd[:, h, :], u_[:, h, :], start=True, stop=True)
                    ins.then_inc(S["a_ready"].sem, 1)
                    for h in range(H):
                        ins = nc.tensor.matmul(PS[:, 1, h * P:(h + 1) * P], intra_t[:, h, :], u_[:, h, :], start=True, stop=True)
                    ins.then_inc(S["b_ready"].sem, 1)
                    pe.wait_ge(*at("c_ready", 1))
                    for h in range(H):
                        ins = nc.tensor.matmul(PS[:, 2, h * P:(h + 1) * P], w_t[:, 4 + h, :], s_[:, h, :], start=True, stop=True)
                    ins.then_inc(S["d_ready"].sem, 1)
                    for h in range(H):
                        ins = nc.tensor.matmul(PS[:, 3, h * P:(h + 1) * P], qkv[:, h, P:2 * P], s_[:, h, :], start=True, stop=True)
                    ins.then_inc(S["e_ready"].sem, 1)
                    pe.wait_ge(*at("f_ready", 1))
                    for h in range(H):
                        ins = nc.tensor.matmul(PS[:, 4, h * P:(h + 1) * P], intra_t[:, 4 + h, :], u_[:, 4 + h, :], start=True, stop=True)
                    ins.then_inc(S["g_ready"].sem, 1)
                    pe.wait_ge(*at("h_ready", 1))
                    for h in range(H):
                        for n in range(2):
                            ins = nc.tensor.transpose(PS[:, 5 + h // 2, (h % 2 * 2 + n) * P:(h % 2 * 2 + n + 1) * P], o_[:, 4 * n + h, :], ident)
                    ins.then_inc(S["transposed"].sem, 1)

                @block.scalar
                def _(act):
                    act.wait_ge(*at("a_ready", 1))
                    nc.scalar.copy(s_, bank4(0)).then_inc(S["c_ready"].sem, 1)
                    act.wait_ge(*at("b_ready", 1))
                    nc.scalar.copy(o_[:, 0:4, :], bank4(1)).then_inc(S["i_ready"].sem, 1)
                    act.wait_ge(*at("i_ready", 1))
                    act.wait_ge(*at("j_ready", 1))
                    for p in range(8):
                        nc.scalar.activation(y[:, p, :], o_[:, p, :], ACT.Square, accum_out=rs[:, p:p + 1]).then_inc(
                            S["squares_ready"].sem, 1)
                    act.wait_ge(*at("inverse_ready", 1))
                    nc.scalar.activation(rr, rs, ACT.Sqrt).then_inc(S["rstd_ready"].sem, 1)

                @block.vector
                def _(dve):
                    dve.wait_ge(*at("d_ready", 1))
                    nc.vector.tensor_tensor(u_[:, 4:8, :], u_[:, 4:8, :], bank4(2), ALU.subtract).then_inc(S["f_ready"].sem, 1)
                    dve.wait_ge(*at("e_ready", 1))
                    dve_chain.link(dve, nc.vector.tensor_tensor(o_[:, 4:8, :], bank4(3), egc[:, 1, :].unsqueeze(2).to_broadcast([P, 4, P]),
                                                                ALU.mult))
                    dve.wait_ge(*at("g_ready", 1))
                    nc.vector.tensor_tensor(o_[:, 4:8, :], o_[:, 4:8, :], bank4(4), ALU.add).then_inc(S["j_ready"].sem, 1)
                    dve.wait_ge(*at("squares_ready", 8))
                    dve_chain.link(dve, nc.vector.tensor_scalar(rs, rs, 1.0 / P, EPS, ALU.mult, ALU.add))
                    nc.vector.reciprocal(rs, rs).then_inc(S["inverse_ready"].sem, 1)
                    dve.wait_ge(*at("rstd_ready", 1))
                    dve_chain.link(dve, nc.vector.tensor_tensor(o_, o_, rr.unsqueeze(2).to_broadcast([P, 8, P]), ALU.mult))
                    nc.vector.tensor_tensor(flat(o_), flat(o_), flat(dz), ALU.mult).then_inc(S["h_ready"].sem, 1)
                    dve.wait_ge(*at("transposed", 1))
                    for n in range(2):
                        dve_chain.add(nc.vector.tensor_scalar(mixed[:, 4 + 2 * n:6 + 2 * n, :],
                                                              PS[:, 5 + n, :].rearrange("p (h t) -> p h t", h=2),
                                                              col("dn_norm_w_2"), None, ALU.mult))

            for n, k in (("a_ready", 1), ("b_ready", 1), ("c_ready", 1), ("d_ready", 1), ("e_ready", 1), ("f_ready", 1), ("g_ready", 1),
                         ("h_ready", 1), ("i_ready", 1), ("j_ready", 1), ("transposed", 1), ("squares_ready", 8), ("inverse_ready", 1),
                         ("rstd_ready", 1)):
                S[n].passed(k)

            first = ws.first["w_out_2"]
            done, n_plain = tile_signals([None, None, None, first, None, None, None, first + 1])
            with nc.Block() as block:

                @block.sync
                def _(sp):
                    ws.load_until(sp, first + 2)

                @block.tensor
                def _(pe):
                    for m in range(KT):
                        if m % 4 == 0:
                            ws.wait(pe, first + m // 4)
                        w = ws.view(first + m // 4)
                        for k in range(KT):
                            ins = nc.tensor.matmul(PS[:, m, 0:LAT], w[:, k, m % 4 * P:m % 4 * P + P], mixed[:, k, :], start=(k == 0),
                                                   stop=(k == KT - 1))
                        ins.then_inc(done[m][0], 1)

                @block.vector
                def _(dve):
                    for m in range(KT):
                        dve.wait_ge(*done[m])
                        dve_chain.add(nc.vector.scalar_tensor_tensor(XT[:, m, 0:LAT], PS[:, m, 0:LAT], MOD[:, 2 * KT + m, 0:1],
                                                                     XT[:, m, 0:LAT], ALU.mult, ALU.add))

            S["tile_ready"].passed(n_plain)

        hybrid_mixer()

        def routed_experts():
            E, K, SLOT, F = 32, 4, 64, 1024
            MAX_BLOCKS = LAT * K // SLOT + E
            W = BIG[:, 0:12 * 2048].rearrange("p (c n) -> p c n", c=12)
            rest = [12 * 2048]

            def take(buf, at, *shape):
                n = 1
                for x in shape:
                    n *= x
                v = buf[:, at[0]:at[0] + n]
                at[0] += n
                names = "abcd"[:len(shape)]
                return v if len(shape) == 1 else v.rearrange(f"p ({' '.join(names)}) -> p {' '.join(names)}",
                                                             **dict(zip(names, shape)))

            htok = take(BIG, rest, 2, D)
            bias1, bias2 = take(BIG, rest, 2 * F), take(BIG, rest, D)
            w_router = take(BIG, rest, KT, E)
            onehot = take(BIG, rest, 2, K, E)
            table = take(BIG, rest, MAX_BLOCKS, E)
            pw = [0]
            gate_, up, sig, act_ = (take(PW, pw, 512) for _ in range(4))
            xt, at_, ys = take(PW, pw, KT, SLOT), take(PW, pw, 4, 2, SLOT), take(PW, pw, 512)
            eq = take(PW, pw, 2, K, SLOT)
            hbuf, hat = HT[:].rearrange("p k t -> p (k t)"), [0]
            drow, grow, eq2 = (take(hbuf, hat, K, LAT) for _ in range(3))
            pick, spread = take(hbuf, hat, 2, SLOT), take(hbuf, hat, LAT)
            sm = [0]
            lg, sel = take(SM, sm, 2, E), take(SM, sm, 2, E)
            v8, gates, idx = take(SM, sm, 2, 8), take(SM, sm, 2, K), take(SM, sm, 2, K)
            gsum, count, blocks, pend, pos = take(SM, sm, 2), take(SM, sm, E), take(SM, sm, E), take(SM, sm, E), take(SM, sm, 2, E)
            dest, slot, tmp = take(SM, sm, 2, K), take(SM, sm, 1), take(SM, sm, E)
            tabf = take(SM, sm, MAX_BLOCKS + 1)
            tabi = take(SM, sm, MAX_BLOCKS + 1).bitcast(I32)
            i8 = take(SM, sm, 2, 8).bitcast(U32)
            sq = PW[:, 1024:3072].rearrange("p (k t) -> p k t", k=KT)
            rstd, rinv = PW[:, 0:LAT], PW[:, LAT:2 * LAT]
            yt_ = BIG[:, 0:2 * D].rearrange("p (a d) -> p a d", a=2)

            def flat(x):
                return x.rearrange("p a b -> p (a b)")

            def norm_parts(gain_then):
                def scalar(act):
                    for k in range(KT):
                        nc.scalar.activation(sq[:, k, :], XT[:, k, 0:LAT], ACT.Square).then_inc(S["squares_ready"].sem, 1)
                    act.wait_ge(*at("inverse_ready", 1))
                    nc.scalar.activation(rstd, rinv, ACT.Sqrt).then_inc(S["rstd_ready"].sem, 1)

                def tensor(pe):
                    for k in range(KT):
                        pe.wait_ge(*at("squares_ready", k + 1))
                        ins = nc.tensor.matmul(PS[:, 7, 0:LAT], ones, sq[:, k, :], start=(k == 0), stop=(k == KT - 1))
                    ins.then_inc(S["square_sum_ready"].sem, 1)

                def vector(dve):
                    dve.wait_ge(*at("square_sum_ready", 1))
                    dve_chain.link(dve, nc.vector.tensor_scalar(rinv, PS[:, 7, 0:LAT], 1.0 / D, EPS, ALU.mult, ALU.add))
                    nc.vector.reciprocal(rinv, rinv).then_inc(S["inverse_ready"].sem, 1)
                    dve.wait_ge(*at("rstd_ready", 1))

                return scalar, tensor, vector

            def norm_passed():
                S["squares_ready"].passed(KT)
                for n in ("square_sum_ready", "inverse_ready", "rstd_ready"):
                    S[n].passed(1)

            n_scalar, n_tensor, n_vector = norm_parts(None)
            with nc.Block() as block:

                @block.sync
                def _(sp):
                    sp.dma_start(w_router, t["w_router_2"].rearrange("(k p) e -> p k e", p=P)).then_inc(S["tokens_loaded"].sem, 16)

                @block.scalar
                def _(act):
                    n_scalar(act)
                    for k in range(KT):
                        act.wait_ge(*at("scaled_ready", k + 1))
                        h = HT[:, k, 0:LAT]
                        nc.scalar.activation(h, h, ACT.Identity, bias=MOD[:, 3 * KT + k, 0:1], scale=GAIN[:, k, 0:1]).then_inc(
                            S["tile_taken"].sem, 1)
                    for n in range(4):
                        act.wait_ge(*at("transposed", n + 1))
                        nc.scalar.copy(htok[:, n // 2, n % 2 * 512:n % 2 * 512 + 512], PS[:, n, :])

                @block.tensor
                def _(pe):
                    n_tensor(pe)
                    pe.wait_ge(*at("tile_taken", KT))
                    pe.wait_ge(*at("tokens_loaded", 16))
                    for n in range(2):
                        for k in range(KT):
                            ins = nc.tensor.matmul(PS[:, 4, n * E:(n + 1) * E], HT[:, k, n * P:(n + 1) * P], w_router[:, k, :], start=(k == 0),
                                                   stop=(k == KT - 1))
                    ins.then_inc(S["scores_ready"].sem, 1)
                    for n in range(4):
                        for j in range(4):
                            ins = nc.tensor.transpose(PS[:, n, j * P:(j + 1) * P], HT[:, n % 2 * 4 + j, n // 2 * P:(n // 2 + 1) * P], ident)
                        ins.then_inc(S["transposed"].sem, 1)
                    pe.wait_ge(*at("a_ready", 1))
                    nc.tensor.matmul(PS[:, 5, 0:E], ones, sel[:, 0, :], start=True, stop=False)
                    nc.tensor.matmul(PS[:, 5, 0:E], ones, sel[:, 1, :], start=False, stop=True)
                    nc.tensor.matmul(PS[:, 5, E:2 * E], const("before"), sel[:, 0, :], start=True, stop=True)
                    nc.tensor.matmul(PS[:, 5, 2 * E:3 * E], const("before"), sel[:, 1, :], start=True, stop=False)
                    nc.tensor.matmul(PS[:, 5, 2 * E:3 * E], ones, sel[:, 0, :], start=False, stop=True).then_inc(S["b_ready"].sem, 1)

                @block.vector
                def _(dve):
                    def link(ins):
                        dve_chain.link(dve, ins)

                    tt, ts = nc.vector.tensor_tensor, nc.vector.tensor_scalar
                    link(nc.vector.scalar_tensor_tensor(GAIN[:, :, 0], MOD[:, 4 * KT:5 * KT, 0], 1.0, col("norm2_w_2"), ALU.add, ALU.mult))
                    n_vector(dve)
                    for k in range(KT):
                        tt(HT[:, k, 0:LAT], XT[:, k, 0:LAT], rstd, ALU.mult).then_inc(S["scaled_ready"].sem, 1)
                    dve.wait_ge(*at("scores_ready", 1))
                    link(tt(lg, PS[:, 4, 0:2 * E].rearrange("p (n e) -> p n e", n=2),
                            bcast("b_router_2").unsqueeze(1).to_broadcast([P, 2, E]), ALU.add))
                    for n in range(2):
                        link(nc.vector.max(v8[:, n, :], lg[:, n, :]))
                        link(nc.vector.max_index(i8[:, n, :], v8[:, n, :], lg[:, n, :]))
                    link(nc.vector.tensor_copy(idx, i8[:, :, 0:K]))
                    for n in range(2):
                        link(tt(onehot[:, n, :, :], const("expert_row").unsqueeze(1).to_broadcast([P, K, E]),
                                idx[:, n, :].unsqueeze(2).to_broadcast([P, K, E]), ALU.is_equal))
                    for n in range(2):
                        link(nc.vector.tensor_reduce(sel[:, n, :], onehot[:, n, :, :].rearrange("p k e -> p e k"), AX, ALU.add))
                    link(tt(gates, v8[:, :, 0:K], v8[:, :, 0:1].to_broadcast([P, 2, K]), ALU.subtract))
                    ts(slot, const("slot_col"), 0.0, None, ALU.add).then_inc(S["a_ready"].sem, 1)
                    dve.wait_ge(*at("b_ready", 1))
                    link(nc.vector.tensor_copy(count, PS[:, 5, 0:E]))
                    link(ts(blocks, count, 0.0, None, ALU.is_gt))
                    for r in range(1, LAT // SLOT):
                        link(nc.vector.scalar_tensor_tensor(blocks, count, float(SLOT * r), blocks, ALU.is_gt, ALU.add))
                    link(nc.vector.tensor_tensor_scan(pend, ones[:, 0:E], blocks, 0.0, ALU.mult, ALU.add))
                    link(tt(tmp, pend, blocks, ALU.subtract))
                    link(nc.vector.scalar_tensor_tensor(pos, tmp.unsqueeze(1).to_broadcast([P, 2, E]), float(SLOT),
                                                        PS[:, 5, E:3 * E].rearrange("p (n e) -> p n e", n=2), ALU.mult, ALU.add))
                    for n in range(2):
                        link(tt(onehot[:, n, :, :], onehot[:, n, :, :], pos[:, n, :].unsqueeze(1).to_broadcast([P, K, E]), ALU.mult))
                        link(nc.vector.tensor_reduce(dest[:, n, :], onehot[:, n, :, :], AX, ALU.add))
                    link(tt(table, pend.unsqueeze(1).to_broadcast([P, MAX_BLOCKS, E]),
                            const("block_row").unsqueeze(2).to_broadcast([P, MAX_BLOCKS, E]), ALU.is_le))
                    link(nc.vector.tensor_reduce(tabf[:, 0:MAX_BLOCKS], table, AX, ALU.add))
                    link(ts(tabf[:, 0:MAX_BLOCKS], tabf[:, 0:MAX_BLOCKS], float(E - 1), None, ALU.min))
                    link(nc.vector.tensor_copy(tabf[:, MAX_BLOCKS:MAX_BLOCKS + 1], pend[:, E - 1:E]))
                    link(nc.vector.tensor_copy(tabi, tabf))

            norm_passed()
            for n, k in (("tile_taken", KT), ("scaled_ready", KT), ("transposed", 4), ("scores_ready", 1), ("a_ready", 1), ("b_ready", 1),
                         ("tokens_loaded", 16)):
                S[n].passed(k)

            def build_pick(dve):
                for n in range(2):
                    dve_chain.link(dve, nc.vector.tensor_tensor(
                        eq[:, n, :, :], const("slot_row").unsqueeze(1).to_broadcast([P, K, SLOT]),
                        dest[:, n, :].unsqueeze(2).to_broadcast([P, K, SLOT]), ALU.is_equal))
            with nc.Block() as block:

                @block.scalar
                def _(act):
                    act_chain.link(act, nc.scalar.activation(gates, gates, ACT.Exp))
                    nc.scalar.copy(tmp[:, 0:1], slot).then_inc(S["a_ready"].sem, 1)

                @block.vector
                def _(dve):
                    dve.wait_ge(*at("a_ready", 1))
                    dve_chain.link(dve, nc.vector.tensor_reduce(gsum, gates, AX, ALU.add))
                    dve_chain.link(dve, nc.vector.reciprocal(gsum, gsum))
                    nc.vector.tensor_tensor(gates, gates, gsum.unsqueeze(2).to_broadcast([P, 2, K]), ALU.mult).then_inc(S["b_ready"].sem, 1)
                    dve.wait_ge(*at("c_ready", 1))
                    for r, dst in enumerate((drow, grow)):
                        for n in range(2):
                            dve_chain.add(nc.vector.tensor_copy(dst[:, :, n * P:(n + 1) * P],
                                                                PS[:, 4 + 2 * r + n, :].rearrange("p (k t) -> p k t", k=K)))
                    dve_chain.add(nc.vector.memset(act_, 0.0))

                @block.tensor
                def _(pe):
                    pe.wait_ge(*at("b_ready", 1))
                    for r, src in enumerate((dest, gates)):
                        for n in range(2):
                            for k in range(K):
                                ins = nc.tensor.matmul(PS[:, 4 + 2 * r + n, k * P:(k + 1) * P], src[:, n, k:k + 1].to_broadcast([P, P]), ident,
                                                       start=True, stop=True)
                    ins.then_inc(S["c_ready"].sem, 1)

            for n in ("a_ready", "b_ready", "c_ready"):
                S[n].passed(1)

            w1 = t["w1_2"].rearrange("e d f -> (e d) f")
            w2 = t["w2_2"].rearrange("e f d -> (e f) d")
            chunk_landed = [ctx.enter_context(nc.semaphore(f"expert_chunk{c}_landed")) for c in range(12)]
            bias_landed = ctx.enter_context(nc.semaphore("expert_bias_landed"))
            used = ctx.enter_context(nc.semaphore("expert_chunk_used"))
            loop = {n: ctx.enter_context(nc.semaphore(n)) for n in (
                "pick_ready spread_ready gathered gathered_copied hidden_ready gate_clipped sigmoid_ready act_ready act_turned "
                "act_copied y_ready y_copied scattered bias_used".split())}

            with nc.Block() as block:

                def trips(eng):
                    return eng.value_load(tabi[0:1, MAX_BLOCKS:MAX_BLOCKS + 1], min_val=LAT * K // SLOT, max_val=MAX_BLOCKS)

                @block.sync
                def _(sp):
                    def load(i, wait):
                        e = sp.value_load(tabi[0:1, bass.ds(i, 1)], min_val=0, max_val=E - 1)
                        for c in range(12):
                            if wait:
                                sp.wait_ge(used, 12 * i + (c - 11))
                            if c < 8:
                                sp.dma_start(W[:, c, :], w1[bass.ds(e * D + c * P, P), :]).then_inc(chunk_landed[c], 16)
                            else:
                                sp.dma_start(W[:, c, :].rearrange("p (j n) -> p j n", j=2),
                                             w2[bass.ds(e * F + (c - 8) * 2 * P, 2 * P), :].rearrange("(j p) n -> p j n", p=P)).then_inc(
                                    chunk_landed[c], 16)
                            if c == 3:
                                if wait:
                                    sp.wait_ge(loop["bias_used"], i)
                                sp.dma_start(bias1[0:1, :], t["b1_2"][bass.ds(e, 1), :]).then_inc(bias_landed, 16)
                                sp.dma_start(bias2[0:1, :], t["b2_2"][bass.ds(e, 1), :]).then_inc(bias_landed, 16)

                    n = trips(sp)
                    load(0, False)
                    with sp.Fori(1, n) as i:
                        load(i, True)

                @block.tensor
                def _(pe):
                    n = trips(pe)
                    for b in range(4):
                        nc.tensor.matmul(PS[:, b, :], ident, act_, start=True, stop=True)
                    with pe.Fori(0, n) as i:
                        pe.wait_ge(loop["pick_ready"], i + 1)
                        for k in range(KT):
                            for a in range(2):
                                ins = nc.tensor.matmul(PS[:, 6, k * SLOT:(k + 1) * SLOT], htok[:, a, k * P:(k + 1) * P], pick[:, a, :],
                                                       start=(a == 0), stop=(a == 1))
                        ins.then_inc(loop["gathered"], 1)
                        pe.wait_ge(loop["gathered_copied"], i + 1)
                        pe.wait_ge(bias_landed, i * 32 + 32)
                        for half in range(2):
                            for g in range(2):
                                nc.tensor.matmul(PS[64 * g:64 * g + 64, 4 + half, :], ones[0:1, 0:SLOT],
                                                 bias1[0:1, half * F + g * 512:half * F + g * 512 + 512], start=True, stop=False)
                        for c in range(8):
                            pe.wait_ge(chunk_landed[c], i * 16 + 16)
                            for half in range(2):
                                for g in range(2):
                                    ins = nc.tensor.matmul(PS[64 * g:64 * g + 64, 4 + half, :], xt[:, c, :],
                                                           W[:, c, half * F + g * 512:half * F + g * 512 + 512], start=False, stop=(c == 7))
                            ins.then_inc(used, 1)
                        pe.wait_ge(loop["act_ready"], i + 1)
                        for j in range(4):
                            ins = nc.tensor.transpose(PS[:, 6, j * P:(j + 1) * P], act_[:, j * P:(j + 1) * P], ident)
                        ins.then_inc(loop["act_turned"], 1)
                        pe.wait_ge(loop["act_copied"], i + 1)
                        for g in range(2):
                            ins = nc.tensor.matmul(PS[64 * g:64 * g + 64, 7, :], ones[0:1, 0:SLOT], bias2[0:1, g * 512:g * 512 + 512],
                                                   start=True, stop=False)
                        ins.then_inc(loop["bias_used"], 1)
                        for k in range(KT):
                            if k % 2 == 0:
                                pe.wait_ge(chunk_landed[8 + k // 2], i * 16 + 16)
                            for g in range(2):
                                ins = nc.tensor.matmul(PS[64 * g:64 * g + 64, 7, :], at_[:, k % 4, k // 4, :],
                                                       W[:, 8 + k // 2, k % 2 * D + g * 512:k % 2 * D + g * 512 + 512], start=False,
                                                       stop=(k == KT - 1))
                            if k % 2 == 1:
                                ins.then_inc(used, 1)
                        pe.wait_ge(loop["y_copied"], i + 1)
                        pe.wait_ge(loop["spread_ready"], i + 1)
                        for a in range(2):
                            for g in range(2):
                                ins = nc.tensor.matmul(PS[:, 2 * a + g, :], spread[64 * g:64 * g + 64, a * P:(a + 1) * P],
                                                       ys[64 * g:64 * g + 64, :], start=False, stop=False, skip_group_check=True)
                        ins.then_inc(loop["scattered"], 1)

                @block.scalar
                def _(act):
                    n = trips(act)
                    with act.Fori(0, n) as i:
                        act.wait_ge(loop["gathered"], i + 1)
                        nc.scalar.copy(xt, PS[:, 6, :].rearrange("p (k s) -> p k s", k=KT)).then_inc(loop["gathered_copied"], 1)
                        act.wait_ge(loop["gate_clipped"], i + 1)
                        nc.scalar.activation(sig, gate_, ACT.Sigmoid, scale=1.702).then_inc(loop["sigmoid_ready"], 1)
                        act.wait_ge(loop["act_turned"], i + 1)
                        nc.scalar.copy(at_, PS[:, 6, :].rearrange("p (j g s) -> p j g s", j=4, g=2)).then_inc(loop["act_copied"], 1)
                        act.wait_ge(used, i * 12 + 12)
                        nc.scalar.copy(ys, PS[:, 7, :]).then_inc(loop["y_copied"], 1)

                @block.vector
                def _(dve):
                    steps = ctx.enter_context(nc.semaphore("block_steps"))

                    def tables(done):
                        for n in range(2):
                            nc.vector.tensor_tensor(eq[:, n, :, :], const("slot_row").unsqueeze(1).to_broadcast([P, K, SLOT]),
                                                    dest[:, n, :].unsqueeze(2).to_broadcast([P, K, SLOT]), ALU.is_equal).then_inc(steps, 1)
                        dve.wait_ge(steps, done(2))
                        nc.vector.tensor_scalar(dest, dest, -float(SLOT), None, ALU.add).then_inc(steps, 1)
                        nc.vector.tensor_reduce(pick[:, 0, :], eq[:, 0, :, :].rearrange("p k s -> p s k"), AX, ALU.add).then_inc(steps, 1)
                        nc.vector.tensor_reduce(pick[:, 1, :], eq[:, 1, :, :].rearrange("p k s -> p s k"), AX, ALU.add).then_inc(
                            loop["pick_ready"], 1)

                    def gates_of_slots(done):
                        nc.vector.scalar_tensor_tensor(eq2, drow, slot, grow, ALU.is_equal, ALU.mult).then_inc(steps, 1)
                        dve.wait_ge(steps, done(5))
                        nc.vector.tensor_scalar(slot, slot, float(SLOT), None, ALU.add).then_inc(steps, 1)
                        nc.vector.tensor_reduce(spread, eq2.rearrange("p k t -> p t k"), AX, ALU.add).then_inc(loop["spread_ready"], 1)

                    n = trips(dve)
                    tables(lambda x: x)
                    gates_of_slots(lambda x: x)
                    with dve.Fori(0, n) as i:
                        dve.wait_ge(used, i * 12 + 8)
                        nc.vector.tensor_scalar(gate_, PS[:, 4, :], 7.0, None, ALU.min).then_inc(loop["gate_clipped"], 1)
                        nc.vector.tensor_scalar(up, PS[:, 5, :], 7.0, -7.0, ALU.min, ALU.max).then_inc(steps, 1)
                        dve.wait_ge(steps, i * 8 + 7)
                        dve.wait_ge(loop["gate_clipped"], i + 1)
                        nc.vector.scalar_tensor_tensor(up, up, 1.0, gate_, ALU.add, ALU.mult).then_inc(steps, 1)
                        dve.wait_ge(steps, i * 8 + 8)
                        dve.wait_ge(loop["sigmoid_ready"], i + 1)
                        nc.vector.tensor_tensor(act_, up, sig, ALU.mult).then_inc(loop["act_ready"], 1)
                        tables(lambda x: i * 8 + (8 + x))
                        dve.wait_ge(loop["scattered"], i + 1)
                        gates_of_slots(lambda x: i * 8 + (8 + x))


            n_scalar, n_tensor, n_vector = norm_parts(None)
            with nc.Block() as block:

                @block.scalar
                def _(act):
                    for b in range(4):
                        nc.scalar.copy(yt_[:, b // 2, b % 2 * 512:b % 2 * 512 + 512], PS[:, b, :]).then_inc(S["a_ready"].sem, 1)
                    act.wait_ge(*at("b_ready", KT))
                    n_scalar(act)

                @block.tensor
                def _(pe):
                    pe.wait_ge(*at("a_ready", 4))
                    for k in range(KT):
                        for n in range(2):
                            ins = nc.tensor.transpose(PS[:, k // 2, (k % 2 * 2 + n) * P:(k % 2 * 2 + n + 1) * P],
                                                      yt_[:, n, k * P:(k + 1) * P], ident)
                        if k % 2:
                            ins.then_inc(S["transposed"].sem, 1)
                    n_tensor(pe)
                    for n in range(2):
                        for k in range(KT):
                            pe.wait_ge(*at("scaled_ready", k + 1))
                            ins = nc.tensor.transpose(PS[:, 2 * n + k // 4, k % 4 * P:(k % 4 + 1) * P], HT[:, k, n * P:(n + 1) * P], ident)
                            if k % 4 == 3:
                                ins.then_inc(S["c_ready"].sem, 1)

                @block.vector
                def _(dve):
                    for k in range(KT):
                        dve.wait_ge(*at("transposed", k // 2 + 1))
                        nc.vector.scalar_tensor_tensor(XT[:, k, 0:LAT], PS[:, k // 2, k % 2 * LAT:(k % 2 + 1) * LAT],
                                                       MOD[:, 5 * KT + k, 0:1], XT[:, k, 0:LAT], ALU.mult, ALU.add).then_inc(S["b_ready"].sem, 1)
                    n_vector(dve)
                    for k in range(KT):
                        nc.vector.scalar_tensor_tensor(HT[:, k, 0:LAT], XT[:, k, 0:LAT], col("final_norm_w_2")[:, k:k + 1], rstd, ALU.mult,
                                                       ALU.mult).then_inc(S["scaled_ready"].sem, 1)
                    for b in range(4):
                        dve.wait_ge(*at("c_ready", b + 1))
                        nc.vector.tensor_copy(htok[:, b // 2, b % 2 * 512:b % 2 * 512 + 512], PS[:, b, :]).then_inc(S["d_ready"].sem, 1)

                @block.sync
                def _(sp):
                    for n in range(2):
                        sp.wait_ge(*at("d_ready", 2 * n + 2))
                        sp.dma_start(out[0, n * P:(n + 1) * P, :], htok[:, n, :]).then_inc(S["stored"].sem, 16)
                    sp.wait_ge(*at("stored", 32))

        routed_experts()


_OUTS = [((1, 256, 1024), "float32")]


def kernel(**inputs):
    import numpy as _np
    import concourse.bacc as _bacc
    from concourse import mybir as _mybir
    from concourse.bass_utils import run_bass_kernel_spmd as _run

    nc = _bacc.Bacc("TRN2", target_bir_lowering=False, num_devices=1)
    arrays, aps = {}, {}

    def give(name, a):
        arrays[f"in_{name}"] = a
        aps[name] = nc.dram_tensor(f"in_{name}", a.shape, _mybir.dt.from_np(a.dtype), kind="ExternalInput").ap()

    rows = {name: k for r in VECTOR_ROWS for name, k in r}
    for name, a in inputs.items():
        a = _np.ascontiguousarray(a)
        if name in rows:
            a = a.reshape(rows[name], P)
        elif name.endswith("_2") and a.ndim > 1:
            a = a.reshape(a.shape[1:])
        elif name.endswith("_2"):
            a = a.reshape(-1)
        if a.ndim == 2 and a.shape[0] == 1:
            a = a.reshape(-1)
        give(name, a)
    table, at = constant_tables()
    give("consts", table)
    shape, dtype = _OUTS[0]
    out = nc.dram_tensor("out_0", shape, _mybir.dt.from_np(_np.dtype(dtype)), kind="ExternalOutput").ap()
    layers_and_experts_kernel(nc, aps, at, out)
    r = _run(nc, [arrays], core_ids=[0])
    return r.results[0]["out_0"]
```

```python
from contextlib import ExitStack

import concourse.bass as bass
from concourse import mybir

F32 = mybir.dt.float32
I32 = mybir.dt.int32
U32 = mybir.dt.uint32
ALU = mybir.AluOpType
ACT = mybir.ActivationFunctionType
AX = mybir.AxisListType.X

P = 128
D = 1024
KT = D // P
LAT = 256
CTX = 256
TOK = LAT + CTX
TT = TOK // P
CH = 512
SLOTS = 3
EPS = 1e-6
NEG = -1e30


class Signal:

    def __init__(self, sem):
        self.sem, self.base = sem, 0

    def at(self, n):
        return self.base + n

    def passed(self, n):
        self.base += n


class Chain:

    def __init__(self, sem):
        self.sem, self.n = sem, 0

    def add(self, ins):
        self.n += 1
        return ins.then_inc(self.sem, 1)

    def link(self, eng, ins):
        self.add(ins)
        eng.wait_ge(self.sem, self.n)


class WeightStream:

    def __init__(self, slots, landed, used):
        self.slots, self.landed, self.used = slots, landed, used
        self.chunks, self.first, self.issued = [], {}, 0

    def add(self, name, w, cuts=None):
        self.first[name] = len(self.chunks)
        rows, cols = w.shape
        kt = rows // P
        cuts = cuts or [*range(0, cols, CH * KT // kt), cols]
        for a, b in zip(cuts, cuts[1:]):
            self.chunks.append((w[:, a:b].rearrange("(k p) n -> p k n", p=P), kt))

    def view(self, n):
        src, kt = self.chunks[n]
        cols = src.shape[2]
        return self.slots[:, n % SLOTS, 0:kt * cols].rearrange("p (k n) -> p k n", k=kt)

    def load_until(self, sp, end):
        while self.issued < min(len(self.chunks), end + SLOTS):
            n = self.issued
            if n >= SLOTS:
                sp.wait_ge(self.used.sem, n - SLOTS + 1)
            sp.dma_start(self.view(n), self.chunks[n][0]).then_inc(self.landed[n % SLOTS].sem, 16)
            self.issued += 1

    def wait(self, pe, n):
        pe.wait_ge(self.landed[n % SLOTS].sem, 16 * (n // SLOTS + 1))


def constant_tables():
    import numpy as np
    p = np.arange(P)
    t = np.arange(LAT)
    tabs = {}
    tabs["ident"] = np.eye(P)
    tabs["ones"] = np.ones((P, P))
    tabs["streams"] = p[:, None] % 32 == np.arange(3)
    swap = np.zeros((P, P))
    swap[p[1::2], p[0::2]] = -1.0
    swap[p[0::2], p[1::2]] = 1.0
    tabs["swap"] = swap
    inv = np.float32(10000.0) ** (-np.arange(16, dtype=np.float32) / np.float32(16))
    ang = np.concatenate([(t // 64).astype(np.float32)[:, None] * inv, (t % 64).astype(np.float32)[:, None] * inv], -1)
    tabs["cos"] = np.cos(ang).T[(p % 64) // 2]
    tabs["sin"] = np.sin(ang).T[(p % 64) // 2]
    q = np.arange(LAT).reshape(2, P)
    dist = (q[:, :, None] - t[None, None, :]).transpose(1, 0, 2)
    tabs["window"] = np.where(np.abs(dist) <= 128, 0.0, NEG).reshape(P, -1)
    n = ((dist >= 0) & (dist <= 128)).astype(int)
    for w, d in ((512, 4), (2048, 16)):
        n = n + ((dist >= 0) & (dist <= w) & (dist % d == 0))
    tabs["dilated"] = np.where(n > 0, 8.0 * np.log(np.maximum(n, 1)), NEG).reshape(P, -1)
    r, c = p[:, None], p[None, :]
    tabs["upto"] = r <= c
    tabs["from"] = r >= c
    tabs["before"] = r < c
    tabs["causal"] = np.where(c <= r, 0.0, NEG)
    tabs["anticausal"] = np.where(c >= r, 0.0, NEG)
    tabs["strict"] = c < r
    for b in (1, 2, 4, 8, 16, 32, 64):
        low = ((r // b) % 2 == 1) & (c // b == r // b - 1)
        tabs[f"low{b}T"] = low.T
        if b == 1:
            tabs["low1"] = low
    tabs["slot_row"] = np.broadcast_to(np.arange(64), (P, 64))
    tabs["slot_col"] = (p % 64)[:, None]
    tabs["expert_row"] = np.broadcast_to(np.arange(32), (P, 32))
    tabs["block_row"] = np.broadcast_to(np.arange(48), (P, 48))
    at, n = {}, 0
    for k, v in tabs.items():
        at[k] = (n, n + v.shape[1])
        n += v.shape[1]
    return np.concatenate([np.asarray(v, np.float32) for v in tabs.values()], 1), at


VECTOR_ROWS = [
    [("l0_b_ada", 24), ("l1_b_ada", 24), ("l2_b_ada", 24), ("l3_b_ada", 24), ("c", 8), ("c_ctx", 8), ("c_2", 8),
     ("l0_g_pre", 8)],
    [("b_ada_2", 48), ("l1_g_pre", 8), ("l2_g_pre", 8), ("l3_g_pre", 8), ("l0_g_post", 8), ("l1_g_post", 8),
     ("l2_g_post", 8), ("l3_g_post", 8), ("norm1_w_2", 8), ("norm2_w_2", 8)],
    [("l2_conv", 40), ("conv_w_2", 48), ("final_norm_w_2", 8), ("l2_g_head", 8), ("l1_g_qa", 2), ("l1_g_kva", 1),
     ("dn_norm_w_2", 1)],
]
BROADCAST = [("l0_sink", 16), ("l3_sink", 16), ("l2_b_gate", 16), ("A_log_2", 4), ("dt_bias_2", 4), ("b_router_2", 32)]


def layers_and_experts_kernel(nc, t, consts_at, out):
    ctx = ExitStack()
    with ctx:
        def sb(name, shape, dt=F32):
            return ctx.enter_context(nc.sbuf_tensor(name, shape, dt))

        def sem(name):
            return Signal(ctx.enter_context(nc.semaphore(name)))

        XT = sb("XT", [P, KT, TOK])
        HT = sb("HT", [P, KT, TOK])
        RING_N = SLOTS * KT * CH
        ARENA_N = 22656
        BIG = sb("BIG", [P, RING_N + ARENA_N])
        PW = sb("PW", [P, 4096])
        n_const = consts_at["block_row"][1]
        CONST = sb("CONST", [P, n_const])
        COLS = sb("COLS", [P, 3, P])
        BC = sb("BC", [P, sum(n for _, n in BROADCAST)])
        COND = sb("COND", [P, KT, 32])
        MOD = sb("MOD", [P, 5, 48])
        GAIN = sb("GAIN", [P, KT, 2])
        GATE = sb("GATE", [P, KT, 2])
        RSTD, RINV = PW[:, 0:TOK], PW[:, TOK:2 * TOK]
        SM = sb("SM", [P, 720])
        ST = sb("ST", [P, 64])

        ring = BIG[:, 0:RING_N].rearrange("p (s n) -> p s n", s=SLOTS)

        class Arena:

            def __init__(self, at=0):
                self.at = at

            def take(self, *shape):
                n = 1
                for s in shape:
                    n *= s
                v = BIG[:, RING_N + self.at:RING_N + self.at + n]
                self.at += n
                assert self.at <= ARENA_N, self.at
                names = "abcd"[:len(shape)]
                return v.rearrange(f"p ({' '.join(names)}) -> p {' '.join(names)}",
                                   **dict(zip(names, shape))) if len(shape) > 1 else v

        SQ = BIG[:, RING_N + KT * TOK:RING_N + 2 * KT * TOK].rearrange("p (k t) -> p k t", k=KT)
        PS = ctx.enter_context(nc.psum_tensor("PS", [P, 8, 512], F32))

        def const(name):
            a, b = consts_at[name]
            return CONST[:, a:b]

        ident, ones = const("ident"), const("ones")
        window = const("window").rearrange("p (t k) -> p t k", t=2)
        dilated = const("dilated").rearrange("p (t k) -> p t k", t=2)

        col_at = {}
        for r, rows in enumerate(VECTOR_ROWS):
            n = 0
            for name, k in rows:
                col_at[name] = (r, n, n + k)
                n += k

        def col(name):
            r, a, b = col_at[name]
            return COLS[:, r, a:b]

        bc_at, n = {}, 0
        for name, k in BROADCAST:
            bc_at[name] = (n, n + k)
            n += k

        def bcast(name):
            return BC[:, bc_at[name][0]:bc_at[name][1]]

        landed = [sem(f"chunk_landed{i}") for i in range(SLOTS)]
        chunk_used = sem("chunk_used")
        ws = WeightStream(ring, landed, chunk_used)
        ADA = ["l0_w_ada", "l1_w_ada", "l2_w_ada", "l3_w_ada", "w_ada_2"]
        BEHIND = {0: [1, 2, 3], 3: [4]}
        ws.add(ADA[0], t[ADA[0]])
        for i in range(4):
            ws.add(f"l{i}_w_in", t[f"l{i}_w_in"], [0, 448, 960, 1472] if i == 1 else None)
            if i == 1:
                ws.add("l1_w_uq", t["l1_w_uq"])
                ws.add("l1_w_ukv", t["l1_w_ukv"])
            for l in BEHIND.get(i, []):
                ws.add(ADA[l], t[ADA[l]])
            ws.add(f"l{i}_w_out", t[f"l{i}_w_out"])
        ws.add("w_in_2", t["w_in_2"])
        ws.add("w_out_2", t["w_out_2"])
        ws.first["end"] = len(ws.chunks)

        dve_chain = Chain(ctx.enter_context(nc.semaphore("dve_chain")))
        act_chain = Chain(ctx.enter_context(nc.semaphore("act_chain")))
        pool_chain = Chain(ctx.enter_context(nc.semaphore("pool_chain")))
        names = ("vectors_loaded tokens_loaded consts_loaded late_loaded transposed transposed_taken cond_ready squares_ready "
                 "square_sum_ready inverse_ready rstd_ready scaled_ready tile_ready tile_taken rope_mixed rope_taken "
                 "scores_ready max_ready exp_ready scores_used probs_ready probs_turned turned_copied heads_ready "
                 "heads_taken stored rows_copied columns_ready columns_taken h_ready normed_ready residual_ready a_ready b_ready c_ready d_ready e_ready f_ready g_ready i_ready j_ready k_ready").split()
        S = {n: sem(n) for n in names}

        def at(name, n):
            return S[name].sem, S[name].at(n)

        def tile_signals(ends):
            said, n = [], 0
            for chunk in ends:
                n += chunk is None
                said.append(at("tile_ready", n) if chunk is None else (chunk_used.sem, chunk + 1))
            return said, n

        class Modulations:

            def __init__(self, layers, rows, bank):
                self.job = [(l, c) for l in layers for c in range((6 if l == 4 else 3) * D // CH)]
                self.rows, self.bank = rows, bank
                self.end = ws.first[ADA[layers[-1]]] + (12 if layers[-1] == 4 else 6)

            def chunk(self, j):
                l, c = self.job[j]
                return ws.first[ADA[l]] + c

            def turned(self, j):
                n = 1 if self.job[j][0] == 4 else 2
                return PS[:, self.bank, 0:4 * n].rearrange("p (m s) -> p m s", s=n)

            def multiply(self, pe, j):
                ws.wait(pe, self.chunk(j))
                if j >= 1:
                    pe.wait_ge(*at("columns_taken", j))
                w = ws.view(self.chunk(j))
                for k in range(KT):
                    g = k % 4 * 32
                    ins = nc.tensor.matmul(PS[g:g + 32, self.bank, :], COND[:, k, :], w[:, k, :], start=(k < 4), stop=(k >= 4),
                                           tile_position=(0, g))
                ins.then_inc(chunk_used.sem, 1)

            def copy(self, act, j):
                act.wait_ge(chunk_used.sem, self.chunk(j) + 1)
                if j >= 1:
                    act.wait_ge(*at("columns_ready", j))
                nc.scalar.copy(self.rows, PS[:, self.bank, :]).then_inc(S["rows_copied"].sem, 1)

            def turn(self, pe, j):
                pe.wait_ge(*at("rows_copied", j + 1))
                o = self.turned(j)
                which = const("streams")[:, 2:3] if self.job[j][0] == 4 else const("streams")[:, 0:2]
                for m in range(4):
                    ins = nc.tensor.matmul(o[:, m, :], self.rows[:, m * P:(m + 1) * P], which, start=True, stop=True)
                ins.then_inc(S["columns_ready"].sem, 1)

            def take(self, dve, j):
                l, c = self.job[j]
                dve.wait_ge(*at("columns_ready", j + 1))
                bias = col("b_ada_2" if l == 4 else f"l{l}_b_ada")[:, 4 * c:4 * c + 4]
                nc.vector.tensor_tensor(modulation(l)[:, 4 * c:4 * c + 4, :], self.turned(j),
                                        bias.unsqueeze(2).to_broadcast([P, 4, 1 if l == 4 else 2]), ALU.add).then_inc(
                    S["columns_taken"].sem, 1)

            def passed(self):
                for n in ("rows_copied", "columns_ready", "columns_taken"):
                    S[n].passed(len(self.job))

        def modulation(l):
            return MOD[:, l, :].rearrange("p (m s) -> p m s", s=1 if l == 4 else 2)

        def square(act, k, tok):
            nc.scalar.activation(SQ[:, k, 0:tok], XT[:, k, 0:tok], ACT.Square).then_inc(S["squares_ready"].sem, 1)

        def sum_squares(pe, tok, bank):
            for k in range(KT):
                pe.wait_ge(*at("squares_ready", k + 1))
                ins = nc.tensor.matmul(PS[:, bank, 0:tok], ones, SQ[:, k, 0:tok], start=(k == 0), stop=(k == KT - 1))
            ins.then_inc(S["square_sum_ready"].sem, 1)

        def inverse(dve, sums, tok, nth=0):
            dve.wait_ge(*at("square_sum_ready", nth + 1))
            dve_chain.link(dve, nc.vector.tensor_scalar(RINV[:, 0:tok], sums, 1.0 / D, EPS, ALU.mult, ALU.add))
            nc.vector.reciprocal(RINV[:, 0:tok], RINV[:, 0:tok]).then_inc(S["inverse_ready"].sem, 1)

        def root(act, tok, nth=0):
            act.wait_ge(*at("inverse_ready", nth + 1))
            nc.scalar.activation(RSTD[:, 0:tok], RINV[:, 0:tok], ACT.Sqrt).then_inc(S["rstd_ready"].sem, 1)

        def norm_vector(dve, l, g_pre, g_post, tok):
            n = 1 if l == 4 else 2
            m = modulation(l)
            if g_post:
                dve_chain.add(nc.vector.tensor_tensor(GATE[:, :, 0:n], m[:, 2 * KT:3 * KT, :], col(g_post).unsqueeze(2).to_broadcast([P, KT, n]),
                                                      ALU.mult))
            dve_chain.link(dve, nc.vector.scalar_tensor_tensor(GAIN[:, :, 0:n], m[:, KT:2 * KT, :], 1.0,
                                                               col(g_pre).unsqueeze(2).to_broadcast([P, KT, n]), ALU.add, ALU.mult))
            for k in range(KT):
                nc.vector.tensor_tensor(HT[:, k, 0:tok], XT[:, k, 0:tok], RSTD[:, 0:tok], ALU.mult).then_inc(S["normed_ready"].sem, 1)

        def norm_scalar(act, l, tok):
            for k in range(KT):
                act.wait_ge(*at("normed_ready", k + 1))
                for s in range(tok // LAT):
                    x = HT[:, k, s * LAT:(s + 1) * LAT]
                    ins = nc.scalar.activation(x, x, ACT.Identity, bias=modulation(l)[:, k, s:s + 1], scale=GAIN[:, k, s:s + 1])
                ins.then_inc(S["h_ready"].sem, 1)

        def norm_passed():
            S["normed_ready"].passed(KT)
            S["h_ready"].passed(KT)

        arena = Arena()
        tok0, _, vec_rows = arena.take(TT, D), arena.take(KT * TOK), arena.take(3, P)
        early = consts_at["streams"][1]
        mods = Modulations([0], arena.take(CH), 7)
        with nc.Block() as block:

            @block.sync
            def _(sp):
                sp.dma_start(vec_rows, t["vector_rows"].rearrange("r p n -> p r n")).then_inc(S["vectors_loaded"].sem, 16)
                sp.dma_start(CONST[:, 0:early], t["consts"][:, 0:early]).then_inc(S["consts_loaded"].sem, 16)
                sp.dma_start(tok0[:, 0:2, :], t["x"].rearrange("o (a p) d -> p (o a) d", p=P)).then_inc(S["tokens_loaded"].sem, 16)
                sp.dma_start(tok0[:, 2:4, :], t["ctx"].rearrange("o (a p) d -> p (o a) d", p=P)).then_inc(S["tokens_loaded"].sem, 16)
                ws.load_until(sp, 0)
                sp.dma_start(BC[:], t["broadcast_row"].partition_broadcast(P)).then_inc(S["late_loaded"].sem, 16)
                sp.dma_start(CONST[:, early:], t["consts"][:, early:]).then_inc(S["late_loaded"].sem, 16)
                ws.load_until(sp, mods.end)

            @block.gpsimd
            def _(pool):
                nc.gpsimd.memset(COND[:], 0.0).then_inc(S["a_ready"].sem, 1)

            @block.tensor
            def _(pe):
                pe.wait_ge(*at("consts_loaded", 16))
                pe.wait_ge(*at("vectors_loaded", 16))
                for r in range(3):
                    ins = nc.tensor.transpose(PS[:, 0, r * P:(r + 1) * P], vec_rows[:, r, :], ident)
                ins.then_inc(S["c_ready"].sem, 1)
                pe.wait_ge(*at("tokens_loaded", 32))
                for k in range(KT):
                    if k == 7:
                        pe.wait_ge(*at("transposed_taken", 1))
                    for a in range(TT):
                        ins = nc.tensor.transpose(PS[:, k + 1 if k < 7 else 1, a * P:(a + 1) * P], tok0[:, a, k * P:(k + 1) * P], ident)
                    ins.then_inc(S["transposed"].sem, 1)
                pe.wait_ge(*at("cond_ready", 1))
                pe.wait_ge(*at("transposed_taken", KT))
                for j in range(len(mods.job)):
                    mods.multiply(pe, j)
                    if j == 2:
                        sum_squares(pe, TOK, 2)
                    mods.turn(pe, j)
                pe.wait_ge(*at("late_loaded", 32))

            @block.scalar
            def _(act):
                act.wait_ge(*at("c_ready", 1))
                act_chain.link(act, nc.scalar.copy(COLS[:], PS[:, 0, 0:3 * P].rearrange("p (r n) -> p r n", r=3)))
                act.wait_ge(*at("a_ready", 1))
                for n, name in enumerate(("c", "c_ctx", "c_2")):
                    ins = nc.scalar.activation(COND[:, :, n], col(name), ACT.Silu)
                ins.then_inc(S["cond_ready"].sem, 1)
                for k in range(KT):
                    act.wait_ge(*at("transposed", k + 1))
                    nc.scalar.copy(XT[:, k, :], PS[:, k + 1 if k < 7 else 1, :]).then_inc(S["transposed_taken"].sem, 1)
                for j in range(3):
                    mods.copy(act, j)
                    if j == 0:
                        for k in range(KT):
                            act.wait_ge(*at("transposed_taken", k + 1))
                            square(act, k, TOK)
                root(act, TOK)
                for j in range(3, len(mods.job)):
                    mods.copy(act, j)

            @block.vector
            def _(dve):
                dve.wait_ge(*at("cond_ready", 1))
                for j in range(len(mods.job)):
                    if j == 2:
                        inverse(dve, PS[:, 2, 0:TOK], TOK)
                    mods.take(dve, j)

        S["consts_loaded"].passed(16)
        S["tokens_loaded"].passed(32)
        S["vectors_loaded"].passed(16)
        S["late_loaded"].passed(32)
        S["transposed"].passed(KT)
        S["transposed_taken"].passed(KT)
        for n in ("cond_ready", "a_ready", "c_ready", "square_sum_ready", "inverse_ready", "rstd_ready"):
            S[n].passed(1)
        S["squares_ready"].passed(KT)
        mods.passed()

        def project_out(w_out, ot, tok):
            first = ws.first[w_out]
            yt = Arena().take(KT, TOK)
            done, n_plain = tile_signals([None, None, None, first, None, None, None, first + 1])
            with nc.Block() as block:

                @block.sync
                def _(sp):
                    ws.load_until(sp, first + 2)

                def sum_tile(pe, m):
                    pe.wait_ge(*at("squares_ready", m + 1))
                    return nc.tensor.matmul(PS[:, 4, 0:tok], ones, SQ[:, m, 0:tok], start=(m == 0), stop=(m == KT - 1))

                @block.tensor
                def _(pe):
                    for m in range(KT):
                        if m % 4 == 0:
                            ws.wait(pe, first + m // 4)
                        w = ws.view(first + m // 4)
                        if m >= 4:
                            pe.wait_ge(*at("tile_taken", m - 3))
                        for k in range(KT):
                            ins = nc.tensor.matmul(PS[:, m % 4, 0:tok], w[:, k, (m % 4) * P:(m % 4 + 1) * P], ot[:, k, 0:tok],
                                                   start=(k == 0), stop=(k == KT - 1))
                        ins.then_inc(done[m][0], 1)
                        if m >= 1:
                            sum_tile(pe, m - 1)
                    sum_tile(pe, KT - 1).then_inc(S["square_sum_ready"].sem, 1)
                    for k in range(KT):
                        pe.wait_ge(*at("squares_ready", KT + k + 1))
                        ins = nc.tensor.matmul(PS[:, 5, 0:tok], ones, SQ[:, k, 0:tok], start=(k == 0), stop=(k == KT - 1))
                    ins.then_inc(S["square_sum_ready"].sem, 1)

                @block.scalar
                def _(act):
                    for m in range(KT):
                        act.wait_ge(*done[m])
                        nc.scalar.activation(SQ[:, m, 0:tok], PS[:, m % 4, 0:tok], ACT.Square).then_inc(S["squares_ready"].sem, 1)
                        for s in range(tok // LAT):
                            sl = slice(s * LAT, (s + 1) * LAT)
                            ins = nc.scalar.activation(yt[:, m, sl], PS[:, m % 4, sl], ACT.Copy, scale=GATE[:, m, s:s + 1])
                        ins.then_inc(S["tile_taken"].sem, 1)
                    root(act, tok)
                    for k in range(KT):
                        act.wait_ge(*at("residual_ready", k + 1))
                        square(act, k, tok)
                    root(act, tok, 1)

                @block.vector
                def _(dve):
                    inverse(dve, PS[:, 4, 0:tok], tok)
                    dve.wait_ge(*at("rstd_ready", 1))
                    dve.wait_ge(*at("tile_taken", KT))
                    for k in range(KT):
                        dve_chain.link(dve, nc.vector.tensor_tensor(yt[:, k, 0:tok], yt[:, k, 0:tok], RSTD[:, 0:tok], ALU.mult))
                        nc.vector.tensor_tensor(XT[:, k, 0:tok], yt[:, k, 0:tok], XT[:, k, 0:tok], ALU.add).then_inc(
                            S["residual_ready"].sem, 1)
                    inverse(dve, PS[:, 5, 0:tok], tok, 1)

            S["tile_ready"].passed(n_plain)
            S["tile_taken"].passed(KT)
            S["residual_ready"].passed(KT)
            S["squares_ready"].passed(2 * KT)
            for n in ("square_sum_ready", "inverse_ready", "rstd_ready"):
                S[n].passed(2)

        def rope_mix(x, n):
            nc.tensor.matmul(PS[:, 4 + n % 2, 0:LAT], const("swap"), x[:, 0:LAT], start=True, stop=True).then_inc(
                S["rope_mixed"].sem, 1)

        def rope_turn(dve, x, n, tmp):
            dve.wait_ge(*at("rope_mixed", n + 1))
            nc.vector.tensor_tensor(tmp, PS[:, 4 + n % 2, 0:LAT], const("sin"), ALU.mult).then_inc(S["rope_taken"].sem, 1)
            dve_chain.link(dve, nc.vector.tensor_tensor(x[:, 0:LAT], x[:, 0:LAT], const("cos"), ALU.mult))
            dve.wait_ge(*at("rope_taken", n + 1))
            dve_chain.link(dve, nc.vector.tensor_tensor(x[:, 0:LAT], x[:, 0:LAT], tmp, ALU.add))

        def attention(units, scale, score, value, mask_of, sink, gate, together=True, mods=None):
            probs = PW[:, 0:2048].rearrange("p (b h k) -> p b h k", b=2, h=2)
            turned = PW[:, 2048:4096].rearrange("p (b h k) -> p b h k", b=2, h=2)
            mx = ST[:, 0:8].rearrange("p (b s) -> p b s", b=2)
            nm = ST[:, 8:16].rearrange("p (b s) -> p b s", b=2)
            den = ST[:, 16:24].rearrange("p (b s) -> p b s", b=2)
            es = ST[:, 24:32].rearrange("p (b s) -> p b s", b=2)
            rd = ST[:, 32:40].rearrange("p (b s) -> p b s", b=2)
            N = len(units)

            def cols(u):
                return u[2][0] * P, (u[2][-1] + 1) * P

            def heads_at(i):
                return PS[:, 6 if mods else 6 + i % 2, :]

            def beside(i, late):
                n, x = 2 * len(mods.job) if mods else 0, 2 * i + late
                return [(y % 2, y // 2) for y in range(x * n // (2 * N), (x + 1) * n // (2 * N))]

            with nc.Block() as block:

                @block.sync
                def _(sp):
                    ws.load_until(sp, mods.end if mods else ws.done)

                @block.tensor
                def _(pe):
                    def scores(i):
                        a, b = cols(units[i])
                        if i >= 2:
                            pe.wait_ge(*at("scores_used", 2 * (i - 1)))
                        for h in range(2):
                            ins = score(h, units[i], slice(a, b), PS[:, 2 * (i % 2) + h, a:b])
                        ins.then_inc(S["scores_ready"].sem, 1)

                    def turn(i):
                        for h in range(2):
                            pe.wait_ge(*at("probs_ready", 2 * i + h + 1))
                            if i >= 1:
                                pe.wait_ge(*at("turned_copied", 2 * i + h - 1))
                            for j, kt in enumerate(units[i][2]):
                                ins = nc.tensor.transpose(PS[:, 4 + h, j * P:(j + 1) * P],
                                                          probs[:, i % 2, h, kt * P:(kt + 1) * P], ident)
                            ins.then_inc(S["probs_turned"].sem, 1)

                    def mix(i):
                        pe.wait_ge(*at("turned_copied", 2 * i + 2))
                        if i >= (1 if mods else 2):
                            pe.wait_ge(*at("heads_taken", i if mods else i - 1))
                        kts = units[i][2]
                        order = [(j, h) for j in range(len(kts)) for h in range(2)]
                        if not together:
                            order.sort(key=lambda x: x[1])
                        for j, h in order:
                            lhs, place = value(units[i], h, kts[j])
                            ins = nc.tensor.matmul(place(heads_at(i)), lhs, turned[:, i % 2, h, j * P:(j + 1) * P],
                                                   start=(j == 0), stop=(j == len(kts) - 1))
                        ins.then_inc(S["heads_ready"].sem, 1)

                    def modulate(i, late):
                        for half, j in beside(i, late):
                            (mods.turn if half else mods.multiply)(pe, j)

                    scores(0)
                    scores(1)
                    for i in range(N):
                        if i + 2 < N:
                            scores(i + 2)
                        modulate(i, 0)
                        turn(i)
                        if i >= 1:
                            mix(i - 1)
                        modulate(i, 1)
                    mix(N - 1)

                @block.scalar
                def _(act):
                    def exps(i):
                        a, b = cols(units[i])
                        act.wait_ge(*at("max_ready", i + 1))
                        if i >= 2:
                            act.wait_ge(*at("probs_turned", 2 * (i - 1)))
                        for h in range(2):
                            nc.scalar.activation(probs[:, i % 2, h, a:b], PS[:, 2 * (i % 2) + h, a:b], ACT.Exp,
                                                 bias=nm[:, i % 2, h:h + 1], scale=scale,
                                                 accum_out=den[:, i % 2, h:h + 1]).then_inc(S["scores_used"].sem, 1)
                            if sink is not None:
                                head = 2 * units[i][0] + h
                                nc.scalar.activation(es[:, i % 2, h:h + 1], sink[:, head:head + 1], ACT.Exp,
                                                     bias=nm[:, i % 2, h:h + 1]).then_inc(S["exp_ready"].sem, 1)

                    def copies(i):
                        n = len(units[i][2]) * P
                        if i >= 2:
                            act.wait_ge(*at("heads_ready", i - 1))
                        for h in range(2):
                            act.wait_ge(*at("probs_turned", 2 * i + h + 1))
                            nc.scalar.copy(turned[:, i % 2, h, 0:n], PS[:, 4 + h, 0:n]).then_inc(S["turned_copied"].sem, 1)

                    def modulate(i, late):
                        for half, j in beside(i, late):
                            if not half:
                                mods.copy(act, j)

                    exps(0)
                    for i in range(N):
                        if i + 1 < N:
                            exps(i + 1)
                        modulate(i, 0)
                        copies(i)
                        modulate(i, 1)

                @block.vector
                def _(dve):
                    def maxima(i):
                        a, b = cols(units[i])
                        s = PS[:, 2 * (i % 2):2 * (i % 2) + 2, :]
                        dve.wait_ge(*at("scores_ready", i + 1))
                        mask = mask_of(units[i])
                        if mask is not None:
                            w = mask.shape[1]
                            dve_chain.link(dve, nc.vector.tensor_tensor(s[:, :, a:a + w], s[:, :, a:a + w],
                                                                        mask.unsqueeze(1).to_broadcast([P, 2, w]), ALU.add))
                        dve_chain.link(dve, nc.vector.tensor_reduce(mx[:, i % 2, 0:2], s[:, :, a:b], AX, ALU.max))
                        if sink is not None:
                            h = 2 * units[i][0]
                            dve_chain.link(dve, nc.vector.scalar_tensor_tensor(
                                mx[:, i % 2, 2:4], mx[:, i % 2, 0:2], scale, sink[:, h:h + 2], ALU.mult, ALU.max))
                            nc.vector.tensor_scalar(nm[:, i % 2, 0:2], mx[:, i % 2, 2:4], -1.0, None, ALU.mult).then_inc(
                                S["max_ready"].sem, 1)
                        else:
                            nc.vector.tensor_scalar(nm[:, i % 2, 0:2], mx[:, i % 2, 0:2], -scale, None, ALU.mult).then_inc(
                                S["max_ready"].sem, 1)

                    def normalise(i):
                        a, b = cols(units[i])
                        dve.wait_ge(*at("scores_used", 2 * i + 2))
                        if sink is not None:
                            dve.wait_ge(*at("exp_ready", 2 * i + 2))
                            dve_chain.link(dve, nc.vector.tensor_tensor(den[:, i % 2, 0:2], den[:, i % 2, 0:2], es[:, i % 2, 0:2],
                                                                        ALU.add))
                        dve_chain.link(dve, nc.vector.reciprocal(rd[:, i % 2, 0:2], den[:, i % 2, 0:2]))
                        for h in range(2):
                            pr = probs[:, i % 2, h, a:b]
                            nc.vector.tensor_scalar(pr, pr, rd[:, i % 2, h:h + 1], None, ALU.mult).then_inc(
                                S["probs_ready"].sem, 1)

                    def gates(i):
                        dve.wait_ge(*at("heads_ready", i + 1))
                        o, z, src = gate(units[i], heads_at(i))
                        if z is None:
                            nc.vector.tensor_copy(o, src).then_inc(S["heads_taken"].sem, 1)
                        else:
                            nc.vector.tensor_tensor(o, src, z, ALU.mult).then_inc(S["heads_taken"].sem, 1)

                    def modulate(i, late):
                        for half, j in beside(i, late):
                            if half:
                                mods.take(dve, j)

                    maxima(0)
                    maxima(1)
                    for i in range(N):
                        normalise(i)
                        modulate(i, 0)
                        if i + 2 < N:
                            maxima(i + 2)
                        if i >= 1:
                            gates(i - 1)
                        modulate(i, 1)
                    gates(N - 1)

            for n, k in (("scores_ready", 1), ("max_ready", 1), ("scores_used", 2), ("exp_ready", 2 if sink is not None else 0),
                         ("probs_ready", 2), ("probs_turned", 2), ("turned_copied", 2), ("heads_ready", 1), ("heads_taken", 1)):
                S[n].passed(k * N)
            if mods:
                mods.passed()

        def window_layer(i, need_ctx):
            w_in = f"l{i}_w_in"
            first = ws.first[w_in]
            a = Arena()
            qt, kt_, zt = a.take(8, TOK), a.take(2, TOK), a.take(8, TOK)
            keys = a.take(4, TOK)
            v = a.take(TT, 256)
            tmp = a.take(LAT)
            mods = Modulations(BEHIND[i], a.take(CH), 7)
            qtok = TOK if need_ctx else LAT
            tiles = [("q", m, m // 4, m % 4 * P, qtok) for m in range(8)]
            tiles += [("k", m, 2, m * P, TOK) for m in range(2)] + [("v", m, 2, 256, 256) for m in range(TT)]
            tiles += [("z", m, 3 + m // 4, m % 4 * P, qtok) for m in range(8)]
            last = [j + 1 == len(tiles) or tiles[j + 1][2] != x[2] for j, x in enumerate(tiles)]
            done, n_plain = tile_signals([first + x[2] if e else None for x, e in zip(tiles, last)])
            roped = [j for j, x in enumerate(tiles) if x[0] in "qk"]
            with nc.Block() as block:

                @block.sync
                def _(sp):
                    ws.load_until(sp, first + 5)

                @block.tensor
                def _(pe):
                    def rope(n):
                        kind, m, _, _, _ = tiles[roped[n]]
                        pe.wait_ge(*at("tile_taken", roped[n] + 1))
                        if n >= 2:
                            pe.wait_ge(*at("rope_taken", n - 1))
                        rope_mix((qt if kind == "q" else kt_)[:, m, :], n)

                    for j, (kind, m, c, x, tok) in enumerate(tiles):
                        if j == 0 or tiles[j - 1][2] != c:
                            ws.wait(pe, first + c)
                        w = ws.view(first + c)
                        if j >= 4:
                            pe.wait_ge(*at("tile_taken", j - 3))
                        for k in range(KT):
                            if j == 0:
                                pe.wait_ge(*at("h_ready", k + 1))
                            if kind == "v":
                                ops = HT[:, k, m * P:(m + 1) * P], w[:, k, x:x + tok]
                            else:
                                ops = w[:, k, x:x + P], HT[:, k, 0:tok]
                            ins = nc.tensor.matmul(PS[:, j % 4, 0:tok], *ops, start=(k == 0), stop=(k == KT - 1))
                        ins.then_inc(done[j][0], 1)
                        if 1 <= j <= len(roped):
                            rope(j - 1)

                @block.scalar
                def _(act):
                    norm_scalar(act, i, TOK)
                    for j, (kind, m, c, x, tok) in enumerate(tiles):
                        act.wait_ge(*done[j])
                        dst = {"q": qt, "k": kt_, "v": v, "z": zt}[kind][:, m, 0:tok]
                        nc.scalar.activation(dst, PS[:, j % 4, 0:tok], ACT.Silu if kind == "z" else ACT.Copy).then_inc(
                            S["tile_taken"].sem, 1)

                @block.vector
                def _(dve):
                    norm_vector(dve, i, f"l{i}_g_pre", f"l{i}_g_post", TOK)
                    for n, j in enumerate(roped):
                        kind, m, _, _, _ = tiles[j]
                        dve.wait_ge(*at("tile_taken", j + 1))
                        rope_turn(dve, (qt if kind == "q" else kt_)[:, m, :], n, tmp)
                    for h in range(4):
                        src = kt_[64 * (h % 2):64 * (h % 2) + 64, h // 2, :]
                        dve_chain.add(nc.vector.tensor_copy(keys[0:64, h, :], src))
                        dve_chain.add(nc.vector.tensor_copy(keys[64:128, h, :], src))

            norm_passed()
            S["tile_ready"].passed(n_plain)
            S["tile_taken"].passed(len(tiles))
            S["rope_mixed"].passed(len(roped))
            S["rope_taken"].passed(len(roped))
            ws.done = first + 5

            def score(h, u, k, out):
                half = slice(64 * h, 64 * h + 64)
                return nc.tensor.matmul(out, qt[half, u[0], u[1] * P:(u[1] + 1) * P], keys[half, u[0] // 2, k], start=True, stop=True)

            def value(u, h, kt):
                j = u[0] // 2
                return v[:, kt, j * 64:(j + 1) * 64], lambda bank: bank[64 * h:64 * h + 64, 0:P]

            def gate(u, bank):
                q = slice(u[1] * P, (u[1] + 1) * P)
                return HT[:, u[0], q], zt[:, u[0], q], bank[:, 0:P]

            units = [(m, q, [0, 1, 2, 3]) for m in range(8) for q in range(2)]
            if need_ctx:
                units += [(m, q, [2, 3]) for m in range(8) for q in (2, 3)]
            attention(units, 64 ** -0.5, score, value, lambda u: window[:, u[1], :] if u[1] < 2 else None,
                      bcast(f"l{i}_sink"), gate, mods=mods)
            project_out(f"l{i}_w_out", HT, qtok)

        window_layer(0, True)

        def latent_layer():
            heads, nope, rot, rank_q, rank_kv = 8, 128, 64, 256, 128
            a = Arena()
            qn, qr, kn = a.take(heads, TOK), a.take(heads // 2, TOK), a.take(heads, TOK)
            kpe, v, zt = a.take(TOK), a.take(TT, heads * P), a.take(8, TOK)
            lowrank, sq, tmp = a.take(3, TOK), a.take(3, TOK), a.take(LAT)
            rstd = [PW[:, 0:TOK], PW[:, TOK:2 * TOK]]
            rinv = [PW[:, 2 * TOK:3 * TOK], PW[:, 3 * TOK:4 * TOK]]
            c_in, c_uq, c_ukv = ws.first["l1_w_in"], ws.first["l1_w_uq"], ws.first["l1_w_ukv"]
            tiles = [("low", m, c_in) for m in range(3)] + [("kpe", 0, c_in)]
            tiles += [("z", m, c_in + 1 + m // 4) for m in range(8)]
            tiles += [("qr", m, c_uq) for m in range(4)] + [("qn", m, c_uq) for m in range(8)]
            tiles += [("kn", m, c_ukv) for m in range(8)] + [("v", m, c_ukv) for m in range(8)]
            last = [j + 1 == len(tiles) or tiles[j + 1][2] != x[2] for j, x in enumerate(tiles)]
            done, n_plain = tile_signals([x[2] if e else None for x, e in zip(tiles, last)])
            roped = [j for j, x in enumerate(tiles) if x[0] in ("kpe", "qr")]
            with nc.Block() as block:

                @block.sync
                def _(sp):
                    ws.load_until(sp, c_ukv + 1)

                @block.tensor
                def _(pe):
                    def rope(n):
                        kind, m, _ = tiles[roped[n]]
                        pe.wait_ge(*at("tile_taken", roped[n] + 1))
                        if n >= 2:
                            pe.wait_ge(*at("rope_taken", n - 1))
                        rope_mix(kpe if kind == "kpe" else qr[:, m, :], n)

                    def square_sums():
                        for n, (x, y) in enumerate(((0, 2), (2, 3))):
                            for m in range(x, y):
                                pe.wait_ge(*at("squares_ready", m + 1))
                                ins = nc.tensor.matmul(PS[:, 6 + n, :], ones, sq[:, m, :], start=(m == x), stop=(m == y - 1))
                            ins.then_inc(S["square_sum_ready"].sem, 1)

                    for j, (kind, m, c) in enumerate(tiles):
                        if j == 0 or tiles[j - 1][2] != c:
                            ws.wait(pe, c)
                        w = ws.view(c)
                        if j >= 4:
                            pe.wait_ge(*at("tile_taken", j - 3))
                        o = PS[:, j % 4, :]
                        if kind in ("low", "z", "kpe"):
                            for k in range(KT):
                                if j == 0:
                                    pe.wait_ge(*at("h_ready", k + 1))
                                x = 384 if kind == "kpe" else m % 4 * P if kind == "z" else m * P
                                n = rot if kind == "kpe" else P
                                for half in range(P // n):
                                    ins = nc.tensor.matmul(o[n * half:n * half + n, :], w[:, k, x:x + n], HT[:, k, :],
                                                           start=(k == 0), stop=(k == KT - 1))
                        elif kind == "qr":
                            pe.wait_ge(*at("scaled_ready", 2))
                            for h in range(2):
                                x = (2 * m + h) * (nope + rot) + nope
                                for k in range(2):
                                    ins = nc.tensor.matmul(o[64 * h:64 * h + 64, :], w[:, k, x:x + rot], lowrank[:, k, :],
                                                           start=(k == 0), stop=(k == 1))
                        elif kind == "qn":
                            x = m * (nope + rot)
                            for k in range(2):
                                ins = nc.tensor.matmul(o, w[:, k, x:x + nope], lowrank[:, k, :], start=(k == 0), stop=(k == 1))
                        elif kind == "kn":
                            pe.wait_ge(*at("scaled_ready", 3))
                            ins = nc.tensor.matmul(o, w[:, 0, m * 256:m * 256 + 128], lowrank[:, 2, :], start=True, stop=True)
                        else:
                            wv = w[:, 0, :].rearrange("p (h n) -> p h n", n=256)[:, m % 2 * 4:m % 2 * 4 + 4, 128:256]
                            ins = nc.tensor.matmul(o, lowrank[:, 2, m // 2 * P:(m // 2 + 1) * P], wv, start=True, stop=True)
                        ins.then_inc(done[j][0], 1)
                        if kind == "z" and m == 0:
                            square_sums()
                            rope(0)
                        if j - 1 in roped[1:]:
                            rope(roped.index(j - 1))

                @block.scalar
                def _(act):
                    norm_scalar(act, 1, TOK)
                    for j, (kind, m, c) in enumerate(tiles):
                        act.wait_ge(*done[j])
                        o = PS[:, j % 4, :]
                        dst = {"low": lowrank[:, m % 3, :], "kpe": kpe, "z": zt[:, m, :], "qr": qr[:, m % 4, :], "qn": qn[:, m, :],
                               "kn": kn[:, m, :], "v": v[:, m // 2, m % 2 * 512:m % 2 * 512 + 512]}[kind]
                        if kind == "low":
                            nc.scalar.activation(sq[:, m, :], o, ACT.Square).then_inc(S["squares_ready"].sem, 1)
                        if kind == "z" and m == 2:
                            for n in range(2):
                                act.wait_ge(*at("inverse_ready", n + 1))
                                nc.scalar.activation(rstd[n], rinv[n], ACT.Sqrt).then_inc(S["rstd_ready"].sem, 1)
                        nc.scalar.activation(dst, o, ACT.Silu if kind == "z" else ACT.Copy).then_inc(S["tile_taken"].sem, 1)

                @block.vector
                def _(dve):
                    norm_vector(dve, 1, "l1_g_pre", "l1_g_post", TOK)
                    for n, width in enumerate((rank_q, rank_kv)):
                        dve.wait_ge(*at("square_sum_ready", n + 1))
                        dve_chain.link(dve, nc.vector.tensor_scalar(rinv[n], PS[:, 6 + n, :], 1.0 / width, EPS, ALU.mult, ALU.add))
                        nc.vector.reciprocal(rinv[n], rinv[n]).then_inc(S["inverse_ready"].sem, 1)
                    dve.wait_ge(*at("tile_taken", 3))
                    for m in range(3):
                        dve.wait_ge(*at("rstd_ready", 1 + m // 2))
                        g = col("l1_g_kva") if m == 2 else col("l1_g_qa")[:, m:m + 1]
                        nc.vector.scalar_tensor_tensor(lowrank[:, m, :], lowrank[:, m, :], g, rstd[m // 2], ALU.mult,
                                                       ALU.mult).then_inc(S["scaled_ready"].sem, 1)
                    for n, j in enumerate(roped):
                        kind, m, _ = tiles[j]
                        dve.wait_ge(*at("tile_taken", j + 1))
                        rope_turn(dve, kpe if kind == "kpe" else qr[:, m, :], n, tmp)

            norm_passed()
            S["tile_ready"].passed(n_plain)
            S["tile_taken"].passed(len(tiles))
            for n, k in (("squares_ready", 3), ("square_sum_ready", 2), ("inverse_ready", 2), ("rstd_ready", 2),
                         ("scaled_ready", 3), ("rope_mixed", len(roped)), ("rope_taken", len(roped))):
                S[n].passed(k)
            ws.done = c_ukv + 1

            def score(h, u, k, out):
                head, q, half = 2 * u[0] + h, slice(u[1] * P, (u[1] + 1) * P), slice(64 * h, 64 * h + 64)
                nc.tensor.matmul(out, qn[:, head, q], kn[:, head, k], start=True, stop=False)
                return nc.tensor.matmul(out, qr[half, u[0], q], kpe[half, k], start=False, stop=True)

            def value(u, h, kt):
                head = 2 * u[0] + h
                return v[:, kt, head * P:(head + 1) * P], lambda bank: bank[:, h * P:(h + 1) * P]

            def gate(u, bank):
                q, pair = slice(u[1] * P, (u[1] + 1) * P), slice(2 * u[0], 2 * u[0] + 2)
                return HT[:, pair, q], zt[:, pair, q], bank[:, 0:2 * P].rearrange("p (h q) -> p h q", h=2)

            units = [(m, q, [0, 1, 2, 3]) for m in range(4) for q in range(2)]
            units += [(m, q, [2, 3]) for m in range(4) for q in (2, 3)]
            attention(units, (nope + rot) ** -0.5, score, value, lambda u: None, None, gate, together=False)
            project_out("l1_w_out", HT, TOK)

        latent_layer()

        def exact_log1p(dve, r, e, x, y):
            dve_chain.link(dve, nc.vector.tensor_scalar(x, e, 1.0 / 3, -0.5, ALU.mult, ALU.add))
            dve_chain.link(dve, nc.vector.tensor_tensor(x, x, e, ALU.mult))
            dve_chain.link(dve, nc.vector.scalar_tensor_tensor(x, x, 1.0, e, ALU.add, ALU.mult))
            dve_chain.link(dve, nc.vector.tensor_tensor(x, x, r, ALU.subtract))
            dve_chain.link(dve, nc.vector.tensor_scalar(y, e, 1e-3, None, ALU.is_lt))
            dve_chain.link(dve, nc.vector.tensor_tensor(x, x, y, ALU.mult))
            dve_chain.link(dve, nc.vector.tensor_tensor(r, r, x, ALU.add))

        def memory_layer():
            H, DV = 4, 256
            order = [[2, 3, 0, 1], [3, 2, 1, 0]]
            a = Arena()
            va = a.take(TT, H, DV + 1)
            qk = a.take(8, TOK)
            ktok = a.take(TT, H, P)
            og = a.take(TT, D)
            raw_at = a.at
            raw = a.take(8, 2, LAT + 4)
            logd = a.take(32, P)
            a2 = Arena(raw_at)
            zt = a2.take(8, TOK)
            hs = HT[:].rearrange("p k t -> p (k t)").rearrange("p (a h v) -> p a h v", a=TT, h=H)
            c_in = ws.first["l2_w_in"]
            taps = col("l2_conv").rearrange("p (j k) -> p j k", j=5)

            small = [0]

            def take(*shape):
                n = 1
                for x in shape:
                    n *= x
                v = SM[:, small[0]:small[0] + n]
                small[0] += n
                names = "abcd"[:len(shape)]
                return v if len(shape) == 1 else v.rearrange(f"p ({' '.join(names)}) -> p {' '.join(names)}",
                                                             **dict(zip(names, shape)))

            gates = take(2, 4, 2, 4)
            logf, ex, t1, t2 = take(2, 4, 4), take(2, 4, 4), take(2, 4, 4), take(2, 4, 4)
            small_cum = small[0]
            cum, tot, u, rowmax, umax = (take(2, 4, 4) for _ in range(5))
            mloc, am, mst = take(2, 4, 4), take(2, 4, 4), take(2, 5, 4)
            keep, gain, at_, nmt, emt, eend, rs, rden = (take(2, 4, 4) for _ in range(8))

            def flat(x):
                return x.rearrange("p a b c -> p (a b c)")

            tiles = [("qk", m, m // 4) for m in range(8)] + [("v", (c, m), 2 + c) for c in range(2) for m in range(TT)]
            tiles += [("o", (c, m), 4 + c) for c in range(2) for m in range(TT)]
            tiles += [("z", m, 6 + m // 4) for m in range(8)] + [("g", 0, 8)]
            last = [j + 1 == len(tiles) or tiles[j + 1][2] != x[2] for j, x in enumerate(tiles)]
            done, n_plain = tile_signals([c_in + x[2] if e else None for x, e in zip(tiles, last)])
            with nc.Block() as block:

                @block.sync
                def _(sp):
                    ws.load_until(sp, c_in + 9)

                @block.gpsimd
                def _(pool):
                    nc.gpsimd.memset(raw[:, :, :, 0:2], 0.0)
                    nc.gpsimd.memset(raw[:, :, :, LAT + 2:LAT + 4], 0.0).then_inc(S["a_ready"].sem, 1)
                    nc.gpsimd.memset(va[:, :, :, DV:DV + 1], 1.0)

                @block.tensor
                def _(pe):
                    for j, (kind, m, c) in enumerate(tiles):
                        if j == 0 or tiles[j - 1][2] != c:
                            ws.wait(pe, c_in + c)
                        w = ws.view(c_in + c)
                        if j >= 4:
                            pe.wait_ge(*at("tile_taken", j - 3))
                        o = PS[:, j % 4, :]
                        for k in range(KT):
                            if j == 0:
                                pe.wait_ge(*at("h_ready", k + 1))
                            if kind in ("qk", "z"):
                                ins = nc.tensor.matmul(o, w[:, k, m % 4 * P:m % 4 * P + P], HT[:, k, :], start=(k == 0), stop=(k == KT - 1))
                            elif kind != "g":
                                ins = nc.tensor.matmul(o, HT[:, k, m[1] * P:(m[1] + 1) * P], w[:, k, :], start=(k == 0), stop=(k == KT - 1))
                        if kind == "g":
                            for n in range(TT):
                                for k in range(KT):
                                    ins = nc.tensor.matmul(o[:, n * 16:n * 16 + 16], HT[:, k, n * P:(n + 1) * P], w[:, k, :],
                                                           start=(k == 0), stop=(k == KT - 1))
                        ins.then_inc(done[j][0], 1)
                        if kind == "o" and m == (1, 3):
                            pe.wait_ge(*at("c_ready", 4))
                            for n in range(TT):
                                for h in range(H):
                                    ins = nc.tensor.transpose(PS[:, 4 + n, h * P:(h + 1) * P], qk[:, 4 + h, n * P:(n + 1) * P], ident)
                                ins.then_inc(S["transposed"].sem, 1)

                @block.scalar
                def _(act):
                    norm_scalar(act, 2, TOK)
                    for j, (kind, m, c) in enumerate(tiles):
                        act.wait_ge(*done[j])
                        o = PS[:, j % 4, :]
                        if kind == "g":
                            break
                        if kind == "qk":
                            dst, o = raw[:, m, :, 2:LAT + 2], o.rearrange("p (s t) -> p s t", s=2)
                        elif kind == "v":
                            dst, o = va[:, m[1], 2 * m[0]:2 * m[0] + 2, 0:DV], o.rearrange("p (h v) -> p h v", h=2)
                        elif kind == "o":
                            dst = og[:, m[1], m[0] * CH:(m[0] + 1) * CH]
                        else:
                            dst = zt[:, m, :]
                            if m == 0:
                                act.wait_ge(*at("b_ready", 8))
                        f = {"o": ACT.Sigmoid, "z": ACT.Silu}.get(kind, ACT.Copy)
                        nc.scalar.activation(dst, o, f).then_inc(S["tile_taken"].sem, 1)
                        if kind == "v" and m[0] == 1:
                            for n in range(2 * m[1], 2 * m[1] + 2):
                                act.wait_ge(*at("b_ready", n + 1))
                                nc.scalar.activation(qk[:, n, :], qk[:, n, :], ACT.Silu).then_inc(S["squares_ready"].sem, 1)
                        if kind == "z" and m < TT:
                            act.wait_ge(*at("transposed", m + 1))
                            nc.scalar.copy(ktok[:, m, :, :], PS[:, 4 + m, :].rearrange("p (h d) -> p h d", h=H)).then_inc(
                                S["d_ready"].sem, 1)

                @block.vector
                def _(dve):
                    norm_vector(dve, 2, "l2_g_pre", "l2_g_post", TOK)
                    dve.wait_ge(*at("a_ready", 1))
                    for m in range(8):
                        dve.wait_ge(*at("tile_taken", m + 1))
                        o = qk[:, m, :].rearrange("p (s t) -> p s t", s=2)
                        dve_chain.link(dve, nc.vector.tensor_scalar(o, raw[:, m, :, 0:LAT], taps[:, 0, m:m + 1], None, ALU.mult))
                        for j in range(1, 5):
                            ins = nc.vector.scalar_tensor_tensor(o, raw[:, m, :, j:j + LAT], taps[:, j, m:m + 1], o, ALU.mult, ALU.add)
                            if j < 4:
                                dve_chain.link(dve, ins)
                        ins.then_inc(S["b_ready"].sem, 1)
                    for m in range(4, 8):
                        dve.wait_ge(*at("squares_ready", m + 1))
                        nc.vector.tensor_scalar(qk[:, m, :], qk[:, m, :], P ** -0.5, None, ALU.mult).then_inc(S["c_ready"].sem, 1)
                    dve.wait_ge(*done[-1])
                    for d in range(2):
                        for j in range(4):
                            n = order[d][j]
                            x = PS[:, (len(tiles) - 1) % 4, n * 16 + d * 8:n * 16 + d * 8 + 8]
                            dve_chain.add(nc.vector.tensor_tensor(gates[:, d, j, :, :], x.rearrange("p (a h) -> p a h", a=2),
                                                                  bcast("l2_b_gate")[:, d * 8:d * 8 + 8].rearrange("p (a h) -> p a h", a=2), ALU.add))

            norm_passed()
            S["tile_ready"].passed(n_plain)
            S["tile_taken"].passed(len(tiles) - 1)
            for n, k in (("a_ready", 1), ("b_ready", 8), ("c_ready", 4), ("d_ready", TT), ("squares_ready", 8), ("transposed", TT)):
                S[n].passed(k)
            ws.done = c_in + 9

            with nc.Block() as block:

                @block.tensor
                def _(pe):
                    pe.wait_ge(*at("b_ready", 1))
                    f = flat(logf)
                    nc.tensor.matmul(PS[:, 0, 0:16], const("upto"), f[:, 0:16], start=True, stop=True)
                    nc.tensor.matmul(PS[:, 0, 16:32], const("from"), f[:, 16:32], start=True, stop=True)
                    nc.tensor.matmul(PS[:, 0, 32:64], ones, f, start=True, stop=True).then_inc(S["c_ready"].sem, 1)
                    pe.wait_ge(*at("d_ready", 1))
                    for g in range(8):
                        if g >= 2:
                            pe.wait_ge(*at("f_ready", g - 1))
                        for i in range(4):
                            c = 4 * g + i
                            ins = nc.tensor.matmul(PS[:, 1 + g % 2, i * P:(i + 1) * P], flat(u)[:, c:c + 1].to_broadcast([P, P]), ident,
                                                   start=True, stop=True)
                        ins.then_inc(S["e_ready"].sem, 1)

                @block.scalar
                def _(act):
                    act.wait_ge(*at("a_ready", 1))
                    act_chain.add(nc.scalar.activation(flat(ex), flat(t1), ACT.Exp, scale=-1.0))
                    act.wait_ge(act_chain.sem, act_chain.n)
                    nc.scalar.activation(flat(logf), flat(ex), ACT.Ln, bias=1.0).then_inc(S["g_ready"].sem, 1)
                    act.wait_ge(*at("k_ready", 1))
                    nc.scalar.activation(flat(keep), flat(am), ACT.Exp)
                    nc.scalar.activation(flat(gain), flat(mloc), ACT.Exp)
                    nc.scalar.activation(flat(at_), flat(t1), ACT.Exp)
                    nc.scalar.activation(flat(emt), flat(nmt), ACT.Exp)
                    nc.scalar.activation(flat(eend), flat(t2), ACT.Exp)

                @block.vector
                def _(dve):
                    ig, fg = gates[:, :, :, 0, :], gates[:, :, :, 1, :]
                    tt, ts = nc.vector.tensor_tensor, nc.vector.tensor_scalar
                    nc.vector.scalar_tensor_tensor(t1, fg, -1.0, fg, ALU.mult, ALU.max).then_inc(S["a_ready"].sem, 1)
                    dve.wait_ge(*at("g_ready", 1))
                    exact_log1p(dve, flat(logf), flat(ex), flat(t2), flat(u))
                    nc.vector.scalar_tensor_tensor(logf, fg, 0.0, logf, ALU.min, ALU.subtract).then_inc(S["b_ready"].sem, 1)
                    dve.wait_ge(*at("c_ready", 1))
                    dve_chain.link(dve, nc.vector.tensor_copy(SM[:, small_cum:small_cum + 64], PS[:, 0, 0:64]))
                    tt(u, ig, cum, ALU.subtract).then_inc(S["d_ready"].sem, 1)
                    for g in range(8):
                        dve.wait_ge(*at("e_ready", g + 1))
                        bank = PS[:, 1 + g % 2, :].rearrange("p (c s) -> p c s", c=4)
                        mask = const("causal" if g < 4 else "anticausal")
                        for i in range(4):
                            c = 4 * g + i
                            ins = dve_chain.add(nc.vector.scalar_tensor_tensor(logd[:, c, :], bank[:, i, :], flat(cum)[:, c:c + 1], mask,
                                                                               ALU.add, ALU.add))
                        nc.vector.tensor_reduce(flat(umax)[:, 4 * g:4 * g + 4], bank, AX, ALU.max).then_inc(S["f_ready"].sem, 1)
                        dve.wait_ge(dve_chain.sem, dve_chain.n)
                        dve_chain.add(nc.vector.tensor_reduce(flat(rowmax)[:, 4 * g:4 * g + 4], logd[:, 4 * g:4 * g + 4, :], AX, ALU.max))
                    dve.wait_ge(*at("f_ready", 8))
                    dve.wait_ge(dve_chain.sem, dve_chain.n)
                    dve_chain.add(tt(mloc, tot, umax, ALU.add))
                    dve_chain.link(dve, nc.vector.memset(mst[:, :, 0, :], NEG))
                    for j in range(4):
                        dve_chain.link(dve, tt(am[:, :, j, :], tot[:, :, j, :], mst[:, :, j, :], ALU.add))
                        dve_chain.link(dve, tt(mst[:, :, j + 1, :], am[:, :, j, :], mloc[:, :, j, :], ALU.max))
                    dve_chain.add(tt(am, am, mst[:, :, 1:5, :], ALU.subtract))
                    dve_chain.add(tt(mloc, mloc, mst[:, :, 1:5, :], ALU.subtract))
                    dve_chain.link(dve, tt(t1, cum, mst[:, :, 0:4, :], ALU.add))
                    dve_chain.link(dve, tt(nmt, t1, rowmax, ALU.max))
                    dve_chain.link(dve, tt(t1, t1, nmt, ALU.subtract))
                    dve_chain.add(ts(nmt, nmt, -1.0, None, ALU.mult))
                    tt(t2, u, umax, ALU.subtract).then_inc(S["k_ready"].sem, 1)

            for n, k in (("a_ready", 1), ("b_ready", 1), ("c_ready", 1), ("d_ready", 1), ("e_ready", 8), ("f_ready", 8),
                         ("g_ready", 1), ("k_ready", 1)):
                S[n].passed(k)

            pw = [0]

            def take_pw(*shape):
                n = 1
                for x in shape:
                    n *= x
                v = PW[:, pw[0]:pw[0] + n]
                pw[0] += n
                names = "abcd"[:len(shape)]
                return v.rearrange(f"p ({' '.join(names)}) -> p {' '.join(names)}", **dict(zip(names, shape)))

            state = take_pw(8, DV + 1)
            dm, sq, sqt, ke = (take_pw(2, P) for _ in range(4))
            inter = take_pw(2, DV + 1)
            added = take_pw(1, DV + 1)[:, 0, :]
            units = [(j, d, h) for j in range(4) for d in range(2) for h in range(H)]
            N = len(units)
            first_at = {}
            for i, (j, d, h) in enumerate(units):
                first_at.setdefault((order[d][j], h), i)
            n_state = sum(j < 3 for j, _, _ in units)
            n_inter = sum(j > 0 for j, _, _ in units)

            def upto(i, which):
                return sum((u[0] < 3) if which == "state" else (u[0] > 0) for u in units[:i])

            with nc.Block() as block:

                @block.tensor
                def _(pe):
                    def logits(i):
                        j, d, h = units[i]
                        t_ = slice(order[d][j] * P, (order[d][j] + 1) * P)
                        if i >= 2:
                            pe.wait_ge(*at("a_ready", i - 1))
                        nc.tensor.matmul(PS[:, i % 2, 0:P], qk[:, h, t_], qk[:, 4 + h, t_], start=True, stop=True).then_inc(
                            S["scores_ready"].sem, 1)

                    def mix(i):
                        j, d, h = units[i]
                        pe.wait_ge(*at("turned_copied", i + 1))
                        if i >= 1:
                            pe.wait_ge(*at("heads_taken", i))
                        nc.tensor.matmul(PS[:, 7, 0:DV], sqt[:, i % 2, :], va[:, order[d][j], h, 0:DV], start=True, stop=True).then_inc(
                            S["heads_ready"].sem, 1)

                    logits(0)
                    for i, (j, d, h) in enumerate(units):
                        n = order[d][j]
                        if i + 1 < N:
                            logits(i + 1)
                        if j < 3:
                            s = upto(i, "state")
                            pe.wait_ge(*at("b_ready", s + 1))
                            if s >= 2:
                                pe.wait_ge(*at("c_ready", s - 1))
                            nc.tensor.matmul(PS[:, 2 + s % 2, 0:DV + 1], ke[:, s % 2, :], va[:, n, h, :], start=True, stop=True).then_inc(
                                S["d_ready"].sem, 1)
                        if j > 0:
                            s = upto(i, "inter")
                            pe.wait_ge(*at("e_ready", s + 1))
                            if s >= 2:
                                pe.wait_ge(*at("f_ready", s - 1))
                            nc.tensor.matmul(PS[:, 4 + s % 2, 0:DV + 1], qk[:, h, n * P:(n + 1) * P], state[:, 4 * d + h, :],
                                             start=True, stop=True).then_inc(S["g_ready"].sem, 1)
                        pe.wait_ge(*at("a_ready", i + 1))
                        if i >= 1:
                            pe.wait_ge(*at("turned_copied", i))
                        nc.tensor.transpose(PS[:, 6, 0:P], sq[:, i % 2, :], ident).then_inc(S["probs_turned"].sem, 1)
                        if i >= 1:
                            mix(i - 1)
                    mix(N - 1)

                @block.scalar
                def _(act):
                    def decays(i):
                        j, d, h = units[i]
                        c = 16 * d + 4 * j + h
                        if i >= 2:
                            act.wait_ge(*at("a_ready", i - 1))
                        nc.scalar.activation(dm[:, i % 2, :], logd[:, c, :], ACT.Exp, bias=flat(nmt)[:, c:c + 1]).then_inc(
                            S["exp_ready"].sem, 1)

                    decays(0)
                    for i, (j, d, h) in enumerate(units):
                        c = 16 * d + 4 * j + h
                        if i + 1 < N:
                            decays(i + 1)
                        if j < 3:
                            s = upto(i, "state")
                            act.wait_ge(*at("d_ready", s + 1))
                            if s >= 1:
                                act.wait_ge(*at("e_ready", s))
                            nc.scalar.activation(added, PS[:, 2 + s % 2, 0:DV + 1], ACT.Copy, scale=flat(gain)[:, c:c + 1]).then_inc(
                                S["c_ready"].sem, 1)
                        if j > 0:
                            s = upto(i, "inter")
                            act.wait_ge(*at("g_ready", s + 1))
                            if i >= 2:
                                act.wait_ge(*at("heads_taken", i - 1))
                            nc.scalar.activation(inter[:, i % 2, :], PS[:, 4 + s % 2, 0:DV + 1], ACT.Copy,
                                                 scale=flat(at_)[:, c:c + 1]).then_inc(S["f_ready"].sem, 1)
                        act.wait_ge(*at("probs_turned", i + 1))
                        if i >= 2:
                            act.wait_ge(*at("heads_ready", i - 1))
                        nc.scalar.copy(sqt[:, i % 2, :], PS[:, 6, 0:P]).then_inc(S["turned_copied"].sem, 1)

                @block.vector
                def _(dve):
                    def end_keys(i):
                        j, d, h = units[i]
                        if j < 3:
                            s = upto(i, "state")
                            if s >= 2:
                                dve.wait_ge(*at("d_ready", s - 1))
                            c = 16 * d + 4 * j + h
                            nc.vector.tensor_scalar(ke[:, s % 2, :], ktok[:, order[d][j], h, :], flat(eend)[:, c:c + 1], None,
                                                    ALU.mult).then_inc(S["b_ready"].sem, 1)

                    def combine(i):
                        j, d, h = units[i]
                        c, n = 16 * d + 4 * j + h, order[d][j]
                        r, w = flat(rden)[:, c:c + 1], hs[:, n, h, :]
                        dve.wait_ge(*at("heads_ready", i + 1))
                        src = PS[:, 7, 0:DV]
                        fresh = first_at[(n, h)] == i
                        if j > 0:
                            x = inter[:, i % 2, 0:DV]
                            dve_chain.link(dve, nc.vector.tensor_tensor(x, src, x, ALU.add))
                            src = x
                        if fresh:
                            nc.vector.tensor_scalar(w, src, r, None, ALU.mult).then_inc(S["heads_taken"].sem, 1)
                        else:
                            nc.vector.scalar_tensor_tensor(w, src, r, w, ALU.mult, ALU.add).then_inc(S["heads_taken"].sem, 1)

                    end_keys(0)
                    for i, (j, d, h) in enumerate(units):
                        c = 16 * d + 4 * j + h
                        if i + 1 < N:
                            end_keys(i + 1)
                        dve.wait_ge(*at("scores_ready", i + 1))
                        dve.wait_ge(*at("exp_ready", i + 1))
                        if i >= 2:
                            dve.wait_ge(*at("probs_turned", i - 1))
                        nc.vector.scalar_tensor_tensor(sq[:, i % 2, :], PS[:, i % 2, 0:P], 1.0, dm[:, i % 2, :], ALU.mult, ALU.mult,
                                                       accum_out=flat(rs)[:, c:c + 1]).then_inc(S["a_ready"].sem, 1)
                        if j < 3:
                            s = upto(i, "state")
                            st = state[:, 4 * d + h, :]
                            dve.wait_ge(*at("c_ready", s + 1))
                            if j == 0:
                                nc.vector.tensor_copy(st, added).then_inc(S["e_ready"].sem, 1)
                            else:
                                dve.wait_ge(*at("g_ready", upto(i, "inter") + 1))
                                nc.vector.scalar_tensor_tensor(st, st, flat(keep)[:, c:c + 1], added, ALU.mult, ALU.add).then_inc(
                                    S["e_ready"].sem, 1)
                        dve.wait_ge(*at("a_ready", i + 1))
                        r, den = flat(rden)[:, c:c + 1], flat(rs)[:, c:c + 1]
                        x = flat(t2)[:, c:c + 1]
                        if j > 0:
                            dve.wait_ge(*at("f_ready", upto(i, "inter") + 1))
                            dve_chain.link(dve, nc.vector.tensor_tensor(den, inter[:, i % 2, DV:DV + 1], den, ALU.add))
                        dve_chain.link(dve, nc.vector.scalar_tensor_tensor(x, den, -1.0, flat(emt)[:, c:c + 1], ALU.mult, ALU.max))
                        dve_chain.link(dve, nc.vector.tensor_tensor(r, den, x, ALU.max))
                        dve_chain.link(dve, nc.vector.reciprocal(r, r))
                        if i >= 1:
                            combine(i - 1)
                    combine(N - 1)

            for n, k in (("scores_ready", N), ("exp_ready", N), ("a_ready", N), ("b_ready", n_state), ("c_ready", n_state),
                         ("d_ready", n_state), ("e_ready", n_state), ("f_ready", n_inter), ("g_ready", n_inter),
                         ("probs_turned", N), ("turned_copied", N), ("heads_ready", N), ("heads_taken", N)):
                S[n].passed(k)

            ot = logd.rearrange("p c s -> p (c s)").rearrange("p (k t) -> p k t", k=KT)
            ss, rr = SM[:, 0:16], SM[:, 16:32]
            with nc.Block() as block:

                @block.sync
                def _(sp):
                    ws.load_until(sp, ws.done)

                @block.vector
                def _(dve):
                    for n in range(TT):
                        x = hs[:, n, :, :].rearrange("p h v -> p (h v)")
                        nc.vector.tensor_tensor(x, x, og[:, n, :], ALU.mult).then_inc(S["a_ready"].sem, 1)
                    dve.wait_ge(*at("squares_ready", 16))
                    dve_chain.link(dve, nc.vector.tensor_scalar(ss, ss, 1.0 / DV, EPS, ALU.mult, ALU.add))
                    nc.vector.reciprocal(ss, ss).then_inc(S["inverse_ready"].sem, 1)
                    dve.wait_ge(*at("rstd_ready", 1))
                    for n in range(TT):
                        for h in range(H):
                            c = n * H + h
                            ins = nc.vector.tensor_scalar(hs[:, n, h, :], hs[:, n, h, :], rr[:, c:c + 1], None, ALU.mult)
                            ins.then_inc(S["b_ready"].sem, 1)
                    for k in range(KT):
                        dve.wait_ge(*at("transposed", k + 1))
                        nc.vector.scalar_tensor_tensor(ot[:, k, :], PS[:, k % 4, :], col("l2_g_head")[:, k:k + 1], zt[:, k, :],
                                                       ALU.mult, ALU.mult).then_inc(S["transposed_taken"].sem, 1)

                @block.scalar
                def _(act):
                    for n in range(TT):
                        act.wait_ge(*at("a_ready", n + 1))
                        for h in range(H):
                            c = n * H + h
                            nc.scalar.activation(PW[:, 0:DV], hs[:, n, h, :], ACT.Square, accum_out=ss[:, c:c + 1]).then_inc(
                                S["squares_ready"].sem, 1)
                            act.wait_ge(*at("squares_ready", c + 1))
                    act.wait_ge(*at("inverse_ready", 1))
                    nc.scalar.activation(rr, ss, ACT.Sqrt).then_inc(S["rstd_ready"].sem, 1)

                @block.tensor
                def _(pe):
                    pe.wait_ge(*at("b_ready", 16))
                    for k in range(KT):
                        if k >= 4:
                            pe.wait_ge(*at("transposed_taken", k - 3))
                        for n in range(TT):
                            ins = nc.tensor.transpose(PS[:, k % 4, n * P:(n + 1) * P], hs[:, n, k // 2, k % 2 * P:k % 2 * P + P], ident)
                        ins.then_inc(S["transposed"].sem, 1)

            for n, k in (("a_ready", TT), ("b_ready", 16), ("squares_ready", 16), ("inverse_ready", 1), ("rstd_ready", 1),
                         ("transposed", KT), ("transposed_taken", KT)):
                S[n].passed(k)
            project_out("l2_w_out", ot, TOK)

        memory_layer()
        window_layer(3, False)

        def hybrid_mixer():
            H = 4
            a = Arena()
            aq, ak, av = a.take(4, LAT), a.take(4, LAT), a.take(2, CH)
            raw = a.take(12, LAT + 3)
            qkv = a.take(12, LAT)
            dz = a.take(2, CH)
            mixed = HT[:, :, 0:LAT]
            c_in = ws.first["w_in_2"]
            taps = col("conv_w_2").rearrange("p (j k) -> p j k", j=4)
            small = [0]

            def take(*shape):
                n = 1
                for x in shape:
                    n *= x
                v = SM[:, small[0]:small[0] + n]
                small[0] += n
                names = "abcd"[:len(shape)]
                return v if len(shape) == 1 else v.rearrange(f"p ({' '.join(names)}) -> p {' '.join(names)}",
                                                             **dict(zip(names, shape)))

            ba = take(2, 8)
            beta, ex, g, t1, t2, x1 = (take(2, 4) for _ in range(6))
            gc, gtot, egc, edec, egl, bg = (take(2, 4) for _ in range(6))

            tiles = [("aq", m, 0) for m in range(4)] + [("ak", m, 1) for m in range(4)] + [("av", m, 2) for m in range(2)]
            tiles += [("qkv", m, 3 + m // 4) for m in range(12)] + [("dz", m, 6) for m in range(2)] + [("ba", 0, 7)]
            last = [j + 1 == len(tiles) or tiles[j + 1][2] != x[2] for j, x in enumerate(tiles)]
            done, n_plain = tile_signals([c_in + x[2] if e else None for x, e in zip(tiles, last)])
            with nc.Block() as block:

                @block.sync
                def _(sp):
                    ws.load_until(sp, c_in + 8)

                @block.gpsimd
                def _(pool):
                    nc.gpsimd.memset(raw[:, :, 0:3], 0.0).then_inc(S["a_ready"].sem, 1)

                @block.tensor
                def _(pe):
                    for j, (kind, m, c) in enumerate(tiles):
                        if j == 0 or tiles[j - 1][2] != c:
                            ws.wait(pe, c_in + c)
                        w = ws.view(c_in + c)
                        if j >= 4:
                            pe.wait_ge(*at("tile_taken", j - 3))
                        o = PS[:, j % 4, :]
                        if kind == "ba":
                            for n in range(2):
                                for k in range(KT):
                                    ins = nc.tensor.matmul(o[:, n * 8:n * 8 + 8], HT[:, k, n * P:(n + 1) * P], w[:, k, :],
                                                           start=(k == 0), stop=(k == KT - 1))
                        else:
                            for k in range(KT):
                                if j == 0:
                                    pe.wait_ge(*at("h_ready", k + 1))
                                if kind in ("av", "dz"):
                                    ins = nc.tensor.matmul(o, HT[:, k, m * P:(m + 1) * P], w[:, k, :], start=(k == 0), stop=(k == KT - 1))
                                else:
                                    ins = nc.tensor.matmul(o[:, 0:LAT], w[:, k, m % 4 * P:m % 4 * P + P], HT[:, k, 0:LAT],
                                                           start=(k == 0), stop=(k == KT - 1))
                        ins.then_inc(done[j][0], 1)

                @block.scalar
                def _(act):
                    norm_scalar(act, 4, LAT)
                    act.wait_ge(*at("a_ready", 1))
                    for j, (kind, m, c) in enumerate(tiles[:-1]):
                        act.wait_ge(*done[j])
                        o = PS[:, j % 4, :]
                        dst, o = {"aq": (aq[:, m % 4, :], o[:, 0:LAT]), "ak": (ak[:, m % 4, :], o[:, 0:LAT]), "av": (av[:, m % 2, :], o),
                                  "qkv": (raw[:, m, 3:LAT + 3], o[:, 0:LAT]), "dz": (dz[:, m % 2, :], o)}[kind]
                        nc.scalar.activation(dst, o, ACT.Silu if kind == "dz" else ACT.Copy).then_inc(S["tile_taken"].sem, 1)
                    for m in range(12):
                        act.wait_ge(*at("b_ready", m + 1))
                        act_chain.add(nc.scalar.activation(qkv[:, m, :], qkv[:, m, :], ACT.Silu))

                @block.vector
                def _(dve):
                    norm_vector(dve, 4, "norm1_w_2", None, LAT)
                    for m in range(12):
                        dve.wait_ge(*at("tile_taken", 11 + m))
                        o = qkv[:, m, :]
                        dve_chain.link(dve, nc.vector.tensor_scalar(o, raw[:, m, 0:LAT], taps[:, 0, m:m + 1], None, ALU.mult))
                        for j in range(1, 4):
                            ins = nc.vector.scalar_tensor_tensor(o, raw[:, m, j:j + LAT], taps[:, j, m:m + 1], o, ALU.mult, ALU.add)
                            if j < 3:
                                dve_chain.link(dve, ins)
                        ins.then_inc(S["b_ready"].sem, 1)
                    dve.wait_ge(*done[-1])
                    dve_chain.add(nc.vector.tensor_copy(ba, PS[:, (len(tiles) - 1) % 4, 0:16].rearrange("p (a n) -> p a n", a=2)))

            norm_passed()
            S["tile_ready"].passed(n_plain)
            S["tile_taken"].passed(len(tiles) - 1)
            S["a_ready"].passed(1)
            S["b_ready"].passed(12)
            ws.done = c_in + 8

            def score(h, u, k, out):
                half = slice(64 * h, 64 * h + 64)
                return nc.tensor.matmul(out, aq[half, u[0], u[1] * P:(u[1] + 1) * P], ak[half, u[0], k], start=True, stop=True)

            def value(u, h, kt):
                head = 2 * u[0] + h
                return av[:, kt, head * 64:head * 64 + 64], lambda bank: bank[64 * h:64 * h + 64, 0:P]

            def gate(u, bank):
                return mixed[:, u[0], u[1] * P:(u[1] + 1) * P], None, bank[:, 0:P]

            units = [(m, q, list(range(q + 1))) for m in range(4) for q in range(2)]
            attention(units, 0.125, score, value, lambda u: dilated[:, u[1], 0:(u[1] + 1) * P], None, gate)

            b = Arena()
            vb, kbg, kd = (b.take(8, P) for _ in range(3))
            b = Arena(a.at)
            kt_, vt, e, amat, amat_t, intra, intra_t = (b.take(8, P) for _ in range(7))
            u_, w_t, o_ = (b.take(8, P) for _ in range(3))
            x = PW[:, 0:1024].rearrange("p (n c) -> p n c", n=8)
            x_t = PW[:, 1024:2048].rearrange("p (n c) -> p n c", n=8)
            y = PW[:, 2048:3072].rearrange("p (n c) -> p n c", n=8)
            lo = PW[:, 3072:4096].rearrange("p (n c) -> p n c", n=8)
            s_ = raw.rearrange("p k t -> p (k t)")[:, 0:512].rearrange("p (h v) -> p h v", h=H)
            norms = raw.rearrange("p k t -> p (k t)")[:, 0:2048].rearrange("p (k t) -> p k t", k=8)
            sq8 = PW[:, 0:2048].rearrange("p (k t) -> p k t", k=8)

            def flat(v):
                return v.rearrange("p a b -> p (a b)")

            def bank4(n):
                return PS[:, n, :].rearrange("p (c s) -> p c s", c=4)

            with nc.Block() as block:

                @block.scalar
                def _(act):
                    for k in range(8):
                        nc.scalar.activation(sq8[:, k, :], qkv[:, k, :], ACT.Square).then_inc(S["squares_ready"].sem, 1)
                    for k in range(8):
                        act.wait_ge(*at("inverse_ready", k + 1))
                        nc.scalar.activation(norms[:, k, :], norms[:, k, :], ACT.Sqrt).then_inc(S["rstd_ready"].sem, 1)
                    act.wait_ge(*at("a_ready", 1))
                    act_chain.link(act, nc.scalar.activation(ex, t1, ACT.Exp, scale=-1.0))
                    nc.scalar.activation(g, ex, ACT.Ln, bias=1.0).then_inc(S["b_ready"].sem, 1)
                    nc.scalar.activation(t2[:, 0, :], bcast("A_log_2"), ACT.Exp).then_inc(S["b_ready"].sem, 1)
                    nc.scalar.activation(beta, ba[:, :, 0:4], ACT.Sigmoid).then_inc(S["b_ready"].sem, 1)
                    for n in range(2):
                        act.wait_ge(*at("transposed", 2 * n + 1))
                        nc.scalar.copy(kt_[:, 4 * n:4 * n + 4, :], bank4(4 + n)).then_inc(S["transposed_taken"].sem, 1)
                        act.wait_ge(*at("transposed", 2 * n + 2))
                        nc.scalar.copy(vt[:, 4 * n:4 * n + 4, :], bank4(6 + n)).then_inc(S["transposed_taken"].sem, 1)

                @block.tensor
                def _(pe):
                    for k in range(8):
                        pe.wait_ge(*at("squares_ready", k + 1))
                        if k >= 4:
                            pe.wait_ge(*at("inverse_ready", k - 3))
                        nc.tensor.matmul(PS[:, k % 4, 0:LAT], ones, sq8[:, k, :], start=True, stop=True).then_inc(
                            S["square_sum_ready"].sem, 1)
                    pe.wait_ge(*at("scaled_ready", 8))
                    for n in range(2):
                        for first, bank in ((4, 4), (8, 6)):
                            for h in range(H):
                                ins = nc.tensor.transpose(PS[:, bank + n, h * P:(h + 1) * P], qkv[:, first + h, n * P:(n + 1) * P], ident)
                            ins.then_inc(S["transposed"].sem, 1)

                @block.vector
                def _(dve):
                    for k in range(8):
                        dve.wait_ge(*at("square_sum_ready", k + 1))
                        dve_chain.link(dve, nc.vector.tensor_scalar(norms[:, k, :], PS[:, k % 4, 0:LAT], EPS, None, ALU.add))
                        nc.vector.reciprocal(norms[:, k, :], norms[:, k, :]).then_inc(S["inverse_ready"].sem, 1)
                    for k in range(8):
                        dve.wait_ge(*at("rstd_ready", k + 1))
                        nc.vector.scalar_tensor_tensor(qkv[:, k, :], qkv[:, k, :], P ** -0.5 if k < 4 else 1.0, norms[:, k, :], ALU.mult,
                                                       ALU.mult).then_inc(S["scaled_ready"].sem, 1)
                    dve_chain.link(dve, nc.vector.tensor_tensor(x1, ba[:, :, 4:8], bcast("dt_bias_2").unsqueeze(1).to_broadcast([P, 2, 4]),
                                                                ALU.add))
                    nc.vector.scalar_tensor_tensor(t1, x1, -1.0, x1, ALU.mult, ALU.max).then_inc(S["a_ready"].sem, 1)
                    dve.wait_ge(*at("b_ready", 1))
                    exact_log1p(dve, flat(g), flat(ex), flat(gc), flat(gtot))
                    dve_chain.link(dve, nc.vector.scalar_tensor_tensor(g, x1, 0.0, g, ALU.max, ALU.add))
                    dve.wait_ge(*at("b_ready", 2))
                    dve_chain.add(nc.vector.scalar_tensor_tensor(g, g, -1.0, t2[:, 0:1, :].to_broadcast([P, 2, 4]), ALU.mult, ALU.mult))

            for n, k in (("squares_ready", 8), ("square_sum_ready", 8), ("inverse_ready", 8), ("rstd_ready", 8), ("scaled_ready", 8),
                         ("transposed", 4), ("transposed_taken", 4), ("a_ready", 1), ("b_ready", 3)):
                S[n].passed(k)

            with nc.Block() as block:

                @block.tensor
                def _(pe):
                    nc.tensor.matmul(PS[:, 0, 0:8], const("upto"), flat(g), start=True, stop=True)
                    nc.tensor.matmul(PS[:, 0, 8:16], ones, flat(g), start=True, stop=True).then_inc(S["a_ready"].sem, 1)
                    for p in range(8):
                        n, h = divmod(p, 4)
                        t_ = slice(n * P, (n + 1) * P)
                        nc.tensor.matmul(PS[:, 1 + n, h * P:(h + 1) * P], qkv[:, 4 + h, t_], qkv[:, 4 + h, t_], start=True, stop=True)
                        ins = nc.tensor.matmul(PS[:, 3 + n, h * P:(h + 1) * P], qkv[:, h, t_], qkv[:, 4 + h, t_], start=True, stop=True)
                    ins.then_inc(S["scores_ready"].sem, 1)
                    pe.wait_ge(*at("b_ready", 1))
                    for p in range(8):
                        ins = nc.tensor.matmul(PS[:, 5 + p // 4, p % 4 * P:(p % 4 + 1) * P], flat(gc)[:, p:p + 1].to_broadcast([P, P]), ident,
                                               start=True, stop=True)
                    ins.then_inc(S["c_ready"].sem, 1)
                    pe.wait_ge(*at("f_ready", 1))
                    pe.wait_ge(*at("d_ready", 2))
                    for p in range(8):
                        ins = nc.tensor.transpose(PS[:, 5 + p // 4, p % 4 * P:(p % 4 + 1) * P], amat[:, p, :], ident)
                    ins.then_inc(S["transposed"].sem, 1)
                    pe.wait_ge(*at("g_ready", 2))
                    for p in range(8):
                        ins = nc.tensor.transpose(PS[:, 3 + p // 4, p % 4 * P:(p % 4 + 1) * P], intra[:, p, :], ident)
                    ins.then_inc(S["transposed"].sem, 1)

                @block.scalar
                def _(act):
                    act.wait_ge(*at("b_ready", 3))
                    nc.scalar.activation(egc, gc, ACT.Exp).then_inc(S["exp_ready"].sem, 1)
                    nc.scalar.activation(edec, edec, ACT.Exp).then_inc(S["exp_ready"].sem, 1)
                    nc.scalar.activation(egl, gtot, ACT.Exp).then_inc(S["exp_ready"].sem, 1)
                    for p in range(8):
                        act.wait_ge(*at("d_ready", 1 + p // 4))
                        nc.scalar.activation(e[:, p, :], e[:, p, :], ACT.Exp, bias=flat(gc)[:, p:p + 1]).then_inc(S["e_ready"].sem, 1)
                    act.wait_ge(*at("transposed", 2))
                    for n in range(2):
                        nc.scalar.copy(intra_t[:, 4 * n:4 * n + 4, :], bank4(3 + n))

                @block.vector
                def _(dve):
                    dve.wait_ge(*at("a_ready", 1))
                    nc.vector.tensor_copy(flat(gc), PS[:, 0, 0:8]).then_inc(S["b_ready"].sem, 1)
                    nc.vector.tensor_copy(flat(gtot), PS[:, 0, 8:16]).then_inc(S["b_ready"].sem, 1)
                    dve.wait_ge(*at("b_ready", 2))
                    nc.vector.tensor_tensor(edec, gtot, gc, ALU.subtract).then_inc(S["b_ready"].sem, 1)
                    dve.wait_ge(*at("c_ready", 1))
                    for n in range(2):
                        nc.vector.scalar_tensor_tensor(e[:, 4 * n:4 * n + 4, :], bank4(5 + n), -1.0,
                                                       const("causal").unsqueeze(1).to_broadcast([P, 4, P]), ALU.mult, ALU.add).then_inc(
                            S["d_ready"].sem, 1)
                    dve.wait_ge(*at("scores_ready", 1))
                    for p in range(8):
                        dve.wait_ge(*at("e_ready", p + 1))
                        dve_chain.add(nc.vector.scalar_tensor_tensor(amat[:, p, :], bank4(1 + p // 4)[:, p % 4, :], flat(beta)[:, p:p + 1],
                                                                     e[:, p, :], ALU.mult, ALU.mult))
                    dve.wait_ge(dve_chain.sem, dve_chain.n)
                    nc.vector.tensor_tensor(amat, amat, const("strict").unsqueeze(1).to_broadcast([P, 8, P]), ALU.mult).then_inc(
                        S["f_ready"].sem, 1)
                    for n in range(2):
                        nc.vector.tensor_tensor(intra[:, 4 * n:4 * n + 4, :], bank4(3 + n), e[:, 4 * n:4 * n + 4, :], ALU.mult).then_inc(
                            S["g_ready"].sem, 1)
                    dve.wait_ge(*at("exp_ready", 3))
                    dve_chain.link(dve, nc.vector.tensor_tensor(bg, beta, egc, ALU.mult))
                    for dst, src, f in ((vb, vt, beta), (kbg, kt_, bg), (kd, kt_, edec)):
                        dve_chain.add(nc.vector.tensor_tensor(dst, src, flat(f).unsqueeze(2).to_broadcast([P, 8, P]), ALU.mult))
                    dve.wait_ge(*at("f_ready", 1))
                    idb = ident.unsqueeze(1).to_broadcast([P, 8, P])
                    dve_chain.link(dve, nc.vector.tensor_tensor(x, amat, const("low1").unsqueeze(1).to_broadcast([P, 8, P]), ALU.mult))
                    dve_chain.link(dve, nc.vector.scalar_tensor_tensor(x, x, -1.0, idb, ALU.mult, ALU.add))
                    dve.wait_ge(*at("transposed", 1))
                    for n in range(2):
                        dve_chain.add(nc.vector.tensor_copy(amat_t[:, 4 * n:4 * n + 4, :], bank4(5 + n)))
                    dve.wait_ge(dve_chain.sem, dve_chain.n)
                    dve_chain.link(dve, nc.vector.tensor_tensor(x_t, amat_t, const("low1T").unsqueeze(1).to_broadcast([P, 8, P]), ALU.mult))
                    dve_chain.link(dve, nc.vector.scalar_tensor_tensor(x_t, x_t, -1.0, idb, ALU.mult, ALU.add))

            for n, k in (("a_ready", 1), ("b_ready", 3), ("c_ready", 1), ("d_ready", 2), ("e_ready", 8), ("f_ready", 1), ("g_ready", 2),
                         ("exp_ready", 3), ("scores_ready", 1), ("transposed", 2)):
                S[n].passed(k)

            levels = (2, 4, 8, 16, 32, 64)
            with nc.Block() as block:

                @block.gpsimd
                def _(pool):
                    for l, bsize in enumerate(levels):
                        if l >= 1:
                            pool.wait_ge(*at("b_ready", l))
                        nc.gpsimd.tensor_tensor(lo, amat_t, const(f"low{bsize}T").unsqueeze(1).to_broadcast([P, 8, P]),
                                                ALU.mult).then_inc(S["a_ready"].sem, 1)

                @block.tensor
                def _(pe):
                    for l in range(len(levels)):
                        pe.wait_ge(*at("a_ready", l + 1))
                        if l >= 1:
                            pe.wait_ge(*at("e_ready", 2 * l))
                            pe.wait_ge(*at("f_ready", 2 * l))
                        for p in range(8):
                            ins = nc.tensor.matmul(PS[:, p // 4, p % 4 * P:(p % 4 + 1) * P], lo[:, p, :], x[:, p, :], start=True, stop=True)
                        ins.then_inc(S["b_ready"].sem, 1)
                        pe.wait_ge(*at("c_ready", 2 * l + 2))
                        for p in range(8):
                            ins = nc.tensor.matmul(PS[:, 2 + p // 4, p % 4 * P:(p % 4 + 1) * P], x_t[:, p, :], y[:, p, :], start=True, stop=True)
                        ins.then_inc(S["d_ready"].sem, 1)
                        for p in range(8):
                            ins = nc.tensor.matmul(PS[:, 4 + p // 4, p % 4 * P:(p % 4 + 1) * P], y[:, p, :], x_t[:, p, :], start=True, stop=True)
                        ins.then_inc(S["g_ready"].sem, 1)
                    pe.wait_ge(*at("f_ready", 2 * len(levels)))
                    for p in range(8):
                        n, h = p // 4, p % 4
                        nc.tensor.matmul(PS[:, n, h * P:(h + 1) * P], x_t[:, p, :], vb[:, p, :], start=True, stop=True)
                        ins = nc.tensor.matmul(PS[:, 2 + n, h * P:(h + 1) * P], kbg[:, p, :], x_t[:, p, :], start=True, stop=True)
                    ins.then_inc(S["scores_ready"].sem, 1)

                @block.scalar
                def _(act):
                    for l in range(len(levels)):
                        act.wait_ge(*at("b_ready", l + 1))
                        if l >= 1:
                            act.wait_ge(*at("g_ready", l))
                        for n in range(2):
                            nc.scalar.copy(y[:, 4 * n:4 * n + 4, :], bank4(n)).then_inc(S["c_ready"].sem, 1)
                    act.wait_ge(*at("scores_ready", 1))
                    for n in range(2):
                        nc.scalar.copy(u_[:, 4 * n:4 * n + 4, :], bank4(n))
                        nc.scalar.copy(w_t[:, 4 * n:4 * n + 4, :], bank4(2 + n))

                @block.vector
                def _(dve):
                    for l in range(len(levels)):
                        dve.wait_ge(*at("d_ready", l + 1))
                        for n in range(2):
                            v = x[:, 4 * n:4 * n + 4, :]
                            nc.vector.tensor_tensor(v, v, bank4(2 + n), ALU.subtract).then_inc(S["e_ready"].sem, 1)
                        dve.wait_ge(*at("g_ready", l + 1))
                        for n in range(2):
                            v = x_t[:, 4 * n:4 * n + 4, :]
                            nc.vector.tensor_tensor(v, v, bank4(4 + n), ALU.subtract).then_inc(S["f_ready"].sem, 1)

            L = len(levels)
            for n, k in (("a_ready", L), ("b_ready", L), ("c_ready", 2 * L), ("d_ready", L), ("e_ready", 2 * L), ("f_ready", 2 * L),
                         ("g_ready", L), ("scores_ready", 1)):
                S[n].passed(k)

            rs, rr = SM[:, 300:308], SM[:, 308:316]
            with nc.Block() as block:

                @block.tensor
                def _(pe):
                    for h in range(H):
                        ins = nc.tensor.matmul(PS[:, 0, h * P:(h + 1) * P], kd[:, h, :], u_[:, h, :], start=True, stop=True)
                    ins.then_inc(S["a_ready"].sem, 1)
                    for h in range(H):
                        ins = nc.tensor.matmul(PS[:, 1, h * P:(h + 1) * P], intra_t[:, h, :], u_[:, h, :], start=True, stop=True)
                    ins.then_inc(S["b_ready"].sem, 1)
                    pe.wait_ge(*at("c_ready", 1))
                    for h in range(H):
                        ins = nc.tensor.matmul(PS[:, 2, h * P:(h + 1) * P], w_t[:, 4 + h, :], s_[:, h, :], start=True, stop=True)
                    ins.then_inc(S["d_ready"].sem, 1)
                    for h in range(H):
                        ins = nc.tensor.matmul(PS[:, 3, h * P:(h + 1) * P], qkv[:, h, P:2 * P], s_[:, h, :], start=True, stop=True)
                    ins.then_inc(S["e_ready"].sem, 1)
                    pe.wait_ge(*at("f_ready", 1))
                    for h in range(H):
                        ins = nc.tensor.matmul(PS[:, 4, h * P:(h + 1) * P], intra_t[:, 4 + h, :], u_[:, 4 + h, :], start=True, stop=True)
                    ins.then_inc(S["g_ready"].sem, 1)
                    pe.wait_ge(*at("k_ready", 1))
                    for h in range(H):
                        for n in range(2):
                            ins = nc.tensor.transpose(PS[:, 5 + h // 2, (h % 2 * 2 + n) * P:(h % 2 * 2 + n + 1) * P], o_[:, 4 * n + h, :], ident)
                    ins.then_inc(S["transposed"].sem, 1)

                @block.scalar
                def _(act):
                    act.wait_ge(*at("a_ready", 1))
                    nc.scalar.copy(s_, bank4(0)).then_inc(S["c_ready"].sem, 1)
                    act.wait_ge(*at("b_ready", 1))
                    nc.scalar.copy(o_[:, 0:4, :], bank4(1)).then_inc(S["i_ready"].sem, 1)
                    act.wait_ge(*at("i_ready", 1))
                    act.wait_ge(*at("j_ready", 1))
                    for p in range(8):
                        nc.scalar.activation(y[:, p, :], o_[:, p, :], ACT.Square, accum_out=rs[:, p:p + 1]).then_inc(
                            S["squares_ready"].sem, 1)
                    act.wait_ge(*at("inverse_ready", 1))
                    nc.scalar.activation(rr, rs, ACT.Sqrt).then_inc(S["rstd_ready"].sem, 1)

                @block.vector
                def _(dve):
                    dve.wait_ge(*at("d_ready", 1))
                    nc.vector.tensor_tensor(u_[:, 4:8, :], u_[:, 4:8, :], bank4(2), ALU.subtract).then_inc(S["f_ready"].sem, 1)
                    dve.wait_ge(*at("e_ready", 1))
                    dve_chain.link(dve, nc.vector.tensor_tensor(o_[:, 4:8, :], bank4(3), egc[:, 1, :].unsqueeze(2).to_broadcast([P, 4, P]),
                                                                ALU.mult))
                    dve.wait_ge(*at("g_ready", 1))
                    nc.vector.tensor_tensor(o_[:, 4:8, :], o_[:, 4:8, :], bank4(4), ALU.add).then_inc(S["j_ready"].sem, 1)
                    dve.wait_ge(*at("squares_ready", 8))
                    dve_chain.link(dve, nc.vector.tensor_scalar(rs, rs, 1.0 / P, EPS, ALU.mult, ALU.add))
                    nc.vector.reciprocal(rs, rs).then_inc(S["inverse_ready"].sem, 1)
                    dve.wait_ge(*at("rstd_ready", 1))
                    dve_chain.link(dve, nc.vector.tensor_tensor(o_, o_, rr.unsqueeze(2).to_broadcast([P, 8, P]), ALU.mult))
                    nc.vector.tensor_tensor(flat(o_), flat(o_), flat(dz), ALU.mult).then_inc(S["k_ready"].sem, 1)
                    dve.wait_ge(*at("transposed", 1))
                    for n in range(2):
                        dve_chain.add(nc.vector.tensor_scalar(mixed[:, 4 + 2 * n:6 + 2 * n, :],
                                                              PS[:, 5 + n, :].rearrange("p (h t) -> p h t", h=2),
                                                              col("dn_norm_w_2"), None, ALU.mult))

            for n, k in (("a_ready", 1), ("b_ready", 1), ("c_ready", 1), ("d_ready", 1), ("e_ready", 1), ("f_ready", 1), ("g_ready", 1),
                         ("k_ready", 1), ("i_ready", 1), ("j_ready", 1), ("transposed", 1), ("squares_ready", 8), ("inverse_ready", 1),
                         ("rstd_ready", 1)):
                S[n].passed(k)

            first = ws.first["w_out_2"]
            done, n_plain = tile_signals([None, None, None, first, None, None, None, first + 1])
            with nc.Block() as block:

                @block.sync
                def _(sp):
                    ws.load_until(sp, first + 2)

                @block.tensor
                def _(pe):
                    for m in range(KT):
                        if m % 4 == 0:
                            ws.wait(pe, first + m // 4)
                        w = ws.view(first + m // 4)
                        for k in range(KT):
                            ins = nc.tensor.matmul(PS[:, m, 0:LAT], w[:, k, m % 4 * P:m % 4 * P + P], mixed[:, k, :], start=(k == 0),
                                                   stop=(k == KT - 1))
                        ins.then_inc(done[m][0], 1)

                @block.vector
                def _(dve):
                    for m in range(KT):
                        dve.wait_ge(*done[m])
                        dve_chain.add(nc.vector.scalar_tensor_tensor(XT[:, m, 0:LAT], PS[:, m, 0:LAT], modulation(4)[:, 2 * KT + m, :],
                                                                     XT[:, m, 0:LAT], ALU.mult, ALU.add))

            S["tile_ready"].passed(n_plain)

        hybrid_mixer()

        def routed_experts():
            E, K, SLOT, F = 32, 4, 64, 1024
            MAX_BLOCKS = LAT * K // SLOT + E
            W = BIG[:, 0:12 * 2048].rearrange("p (c n) -> p c n", c=12)
            rest = [12 * 2048]

            def take(buf, at, *shape):
                n = 1
                for x in shape:
                    n *= x
                v = buf[:, at[0]:at[0] + n]
                at[0] += n
                names = "abcd"[:len(shape)]
                return v if len(shape) == 1 else v.rearrange(f"p ({' '.join(names)}) -> p {' '.join(names)}",
                                                             **dict(zip(names, shape)))

            htok = take(BIG, rest, 2, D)
            bias1 = take(BIG, rest, 2 * F)
            bias2 = take(BIG, rest, D)
            w_router = take(BIG, rest, KT, E)
            onehot, placed = take(BIG, rest, 2, K, E), take(BIG, rest, 2, K, E)
            gates_of = take(BIG, rest, 2, E)
            gates_by = take(BIG, rest, LAT)
            table = take(BIG, rest, MAX_BLOCKS, E)
            pw = [0]
            gate_, up, sig, act_ = (take(PW, pw, 512) for _ in range(4))
            xt, at_, ys = take(PW, pw, KT, SLOT), take(PW, pw, 4, 2, SLOT), take(PW, pw, 512)
            eq = take(PW, pw, 2, K, SLOT)
            hbuf, hat = HT[:].rearrange("p k t -> p (k t)"), [0]
            drow, grow, eq2 = (take(hbuf, hat, K, LAT) for _ in range(3))
            pick, spread = take(hbuf, hat, 2, SLOT), take(hbuf, hat, LAT)
            sm = [0]
            lg, sel = take(SM, sm, 2, E), take(SM, sm, 2, E)
            v8, gates, idx = take(SM, sm, 2, 8), take(SM, sm, 2, K), take(SM, sm, 2, K)
            gsum, count, blocks, pend, pos = take(SM, sm, 2), take(SM, sm, E), take(SM, sm, E), take(SM, sm, E), take(SM, sm, 2, E)
            dest, slot, tmp = take(SM, sm, 2, K), take(SM, sm, 1), take(SM, sm, E)
            tabf = take(SM, sm, MAX_BLOCKS + 1)
            tabi = take(SM, sm, MAX_BLOCKS + 1).bitcast(I32)
            i8 = take(SM, sm, 2, 8).bitcast(U32)
            sq = PW[:, 1024:3072].rearrange("p (k t) -> p k t", k=KT)
            rstd, rinv = PW[:, 0:LAT], PW[:, LAT:2 * LAT]
            yt_ = BIG[:, 0:2 * D].rearrange("p (a d) -> p a d", a=2)

            def flat(x):
                return x.rearrange("p a b -> p (a b)")

            def norm_parts(gain_then):
                def scalar(act):
                    for k in range(KT):
                        nc.scalar.activation(sq[:, k, :], XT[:, k, 0:LAT], ACT.Square).then_inc(S["squares_ready"].sem, 1)
                    act.wait_ge(*at("inverse_ready", 1))
                    nc.scalar.activation(rstd, rinv, ACT.Sqrt).then_inc(S["rstd_ready"].sem, 1)

                def tensor(pe):
                    for k in range(KT):
                        pe.wait_ge(*at("squares_ready", k + 1))
                        ins = nc.tensor.matmul(PS[:, 7, 0:LAT], ones, sq[:, k, :], start=(k == 0), stop=(k == KT - 1))
                    ins.then_inc(S["square_sum_ready"].sem, 1)

                def vector(dve):
                    dve.wait_ge(*at("square_sum_ready", 1))
                    dve_chain.link(dve, nc.vector.tensor_scalar(rinv, PS[:, 7, 0:LAT], 1.0 / D, EPS, ALU.mult, ALU.add))
                    nc.vector.reciprocal(rinv, rinv).then_inc(S["inverse_ready"].sem, 1)
                    dve.wait_ge(*at("rstd_ready", 1))

                return scalar, tensor, vector

            def own_norm_passed():
                S["squares_ready"].passed(KT)
                for n in ("square_sum_ready", "inverse_ready", "rstd_ready"):
                    S[n].passed(1)

            n_scalar, n_tensor, n_vector = norm_parts(None)
            with nc.Block() as block:

                @block.sync
                def _(sp):
                    sp.dma_start(w_router, t["w_router_2"].rearrange("(k p) e -> p k e", p=P)).then_inc(S["tokens_loaded"].sem, 16)

                @block.scalar
                def _(act):
                    n_scalar(act)
                    for k in range(KT):
                        act.wait_ge(*at("scaled_ready", k + 1))
                        h = HT[:, k, 0:LAT]
                        nc.scalar.activation(h, h, ACT.Identity, bias=modulation(4)[:, 3 * KT + k, :], scale=GAIN[:, k, 0:1]).then_inc(
                            S["tile_taken"].sem, 1)
                    for n in range(4):
                        act.wait_ge(*at("transposed", n + 1))
                        nc.scalar.copy(htok[:, n // 2, n % 2 * 512:n % 2 * 512 + 512], PS[:, n, :])

                @block.tensor
                def _(pe):
                    n_tensor(pe)
                    pe.wait_ge(*at("tile_taken", KT))
                    pe.wait_ge(*at("tokens_loaded", 16))
                    for n in range(2):
                        for k in range(KT):
                            ins = nc.tensor.matmul(PS[:, 4, n * E:(n + 1) * E], HT[:, k, n * P:(n + 1) * P], w_router[:, k, :], start=(k == 0),
                                                   stop=(k == KT - 1))
                    ins.then_inc(S["scores_ready"].sem, 1)
                    for n in range(4):
                        for j in range(4):
                            ins = nc.tensor.transpose(PS[:, n, j * P:(j + 1) * P], HT[:, n % 2 * 4 + j, n // 2 * P:(n // 2 + 1) * P], ident)
                        ins.then_inc(S["transposed"].sem, 1)
                    pe.wait_ge(*at("a_ready", 1))
                    nc.tensor.matmul(PS[:, 5, 0:E], ones, sel[:, 0, :], start=True, stop=False)
                    nc.tensor.matmul(PS[:, 5, 0:E], ones, sel[:, 1, :], start=False, stop=True)
                    nc.tensor.matmul(PS[:, 5, E:2 * E], const("before"), sel[:, 0, :], start=True, stop=True)
                    nc.tensor.matmul(PS[:, 5, 2 * E:3 * E], const("before"), sel[:, 1, :], start=True, stop=False)
                    nc.tensor.matmul(PS[:, 5, 2 * E:3 * E], ones, sel[:, 0, :], start=False, stop=True).then_inc(S["b_ready"].sem, 1)

                @block.vector
                def _(dve):
                    def link(ins):
                        dve_chain.link(dve, ins)

                    tt, ts = nc.vector.tensor_tensor, nc.vector.tensor_scalar
                    link(nc.vector.scalar_tensor_tensor(GAIN[:, :, 0], modulation(4)[:, 4 * KT:5 * KT, 0], 1.0, col("norm2_w_2"), ALU.add, ALU.mult))
                    n_vector(dve)
                    for k in range(KT):
                        tt(HT[:, k, 0:LAT], XT[:, k, 0:LAT], rstd, ALU.mult).then_inc(S["scaled_ready"].sem, 1)
                    dve.wait_ge(*at("scores_ready", 1))
                    link(tt(lg, PS[:, 4, 0:2 * E].rearrange("p (n e) -> p n e", n=2),
                            bcast("b_router_2").unsqueeze(1).to_broadcast([P, 2, E]), ALU.add))
                    for n in range(2):
                        link(nc.vector.max(v8[:, n, :], lg[:, n, :]))
                        link(nc.vector.max_index(i8[:, n, :], v8[:, n, :], lg[:, n, :]))
                    link(nc.vector.tensor_copy(idx, i8[:, :, 0:K]))
                    for n in range(2):
                        link(tt(onehot[:, n, :, :], const("expert_row").unsqueeze(1).to_broadcast([P, K, E]),
                                idx[:, n, :].unsqueeze(2).to_broadcast([P, K, E]), ALU.is_equal))
                    for n in range(2):
                        link(nc.vector.tensor_reduce(sel[:, n, :], onehot[:, n, :, :].rearrange("p k e -> p e k"), AX, ALU.add))
                    link(tt(gates, v8[:, :, 0:K], v8[:, :, 0:1].to_broadcast([P, 2, K]), ALU.subtract))
                    ts(slot, const("slot_col"), 0.0, None, ALU.add).then_inc(S["a_ready"].sem, 1)
                    dve.wait_ge(*at("b_ready", 1))
                    link(nc.vector.tensor_copy(count, PS[:, 5, 0:E]))
                    link(ts(blocks, count, 0.0, None, ALU.is_gt))
                    for r in range(1, LAT // SLOT):
                        link(nc.vector.scalar_tensor_tensor(blocks, count, float(SLOT * r), blocks, ALU.is_gt, ALU.add))
                    link(nc.vector.tensor_tensor_scan(pend, ones[:, 0:E], blocks, 0.0, ALU.mult, ALU.add))
                    link(tt(tmp, pend, blocks, ALU.subtract))
                    link(nc.vector.scalar_tensor_tensor(pos, tmp.unsqueeze(1).to_broadcast([P, 2, E]), float(SLOT),
                                                        PS[:, 5, E:3 * E].rearrange("p (n e) -> p n e", n=2), ALU.mult, ALU.add))
                    for n in range(2):
                        link(tt(placed[:, n, :, :], onehot[:, n, :, :], pos[:, n, :].unsqueeze(1).to_broadcast([P, K, E]), ALU.mult))
                        link(nc.vector.tensor_reduce(dest[:, n, :], placed[:, n, :, :], AX, ALU.add))
                    link(tt(table, pend.unsqueeze(1).to_broadcast([P, MAX_BLOCKS, E]),
                            const("block_row").unsqueeze(2).to_broadcast([P, MAX_BLOCKS, E]), ALU.is_le))
                    link(nc.vector.tensor_reduce(tabf[:, 0:MAX_BLOCKS], table, AX, ALU.add))
                    link(ts(tabf[:, 0:MAX_BLOCKS], tabf[:, 0:MAX_BLOCKS], float(E - 1), None, ALU.min))
                    link(nc.vector.tensor_copy(tabf[:, MAX_BLOCKS:MAX_BLOCKS + 1], pend[:, E - 1:E]))
                    link(nc.vector.tensor_copy(tabi, tabf))

            own_norm_passed()
            for n, k in (("tile_taken", KT), ("scaled_ready", KT), ("transposed", 4), ("scores_ready", 1), ("a_ready", 1), ("b_ready", 1),
                         ("tokens_loaded", 16)):
                S[n].passed(k)

            with nc.Block() as block:

                @block.sync
                def _(sp):
                    sp.dma_start(bias2[0:E, :], t["b2_2"]).then_inc(S["tokens_loaded"].sem, 16)

                @block.scalar
                def _(act):
                    act_chain.link(act, nc.scalar.activation(gates, gates, ACT.Exp))
                    nc.scalar.copy(tmp[:, 0:1], slot).then_inc(S["a_ready"].sem, 1)
                    act.wait_ge(*at("transposed", 1))
                    nc.scalar.copy(gates_by[0:E, :], PS[0:E, 0, 0:LAT]).then_inc(S["e_ready"].sem, 1)

                @block.vector
                def _(dve):
                    dve.wait_ge(*at("a_ready", 1))
                    dve_chain.link(dve, nc.vector.tensor_reduce(gsum, gates, AX, ALU.add))
                    dve_chain.link(dve, nc.vector.reciprocal(gsum, gsum))
                    nc.vector.tensor_tensor(gates, gates, gsum.unsqueeze(2).to_broadcast([P, 2, K]), ALU.mult).then_inc(S["b_ready"].sem, 1)
                    dve.wait_ge(*at("b_ready", 1))
                    for n in range(2):
                        dve_chain.link(dve, nc.vector.tensor_tensor(
                            placed[:, n, :, :], onehot[:, n, :, :], gates[:, n, :].unsqueeze(2).to_broadcast([P, K, E]), ALU.mult))
                        nc.vector.tensor_reduce(gates_of[:, n, :], placed[:, n, :, :].rearrange("p k e -> p e k"), AX,
                                                ALU.add).then_inc(S["d_ready"].sem, 1)
                    dve.wait_ge(*at("c_ready", 1))
                    for r, dst in enumerate((drow, grow)):
                        for n in range(2):
                            dve_chain.add(nc.vector.tensor_copy(dst[:, :, n * P:(n + 1) * P],
                                                                PS[:, 4 + 2 * r + n, :].rearrange("p (k t) -> p k t", k=K)))
                    dve_chain.add(nc.vector.memset(act_, 0.0))

                @block.tensor
                def _(pe):
                    pe.wait_ge(*at("b_ready", 1))
                    for r, src in enumerate((dest, gates)):
                        for n in range(2):
                            for k in range(K):
                                ins = nc.tensor.matmul(PS[:, 4 + 2 * r + n, k * P:(k + 1) * P], src[:, n, k:k + 1].to_broadcast([P, P]), ident,
                                                       start=True, stop=True)
                    ins.then_inc(S["c_ready"].sem, 1)
                    pe.wait_ge(*at("d_ready", 2))
                    for n in range(2):
                        ins = nc.tensor.transpose(PS[0:E, 0, n * P:(n + 1) * P], gates_of[:, n, :], ident)
                    ins.then_inc(S["transposed"].sem, 1)
                    pe.wait_ge(*at("e_ready", 1))
                    pe.wait_ge(*at("tokens_loaded", 16))
                    for a in range(2):
                        for g in range(2):
                            nc.tensor.matmul(PS[:, 2 * a + g, :], gates_by[0:E, a * P:(a + 1) * P], bias2[0:E, g * 512:g * 512 + 512],
                                             start=True, stop=True)

            for n in ("a_ready", "b_ready", "c_ready", "e_ready", "transposed"):
                S[n].passed(1)
            S["d_ready"].passed(2)
            S["tokens_loaded"].passed(16)

            w1 = t["w1_2"].rearrange("e d f -> (e d) f")
            w2 = t["w2_2"].rearrange("e f d -> (e f) d")
            chunk_landed = [ctx.enter_context(nc.semaphore(f"expert_chunk{c}_landed")) for c in range(12)]
            bias_landed = ctx.enter_context(nc.semaphore("expert_bias_landed"))
            used = ctx.enter_context(nc.semaphore("expert_chunk_used"))
            loop = {n: ctx.enter_context(nc.semaphore(n)) for n in (
                "pick_ready spread_ready gathered gathered_copied gate_clipped sigmoid_ready act_ready act_turned "
                "act_copied y_copied scattered bias_used".split())}

            with nc.Block() as block:

                def trips(eng):
                    return eng.value_load(tabi[0:1, MAX_BLOCKS:MAX_BLOCKS + 1], min_val=LAT * K // SLOT, max_val=MAX_BLOCKS)

                @block.sync
                def _(sp):
                    def load(i, wait):
                        e = sp.value_load(tabi[0:1, bass.ds(i, 1)], min_val=0, max_val=E - 1)
                        if wait:
                            sp.wait_ge(loop["bias_used"], i)
                        sp.dma_start(bias1[0:1, :], t["b1_2"][bass.ds(e, 1), :]).then_inc(bias_landed, 16)
                        for c in range(12):
                            if wait:
                                sp.wait_ge(used, 12 * i + (c - 11))
                            if c < 8:
                                sp.dma_start(W[:, c, :], w1[bass.ds(e * D + c * P, P), :]).then_inc(chunk_landed[c], 16)
                            else:
                                sp.dma_start(W[:, c, :].rearrange("p (j n) -> p j n", j=2),
                                             w2[bass.ds(e * F + (c - 8) * 2 * P, 2 * P), :].rearrange("(j p) n -> p j n", p=P)).then_inc(
                                    chunk_landed[c], 16)

                    n = trips(sp)
                    load(0, False)
                    with sp.Fori(1, n) as i:
                        load(i, True)

                @block.tensor
                def _(pe):
                    def gather():
                        for k in range(KT):
                            for a in range(2):
                                ins = nc.tensor.matmul(PS[:, 6, k * SLOT:(k + 1) * SLOT], htok[:, a, k * P:(k + 1) * P], pick[:, a, :],
                                                       start=(a == 0), stop=(a == 1))
                        ins.then_inc(loop["gathered"], 1)

                    def scatter():
                        for a in range(2):
                            for g in range(2):
                                ins = nc.tensor.matmul(PS[:, 2 * a + g, :], spread[64 * g:64 * g + 64, a * P:(a + 1) * P],
                                                       ys[64 * g:64 * g + 64, :], start=False, stop=False, skip_group_check=True)
                        ins.then_inc(loop["scattered"], 1)

                    n = trips(pe)
                    pe.wait_ge(loop["pick_ready"], 1)
                    gather()
                    with pe.Fori(0, n) as i:
                        pe.wait_ge(bias_landed, i * 16 + 16)
                        for half in range(2):
                            for g in range(2):
                                ins = nc.tensor.matmul(PS[64 * g:64 * g + 64, 4 + half, :], ones[0:1, 0:SLOT],
                                                       bias1[0:1, half * F + g * 512:half * F + g * 512 + 512], start=True, stop=False)
                        ins.then_inc(loop["bias_used"], 1)
                        pe.wait_ge(loop["gathered_copied"], i + 1)
                        for c in range(8):
                            pe.wait_ge(chunk_landed[c], i * 16 + 16)
                            for half in range(2):
                                for g in range(2):
                                    ins = nc.tensor.matmul(PS[64 * g:64 * g + 64, 4 + half, :], xt[:, c, :],
                                                           W[:, c, half * F + g * 512:half * F + g * 512 + 512], start=False, stop=(c == 7))
                            ins.then_inc(used, 1)
                        pe.wait_ge(loop["pick_ready"], i + 2)
                        gather()
                        pe.wait_ge(loop["spread_ready"], i + 1)
                        pe.wait_ge(loop["y_copied"], i + 1)
                        scatter()
                        pe.wait_ge(loop["gathered_copied"], i + 2)
                        pe.wait_ge(loop["act_ready"], i + 1)
                        for j in range(4):
                            ins = nc.tensor.transpose(PS[:, 6, j * P:(j + 1) * P], act_[:, j * P:(j + 1) * P], ident)
                        ins.then_inc(loop["act_turned"], 1)
                        pe.wait_ge(loop["act_copied"], i + 1)
                        for k in range(KT):
                            if k % 2 == 0:
                                pe.wait_ge(chunk_landed[8 + k // 2], i * 16 + 16)
                            for g in range(2):
                                ins = nc.tensor.matmul(PS[64 * g:64 * g + 64, 7, :], at_[:, k % 4, k // 4, :],
                                                       W[:, 8 + k // 2, k % 2 * D + g * 512:k % 2 * D + g * 512 + 512], start=(k == 0),
                                                       stop=(k == KT - 1))
                            if k % 2 == 1:
                                ins.then_inc(used, 1)
                    pe.wait_ge(loop["spread_ready"], n + 1)
                    pe.wait_ge(loop["y_copied"], n + 1)
                    scatter()

                @block.scalar
                def _(act):
                    n = trips(act)
                    nc.scalar.copy(ys, act_).then_inc(loop["y_copied"], 1)
                    act.wait_ge(loop["gathered"], 1)
                    nc.scalar.copy(xt, PS[:, 6, :].rearrange("p (k s) -> p k s", k=KT)).then_inc(loop["gathered_copied"], 1)
                    with act.Fori(0, n) as i:
                        act.wait_ge(loop["gate_clipped"], i + 1)
                        nc.scalar.activation(sig, gate_, ACT.Sigmoid, scale=1.702).then_inc(loop["sigmoid_ready"], 1)
                        act.wait_ge(loop["gathered"], i + 2)
                        nc.scalar.copy(xt, PS[:, 6, :].rearrange("p (k s) -> p k s", k=KT)).then_inc(loop["gathered_copied"], 1)
                        act.wait_ge(loop["act_turned"], i + 1)
                        nc.scalar.copy(at_, PS[:, 6, :].rearrange("p (j g s) -> p j g s", j=4, g=2)).then_inc(loop["act_copied"], 1)
                        act.wait_ge(used, i * 12 + 12)
                        nc.scalar.copy(ys, PS[:, 7, :]).then_inc(loop["y_copied"], 1)

                @block.vector
                def _(dve):
                    steps = ctx.enter_context(nc.semaphore("block_steps"))

                    def tables(done):
                        for n in range(2):
                            nc.vector.tensor_tensor(eq[:, n, :, :], const("slot_row").unsqueeze(1).to_broadcast([P, K, SLOT]),
                                                    dest[:, n, :].unsqueeze(2).to_broadcast([P, K, SLOT]), ALU.is_equal).then_inc(steps, 1)
                        dve.wait_ge(steps, done(2))
                        nc.vector.tensor_scalar(dest, dest, -float(SLOT), None, ALU.add).then_inc(steps, 1)
                        nc.vector.tensor_reduce(pick[:, 0, :], eq[:, 0, :, :].rearrange("p k s -> p s k"), AX, ALU.add).then_inc(steps, 1)
                        nc.vector.tensor_reduce(pick[:, 1, :], eq[:, 1, :, :].rearrange("p k s -> p s k"), AX, ALU.add).then_inc(
                            loop["pick_ready"], 1)

                    n = trips(dve)
                    tables(lambda x: x)
                    nc.vector.memset(spread, 0.0).then_inc(loop["spread_ready"], 1)
                    dve.wait_ge(steps, 4)
                    dve.wait_ge(loop["gathered"], 1)
                    tables(lambda x: 4 + x)
                    with dve.Fori(0, n) as i:
                        dve.wait_ge(used, i * 12 + 8)
                        nc.vector.tensor_scalar(gate_, PS[:, 4, :], 7.0, None, ALU.min).then_inc(loop["gate_clipped"], 1)
                        nc.vector.tensor_scalar(up, PS[:, 5, :], 7.0, -7.0, ALU.min, ALU.max).then_inc(steps, 1)
                        dve.wait_ge(steps, i * 8 + 9)
                        dve.wait_ge(loop["gate_clipped"], i + 1)
                        nc.vector.scalar_tensor_tensor(up, up, 1.0, gate_, ALU.add, ALU.mult).then_inc(steps, 1)
                        dve.wait_ge(steps, i * 8 + 10)
                        dve.wait_ge(loop["sigmoid_ready"], i + 1)
                        nc.vector.tensor_tensor(act_, up, sig, ALU.mult).then_inc(loop["act_ready"], 1)
                        nc.vector.scalar_tensor_tensor(eq2, drow, slot, grow, ALU.is_equal, ALU.mult).then_inc(steps, 1)
                        dve.wait_ge(steps, i * 8 + 11)
                        nc.vector.tensor_scalar(slot, slot, float(SLOT), None, ALU.add).then_inc(steps, 1)
                        dve.wait_ge(loop["scattered"], i + 1)
                        nc.vector.tensor_reduce(spread, eq2.rearrange("p k t -> p t k"), AX, ALU.add).then_inc(loop["spread_ready"], 1)
                        dve.wait_ge(loop["gathered"], i + 2)
                        tables(lambda x: i * 8 + (12 + x))


            n_scalar, n_tensor, n_vector = norm_parts(None)
            with nc.Block() as block:

                @block.scalar
                def _(act):
                    for b in range(4):
                        nc.scalar.copy(yt_[:, b // 2, b % 2 * 512:b % 2 * 512 + 512], PS[:, b, :]).then_inc(S["a_ready"].sem, 1)
                    act.wait_ge(*at("b_ready", KT))
                    n_scalar(act)

                @block.tensor
                def _(pe):
                    pe.wait_ge(*at("a_ready", 4))
                    for k in range(KT):
                        for n in range(2):
                            ins = nc.tensor.transpose(PS[:, k // 2, (k % 2 * 2 + n) * P:(k % 2 * 2 + n + 1) * P],
                                                      yt_[:, n, k * P:(k + 1) * P], ident)
                        if k % 2:
                            ins.then_inc(S["transposed"].sem, 1)
                    n_tensor(pe)
                    for n in range(2):
                        for k in range(KT):
                            pe.wait_ge(*at("scaled_ready", k + 1))
                            ins = nc.tensor.transpose(PS[:, 2 * n + k // 4, k % 4 * P:(k % 4 + 1) * P], HT[:, k, n * P:(n + 1) * P], ident)
                            if k % 4 == 3:
                                ins.then_inc(S["c_ready"].sem, 1)

                @block.vector
                def _(dve):
                    for k in range(KT):
                        dve.wait_ge(*at("transposed", k // 2 + 1))
                        nc.vector.scalar_tensor_tensor(XT[:, k, 0:LAT], PS[:, k // 2, k % 2 * LAT:(k % 2 + 1) * LAT],
                                                       modulation(4)[:, 5 * KT + k, :], XT[:, k, 0:LAT], ALU.mult, ALU.add).then_inc(S["b_ready"].sem, 1)
                    n_vector(dve)
                    for k in range(KT):
                        nc.vector.scalar_tensor_tensor(HT[:, k, 0:LAT], XT[:, k, 0:LAT], col("final_norm_w_2")[:, k:k + 1], rstd, ALU.mult,
                                                       ALU.mult).then_inc(S["scaled_ready"].sem, 1)
                    for b in range(4):
                        dve.wait_ge(*at("c_ready", b + 1))
                        nc.vector.tensor_copy(htok[:, b // 2, b % 2 * 512:b % 2 * 512 + 512], PS[:, b, :]).then_inc(S["d_ready"].sem, 1)

                @block.sync
                def _(sp):
                    for n in range(2):
                        sp.wait_ge(*at("d_ready", 2 * n + 2))
                        sp.dma_start(out[0, n * P:(n + 1) * P, :], htok[:, n, :]).then_inc(S["stored"].sem, 16)
                    sp.wait_ge(*at("stored", 32))

        routed_experts()


_OUTS = [((1, 256, 1024), "float32")]


def kernel(**inputs):
    import numpy as _np
    import concourse.bacc as _bacc
    from concourse import mybir as _mybir
    from concourse.bass_utils import run_bass_kernel_spmd as _run

    nc = _bacc.Bacc("TRN2", target_bir_lowering=False, num_devices=1)
    arrays, aps = {}, {}

    def give(name, a):
        arrays[f"in_{name}"] = a
        aps[name] = nc.dram_tensor(f"in_{name}", a.shape, _mybir.dt.from_np(a.dtype), kind="ExternalInput").ap()

    inputs = {name: _np.ascontiguousarray(a) for name, a in inputs.items()}
    packed = {name for r in VECTOR_ROWS for name, _ in r} | {name for name, _ in BROADCAST}
    rows = [_np.concatenate([inputs[name].reshape(k, P) for name, k in r]) for r in VECTOR_ROWS]
    give("vector_rows", _np.stack([_np.concatenate([r, _np.zeros((P - len(r), P), r.dtype)]) for r in rows]))
    give("broadcast_row", _np.concatenate([inputs[name].reshape(-1) for name, _ in BROADCAST]))
    for name, a in inputs.items():
        if name in packed:
            continue
        if name.endswith("_2") and a.ndim > 1:
            a = a.reshape(a.shape[1:])
        give(name, a)
    table, at = constant_tables()
    give("consts", table)
    shape, dtype = _OUTS[0]
    out = nc.dram_tensor("out_0", shape, _mybir.dt.from_np(_np.dtype(dtype)), kind="ExternalOutput").ap()
    layers_and_experts_kernel(nc, aps, at, out)
    r = _run(nc, [arrays], core_ids=[0])
    return r.results[0]["out_0"]
```

```python
from contextlib import ExitStack

import concourse.bass as bass
from concourse import mybir

F32 = mybir.dt.float32
I32 = mybir.dt.int32
U32 = mybir.dt.uint32
ALU = mybir.AluOpType
ACT = mybir.ActivationFunctionType
AX = mybir.AxisListType.X

P = 128
D = 1024
KT = D // P
LAT = 256
CTX = 256
TOK = LAT + CTX
TT = TOK // P
CH = 512
SLOTS = 3
EPS = 1e-6
NEG = -1e30


class Signal:

    def __init__(self, sem):
        self.sem, self.base = sem, 0

    def at(self, n):
        return self.base + n

    def passed(self, n):
        self.base += n


class Chain:

    def __init__(self, sem):
        self.sem, self.n = sem, 0

    def add(self, ins):
        self.n += 1
        return ins.then_inc(self.sem, 1)

    def link(self, eng, ins):
        self.add(ins)
        eng.wait_ge(self.sem, self.n)


class WeightStream:

    def __init__(self, slots, landed, used):
        self.slots, self.landed, self.used = slots, landed, used
        self.chunks, self.first, self.issued = [], {}, 0

    def add(self, name, w, cuts=None):
        self.first[name] = len(self.chunks)
        rows, cols = w.shape
        kt = rows // P
        cuts = cuts or [*range(0, cols, CH * KT // kt), cols]
        for a, b in zip(cuts, cuts[1:]):
            self.chunks.append((w[:, a:b].rearrange("(k p) n -> p k n", p=P), kt))

    def view(self, n):
        src, kt = self.chunks[n]
        cols = src.shape[2]
        return self.slots[:, n % SLOTS, 0:kt * cols].rearrange("p (k n) -> p k n", k=kt)

    def load_until(self, sp, end):
        while self.issued < min(len(self.chunks), end + SLOTS):
            n = self.issued
            if n >= SLOTS:
                sp.wait_ge(self.used.sem, n - SLOTS + 1)
            sp.dma_start(self.view(n), self.chunks[n][0]).then_inc(self.landed[n % SLOTS].sem, 16)
            self.issued += 1

    def wait(self, pe, n):
        pe.wait_ge(self.landed[n % SLOTS].sem, 16 * (n // SLOTS + 1))


def constant_tables():
    import numpy as np
    p = np.arange(P)
    t = np.arange(LAT)
    tabs = {}
    tabs["ident"] = np.eye(P)
    tabs["ones"] = np.ones((P, P))
    pick = [(h, s) for h in range(2) for s in range(2)] + [(h, 2) for h in range(2)]
    tabs["streams"] = np.stack([(p % 32 == s) & (p // 32 % 2 == h) for h, s in pick], 1)
    tabs["eps"] = np.full((P, 1), EPS)
    swap = np.zeros((P, P))
    swap[p[1::2], p[0::2]] = -1.0
    swap[p[0::2], p[1::2]] = 1.0
    tabs["swap"] = swap
    inv = np.float32(10000.0) ** (-np.arange(16, dtype=np.float32) / np.float32(16))
    ang = np.concatenate([(t // 64).astype(np.float32)[:, None] * inv, (t % 64).astype(np.float32)[:, None] * inv], -1)
    tabs["cos"] = np.cos(ang).T[(p % 64) // 2]
    tabs["sin"] = np.sin(ang).T[(p % 64) // 2]
    q = np.arange(LAT).reshape(2, P)
    dist = (q[:, :, None] - t[None, None, :]).transpose(1, 0, 2)
    tabs["window"] = np.where(np.abs(dist) <= 128, 0.0, NEG).reshape(P, -1)
    n = ((dist >= 0) & (dist <= 128)).astype(int)
    for w, d in ((512, 4), (2048, 16)):
        n = n + ((dist >= 0) & (dist <= w) & (dist % d == 0))
    tabs["dilated"] = np.where(n > 0, 8.0 * np.log(np.maximum(n, 1)), NEG).reshape(P, -1)
    r, c = p[:, None], p[None, :]
    tabs["upto"] = r <= c
    tabs["from"] = r >= c
    tabs["before"] = r < c
    tabs["causal"] = np.where(c <= r, 0.0, NEG)
    tabs["anticausal"] = np.where(c >= r, 0.0, NEG)
    tabs["strict"] = c < r
    for b in (1, 2, 4, 8, 16, 32, 64):
        low = ((r // b) % 2 == 1) & (c // b == r // b - 1)
        tabs[f"low{b}T"] = low.T
        if b == 1:
            tabs["low1"] = low
    tabs["slot_row"] = np.broadcast_to(np.arange(64), (P, 64))
    tabs["slot_col"] = (p % 64)[:, None]
    tabs["expert_row"] = np.broadcast_to(np.arange(32), (P, 32))
    tabs["partition"] = p[:, None]
    at, n = {}, 0
    for k, v in tabs.items():
        at[k] = (n, n + v.shape[1])
        n += v.shape[1]
    return np.concatenate([np.asarray(v, np.float32) for v in tabs.values()], 1), at


VECTOR_ROWS = [
    [("l0_b_ada", 24), ("l1_b_ada", 24), ("l2_b_ada", 24), ("l3_b_ada", 24), ("c", 8), ("c_ctx", 8), ("c_2", 8),
     ("l0_g_pre", 8)],
    [("b_ada_2", 48), ("l1_g_pre", 8), ("l2_g_pre", 8), ("l3_g_pre", 8), ("l0_g_post", 8), ("l1_g_post", 8),
     ("l2_g_post", 8), ("l3_g_post", 8), ("norm1_w_2", 8), ("norm2_w_2", 8)],
    [("l2_conv", 40), ("conv_w_2", 48), ("l2_g_head", 8), ("l1_g_qa", 2), ("l1_g_kva", 1),
     ("dn_norm_w_2", 1)],
]
BROADCAST = [("l0_sink", 16), ("l3_sink", 16), ("l2_b_gate", 16), ("A_log_2", 4), ("dt_bias_2", 4), ("b_router_2", 32)]


def layers_and_experts_kernel(nc, t, consts_at, out):
    ctx = ExitStack()
    with ctx:
        def sb(name, shape, dt=F32):
            return ctx.enter_context(nc.sbuf_tensor(name, shape, dt))

        def sem(name):
            return Signal(ctx.enter_context(nc.semaphore(name)))

        XT = sb("XT", [P, KT, TOK])
        HT = sb("HT", [P, KT, TOK])
        RING_N = SLOTS * KT * CH
        ARENA_N = 22656
        BIG = sb("BIG", [P, RING_N + ARENA_N])
        PW = sb("PW", [P, 4096])
        n_const = consts_at["partition"][1]
        CONST = sb("CONST", [P, n_const])
        COLS = sb("COLS", [P, 3, P])
        BC = sb("BC", [P, sum(n for _, n in BROADCAST)])
        COND = sb("COND", [P, KT, 32])
        MOD = sb("MOD", [P, 5, 48])
        GAIN = sb("GAIN", [P, KT, 2])
        GATE = sb("GATE", [P, KT, 2])
        RSTD, RMS = PW[:, 0:TOK], PW[:, TOK:2 * TOK]
        SM = sb("SM", [P, 720])
        ST = sb("ST", [P, 64])

        ring = BIG[:, 0:RING_N].rearrange("p (s n) -> p s n", s=SLOTS)

        class Arena:

            def __init__(self, at=0):
                self.at = at

            def take(self, *shape):
                n = 1
                for s in shape:
                    n *= s
                v = BIG[:, RING_N + self.at:RING_N + self.at + n]
                self.at += n
                assert self.at <= ARENA_N, self.at
                names = "abcd"[:len(shape)]
                return v.rearrange(f"p ({' '.join(names)}) -> p {' '.join(names)}",
                                   **dict(zip(names, shape))) if len(shape) > 1 else v

        YT = BIG[:, RING_N:RING_N + KT * TOK].rearrange("p (k t) -> p k t", k=KT)
        SQ = BIG[:, RING_N + KT * TOK:RING_N + 2 * KT * TOK].rearrange("p (k t) -> p k t", k=KT)
        PS = ctx.enter_context(nc.psum_tensor("PS", [P, 8, 512], F32))

        def const(name):
            a, b = consts_at[name]
            return CONST[:, a:b]

        ident, ones = const("ident"), const("ones")
        window = const("window").rearrange("p (t k) -> p t k", t=2)
        dilated = const("dilated").rearrange("p (t k) -> p t k", t=2)

        col_at = {}
        for r, rows in enumerate(VECTOR_ROWS):
            n = 0
            for name, k in rows:
                col_at[name] = (r, n, n + k)
                n += k

        def col(name):
            r, a, b = col_at[name]
            return COLS[:, r, a:b]

        bc_at, n = {}, 0
        for name, k in BROADCAST:
            bc_at[name] = (n, n + k)
            n += k

        def bcast(name):
            return BC[:, bc_at[name][0]:bc_at[name][1]]

        landed = [sem(f"chunk_landed{i}") for i in range(SLOTS)]
        chunk_used = sem("chunk_used")
        ws = WeightStream(ring, landed, chunk_used)
        ADA = ["l0_w_ada", "l1_w_ada", "l2_w_ada", "l3_w_ada", "w_ada_2"]
        ws.add(ADA[0], t[ADA[0]][:, 0:2 * D])
        for i in range(4):
            if i == 2:
                for name, part in (("l2_w_in", slice(0, 3072)), ("l2_w_gates", slice(4096, 4112)), ("l2_w_z", slice(3072, 4096))):
                    ws.add(name, t["l2_w_in"][:, part])
            else:
                ws.add(f"l{i}_w_in", t[f"l{i}_w_in"], [0, 448, 960, 1472] if i == 1 else None)
            if i == 1:
                ws.add("l1_w_uq", t["l1_w_uq"])
                ws.add("l1_w_ukv", t["l1_w_ukv"])
            if i == 0:
                ws.add("l0_w_ada_gate", t[ADA[0]][:, 2 * D:])
            for l in {0: [1, 2, 3], 3: [4]}.get(i, []):
                ws.add(ADA[l], t[ADA[l]])
            ws.add(f"l{i}_w_out", t[f"l{i}_w_out"])
        ws.add("w_in_2", t["w_in_2"][:, 1536:3072])
        for part in (slice(3584, 3592), slice(0, 1536), slice(3072, 3584)):
            ws.add("w_in_2_rest", t["w_in_2"][:, part])
        ws.add("w_out_2", t["w_out_2"])
        ws.first["end"] = len(ws.chunks)

        def modulation_chunks(l, a, b, name=None):
            return [(l, c, ws.first[name or ADA[l]] + c - (a if name else 0)) for c in range(a, b)]

        BESIDE = {0: modulation_chunks(0, 4, 6, "l0_w_ada_gate") + [x for l in (1, 2, 3) for x in modulation_chunks(l, 0, 6)],
                  3: modulation_chunks(4, 0, 12)}

        dve_chain = Chain(ctx.enter_context(nc.semaphore("dve_chain")))
        act_chain = Chain(ctx.enter_context(nc.semaphore("act_chain")))
        pool_chain = Chain(ctx.enter_context(nc.semaphore("pool_chain")))
        names = ("vectors_loaded tokens_loaded consts_loaded late_loaded transposed transposed_taken cond_ready squares_ready "
                 "square_sum_ready rms_ready inverse_ready rstd_ready scaled_ready tile_ready tile_taken rope_mixed rope_taken "
                 "scores_ready max_ready exp_ready scores_used probs_ready probs_turned turned_copied heads_ready "
                 "heads_taken rows_copied columns_ready columns_taken h_ready normed_ready residual_ready a_ready b_ready c_ready d_ready e_ready f_ready g_ready i_ready j_ready k_ready").split()
        S = {n: sem(n) for n in names}

        def at(name, n):
            return S[name].sem, S[name].at(n)

        def tile_signals(ends):
            said, n = [], 0
            for chunk in ends:
                n += chunk is None
                said.append(at("tile_ready", n) if chunk is None else (chunk_used.sem, chunk + 1))
            return said, n

        class Modulations:

            def __init__(self, job, rows, bank):
                self.job, self.rows, self.bank = job, rows, bank
                self.end = job[-1][2] + 1

            def turned(self, j):
                n = 1 if self.job[j][0] == 4 else 2
                return PS[:, self.bank, 0:4 * n].rearrange("p (q h s) -> p h q s", h=2, s=n)

            def multiply(self, pe, j):
                chunk = self.job[j][2]
                ws.wait(pe, chunk)
                if j >= 1:
                    pe.wait_ge(*at("columns_taken", j))
                w = ws.view(chunk)
                for k in range(KT):
                    for half in range(2):
                        g = 32 * (k % 2 * 2 + half)
                        ins = nc.tensor.matmul(PS[g:g + 32, self.bank, 0:256], COND[:, k, :], w[:, k, half * 256:half * 256 + 256],
                                               start=(k < 2), stop=(k >= KT - 2), tile_position=(0, g))
                ins.then_inc(chunk_used.sem, 1)

            def copy(self, act, j):
                act.wait_ge(chunk_used.sem, self.job[j][2] + 1)
                if j >= 1:
                    act.wait_ge(*at("columns_ready", j))
                nc.scalar.copy(self.rows, PS[:, self.bank, 0:256]).then_inc(S["rows_copied"].sem, 1)

            def turn(self, pe, j):
                pe.wait_ge(*at("rows_copied", j + 1))
                which = const("streams")[:, 4:6] if self.job[j][0] == 4 else const("streams")[:, 0:4]
                n = which.shape[1]
                for q in range(2):
                    ins = nc.tensor.matmul(PS[:, self.bank, q * n:(q + 1) * n], self.rows[:, q * P:(q + 1) * P], which, start=True, stop=True)
                ins.then_inc(S["columns_ready"].sem, 1)

            def take(self, dve, j):
                l, c, _ = self.job[j]
                dve.wait_ge(*at("columns_ready", j + 1))
                bias = col("b_ada_2" if l == 4 else f"l{l}_b_ada")[:, 4 * c:4 * c + 4]
                nc.vector.tensor_tensor(modulation(l)[:, 4 * c:4 * c + 4, :].rearrange("p (h q) s -> p h q s", h=2), self.turned(j),
                                        bias.rearrange("p (h q) -> p h q", h=2).unsqueeze(3).to_broadcast([P, 2, 2, 1 if l == 4 else 2]),
                                        ALU.add).then_inc(
                    S["columns_taken"].sem, 1)

            def passed(self):
                for n in ("rows_copied", "columns_ready", "columns_taken"):
                    S[n].passed(len(self.job))

        def modulation(l):
            return MOD[:, l, :].rearrange("p (m s) -> p m s", s=1 if l == 4 else 2)

        LATENT, CONTEXT, ALL = slice(0, LAT), slice(LAT, TOK), slice(0, TOK)

        def square(act, k, tok, sq):
            nc.scalar.activation(sq[:, k, tok], XT[:, k, tok], ACT.Square).then_inc(S["squares_ready"].sem, 1)

        def sum_squares(pe, tok, sums, sq):
            for k in range(KT):
                pe.wait_ge(*at("squares_ready", k + 1))
                ins = nc.tensor.matmul(sums, ones, sq[:, k, tok], start=(k == 0), stop=(k == KT - 1))
            ins.then_inc(S["square_sum_ready"].sem, 1)

        def root(act, sums, tok, nth=0):
            act.wait_ge(*at("square_sum_ready", nth + 1))
            nc.scalar.activation(RMS[:, tok], sums, ACT.Sqrt, bias=const("eps"), scale=1.0 / D).then_inc(S["rms_ready"].sem, 1)

        def inverse(dve, tok, nth=0):
            dve.wait_ge(*at("rms_ready", nth + 1))
            dve_chain.link(dve, nc.vector.reciprocal(RSTD[:, tok], RMS[:, tok]))

        def residual(dve, tok):
            for k in range(KT):
                dve_chain.link(dve, nc.vector.tensor_tensor(YT[:, k, tok], YT[:, k, tok], RSTD[:, tok], ALU.mult))
                nc.vector.tensor_tensor(XT[:, k, tok], YT[:, k, tok], XT[:, k, tok], ALU.add).then_inc(S["residual_ready"].sem, 1)

        def norm_vector(dve, l, g_pre, streams, pending=False, part=0):
            m = modulation(l)[:, 3 * KT * part:, :]
            dve_chain.link(dve, nc.vector.scalar_tensor_tensor(GAIN[:, :, 0:streams], m[:, KT:2 * KT, :], 1.0,
                                                               col(g_pre).unsqueeze(2).to_broadcast([P, KT, streams]), ALU.add, ALU.mult))
            for tok in (LATENT, CONTEXT)[:streams]:
                if pending and tok is CONTEXT:
                    inverse(dve, CONTEXT)
                    residual(dve, CONTEXT)
                    inverse(dve, CONTEXT, 1)
                for k in range(KT):
                    nc.vector.tensor_tensor(HT[:, k, tok], XT[:, k, tok], RSTD[:, tok], ALU.mult).then_inc(S["normed_ready"].sem, 1)

        def norm_scalar(act, l, streams, pending=False, part=0):
            if pending:
                root(act, PS[:, 6, 0:LAT], CONTEXT)
            for s, tok in enumerate((LATENT, CONTEXT)[:streams]):
                if pending and tok is CONTEXT:
                    for k in range(KT):
                        act.wait_ge(*at("residual_ready", k + 1))
                        square(act, k, CONTEXT, SQ)
                    root(act, PS[:, 7, 0:LAT], CONTEXT, 1)
                for k in range(KT):
                    act.wait_ge(*at("normed_ready", s * KT + k + 1))
                    nc.scalar.activation(HT[:, k, tok], HT[:, k, tok], ACT.Identity, bias=modulation(l)[:, 3 * KT * part + k, s:s + 1],
                                         scale=GAIN[:, k, s:s + 1]).then_inc(S["h_ready"].sem, 1)

        def first_tiles(pe, pending, tiles, product):
            if pending:
                nc.tensor.matmul(PS[:, 6, 0:LAT], ones, SQ[:, 0, CONTEXT], start=True, stop=True).then_inc(
                    S["square_sum_ready"].sem, 1)
            for s, tok in enumerate((LATENT, CONTEXT)):
                for j, streams, done in tiles:
                    if pending and tok is LATENT and j == 3:
                        sum_squares(pe, CONTEXT, PS[:, 7, 0:LAT], SQ)
                    if s < streams:
                        for k in range(KT):
                            pe.wait_ge(*at("h_ready", s * KT + k + 1))
                            ins = product(j, k, tok)
                        if s == streams - 1:
                            ins.then_inc(done[0], 1)

        def norm_passed(streams, pending=False):
            S["normed_ready"].passed(KT * streams)
            S["h_ready"].passed(KT * streams)
            if pending:
                S["residual_ready"].passed(KT)
                S["squares_ready"].passed(KT)
                S["square_sum_ready"].passed(2)
                S["rms_ready"].passed(2)

        arena = Arena()
        tok0, _, vec_rows = arena.take(TT, D), arena.take(KT * TOK), arena.take(3, P)
        early = consts_at["eps"][1]
        mods = Modulations(modulation_chunks(0, 0, 4), arena.take(256), 7)
        with nc.Block() as block:

            @block.sync
            def _(sp):
                sp.dma_start(vec_rows, t["vector_rows"].rearrange("r p n -> p r n")).then_inc(S["vectors_loaded"].sem, 16)
                sp.dma_start(CONST[:, 0:early], t["consts"][:, 0:early]).then_inc(S["consts_loaded"].sem, 16)
                sp.dma_start(tok0[:, 0:2, :], t["x"].rearrange("o (a p) d -> p (o a) d", p=P)).then_inc(S["tokens_loaded"].sem, 16)
                sp.dma_start(tok0[:, 2:4, :], t["ctx"].rearrange("o (a p) d -> p (o a) d", p=P)).then_inc(S["tokens_loaded"].sem, 16)
                ws.load_until(sp, 1)
                sp.dma_start(BC[:], t["broadcast_row"].partition_broadcast(P)).then_inc(S["late_loaded"].sem, 16)
                sp.dma_start(CONST[:, early:], t["consts"][:, early:]).then_inc(S["late_loaded"].sem, 16)
                ws.load_until(sp, mods.end)

            @block.gpsimd
            def _(pool):
                nc.gpsimd.memset(COND[:], 0.0).then_inc(S["a_ready"].sem, 1)

            @block.tensor
            def _(pe):
                pe.wait_ge(*at("consts_loaded", 16))
                pe.wait_ge(*at("vectors_loaded", 16))
                for r in range(3):
                    ins = nc.tensor.transpose(PS[:, 0, r * P:(r + 1) * P], vec_rows[:, r, :], ident)
                ins.then_inc(S["c_ready"].sem, 1)
                pe.wait_ge(*at("tokens_loaded", 32))
                for k in range(KT):
                    if k == 0 or k >= 6:
                        pe.wait_ge(*at("transposed_taken", k - 5) if k else at("cond_ready", 1))
                    for a in range(TT):
                        ins = nc.tensor.transpose(PS[:, k % 6, a * P:(a + 1) * P], tok0[:, a, k * P:(k + 1) * P], ident)
                    ins.then_inc(S["transposed"].sem, 1)
                sum_squares(pe, ALL, PS[:, 6, :], SQ)
                for j in range(len(mods.job)):
                    mods.multiply(pe, j)
                    mods.turn(pe, j)
                pe.wait_ge(*at("late_loaded", 32))

            @block.scalar
            def _(act):
                act.wait_ge(*at("c_ready", 1))
                act_chain.link(act, nc.scalar.copy(COLS[:], PS[:, 0, 0:3 * P].rearrange("p (r n) -> p r n", r=3)))
                act.wait_ge(*at("a_ready", 1))
                for n, name in enumerate(("c", "c_ctx", "c_2")):
                    ins = nc.scalar.activation(COND[:, :, n], col(name), ACT.Silu)
                ins.then_inc(S["cond_ready"].sem, 1)
                for k in range(KT):
                    act.wait_ge(*at("transposed_taken", k + 1))
                    square(act, k, ALL, SQ)
                root(act, PS[:, 6, :], ALL)
                for j in range(len(mods.job)):
                    mods.copy(act, j)

            @block.vector
            def _(dve):
                for k in range(KT):
                    dve.wait_ge(*at("transposed", k + 1))
                    nc.vector.tensor_copy(XT[:, k, :], PS[:, k % 6, :]).then_inc(S["transposed_taken"].sem, 1)
                inverse(dve, ALL)
                dve.wait_ge(*at("cond_ready", 1))
                for j in range(len(mods.job)):
                    mods.take(dve, j)

        S["consts_loaded"].passed(16)
        S["tokens_loaded"].passed(32)
        S["vectors_loaded"].passed(16)
        S["late_loaded"].passed(32)
        S["transposed"].passed(KT)
        S["transposed_taken"].passed(KT)
        for n in ("cond_ready", "a_ready", "c_ready", "square_sum_ready", "rms_ready"):
            S[n].passed(1)
        S["squares_ready"].passed(KT)
        mods.passed()

        def project_out(l, ot, streams):
            first = ws.first[f"l{l}_w_out"]
            tiles = [(s, m) for s in range(streams) for m in range(KT)]
            done, n_plain = tile_signals([first + m // 4 if s == streams - 1 and m % 4 == 3 else None for s, m in tiles])
            beside = streams == 2
            with nc.Block() as block:

                @block.sync
                def _(sp):
                    ws.load_until(sp, first + 2)

                @block.tensor
                def _(pe):
                    def sum_tiles():
                        pe.wait_ge(*at("c_ready", 1))
                        nc.tensor.matmul(PS[:, 4, 0:LAT], ones, SQ[:, 0, LATENT], start=True, stop=True).then_inc(
                            S["square_sum_ready"].sem, 1)

                    for j, (s, m) in enumerate(tiles):
                        if s == 0 and m % 4 == 0:
                            ws.wait(pe, first + m // 4)
                        w = ws.view(first + m // 4)
                        if j >= 4:
                            pe.wait_ge(*at("tile_taken", j - 3))
                        for k in range(KT):
                            ins = nc.tensor.matmul(PS[:, j % 4, 0:LAT], w[:, k, (m % 4) * P:(m % 4 + 1) * P],
                                                   ot[:, k, s * LAT:(s + 1) * LAT], start=(k == 0), stop=(k == KT - 1))
                        ins.then_inc(done[j][0], 1)
                        if (s, m) == (1, 0):
                            sum_tiles()
                        if (s, m) == (1, 5):
                            sum_squares(pe, LATENT, PS[:, 5, 0:LAT], SQ)
                    if not beside:
                        sum_tiles()
                        sum_squares(pe, LATENT, PS[:, 5, 0:LAT], SQ)

                @block.scalar
                def _(act):
                    def squares():
                        for k in range(KT):
                            act.wait_ge(*at("residual_ready", k + 1))
                            square(act, k, LATENT, SQ)

                    act.wait_ge(*at("b_ready", 1))
                    for j, (s, m) in enumerate(tiles):
                        act.wait_ge(*done[j])
                        tok = slice(s * LAT, (s + 1) * LAT)
                        nc.scalar.activation(SQ[:, m, tok], PS[:, j % 4, 0:LAT], ACT.Square).then_inc(S["a_ready"].sem, 1)
                        nc.scalar.activation(YT[:, m, tok], PS[:, j % 4, 0:LAT], ACT.Copy, scale=GATE[:, m, s:s + 1]).then_inc(
                            S["tile_taken"].sem, 1)
                        if (s, m) == (1, 0):
                            root(act, PS[:, 4, 0:LAT], LATENT)
                        if (s, m) == (1, 4):
                            squares()
                        if (s, m) == (1, 6):
                            root(act, PS[:, 5, 0:LAT], LATENT, 1)
                    if not beside:
                        root(act, PS[:, 4, 0:LAT], LATENT)
                        squares()
                        root(act, PS[:, 5, 0:LAT], LATENT, 1)

                @block.vector
                def _(dve):
                    def sum_tiles(s):
                        tok = slice(s * LAT, (s + 1) * LAT)
                        for m in range(1, KT):
                            dve.wait_ge(*at("a_ready", s * KT + m + 1))
                            ins = nc.vector.tensor_tensor(SQ[:, 0, tok], SQ[:, 0, tok], SQ[:, m, tok], ALU.add)
                            if m < KT - 1:
                                dve_chain.link(dve, ins)
                        ins.then_inc(S["c_ready"].sem, 1)

                    nc.vector.tensor_tensor(GATE[:], modulation(l)[:, 2 * KT:3 * KT, :],
                                            col(f"l{l}_g_post").unsqueeze(2).to_broadcast([P, KT, 2]), ALU.mult).then_inc(S["b_ready"].sem, 1)
                    sum_tiles(0)
                    inverse(dve, LATENT)
                    dve.wait_ge(*at("tile_taken", KT))
                    residual(dve, LATENT)
                    inverse(dve, LATENT, 1)
                    if beside:
                        sum_tiles(1)

            S["tile_ready"].passed(n_plain)
            S["tile_taken"].passed(KT * streams)
            S["a_ready"].passed(KT * streams)
            S["b_ready"].passed(1)
            S["c_ready"].passed(streams)
            S["residual_ready"].passed(KT)
            S["squares_ready"].passed(KT)
            for n in ("square_sum_ready", "rms_ready"):
                S[n].passed(2)

        def rope_mix(x, n):
            nc.tensor.matmul(PS[:, 4 + n % 2, 0:LAT], const("swap"), x[:, 0:LAT], start=True, stop=True).then_inc(
                S["rope_mixed"].sem, 1)

        def rope_turn(dve, x, n, tmp):
            dve.wait_ge(*at("rope_mixed", n + 1))
            nc.vector.tensor_tensor(tmp, PS[:, 4 + n % 2, 0:LAT], const("sin"), ALU.mult).then_inc(S["rope_taken"].sem, 1)
            dve_chain.link(dve, nc.vector.tensor_tensor(x[:, 0:LAT], x[:, 0:LAT], const("cos"), ALU.mult))
            dve.wait_ge(*at("rope_taken", n + 1))
            dve_chain.link(dve, nc.vector.tensor_tensor(x[:, 0:LAT], x[:, 0:LAT], tmp, ALU.add))

        def attention(units, scale, score, value, mask_of, sink, gate, together=True, mods=None):
            probs = PW[:, 0:2048].rearrange("p (b h k) -> p b h k", b=2, h=2)
            turned = PW[:, 2048:4096].rearrange("p (b h k) -> p b h k", b=2, h=2)
            mx = ST[:, 0:8].rearrange("p (b s) -> p b s", b=2)
            nm = ST[:, 8:16].rearrange("p (b s) -> p b s", b=2)
            den = ST[:, 16:24].rearrange("p (b s) -> p b s", b=2)
            es = ST[:, 24:32].rearrange("p (b s) -> p b s", b=2)
            rd = ST[:, 32:40].rearrange("p (b s) -> p b s", b=2)
            N = len(units)

            def cols(u):
                return u[2][0] * P, (u[2][-1] + 1) * P

            def heads_at(i):
                return PS[:, 6 if mods else 6 + i % 2, :]

            def beside(i, late):
                n, x = 2 * len(mods.job) if mods else 0, 2 * i + late
                return [(y % 2, y // 2) for y in range(x * n // (2 * N), (x + 1) * n // (2 * N))]

            with nc.Block() as block:

                @block.sync
                def _(sp):
                    ws.load_until(sp, mods.end if mods else ws.done)

                @block.tensor
                def _(pe):
                    def scores(i):
                        a, b = cols(units[i])
                        if i >= 2:
                            pe.wait_ge(*at("scores_used", 2 * (i - 1)))
                        for h in range(2):
                            ins = score(h, units[i], slice(a, b), PS[:, 2 * (i % 2) + h, a:b])
                        ins.then_inc(S["scores_ready"].sem, 1)

                    def turn(i):
                        for h in range(2):
                            pe.wait_ge(*at("probs_ready", 2 * i + h + 1))
                            if i >= 1:
                                pe.wait_ge(*at("turned_copied", 2 * i + h - 1))
                            for j, kt in enumerate(units[i][2]):
                                ins = nc.tensor.transpose(PS[:, 4 + h, j * P:(j + 1) * P],
                                                          probs[:, i % 2, h, kt * P:(kt + 1) * P], ident)
                            ins.then_inc(S["probs_turned"].sem, 1)

                    def mix(i):
                        pe.wait_ge(*at("turned_copied", 2 * i + 2))
                        if i >= (1 if mods else 2):
                            pe.wait_ge(*at("heads_taken", i if mods else i - 1))
                        kts = units[i][2]
                        order = [(j, h) for j in range(len(kts)) for h in range(2)]
                        if not together:
                            order.sort(key=lambda x: x[1])
                        for j, h in order:
                            lhs, place = value(units[i], h, kts[j])
                            ins = nc.tensor.matmul(place(heads_at(i)), lhs, turned[:, i % 2, h, j * P:(j + 1) * P],
                                                   start=(j == 0), stop=(j == len(kts) - 1))
                        ins.then_inc(S["heads_ready"].sem, 1)

                    def modulate(i, late):
                        for half, j in beside(i, late):
                            (mods.turn if half else mods.multiply)(pe, j)

                    scores(0)
                    scores(1)
                    for i in range(N):
                        if i + 2 < N:
                            scores(i + 2)
                        modulate(i, 0)
                        turn(i)
                        if i >= 1:
                            mix(i - 1)
                        modulate(i, 1)
                    mix(N - 1)

                @block.scalar
                def _(act):
                    def exps(i):
                        a, b = cols(units[i])
                        act.wait_ge(*at("max_ready", i + 1))
                        if i >= 2:
                            act.wait_ge(*at("probs_turned", 2 * (i - 1)))
                        for h in range(2):
                            nc.scalar.activation(probs[:, i % 2, h, a:b], PS[:, 2 * (i % 2) + h, a:b], ACT.Exp,
                                                 bias=nm[:, i % 2, h:h + 1], scale=scale,
                                                 accum_out=den[:, i % 2, h:h + 1]).then_inc(S["scores_used"].sem, 1)
                            if sink is not None:
                                head = 2 * units[i][0] + h
                                nc.scalar.activation(es[:, i % 2, h:h + 1], sink[:, head:head + 1], ACT.Exp,
                                                     bias=nm[:, i % 2, h:h + 1]).then_inc(S["exp_ready"].sem, 1)

                    def copies(i):
                        n = len(units[i][2]) * P
                        if i >= 2:
                            act.wait_ge(*at("heads_ready", i - 1))
                        for h in range(2):
                            act.wait_ge(*at("probs_turned", 2 * i + h + 1))
                            nc.scalar.copy(turned[:, i % 2, h, 0:n], PS[:, 4 + h, 0:n]).then_inc(S["turned_copied"].sem, 1)

                    def modulate(i, late):
                        for half, j in beside(i, late):
                            if not half:
                                mods.copy(act, j)

                    exps(0)
                    for i in range(N):
                        if i + 1 < N:
                            exps(i + 1)
                        modulate(i, 0)
                        copies(i)
                        modulate(i, 1)

                @block.vector
                def _(dve):
                    def maxima(i):
                        a, b = cols(units[i])
                        s = PS[:, 2 * (i % 2):2 * (i % 2) + 2, :]
                        dve.wait_ge(*at("scores_ready", i + 1))
                        mask = mask_of(units[i])
                        if mask is not None:
                            w = mask.shape[1]
                            dve_chain.link(dve, nc.vector.tensor_tensor(s[:, :, a:a + w], s[:, :, a:a + w],
                                                                        mask.unsqueeze(1).to_broadcast([P, 2, w]), ALU.add))
                        dve_chain.link(dve, nc.vector.tensor_reduce(mx[:, i % 2, 0:2], s[:, :, a:b], AX, ALU.max))
                        if sink is not None:
                            h = 2 * units[i][0]
                            dve_chain.link(dve, nc.vector.scalar_tensor_tensor(
                                mx[:, i % 2, 2:4], mx[:, i % 2, 0:2], scale, sink[:, h:h + 2], ALU.mult, ALU.max))
                            nc.vector.tensor_scalar(nm[:, i % 2, 0:2], mx[:, i % 2, 2:4], -1.0, None, ALU.mult).then_inc(
                                S["max_ready"].sem, 1)
                        else:
                            nc.vector.tensor_scalar(nm[:, i % 2, 0:2], mx[:, i % 2, 0:2], -scale, None, ALU.mult).then_inc(
                                S["max_ready"].sem, 1)

                    def normalise(i):
                        a, b = cols(units[i])
                        dve.wait_ge(*at("scores_used", 2 * i + 2))
                        if sink is not None:
                            dve.wait_ge(*at("exp_ready", 2 * i + 2))
                            dve_chain.link(dve, nc.vector.tensor_tensor(den[:, i % 2, 0:2], den[:, i % 2, 0:2], es[:, i % 2, 0:2],
                                                                        ALU.add))
                        dve_chain.link(dve, nc.vector.reciprocal(rd[:, i % 2, 0:2], den[:, i % 2, 0:2]))
                        for h in range(2):
                            pr = probs[:, i % 2, h, a:b]
                            nc.vector.tensor_scalar(pr, pr, rd[:, i % 2, h:h + 1], None, ALU.mult).then_inc(
                                S["probs_ready"].sem, 1)

                    def gates(i):
                        dve.wait_ge(*at("heads_ready", i + 1))
                        o, z, src = gate(units[i], heads_at(i))
                        if z is None:
                            nc.vector.tensor_copy(o, src).then_inc(S["heads_taken"].sem, 1)
                        else:
                            nc.vector.tensor_tensor(o, src, z, ALU.mult).then_inc(S["heads_taken"].sem, 1)

                    def modulate(i, late):
                        for half, j in beside(i, late):
                            if half:
                                mods.take(dve, j)

                    maxima(0)
                    maxima(1)
                    for i in range(N):
                        normalise(i)
                        modulate(i, 0)
                        if i + 2 < N:
                            maxima(i + 2)
                        if i >= 1:
                            gates(i - 1)
                        modulate(i, 1)
                    gates(N - 1)

            for n, k in (("scores_ready", 1), ("max_ready", 1), ("scores_used", 2), ("exp_ready", 2 if sink is not None else 0),
                         ("probs_ready", 2), ("probs_turned", 2), ("turned_copied", 2), ("heads_ready", 1), ("heads_taken", 1)):
                S[n].passed(k * N)
            if mods:
                mods.passed()

        def window_layer(i, need_ctx):
            w_in = f"l{i}_w_in"
            first = ws.first[w_in]
            a = Arena()
            qt, kt_, zt = a.take(8, TOK), a.take(2, TOK), a.take(8, TOK)
            keys = a.take(4, TOK)
            v = a.take(TT, 256)
            tmp = a.take(LAT)
            mods = Modulations(BESIDE[i], a.take(256), 7)
            qtok = TOK if need_ctx else LAT
            pending = i > 0
            tiles = [("q", m, m // 4, m % 4 * P, qtok) for m in range(8)]
            tiles += [("k", m, 2, m * P, TOK) for m in range(2)] + [("v", m, 2, 256, 256) for m in range(TT)]
            tiles += [("z", m, 3 + m // 4, m % 4 * P, qtok) for m in range(8)]
            last = [j + 1 == len(tiles) or tiles[j + 1][2] != x[2] for j, x in enumerate(tiles)]
            done, n_plain = tile_signals([first + x[2] if e else None for x, e in zip(tiles, last)])
            roped = [j for j, x in enumerate(tiles) if x[0] in "qk"]
            with nc.Block() as block:

                @block.sync
                def _(sp):
                    ws.load_until(sp, first + 5)

                @block.tensor
                def _(pe):
                    def rope(n):
                        kind, m, _, _, _ = tiles[roped[n]]
                        pe.wait_ge(*at("tile_taken", roped[n] + 1))
                        if n >= 2:
                            pe.wait_ge(*at("rope_taken", n - 1))
                        rope_mix((qt if kind == "q" else kt_)[:, m, :], n)

                    def latent_or_context(j, k, t):
                        return nc.tensor.matmul(PS[:, j, t], ws.view(first)[:, k, j * P:(j + 1) * P], HT[:, k, t], start=(k == 0),
                                                stop=(k == KT - 1))

                    ws.wait(pe, first)
                    first_tiles(pe, pending, [(j, qtok // LAT, done[j]) for j in range(4)], latent_or_context)
                    for j, (kind, m, c, x, tok) in enumerate(tiles):
                        if j >= 4:
                            if tiles[j - 1][2] != c:
                                ws.wait(pe, first + c)
                            w = ws.view(first + c)
                            pe.wait_ge(*at("tile_taken", j - 3))
                            if j == 8:
                                pe.wait_ge(*at("h_ready", 2 * KT))
                            for k in range(KT):
                                if kind == "v":
                                    ops = HT[:, k, m * P:(m + 1) * P], w[:, k, x:x + tok]
                                else:
                                    ops = w[:, k, x:x + P], HT[:, k, 0:tok]
                                ins = nc.tensor.matmul(PS[:, j % 4, 0:tok], *ops, start=(k == 0), stop=(k == KT - 1))
                            ins.then_inc(done[j][0], 1)
                        if 1 <= j <= len(roped):
                            rope(j - 1)

                @block.scalar
                def _(act):
                    norm_scalar(act, i, 2, pending)
                    for j, (kind, m, c, x, tok) in enumerate(tiles):
                        act.wait_ge(*done[j])
                        dst = {"q": qt, "k": kt_, "v": v, "z": zt}[kind][:, m, 0:tok]
                        nc.scalar.activation(dst, PS[:, j % 4, 0:tok], ACT.Silu if kind == "z" else ACT.Copy).then_inc(
                            S["tile_taken"].sem, 1)

                @block.vector
                def _(dve):
                    norm_vector(dve, i, f"l{i}_g_pre", 2, pending)
                    for n, j in enumerate(roped):
                        kind, m, _, _, _ = tiles[j]
                        dve.wait_ge(*at("tile_taken", j + 1))
                        rope_turn(dve, (qt if kind == "q" else kt_)[:, m, :], n, tmp)
                    for h in range(4):
                        src = kt_[64 * (h % 2):64 * (h % 2) + 64, h // 2, :]
                        dve_chain.add(nc.vector.tensor_copy(keys[0:64, h, :], src))
                        dve_chain.add(nc.vector.tensor_copy(keys[64:128, h, :], src))

            norm_passed(2, pending)
            S["tile_ready"].passed(n_plain)
            S["tile_taken"].passed(len(tiles))
            S["rope_mixed"].passed(len(roped))
            S["rope_taken"].passed(len(roped))
            ws.done = first + 5

            def score(h, u, k, out):
                half = slice(64 * h, 64 * h + 64)
                return nc.tensor.matmul(out, qt[half, u[0], u[1] * P:(u[1] + 1) * P], keys[half, u[0] // 2, k], start=True, stop=True)

            def value(u, h, kt):
                j = u[0] // 2
                return v[:, kt, j * 64:(j + 1) * 64], lambda bank: bank[64 * h:64 * h + 64, 0:P]

            def gate(u, bank):
                q = slice(u[1] * P, (u[1] + 1) * P)
                return HT[:, u[0], q], zt[:, u[0], q], bank[:, 0:P]

            units = [(m, q, [0, 1, 2, 3]) for m in range(8) for q in range(2)]
            if need_ctx:
                units += [(m, q, [2, 3]) for m in range(8) for q in (2, 3)]
            attention(units, 64 ** -0.5, score, value, lambda u: window[:, u[1], :] if u[1] < 2 else None,
                      bcast(f"l{i}_sink"), gate, mods=mods)
            project_out(i, HT, qtok // LAT)

        window_layer(0, True)

        def latent_layer():
            heads, nope, rot, rank_q, rank_kv = 8, 128, 64, 256, 128
            a = Arena()
            qn, qr, kn = a.take(heads, TOK), a.take(heads // 2, TOK), a.take(heads, TOK)
            kpe, v, zt = a.take(TOK), a.take(TT, heads * P), a.take(8, TOK)
            lowrank, sq, tmp = a.take(3, TOK), a.take(3, TOK), a.take(LAT)
            rstd = [PW[:, 0:TOK], PW[:, TOK:2 * TOK]]
            rinv = [PW[:, 2 * TOK:3 * TOK], PW[:, 3 * TOK:4 * TOK]]
            c_in, c_uq, c_ukv = ws.first["l1_w_in"], ws.first["l1_w_uq"], ws.first["l1_w_ukv"]
            tiles = [("low", m, c_in) for m in range(3)] + [("kpe", 0, c_in)]
            tiles += [("z", m, c_in + 1 + m // 4) for m in range(8)]
            tiles += [("qr", m, c_uq) for m in range(4)] + [("qn", m, c_uq) for m in range(8)]
            tiles += [("kn", m, c_ukv) for m in range(8)] + [("v", m, c_ukv) for m in range(8)]
            last = [j + 1 == len(tiles) or tiles[j + 1][2] != x[2] for j, x in enumerate(tiles)]
            done, n_plain = tile_signals([x[2] if e else None for x, e in zip(tiles, last)])
            roped = [j for j, x in enumerate(tiles) if x[0] in ("kpe", "qr")]
            with nc.Block() as block:

                @block.sync
                def _(sp):
                    ws.load_until(sp, c_ukv + 1)

                @block.tensor
                def _(pe):
                    def rope(n):
                        kind, m, _ = tiles[roped[n]]
                        pe.wait_ge(*at("tile_taken", roped[n] + 1))
                        if n >= 2:
                            pe.wait_ge(*at("rope_taken", n - 1))
                        rope_mix(kpe if kind == "kpe" else qr[:, m, :], n)

                    def square_sums():
                        for n, (x, y) in enumerate(((0, 2), (2, 3))):
                            for m in range(x, y):
                                pe.wait_ge(*at("a_ready", m + 1))
                                ins = nc.tensor.matmul(PS[:, 6 + n, :], ones, sq[:, m, :], start=(m == x), stop=(m == y - 1))
                            ins.then_inc(S["b_ready"].sem, 1)

                    def latent_or_context(j, k, t):
                        w = ws.view(c_in)
                        if tiles[j][0] == "low":
                            return nc.tensor.matmul(PS[:, j, t], w[:, k, j * P:(j + 1) * P], HT[:, k, t], start=(k == 0), stop=(k == KT - 1))
                        for half in range(2):
                            ins = nc.tensor.matmul(PS[rot * half:rot * half + rot, j, t], w[:, k, 384:384 + rot], HT[:, k, t],
                                                   start=(k == 0), stop=(k == KT - 1))
                        return ins

                    ws.wait(pe, c_in)
                    first_tiles(pe, True, [(j, 2, done[j]) for j in range(4)], latent_or_context)
                    for j, (kind, m, c) in enumerate(tiles):
                        if j < 4:
                            continue
                        if tiles[j - 1][2] != c:
                            ws.wait(pe, c)
                        w = ws.view(c)
                        pe.wait_ge(*at("tile_taken", j - 3))
                        o = PS[:, j % 4, :]
                        if kind == "z":
                            for k in range(KT):
                                ins = nc.tensor.matmul(o, w[:, k, m % 4 * P:m % 4 * P + P], HT[:, k, :], start=(k == 0), stop=(k == KT - 1))
                        elif kind == "qr":
                            pe.wait_ge(*at("scaled_ready", 2))
                            for h in range(2):
                                x = (2 * m + h) * (nope + rot) + nope
                                for k in range(2):
                                    ins = nc.tensor.matmul(o[64 * h:64 * h + 64, :], w[:, k, x:x + rot], lowrank[:, k, :],
                                                           start=(k == 0), stop=(k == 1))
                        elif kind == "qn":
                            x = m * (nope + rot)
                            for k in range(2):
                                ins = nc.tensor.matmul(o, w[:, k, x:x + nope], lowrank[:, k, :], start=(k == 0), stop=(k == 1))
                        elif kind == "kn":
                            pe.wait_ge(*at("scaled_ready", 3))
                            ins = nc.tensor.matmul(o, w[:, 0, m * 256:m * 256 + 128], lowrank[:, 2, :], start=True, stop=True)
                        else:
                            wv = w[:, 0, :].rearrange("p (h n) -> p h n", n=256)[:, m % 2 * 4:m % 2 * 4 + 4, 128:256]
                            ins = nc.tensor.matmul(o, lowrank[:, 2, m // 2 * P:(m // 2 + 1) * P], wv, start=True, stop=True)
                        ins.then_inc(done[j][0], 1)
                        if kind == "z" and m == 0:
                            square_sums()
                            rope(0)
                        if j - 1 in roped[1:]:
                            rope(roped.index(j - 1))

                @block.scalar
                def _(act):
                    norm_scalar(act, 1, 2, True)
                    for j, (kind, m, c) in enumerate(tiles):
                        act.wait_ge(*done[j])
                        o = PS[:, j % 4, :]
                        dst = {"low": lowrank[:, m % 3, :], "kpe": kpe, "z": zt[:, m, :], "qr": qr[:, m % 4, :], "qn": qn[:, m, :],
                               "kn": kn[:, m, :], "v": v[:, m // 2, m % 2 * 512:m % 2 * 512 + 512]}[kind]
                        if kind == "low":
                            nc.scalar.activation(sq[:, m, :], o, ACT.Square).then_inc(S["a_ready"].sem, 1)
                        if kind == "z" and m == 2:
                            for n in range(2):
                                act.wait_ge(*at("inverse_ready", n + 1))
                                nc.scalar.activation(rstd[n], rinv[n], ACT.Sqrt).then_inc(S["rstd_ready"].sem, 1)
                        nc.scalar.activation(dst, o, ACT.Silu if kind == "z" else ACT.Copy).then_inc(S["tile_taken"].sem, 1)

                @block.vector
                def _(dve):
                    norm_vector(dve, 1, "l1_g_pre", 2, True)
                    for n, width in enumerate((rank_q, rank_kv)):
                        dve.wait_ge(*at("b_ready", n + 1))
                        dve_chain.link(dve, nc.vector.tensor_scalar(rinv[n], PS[:, 6 + n, :], 1.0 / width, EPS, ALU.mult, ALU.add))
                        nc.vector.reciprocal(rinv[n], rinv[n]).then_inc(S["inverse_ready"].sem, 1)
                    dve.wait_ge(*at("tile_taken", 3))
                    for m in range(3):
                        dve.wait_ge(*at("rstd_ready", 1 + m // 2))
                        g = col("l1_g_kva") if m == 2 else col("l1_g_qa")[:, m:m + 1]
                        nc.vector.scalar_tensor_tensor(lowrank[:, m, :], lowrank[:, m, :], g, rstd[m // 2], ALU.mult,
                                                       ALU.mult).then_inc(S["scaled_ready"].sem, 1)
                    for n, j in enumerate(roped):
                        kind, m, _ = tiles[j]
                        dve.wait_ge(*at("tile_taken", j + 1))
                        rope_turn(dve, kpe if kind == "kpe" else qr[:, m, :], n, tmp)

            norm_passed(2, True)
            S["tile_ready"].passed(n_plain)
            S["tile_taken"].passed(len(tiles))
            for n, k in (("a_ready", 3), ("b_ready", 2), ("inverse_ready", 2), ("rstd_ready", 2),
                         ("scaled_ready", 3), ("rope_mixed", len(roped)), ("rope_taken", len(roped))):
                S[n].passed(k)
            ws.done = c_ukv + 1

            def score(h, u, k, out):
                head, q, half = 2 * u[0] + h, slice(u[1] * P, (u[1] + 1) * P), slice(64 * h, 64 * h + 64)
                nc.tensor.matmul(out, qn[:, head, q], kn[:, head, k], start=True, stop=False)
                return nc.tensor.matmul(out, qr[half, u[0], q], kpe[half, k], start=False, stop=True)

            def value(u, h, kt):
                head = 2 * u[0] + h
                return v[:, kt, head * P:(head + 1) * P], lambda bank: bank[:, h * P:(h + 1) * P]

            def gate(u, bank):
                q, pair = slice(u[1] * P, (u[1] + 1) * P), slice(2 * u[0], 2 * u[0] + 2)
                return HT[:, pair, q], zt[:, pair, q], bank[:, 0:2 * P].rearrange("p (h q) -> p h q", h=2)

            units = [(m, q, [0, 1, 2, 3]) for m in range(4) for q in range(2)]
            units += [(m, q, [2, 3]) for m in range(4) for q in (2, 3)]
            attention(units, (nope + rot) ** -0.5, score, value, lambda u: None, None, gate, together=False)
            project_out(1, HT, 2)

        latent_layer()

        def exact_log1p(dve, r, e, x, y):
            dve_chain.link(dve, nc.vector.tensor_scalar(x, e, 1.0 / 3, -0.5, ALU.mult, ALU.add))
            dve_chain.link(dve, nc.vector.tensor_tensor(x, x, e, ALU.mult))
            dve_chain.link(dve, nc.vector.scalar_tensor_tensor(x, x, 1.0, e, ALU.add, ALU.mult))
            dve_chain.link(dve, nc.vector.tensor_tensor(x, x, r, ALU.subtract))
            dve_chain.link(dve, nc.vector.tensor_scalar(y, e, 1e-3, None, ALU.is_lt))
            dve_chain.link(dve, nc.vector.tensor_tensor(x, x, y, ALU.mult))
            dve_chain.link(dve, nc.vector.tensor_tensor(r, r, x, ALU.add))

        def memory_layer():
            H, DV = 4, 256
            order = [[2, 3, 0, 1], [3, 2, 1, 0]]
            a = Arena()
            va = a.take(TT, H, DV + 1)
            qk = a.take(8, TOK)
            ktok = a.take(TT, H, P)
            og = a.take(TT, D)
            raw_at = a.at
            raw = a.take(8, 2, LAT + 4)
            logd = a.take(32, P)
            a2 = Arena(raw_at)
            zt = a2.take(8, TOK)
            c_in = ws.first["l2_w_in"]
            hs = ring[:, ws.first["l2_w_z"] % SLOTS, :].rearrange("p (a h v) -> p a h v", a=TT, h=H)
            taps = col("l2_conv").rearrange("p (j k) -> p j k", j=5)

            small = [0]

            def take(*shape):
                n = 1
                for x in shape:
                    n *= x
                v = SM[:, small[0]:small[0] + n]
                small[0] += n
                names = "abcd"[:len(shape)]
                return v if len(shape) == 1 else v.rearrange(f"p ({' '.join(names)}) -> p {' '.join(names)}",
                                                             **dict(zip(names, shape)))

            gates = take(2, 4, 2, 4)
            logf, ex, t1, t2 = take(2, 4, 4), take(2, 4, 4), take(2, 4, 4), take(2, 4, 4)
            small_cum = small[0]
            cum, tot, u, rowmax, umax = (take(2, 4, 4) for _ in range(5))
            mloc, am, mst = take(2, 4, 4), take(2, 4, 4), take(2, 5, 4)
            keep, gain, at_, nmt, emt, eend, rs, rden = (take(2, 4, 4) for _ in range(8))

            def flat(x):
                return x.rearrange("p a b c -> p (a b c)")

            tiles = [("qk", m, m // 4) for m in range(8)] + [("v", (c, m), 2 + c) for c in range(2) for m in range(TT)]
            tiles += [("o", (c, m), 4 + c) for c in range(2) for m in range(TT)]
            tiles += [("g", 0, 6)]
            last = [j + 1 == len(tiles) or tiles[j + 1][2] != x[2] for j, x in enumerate(tiles)]
            done, n_plain = tile_signals([c_in + x[2] if e else None for x, e in zip(tiles, last)])
            with nc.Block() as block:

                @block.sync
                def _(sp):
                    ws.load_until(sp, c_in + 7)

                @block.gpsimd
                def _(pool):
                    pool.wait_ge(*at("h_ready", 2 * KT))
                    nc.gpsimd.memset(raw[:, :, :, 0:2], 0.0)
                    nc.gpsimd.memset(raw[:, :, :, LAT + 2:LAT + 4], 0.0).then_inc(S["a_ready"].sem, 1)
                    nc.gpsimd.memset(va[:, :, :, DV:DV + 1], 1.0)

                @block.tensor
                def _(pe):
                    def latent_or_context(j, k, t):
                        return nc.tensor.matmul(PS[:, j, t], ws.view(c_in)[:, k, j * P:(j + 1) * P], HT[:, k, t], start=(k == 0),
                                                stop=(k == KT - 1))

                    ws.wait(pe, c_in)
                    first_tiles(pe, True, [(j, 2, done[j]) for j in range(4)], latent_or_context)
                    for j, (kind, m, c) in enumerate(tiles):
                        if j < 4:
                            continue
                        if tiles[j - 1][2] != c:
                            ws.wait(pe, c_in + c)
                        w = ws.view(c_in + c)
                        pe.wait_ge(*at("tile_taken", j - 3))
                        o = PS[:, j % 4, :]
                        for k in range(KT):
                            if kind == "qk":
                                ins = nc.tensor.matmul(o, w[:, k, m % 4 * P:m % 4 * P + P], HT[:, k, :], start=(k == 0), stop=(k == KT - 1))
                            elif kind != "g":
                                ins = nc.tensor.matmul(o, HT[:, k, m[1] * P:(m[1] + 1) * P], w[:, k, :], start=(k == 0), stop=(k == KT - 1))
                        if kind == "g":
                            for n in range(TT):
                                for k in range(KT):
                                    ins = nc.tensor.matmul(o[:, n * 16:n * 16 + 16], HT[:, k, n * P:(n + 1) * P], w[:, k, :],
                                                           start=(k == 0), stop=(k == KT - 1))
                        ins.then_inc(done[j][0], 1)
                        if kind == "o" and m == (1, 3):
                            pe.wait_ge(*at("c_ready", 4))
                            for n in range(TT):
                                for h in range(H):
                                    ins = nc.tensor.transpose(PS[:, 4 + n, h * P:(h + 1) * P], qk[:, 4 + h, n * P:(n + 1) * P], ident)
                                ins.then_inc(S["transposed"].sem, 1)

                @block.scalar
                def _(act):
                    norm_scalar(act, 2, 2, True)
                    for j, (kind, m, c) in enumerate(tiles):
                        act.wait_ge(*done[j])
                        o = PS[:, j % 4, :]
                        if kind == "g":
                            break
                        if kind == "qk":
                            dst, o = raw[:, m, :, 2:LAT + 2], o.rearrange("p (s t) -> p s t", s=2)
                        elif kind == "v":
                            dst, o = va[:, m[1], 2 * m[0]:2 * m[0] + 2, 0:DV], o.rearrange("p (h v) -> p h v", h=2)
                        else:
                            dst = og[:, m[1], m[0] * CH:(m[0] + 1) * CH]
                        nc.scalar.activation(dst, o, ACT.Sigmoid if kind == "o" else ACT.Copy).then_inc(S["tile_taken"].sem, 1)
                        if kind == "v" and m[0] == 1:
                            for n in range(2 * m[1], 2 * m[1] + 2):
                                act.wait_ge(*at("b_ready", n + 1))
                                nc.scalar.activation(qk[:, n, :], qk[:, n, :], ACT.Silu).then_inc(S["scaled_ready"].sem, 1)
                    for n in range(TT):
                        act.wait_ge(*at("transposed", n + 1))
                        nc.scalar.copy(ktok[:, n, :, :], PS[:, 4 + n, :].rearrange("p (h d) -> p h d", h=H)).then_inc(
                            S["d_ready"].sem, 1)

                @block.vector
                def _(dve):
                    norm_vector(dve, 2, "l2_g_pre", 2, True)
                    dve.wait_ge(*at("a_ready", 1))
                    for m in range(8):
                        dve.wait_ge(*at("tile_taken", m + 1))
                        o = qk[:, m, :].rearrange("p (s t) -> p s t", s=2)
                        dve_chain.link(dve, nc.vector.tensor_scalar(o, raw[:, m, :, 0:LAT], taps[:, 0, m:m + 1], None, ALU.mult))
                        for j in range(1, 5):
                            ins = nc.vector.scalar_tensor_tensor(o, raw[:, m, :, j:j + LAT], taps[:, j, m:m + 1], o, ALU.mult, ALU.add)
                            if j < 4:
                                dve_chain.link(dve, ins)
                        ins.then_inc(S["b_ready"].sem, 1)
                    for m in range(4, 8):
                        dve.wait_ge(*at("scaled_ready", m + 1))
                        nc.vector.tensor_scalar(qk[:, m, :], qk[:, m, :], P ** -0.5, None, ALU.mult).then_inc(S["c_ready"].sem, 1)
                    dve.wait_ge(*done[-1])
                    for d in range(2):
                        for j in range(4):
                            n = order[d][j]
                            x = PS[:, (len(tiles) - 1) % 4, n * 16 + d * 8:n * 16 + d * 8 + 8]
                            dve_chain.add(nc.vector.tensor_tensor(gates[:, d, j, :, :], x.rearrange("p (a h) -> p a h", a=2),
                                                                  bcast("l2_b_gate")[:, d * 8:d * 8 + 8].rearrange("p (a h) -> p a h", a=2), ALU.add))

            norm_passed(2, True)
            S["tile_ready"].passed(n_plain)
            S["tile_taken"].passed(len(tiles) - 1)
            for n, k in (("a_ready", 1), ("b_ready", 8), ("c_ready", 4), ("d_ready", TT), ("scaled_ready", 8), ("transposed", TT)):
                S[n].passed(k)
            z_in, early_z = c_in + 7, 4
            z_done, z_plain = tile_signals([None, None, None, z_in, None, None, None, z_in + 1])

            def z_product(pe, m, k, bank):
                if m % 4 == 0 and k == 0:
                    ws.wait(pe, z_in + m // 4)
                ins = nc.tensor.matmul(PS[:, bank, :], ws.view(z_in + m // 4)[:, k, m % 4 * P:m % 4 * P + P], HT[:, k, :], start=(k == 0),
                                       stop=(k == KT - 1))
                if k == KT - 1:
                    ins.then_inc(z_done[m][0], 1)

            ws.done = z_in

            with nc.Block() as block:

                @block.sync
                def _(sp):
                    ws.load_until(sp, z_in)

                @block.tensor
                def _(pe):
                    for k in range(KT):
                        z_product(pe, 0, k, 4)
                    pe.wait_ge(*at("b_ready", 1))
                    f = flat(logf)
                    nc.tensor.matmul(PS[:, 0, 0:16], const("upto"), f[:, 0:16], start=True, stop=True)
                    nc.tensor.matmul(PS[:, 0, 16:32], const("from"), f[:, 16:32], start=True, stop=True)
                    nc.tensor.matmul(PS[:, 0, 32:64], ones, f, start=True, stop=True).then_inc(S["c_ready"].sem, 1)
                    for k in range(2):
                        z_product(pe, 1, k, 5)
                    pe.wait_ge(*at("d_ready", 1))
                    for g in range(8):
                        if g >= 2:
                            pe.wait_ge(*at("f_ready", g - 1))
                        for i in range(4):
                            c = 4 * g + i
                            ins = nc.tensor.matmul(PS[:, 1 + g % 2, i * P:(i + 1) * P], flat(u)[:, c:c + 1].to_broadcast([P, P]), ident,
                                                   start=True, stop=True)
                        ins.then_inc(S["e_ready"].sem, 1)
                        if 1 <= g < 7:
                            z_product(pe, 1, g + 1, 5)
                    for m in (2, 3):
                        for k in range(KT):
                            z_product(pe, m, k, 4 + m)

                @block.scalar
                def _(act):
                    act.wait_ge(*at("a_ready", 1))
                    act_chain.add(nc.scalar.activation(flat(ex), flat(t1), ACT.Exp, scale=-1.0))
                    act.wait_ge(act_chain.sem, act_chain.n)
                    nc.scalar.activation(flat(logf), flat(ex), ACT.Ln, bias=1.0).then_inc(S["g_ready"].sem, 1)
                    act.wait_ge(*at("k_ready", 1))
                    nc.scalar.activation(flat(keep), flat(am), ACT.Exp)
                    nc.scalar.activation(flat(gain), flat(mloc), ACT.Exp)
                    nc.scalar.activation(flat(at_), flat(t1), ACT.Exp)
                    nc.scalar.activation(flat(emt), flat(nmt), ACT.Exp)
                    nc.scalar.activation(flat(eend), flat(t2), ACT.Exp)
                    for m in range(early_z):
                        act.wait_ge(*z_done[m])
                        nc.scalar.copy(zt[:, m, :], PS[:, 4 + m, :])

                @block.vector
                def _(dve):
                    ig, fg = gates[:, :, :, 0, :], gates[:, :, :, 1, :]
                    tt, ts = nc.vector.tensor_tensor, nc.vector.tensor_scalar
                    nc.vector.scalar_tensor_tensor(t1, fg, -1.0, fg, ALU.mult, ALU.max).then_inc(S["a_ready"].sem, 1)
                    dve.wait_ge(*at("g_ready", 1))
                    exact_log1p(dve, flat(logf), flat(ex), flat(t2), flat(u))
                    nc.vector.scalar_tensor_tensor(logf, fg, 0.0, logf, ALU.min, ALU.subtract).then_inc(S["b_ready"].sem, 1)
                    dve.wait_ge(*at("c_ready", 1))
                    dve_chain.link(dve, nc.vector.tensor_copy(SM[:, small_cum:small_cum + 64], PS[:, 0, 0:64]))
                    tt(u, ig, cum, ALU.subtract).then_inc(S["d_ready"].sem, 1)
                    for g in range(8):
                        dve.wait_ge(*at("e_ready", g + 1))
                        bank = PS[:, 1 + g % 2, :].rearrange("p (c s) -> p c s", c=4)
                        mask = const("causal" if g < 4 else "anticausal")
                        for i in range(4):
                            c = 4 * g + i
                            ins = dve_chain.add(nc.vector.scalar_tensor_tensor(logd[:, c, :], bank[:, i, :], flat(cum)[:, c:c + 1], mask,
                                                                               ALU.add, ALU.add))
                        nc.vector.tensor_reduce(flat(umax)[:, 4 * g:4 * g + 4], bank, AX, ALU.max).then_inc(S["f_ready"].sem, 1)
                        dve.wait_ge(dve_chain.sem, dve_chain.n)
                        dve_chain.add(nc.vector.tensor_reduce(flat(rowmax)[:, 4 * g:4 * g + 4], logd[:, 4 * g:4 * g + 4, :], AX, ALU.max))
                    dve.wait_ge(*at("f_ready", 8))
                    dve.wait_ge(dve_chain.sem, dve_chain.n)
                    dve_chain.add(tt(mloc, tot, umax, ALU.add))
                    dve_chain.link(dve, nc.vector.memset(mst[:, :, 0, :], NEG))
                    for j in range(4):
                        dve_chain.link(dve, tt(am[:, :, j, :], tot[:, :, j, :], mst[:, :, j, :], ALU.add))
                        dve_chain.link(dve, tt(mst[:, :, j + 1, :], am[:, :, j, :], mloc[:, :, j, :], ALU.max))
                    dve_chain.add(tt(am, am, mst[:, :, 1:5, :], ALU.subtract))
                    dve_chain.add(tt(mloc, mloc, mst[:, :, 1:5, :], ALU.subtract))
                    dve_chain.link(dve, tt(t1, cum, mst[:, :, 0:4, :], ALU.add))
                    dve_chain.link(dve, tt(nmt, t1, rowmax, ALU.max))
                    dve_chain.link(dve, tt(t1, t1, nmt, ALU.subtract))
                    dve_chain.add(ts(nmt, nmt, -1.0, None, ALU.mult))
                    tt(t2, u, umax, ALU.subtract).then_inc(S["k_ready"].sem, 1)

            for n, k in (("a_ready", 1), ("b_ready", 1), ("c_ready", 1), ("d_ready", 1), ("e_ready", 8), ("f_ready", 8),
                         ("g_ready", 1), ("k_ready", 1)):
                S[n].passed(k)

            pw = [0]

            def take_pw(*shape):
                n = 1
                for x in shape:
                    n *= x
                v = PW[:, pw[0]:pw[0] + n]
                pw[0] += n
                names = "abcd"[:len(shape)]
                return v.rearrange(f"p ({' '.join(names)}) -> p {' '.join(names)}", **dict(zip(names, shape)))

            state = take_pw(8, DV + 1)
            dm, sq, sqt, ke = (take_pw(2, P) for _ in range(4))
            inter = take_pw(2, DV + 1)
            added = take_pw(1, DV + 1)[:, 0, :]
            units = [(j, d, h) for j in range(4) for d in range(2) for h in range(H)]
            N = len(units)
            first_at = {}
            for i, (j, d, h) in enumerate(units):
                first_at.setdefault((order[d][j], h), i)
            n_state = sum(j < 3 for j, _, _ in units)
            n_inter = sum(j > 0 for j, _, _ in units)

            def upto(i, which):
                return sum((u[0] < 3) if which == "state" else (u[0] > 0) for u in units[:i])

            late_z = (8 - early_z) * KT

            def z_parts(i):
                return [(early_z + n // KT, n % KT, 3 + n // KT % 2 * 2) for n in range(i * late_z // N, (i + 1) * late_z // N)]

            with nc.Block() as block:

                @block.sync
                def _(sp):
                    ws.load_until(sp, z_in)

                @block.tensor
                def _(pe):
                    def logits(i):
                        j, d, h = units[i]
                        t_ = slice(order[d][j] * P, (order[d][j] + 1) * P)
                        if i >= 2:
                            pe.wait_ge(*at("a_ready", i - 1))
                        nc.tensor.matmul(PS[:, i % 2, 0:P], qk[:, h, t_], qk[:, 4 + h, t_], start=True, stop=True).then_inc(
                            S["scores_ready"].sem, 1)

                    def mix(i):
                        j, d, h = units[i]
                        pe.wait_ge(*at("turned_copied", i + 1))
                        if i >= 1:
                            pe.wait_ge(*at("heads_taken", i))
                        nc.tensor.matmul(PS[:, 7, 0:DV], sqt[:, i % 2, :], va[:, order[d][j], h, 0:DV], start=True, stop=True).then_inc(
                            S["heads_ready"].sem, 1)

                    logits(0)
                    for i, (j, d, h) in enumerate(units):
                        n = order[d][j]
                        if i + 1 < N:
                            logits(i + 1)
                        if j < 3:
                            s = upto(i, "state")
                            pe.wait_ge(*at("b_ready", s + 1))
                            if s >= 1:
                                pe.wait_ge(*at("c_ready", s))
                            nc.tensor.matmul(PS[:, 2, 0:DV + 1], ke[:, s % 2, :], va[:, n, h, :], start=True, stop=True).then_inc(
                                S["d_ready"].sem, 1)
                        if j > 0:
                            s = upto(i, "inter")
                            pe.wait_ge(*at("e_ready", s + 1))
                            if s >= 1:
                                pe.wait_ge(*at("f_ready", s))
                            nc.tensor.matmul(PS[:, 4, 0:DV + 1], qk[:, h, n * P:(n + 1) * P], state[:, 4 * d + h, :],
                                             start=True, stop=True).then_inc(S["g_ready"].sem, 1)
                        for m, k, bank in z_parts(i):
                            if k == 0 and m >= early_z + 2:
                                pe.wait_ge(*at("tile_taken", m - early_z - 1))
                            z_product(pe, m, k, bank)
                        pe.wait_ge(*at("a_ready", i + 1))
                        if i >= 1:
                            pe.wait_ge(*at("turned_copied", i))
                        nc.tensor.transpose(PS[:, 6, 0:P], sq[:, i % 2, :], ident).then_inc(S["probs_turned"].sem, 1)
                        if i >= 1:
                            mix(i - 1)
                    mix(N - 1)

                @block.scalar
                def _(act):
                    def decays(i):
                        j, d, h = units[i]
                        c = 16 * d + 4 * j + h
                        if i >= 2:
                            act.wait_ge(*at("a_ready", i - 1))
                        nc.scalar.activation(dm[:, i % 2, :], logd[:, c, :], ACT.Exp, bias=flat(nmt)[:, c:c + 1]).then_inc(
                            S["exp_ready"].sem, 1)

                    decays(0)
                    for i, (j, d, h) in enumerate(units):
                        c = 16 * d + 4 * j + h
                        if i + 1 < N:
                            decays(i + 1)
                        if j < 3:
                            s = upto(i, "state")
                            act.wait_ge(*at("d_ready", s + 1))
                            if s >= 1:
                                act.wait_ge(*at("e_ready", s))
                            nc.scalar.activation(added, PS[:, 2, 0:DV + 1], ACT.Copy, scale=flat(gain)[:, c:c + 1]).then_inc(
                                S["c_ready"].sem, 1)
                        if j > 0:
                            s = upto(i, "inter")
                            act.wait_ge(*at("g_ready", s + 1))
                            if i >= 2:
                                act.wait_ge(*at("heads_taken", i - 1))
                            nc.scalar.activation(inter[:, i % 2, :], PS[:, 4, 0:DV + 1], ACT.Copy,
                                                 scale=flat(at_)[:, c:c + 1]).then_inc(S["f_ready"].sem, 1)
                        act.wait_ge(*at("probs_turned", i + 1))
                        if i >= 2:
                            act.wait_ge(*at("heads_ready", i - 1))
                        nc.scalar.copy(sqt[:, i % 2, :], PS[:, 6, 0:P]).then_inc(S["turned_copied"].sem, 1)
                        for m, k, bank in z_parts(i):
                            if k == KT - 1:
                                act.wait_ge(*z_done[m])
                                nc.scalar.copy(zt[:, m, :], PS[:, bank, :]).then_inc(S["tile_taken"].sem, 1)

                @block.vector
                def _(dve):
                    def end_keys(i):
                        j, d, h = units[i]
                        if j < 3:
                            s = upto(i, "state")
                            if s >= 2:
                                dve.wait_ge(*at("d_ready", s - 1))
                            c = 16 * d + 4 * j + h
                            nc.vector.tensor_scalar(ke[:, s % 2, :], ktok[:, order[d][j], h, :], flat(eend)[:, c:c + 1], None,
                                                    ALU.mult).then_inc(S["b_ready"].sem, 1)

                    def combine(i):
                        j, d, h = units[i]
                        c, n = 16 * d + 4 * j + h, order[d][j]
                        r, w = flat(rden)[:, c:c + 1], hs[:, n, h, :]
                        dve.wait_ge(*at("heads_ready", i + 1))
                        src = PS[:, 7, 0:DV]
                        fresh = first_at[(n, h)] == i
                        if j > 0:
                            x = inter[:, i % 2, 0:DV]
                            dve_chain.link(dve, nc.vector.tensor_tensor(x, src, x, ALU.add))
                            src = x
                        if fresh:
                            nc.vector.tensor_scalar(w, src, r, None, ALU.mult).then_inc(S["heads_taken"].sem, 1)
                        else:
                            nc.vector.scalar_tensor_tensor(w, src, r, w, ALU.mult, ALU.add).then_inc(S["heads_taken"].sem, 1)

                    end_keys(0)
                    for i, (j, d, h) in enumerate(units):
                        c = 16 * d + 4 * j + h
                        if i + 1 < N:
                            end_keys(i + 1)
                        dve.wait_ge(*at("scores_ready", i + 1))
                        dve.wait_ge(*at("exp_ready", i + 1))
                        if i >= 2:
                            dve.wait_ge(*at("probs_turned", i - 1))
                        nc.vector.scalar_tensor_tensor(sq[:, i % 2, :], PS[:, i % 2, 0:P], 1.0, dm[:, i % 2, :], ALU.mult, ALU.mult,
                                                       accum_out=flat(rs)[:, c:c + 1]).then_inc(S["a_ready"].sem, 1)
                        if j < 3:
                            s = upto(i, "state")
                            st = state[:, 4 * d + h, :]
                            dve.wait_ge(*at("c_ready", s + 1))
                            if j == 0:
                                nc.vector.tensor_copy(st, added).then_inc(S["e_ready"].sem, 1)
                            else:
                                dve.wait_ge(*at("g_ready", upto(i, "inter") + 1))
                                nc.vector.scalar_tensor_tensor(st, st, flat(keep)[:, c:c + 1], added, ALU.mult, ALU.add).then_inc(
                                    S["e_ready"].sem, 1)
                        dve.wait_ge(*at("a_ready", i + 1))
                        r, den = flat(rden)[:, c:c + 1], flat(rs)[:, c:c + 1]
                        x = flat(t2)[:, c:c + 1]
                        if j > 0:
                            dve.wait_ge(*at("f_ready", upto(i, "inter") + 1))
                            dve_chain.link(dve, nc.vector.tensor_tensor(den, inter[:, i % 2, DV:DV + 1], den, ALU.add))
                        dve_chain.link(dve, nc.vector.scalar_tensor_tensor(x, den, -1.0, flat(emt)[:, c:c + 1], ALU.mult, ALU.max))
                        dve_chain.link(dve, nc.vector.tensor_tensor(r, den, x, ALU.max))
                        dve_chain.link(dve, nc.vector.reciprocal(r, r))
                        if i >= 1:
                            combine(i - 1)
                    combine(N - 1)

            for n, k in (("scores_ready", N), ("exp_ready", N), ("a_ready", N), ("b_ready", n_state), ("c_ready", n_state),
                         ("d_ready", n_state), ("e_ready", n_state), ("f_ready", n_inter), ("g_ready", n_inter),
                         ("probs_turned", N), ("turned_copied", N), ("heads_ready", N), ("heads_taken", N)):
                S[n].passed(k)
            S["tile_ready"].passed(z_plain)
            S["tile_taken"].passed(8 - early_z)

            ot = logd.rearrange("p c s -> p (c s)").rearrange("p (k t) -> p k t", k=KT)
            ss, rr = SM[:, 0:16], SM[:, 16:32]
            squares = PW[:].rearrange("p (n h v) -> p n h v", n=TT, h=H)
            shared = [(n, h) for n in range(2, TT) for h in range(2, H)]

            with nc.Block() as block:

                @block.sync
                def _(sp):
                    ws.load_until(sp, ws.done)

                @block.vector
                def _(dve):
                    for n in range(TT):
                        x = hs[:, n, :, :].rearrange("p h v -> p (h v)")
                        nc.vector.tensor_tensor(x, x, og[:, n, :], ALU.mult).then_inc(S["a_ready"].sem, 1)
                    dve.wait_ge(*at("a_ready", TT))
                    for n, h in shared:
                        ins = nc.vector.scalar_tensor_tensor(squares[:, n, h, :], hs[:, n, h, :], 1.0, hs[:, n, h, :], ALU.mult, ALU.mult,
                                                             accum_out=ss[:, n * H + h:n * H + h + 1])
                        dve_chain.link(dve, ins)
                    dve.wait_ge(*at("squares_ready", 16 - len(shared)))
                    dve_chain.link(dve, nc.vector.tensor_scalar(ss, ss, 1.0 / DV, EPS, ALU.mult, ALU.add))
                    nc.vector.reciprocal(ss, ss).then_inc(S["inverse_ready"].sem, 1)
                    dve.wait_ge(*at("rstd_ready", 1))
                    for h in range(H):
                        for n in range(TT):
                            c = n * H + h
                            ins = nc.vector.tensor_scalar(hs[:, n, h, :], hs[:, n, h, :], rr[:, c:c + 1], None, ALU.mult)
                            ins.then_inc(S["b_ready"].sem, 1)
                    for k in range(KT):
                        dve.wait_ge(*at("transposed", k + 1))
                        dve.wait_ge(*at("scaled_ready", k + 1))
                        nc.vector.scalar_tensor_tensor(ot[:, k, :], PS[:, k % 4, :], col("l2_g_head")[:, k:k + 1], zt[:, k, :],
                                                       ALU.mult, ALU.mult).then_inc(S["transposed_taken"].sem, 1)

                @block.scalar
                def _(act):
                    for n in range(TT):
                        act.wait_ge(*at("a_ready", n + 1))
                        for h in range(H):
                            if (n, h) not in shared:
                                c = n * H + h
                                nc.scalar.activation(squares[:, n, h, :], hs[:, n, h, :], ACT.Square, accum_out=ss[:, c:c + 1]).then_inc(
                                    S["squares_ready"].sem, 1)
                    act.wait_ge(*at("inverse_ready", 1))
                    nc.scalar.activation(rr, ss, ACT.Sqrt).then_inc(S["rstd_ready"].sem, 1)
                    for k in range(KT):
                        nc.scalar.activation(zt[:, k, :], zt[:, k, :], ACT.Silu).then_inc(S["scaled_ready"].sem, 1)

                @block.tensor
                def _(pe):
                    for k in range(KT):
                        pe.wait_ge(*at("b_ready", TT * (k // 2 + 1)))
                        if k >= 4:
                            pe.wait_ge(*at("transposed_taken", k - 3))
                        for n in range(TT):
                            ins = nc.tensor.transpose(PS[:, k % 4, n * P:(n + 1) * P], hs[:, n, k // 2, k % 2 * P:k % 2 * P + P], ident)
                        ins.then_inc(S["transposed"].sem, 1)

            for n, k in (("a_ready", TT), ("b_ready", 16), ("squares_ready", 16 - len(shared)), ("inverse_ready", 1), ("rstd_ready", 1),
                         ("scaled_ready", KT), ("transposed", KT), ("transposed_taken", KT)):
                S[n].passed(k)
            project_out(2, ot, 2)

        memory_layer()
        window_layer(3, False)

        expert_weights = BIG[:, 0:12 * 2048].rearrange("p (c n) -> p c n", c=12)
        chunk_landed = [ctx.enter_context(nc.semaphore(f"expert_chunk{c}_landed")) for c in range(12)]

        def load_expert_chunk(sp, e, c):
            if c < 8:
                src, dst = t["w1_2"].rearrange("e d f -> (e d) f")[bass.ds(e * D + c * P, P), :], expert_weights[:, c, :]
            else:
                src = t["w2_2"].rearrange("e f d -> (e f) d")[bass.ds(e * D + (c - 8) * 2 * P, 2 * P), :].rearrange("(j p) n -> p j n", p=P)
                dst = expert_weights[:, c, :].rearrange("p (j n) -> p j n", j=2)
            sp.dma_start(dst, src).then_inc(chunk_landed[c], 16)

        free_slot = (ws.first["w_out_2"] + 2) % SLOTS
        early_chunks = [2 * free_slot, 2 * free_slot + 1, *range(6, 12)]

        hybrid_squares = PW[:, 2 * TOK:2 * TOK + KT * LAT].rearrange("p (k t) -> p k t", k=KT)

        def hybrid_mixer():
            H = 4
            a = Arena()
            aq, ak, av = a.take(4, LAT), a.take(4, LAT), a.take(2, CH)
            raw = a.take(12, LAT + 3)
            qkv = a.take(12, LAT)
            dz = a.take(2, CH)
            mixed = HT[:, :, 0:LAT]
            c_in = ws.first["w_in_2"]
            taps = col("conv_w_2").rearrange("p (j k) -> p j k", j=4)
            small = [0]

            def take(*shape):
                n = 1
                for x in shape:
                    n *= x
                v = SM[:, small[0]:small[0] + n]
                small[0] += n
                names = "abcd"[:len(shape)]
                return v if len(shape) == 1 else v.rearrange(f"p ({' '.join(names)}) -> p {' '.join(names)}",
                                                             **dict(zip(names, shape)))

            ba = take(2, 8)
            beta, ex, g, t1, t2, x1 = (take(2, 4) for _ in range(6))
            gc, gtot, egc, edec, egl, bg = (take(2, 4) for _ in range(6))

            b = Arena(a.at)
            kt_, vt, e, amat, amat_t, intra, intra_t = (b.take(8, P) for _ in range(7))
            u_, w_t, o_, kbg = (b.take(8, P) for _ in range(4))
            kd, vb = (raw.rearrange("p k t -> p (k t)")[:, 512 + 1024 * n:1536 + 1024 * n].rearrange("p (n c) -> p n c", n=8) for n in range(2))
            x = PW[:, 0:1024].rearrange("p (n c) -> p n c", n=8)
            x_t = PW[:, 1024:2048].rearrange("p (n c) -> p n c", n=8)
            y = PW[:, 2048:3072].rearrange("p (n c) -> p n c", n=8)
            lo = PW[:, 3072:4096].rearrange("p (n c) -> p n c", n=8)
            s_ = raw.rearrange("p k t -> p (k t)")[:, 0:512].rearrange("p (h v) -> p h v", h=H)
            norms = raw.rearrange("p k t -> p (k t)")[:, 0:2048].rearrange("p (k t) -> p k t", k=8)
            sq8 = PW[:, 0:2048].rearrange("p (k t) -> p k t", k=8)

            def flat(v):
                return v.rearrange("p a b -> p (a b)")

            def bank4(n):
                return PS[:, n, :].rearrange("p (c s) -> p c s", c=4)

            tiles = [("qkv", m, m // 4) for m in range(12)] + [("ba", 0, 3)]
            tiles += [("aq", m, 4) for m in range(4)] + [("ak", m, 5) for m in range(4)]
            last = [j + 1 == len(tiles) or tiles[j + 1][2] != x[2] for j, x in enumerate(tiles)]
            done, n_plain = tile_signals([c_in + x[2] if e else None for x, e in zip(tiles, last)])
            with nc.Block() as block:

                @block.sync
                def _(sp):
                    ws.load_until(sp, c_in + 6)

                @block.gpsimd
                def _(pool):
                    nc.gpsimd.memset(raw[:, :, 0:3], 0.0).then_inc(S["a_ready"].sem, 1)

                @block.tensor
                def _(pe):
                    for j, (kind, m, c) in enumerate(tiles):
                        if j == 0 or tiles[j - 1][2] != c:
                            ws.wait(pe, c_in + c)
                        w = ws.view(c_in + c)
                        if j >= 4:
                            pe.wait_ge(*at("tile_taken", j - 3))
                        o = PS[:, j % 4, :]
                        if kind == "ba":
                            for n in range(2):
                                for k in range(KT):
                                    ins = nc.tensor.matmul(o[:, n * 8:n * 8 + 8], HT[:, k, n * P:(n + 1) * P], w[:, k, :],
                                                           start=(k == 0), stop=(k == KT - 1))
                        else:
                            for k in range(KT):
                                if j == 0:
                                    pe.wait_ge(*at("h_ready", k + 1))
                                ins = nc.tensor.matmul(o[:, 0:LAT], w[:, k, m % 4 * P:m % 4 * P + P], HT[:, k, 0:LAT],
                                                       start=(k == 0), stop=(k == KT - 1))
                        ins.then_inc(done[j][0], 1)
                        if 4 <= j < 12:
                            k = j - 4
                            pe.wait_ge(*at("squares_ready", k + 1))
                            if k >= 2:
                                pe.wait_ge(*at("inverse_ready", k - 1))
                            nc.tensor.matmul(PS[:, 4 + k % 2, 0:LAT], ones, sq8[:, k, :], start=True, stop=True).then_inc(
                                S["square_sum_ready"].sem, 1)
                        if kind == "ak" and m >= 2:
                            if m == 2:
                                pe.wait_ge(*at("scaled_ready", 8))
                            else:
                                pe.wait_ge(*at("transposed_taken", 2))
                            for first, bank in ((4, 6), (8, 7)):
                                for h in range(H):
                                    ins = nc.tensor.transpose(PS[:, bank, h * P:(h + 1) * P], qkv[:, first + h, (m - 2) * P:(m - 1) * P], ident)
                                ins.then_inc(S["transposed"].sem, 1)

                @block.scalar
                def _(act):
                    norm_scalar(act, 4, 1)
                    act.wait_ge(*at("a_ready", 1))
                    for j, (kind, m, c) in enumerate(tiles):
                        act.wait_ge(*done[j])
                        o = PS[:, j % 4, :]
                        dst, o = {"aq": (aq[:, m % 4, :], o[:, 0:LAT]), "ak": (ak[:, m % 4, :], o[:, 0:LAT]),
                                  "qkv": (raw[:, m, 3:LAT + 3], o[:, 0:LAT]), "ba": (ba, o[:, 0:16].rearrange("p (a n) -> p a n", a=2))}[kind]
                        nc.scalar.copy(dst, o).then_inc(S["tile_taken"].sem, 1)
                        if 2 <= j < 14:
                            k = j - 2
                            act.wait_ge(*at("b_ready", k + 1))
                            ins = nc.scalar.activation(qkv[:, k, :], qkv[:, k, :], ACT.Silu)
                            act_chain.link(act, ins)
                            if k < 8:
                                nc.scalar.activation(sq8[:, k, :], qkv[:, k, :], ACT.Square).then_inc(S["squares_ready"].sem, 1)
                        if j == 17:
                            for k in range(8):
                                act.wait_ge(*at("inverse_ready", k + 1))
                                nc.scalar.activation(norms[:, k, :], norms[:, k, :], ACT.Sqrt).then_inc(S["rstd_ready"].sem, 1)
                        if j == 18:
                            act.wait_ge(*at("c_ready", 1))
                            act_chain.link(act, nc.scalar.activation(ex, t1, ACT.Exp, scale=-1.0))
                            nc.scalar.activation(g, ex, ACT.Ln, bias=1.0).then_inc(S["d_ready"].sem, 1)
                            nc.scalar.activation(t2[:, 0, :], bcast("A_log_2"), ACT.Exp).then_inc(S["d_ready"].sem, 1)
                            nc.scalar.activation(beta, ba[:, :, 0:4], ACT.Sigmoid).then_inc(S["d_ready"].sem, 1)
                        if kind == "ak" and m >= 2:
                            n = m - 2
                            act.wait_ge(*at("transposed", 2 * n + 1))
                            nc.scalar.copy(kt_[:, 4 * n:4 * n + 4, :], bank4(6)).then_inc(S["transposed_taken"].sem, 1)
                            act.wait_ge(*at("transposed", 2 * n + 2))
                            nc.scalar.copy(vt[:, 4 * n:4 * n + 4, :], bank4(7)).then_inc(S["transposed_taken"].sem, 1)

                @block.vector
                def _(dve):
                    norm_vector(dve, 4, "norm1_w_2", 1)

                    def norm_of(k):
                        dve.wait_ge(*at("square_sum_ready", k + 1))
                        dve_chain.link(dve, nc.vector.tensor_scalar(norms[:, k, :], PS[:, 4 + k % 2, 0:LAT], EPS, None, ALU.add))
                        nc.vector.reciprocal(norms[:, k, :], norms[:, k, :]).then_inc(S["inverse_ready"].sem, 1)

                    for m in range(12):
                        dve.wait_ge(*at("tile_taken", 1 + m))
                        o = qkv[:, m, :]
                        dve_chain.link(dve, nc.vector.tensor_scalar(o, raw[:, m, 0:LAT], taps[:, 0, m:m + 1], None, ALU.mult))
                        for j in range(1, 4):
                            ins = nc.vector.scalar_tensor_tensor(o, raw[:, m, j:j + LAT], taps[:, j, m:m + 1], o, ALU.mult, ALU.add)
                            if j < 3:
                                dve_chain.link(dve, ins)
                        ins.then_inc(S["b_ready"].sem, 1)
                        if m >= 4:
                            norm_of(m - 4)
                    for k in range(8):
                        dve.wait_ge(*at("rstd_ready", k + 1))
                        nc.vector.scalar_tensor_tensor(qkv[:, k, :], qkv[:, k, :], P ** -0.5 if k < 4 else 1.0, norms[:, k, :], ALU.mult,
                                                       ALU.mult).then_inc(S["scaled_ready"].sem, 1)
                    dve.wait_ge(*at("tile_taken", 13))
                    dve_chain.link(dve, nc.vector.tensor_tensor(x1, ba[:, :, 4:8], bcast("dt_bias_2").unsqueeze(1).to_broadcast([P, 2, 4]),
                                                                ALU.add))
                    nc.vector.scalar_tensor_tensor(t1, x1, -1.0, x1, ALU.mult, ALU.max).then_inc(S["c_ready"].sem, 1)
                    dve.wait_ge(*at("d_ready", 1))
                    exact_log1p(dve, flat(g), flat(ex), flat(gc), flat(gtot))
                    dve_chain.link(dve, nc.vector.scalar_tensor_tensor(g, x1, 0.0, g, ALU.max, ALU.add))
                    dve.wait_ge(*at("d_ready", 2))
                    dve_chain.add(nc.vector.scalar_tensor_tensor(g, g, -1.0, t2[:, 0:1, :].to_broadcast([P, 2, 4]), ALU.mult, ALU.mult))

            S["tile_ready"].passed(n_plain)
            S["tile_taken"].passed(len(tiles))
            norm_passed(1)
            for n, k in (("a_ready", 1), ("b_ready", 12), ("c_ready", 1), ("d_ready", 3), ("squares_ready", 8), ("square_sum_ready", 8),
                         ("inverse_ready", 8), ("rstd_ready", 8), ("scaled_ready", 8), ("transposed", 4), ("transposed_taken", 4)):
                S[n].passed(k)

            av_done, n_plain = tile_signals([None, c_in + 6])
            with nc.Block() as block:

                @block.sync
                def _(sp):
                    ws.load_until(sp, c_in + 7)

                @block.tensor
                def _(pe):
                    def values(m):
                        w = ws.view(c_in + 6)
                        for k in range(KT):
                            ins = nc.tensor.matmul(PS[:, 7, :], HT[:, k, m * P:(m + 1) * P], w[:, k, :], start=(k == 0), stop=(k == KT - 1))
                        ins.then_inc(av_done[m][0], 1)

                    nc.tensor.matmul(PS[:, 0, 0:8], const("upto"), flat(g), start=True, stop=True)
                    nc.tensor.matmul(PS[:, 0, 8:16], ones, flat(g), start=True, stop=True).then_inc(S["a_ready"].sem, 1)
                    for p in range(8):
                        n, h = divmod(p, 4)
                        t_ = slice(n * P, (n + 1) * P)
                        nc.tensor.matmul(PS[:, 1 + n, h * P:(h + 1) * P], qkv[:, 4 + h, t_], qkv[:, 4 + h, t_], start=True, stop=True)
                        ins = nc.tensor.matmul(PS[:, 3 + n, h * P:(h + 1) * P], qkv[:, h, t_], qkv[:, 4 + h, t_], start=True, stop=True)
                    ins.then_inc(S["scores_ready"].sem, 1)
                    pe.wait_ge(*at("b_ready", 1))
                    for p in range(8):
                        ins = nc.tensor.matmul(PS[:, 5 + p // 4, p % 4 * P:(p % 4 + 1) * P], flat(gc)[:, p:p + 1].to_broadcast([P, P]), ident,
                                               start=True, stop=True)
                    ins.then_inc(S["c_ready"].sem, 1)
                    ws.wait(pe, c_in + 6)
                    values(0)
                    pe.wait_ge(*at("f_ready", 1))
                    pe.wait_ge(*at("d_ready", 2))
                    for p in range(8):
                        ins = nc.tensor.transpose(PS[:, 5 + p // 4, p % 4 * P:(p % 4 + 1) * P], amat[:, p, :], ident)
                    ins.then_inc(S["transposed"].sem, 1)
                    pe.wait_ge(*at("tile_taken", 1))
                    values(1)
                    pe.wait_ge(*at("g_ready", 2))
                    for p in range(8):
                        ins = nc.tensor.transpose(PS[:, 3 + p // 4, p % 4 * P:(p % 4 + 1) * P], intra[:, p, :], ident)
                    ins.then_inc(S["transposed"].sem, 1)

                @block.scalar
                def _(act):
                    act.wait_ge(*at("b_ready", 3))
                    nc.scalar.activation(egc, gc, ACT.Exp).then_inc(S["exp_ready"].sem, 1)
                    nc.scalar.activation(edec, edec, ACT.Exp).then_inc(S["exp_ready"].sem, 1)
                    nc.scalar.activation(egl, gtot, ACT.Exp).then_inc(S["exp_ready"].sem, 1)
                    for p in range(8):
                        act.wait_ge(*at("d_ready", 1 + p // 4))
                        nc.scalar.activation(e[:, p, :], e[:, p, :], ACT.Exp, bias=flat(gc)[:, p:p + 1]).then_inc(S["e_ready"].sem, 1)
                    for m in range(2):
                        act.wait_ge(*av_done[m])
                        nc.scalar.copy(av[:, m, :], PS[:, 7, :]).then_inc(S["tile_taken"].sem, 1)
                    act.wait_ge(*at("transposed", 2))
                    for n in range(2):
                        nc.scalar.copy(intra_t[:, 4 * n:4 * n + 4, :], bank4(3 + n))

                @block.vector
                def _(dve):
                    dve.wait_ge(*at("a_ready", 1))
                    nc.vector.tensor_copy(flat(gc), PS[:, 0, 0:8]).then_inc(S["b_ready"].sem, 1)
                    nc.vector.tensor_copy(flat(gtot), PS[:, 0, 8:16]).then_inc(S["b_ready"].sem, 1)
                    dve.wait_ge(*at("b_ready", 2))
                    nc.vector.tensor_tensor(edec, gtot, gc, ALU.subtract).then_inc(S["b_ready"].sem, 1)
                    dve.wait_ge(*at("c_ready", 1))
                    for n in range(2):
                        nc.vector.scalar_tensor_tensor(e[:, 4 * n:4 * n + 4, :], bank4(5 + n), -1.0,
                                                       const("causal").unsqueeze(1).to_broadcast([P, 4, P]), ALU.mult, ALU.add).then_inc(
                            S["d_ready"].sem, 1)
                    dve.wait_ge(*at("scores_ready", 1))
                    for p in range(8):
                        dve.wait_ge(*at("e_ready", p + 1))
                        dve_chain.add(nc.vector.scalar_tensor_tensor(amat[:, p, :], bank4(1 + p // 4)[:, p % 4, :], flat(beta)[:, p:p + 1],
                                                                     e[:, p, :], ALU.mult, ALU.mult))
                    dve.wait_ge(dve_chain.sem, dve_chain.n)
                    nc.vector.tensor_tensor(amat, amat, const("strict").unsqueeze(1).to_broadcast([P, 8, P]), ALU.mult).then_inc(
                        S["f_ready"].sem, 1)
                    for n in range(2):
                        nc.vector.tensor_tensor(intra[:, 4 * n:4 * n + 4, :], bank4(3 + n), e[:, 4 * n:4 * n + 4, :], ALU.mult).then_inc(
                            S["g_ready"].sem, 1)
                    dve.wait_ge(*at("exp_ready", 3))
                    dve_chain.link(dve, nc.vector.tensor_tensor(bg, beta, egc, ALU.mult))
                    for dst, src, f in ((vb, vt, beta), (kbg, kt_, bg), (kd, kt_, edec)):
                        dve_chain.add(nc.vector.tensor_tensor(dst, src, flat(f).unsqueeze(2).to_broadcast([P, 8, P]), ALU.mult))
                    dve.wait_ge(*at("f_ready", 1))
                    idb = ident.unsqueeze(1).to_broadcast([P, 8, P])
                    dve_chain.link(dve, nc.vector.tensor_tensor(x, amat, const("low1").unsqueeze(1).to_broadcast([P, 8, P]), ALU.mult))
                    dve_chain.link(dve, nc.vector.scalar_tensor_tensor(x, x, -1.0, idb, ALU.mult, ALU.add))
                    dve.wait_ge(*at("transposed", 1))
                    for n in range(2):
                        dve_chain.add(nc.vector.tensor_copy(amat_t[:, 4 * n:4 * n + 4, :], bank4(5 + n)))
                    dve.wait_ge(dve_chain.sem, dve_chain.n)
                    dve_chain.link(dve, nc.vector.tensor_tensor(x_t, amat_t, const("low1T").unsqueeze(1).to_broadcast([P, 8, P]), ALU.mult))
                    dve_chain.link(dve, nc.vector.scalar_tensor_tensor(x_t, x_t, -1.0, idb, ALU.mult, ALU.add))

            for n, k in (("a_ready", 1), ("b_ready", 3), ("c_ready", 1), ("d_ready", 2), ("e_ready", 8), ("f_ready", 1), ("g_ready", 2),
                         ("exp_ready", 3), ("scores_ready", 1), ("transposed", 2)):
                S[n].passed(k)
            S["tile_ready"].passed(n_plain)
            S["tile_taken"].passed(2)

            levels = (2, 4, 8, 16, 32, 64)
            L = len(levels)
            dz_done, n_plain = tile_signals([None, c_in + 7])
            with nc.Block() as block:

                @block.sync
                def _(sp):
                    ws.load_until(sp, c_in + 8)

                @block.gpsimd
                def _(pool):
                    for l, bsize in enumerate(levels):
                        if l >= 1:
                            pool.wait_ge(*at("b_ready", 2 * l))
                        nc.gpsimd.tensor_tensor(lo, amat_t, const(f"low{bsize}T").unsqueeze(1).to_broadcast([P, 8, P]),
                                                ALU.mult).then_inc(S["a_ready"].sem, 1)

                @block.tensor
                def _(pe):
                    def gate_part(i):
                        m, w = i // 4, ws.view(c_in + 7)
                        for k in range(i % 4 * 2, i % 4 * 2 + 2):
                            ins = nc.tensor.matmul(PS[:, 6 + m, :], HT[:, k, m * P:(m + 1) * P], w[:, k, :], start=(k == 0), stop=(k == KT - 1))
                        if i % 4 == 3:
                            ins.then_inc(dz_done[m][0], 1)

                    ws.wait(pe, c_in + 7)
                    for l in range(L):
                        pe.wait_ge(*at("a_ready", l + 1))
                        for n in range(2):
                            if l >= 1:
                                pe.wait_ge(*at("e_ready", 2 * l + n - 1))
                                pe.wait_ge(*at("f_ready", 2 * l + n - 1))
                            for p in range(4 * n, 4 * n + 4):
                                ins = nc.tensor.matmul(bank4(n)[:, p % 4, :], lo[:, p, :], x[:, p, :], start=True, stop=True)
                            ins.then_inc(S["b_ready"].sem, 1)
                        if l < 4:
                            gate_part(2 * l)
                        for n in range(2):
                            pe.wait_ge(*at("c_ready", 2 * l + n + 1))
                            if l < L - 1:
                                for p in range(4 * n, 4 * n + 4):
                                    ins = nc.tensor.matmul(bank4(2 + n)[:, p % 4, :], x_t[:, p, :], y[:, p, :], start=True, stop=True)
                                ins.then_inc(S["d_ready"].sem, 1)
                            for p in range(4 * n, 4 * n + 4):
                                ins = nc.tensor.matmul(bank4(4 + n)[:, p % 4, :], y[:, p, :], x_t[:, p, :], start=True, stop=True)
                            ins.then_inc(S["g_ready"].sem, 1)
                        if l < 4:
                            gate_part(2 * l + 1)
                    pe.wait_ge(*at("f_ready", 2 * L))
                    for p in range(8):
                        n, h = p // 4, p % 4
                        nc.tensor.matmul(PS[:, n, h * P:(h + 1) * P], x_t[:, p, :], vb[:, p, :], start=True, stop=True)
                        ins = nc.tensor.matmul(PS[:, 2 + n, h * P:(h + 1) * P], kbg[:, p, :], x_t[:, p, :], start=True, stop=True)
                    ins.then_inc(S["scores_ready"].sem, 1)

                @block.scalar
                def _(act):
                    for l in range(L):
                        for n in range(2):
                            act.wait_ge(*at("b_ready", 2 * l + n + 1))
                            if l >= 1:
                                act.wait_ge(*at("g_ready", 2 * l + n - 1))
                            nc.scalar.copy(y[:, 4 * n:4 * n + 4, :], bank4(n)).then_inc(S["c_ready"].sem, 1)
                    for m in range(2):
                        act.wait_ge(*dz_done[m])
                        nc.scalar.activation(dz[:, m, :], PS[:, 6 + m, :], ACT.Silu)
                    act.wait_ge(*at("scores_ready", 1))
                    for n in range(2):
                        nc.scalar.copy(u_[:, 4 * n:4 * n + 4, :], bank4(n))
                        nc.scalar.copy(w_t[:, 4 * n:4 * n + 4, :], bank4(2 + n))

                @block.vector
                def _(dve):
                    for l in range(L):
                        for n in range(2):
                            if l < L - 1:
                                dve.wait_ge(*at("d_ready", 2 * l + n + 1))
                                v = x[:, 4 * n:4 * n + 4, :]
                                nc.vector.tensor_tensor(v, v, bank4(2 + n), ALU.subtract).then_inc(S["e_ready"].sem, 1)
                            dve.wait_ge(*at("g_ready", 2 * l + n + 1))
                            v = x_t[:, 4 * n:4 * n + 4, :]
                            nc.vector.tensor_tensor(v, v, bank4(4 + n), ALU.subtract).then_inc(S["f_ready"].sem, 1)

            for n, k in (("a_ready", L), ("b_ready", 2 * L), ("c_ready", 2 * L), ("d_ready", 2 * L - 2), ("e_ready", 2 * L - 2),
                         ("f_ready", 2 * L), ("g_ready", 2 * L), ("scores_ready", 1)):
                S[n].passed(k)
            S["tile_ready"].passed(n_plain)

            rs, rr = SM[:, 300:308], SM[:, 308:316]
            with nc.Block() as block:

                @block.tensor
                def _(pe):
                    for h in range(H):
                        ins = nc.tensor.matmul(PS[:, 0, h * P:(h + 1) * P], kd[:, h, :], u_[:, h, :], start=True, stop=True)
                    ins.then_inc(S["a_ready"].sem, 1)
                    for h in range(H):
                        ins = nc.tensor.matmul(PS[:, 1, h * P:(h + 1) * P], intra_t[:, h, :], u_[:, h, :], start=True, stop=True)
                    ins.then_inc(S["b_ready"].sem, 1)
                    pe.wait_ge(*at("c_ready", 1))
                    for h in range(H):
                        ins = nc.tensor.matmul(PS[:, 2, h * P:(h + 1) * P], w_t[:, 4 + h, :], s_[:, h, :], start=True, stop=True)
                    ins.then_inc(S["d_ready"].sem, 1)
                    for h in range(H):
                        ins = nc.tensor.matmul(PS[:, 3, h * P:(h + 1) * P], qkv[:, h, P:2 * P], s_[:, h, :], start=True, stop=True)
                    ins.then_inc(S["e_ready"].sem, 1)
                    pe.wait_ge(*at("f_ready", 1))
                    for h in range(H):
                        ins = nc.tensor.matmul(PS[:, 4, h * P:(h + 1) * P], intra_t[:, 4 + h, :], u_[:, 4 + h, :], start=True, stop=True)
                    ins.then_inc(S["g_ready"].sem, 1)
                    pe.wait_ge(*at("k_ready", 1))
                    for h in range(H):
                        for n in range(2):
                            ins = nc.tensor.transpose(PS[:, 5 + h // 2, (h % 2 * 2 + n) * P:(h % 2 * 2 + n + 1) * P], o_[:, 4 * n + h, :], ident)
                    ins.then_inc(S["transposed"].sem, 1)

                @block.scalar
                def _(act):
                    act.wait_ge(*at("a_ready", 1))
                    nc.scalar.copy(s_, bank4(0)).then_inc(S["c_ready"].sem, 1)
                    act.wait_ge(*at("b_ready", 1))
                    nc.scalar.copy(o_[:, 0:4, :], bank4(1)).then_inc(S["i_ready"].sem, 1)
                    act.wait_ge(*at("i_ready", 1))
                    act.wait_ge(*at("j_ready", 1))
                    for p in range(8):
                        nc.scalar.activation(y[:, p, :], o_[:, p, :], ACT.Square, accum_out=rs[:, p:p + 1]).then_inc(
                            S["squares_ready"].sem, 1)
                    act.wait_ge(*at("inverse_ready", 1))
                    nc.scalar.activation(rr, rs, ACT.Sqrt).then_inc(S["rstd_ready"].sem, 1)

                @block.vector
                def _(dve):
                    dve.wait_ge(*at("d_ready", 1))
                    nc.vector.tensor_tensor(u_[:, 4:8, :], u_[:, 4:8, :], bank4(2), ALU.subtract).then_inc(S["f_ready"].sem, 1)
                    dve.wait_ge(*at("e_ready", 1))
                    dve_chain.link(dve, nc.vector.tensor_tensor(o_[:, 4:8, :], bank4(3), egc[:, 1, :].unsqueeze(2).to_broadcast([P, 4, P]),
                                                                ALU.mult))
                    dve.wait_ge(*at("g_ready", 1))
                    nc.vector.tensor_tensor(o_[:, 4:8, :], o_[:, 4:8, :], bank4(4), ALU.add).then_inc(S["j_ready"].sem, 1)
                    dve.wait_ge(*at("squares_ready", 8))
                    dve_chain.link(dve, nc.vector.tensor_scalar(rs, rs, 1.0 / P, EPS, ALU.mult, ALU.add))
                    nc.vector.reciprocal(rs, rs).then_inc(S["inverse_ready"].sem, 1)
                    dve.wait_ge(*at("rstd_ready", 1))
                    dve_chain.link(dve, nc.vector.tensor_tensor(o_, o_, rr.unsqueeze(2).to_broadcast([P, 8, P]), ALU.mult))
                    nc.vector.tensor_tensor(flat(o_), flat(o_), flat(dz), ALU.mult).then_inc(S["k_ready"].sem, 1)
                    dve.wait_ge(*at("transposed", 1))
                    for n in range(2):
                        dve_chain.add(nc.vector.tensor_scalar(mixed[:, 4 + 2 * n:6 + 2 * n, :],
                                                              PS[:, 5 + n, :].rearrange("p (h t) -> p h t", h=2),
                                                              col("dn_norm_w_2"), None, ALU.mult))

            for n, k in (("a_ready", 1), ("b_ready", 1), ("c_ready", 1), ("d_ready", 1), ("e_ready", 1), ("f_ready", 1), ("g_ready", 1),
                         ("k_ready", 1), ("i_ready", 1), ("j_ready", 1), ("transposed", 1), ("squares_ready", 8), ("inverse_ready", 1),
                         ("rstd_ready", 1)):
                S[n].passed(k)

            def score(h, u, k, out):
                half = slice(64 * h, 64 * h + 64)
                return nc.tensor.matmul(out, aq[half, u[0], u[1] * P:(u[1] + 1) * P], ak[half, u[0], k], start=True, stop=True)

            def value(u, h, kt):
                head = 2 * u[0] + h
                return av[:, kt, head * 64:head * 64 + 64], lambda bank: bank[64 * h:64 * h + 64, 0:P]

            def gate(u, bank):
                return mixed[:, u[0], u[1] * P:(u[1] + 1) * P], None, bank[:, 0:P]

            units = [(m, q, list(range(q + 1))) for m in range(4) for q in range(2)]
            ws.done = c_in + 8
            attention(units, 0.125, score, value, lambda u: dilated[:, u[1], 0:(u[1] + 1) * P], None, gate)

            first = ws.first["w_out_2"]
            done, n_plain = tile_signals([None, None, None, first, None, None, None, first + 1])
            with nc.Block() as block:

                @block.sync
                def _(sp):
                    ws.load_until(sp, first + 2)
                    for c in early_chunks:
                        load_expert_chunk(sp, 0, c)

                @block.tensor
                def _(pe):
                    for m in range(KT):
                        if m % 4 == 0:
                            ws.wait(pe, first + m // 4)
                        w = ws.view(first + m // 4)
                        for k in range(KT):
                            ins = nc.tensor.matmul(PS[:, m, 0:LAT], w[:, k, m % 4 * P:m % 4 * P + P], mixed[:, k, :], start=(k == 0),
                                                   stop=(k == KT - 1))
                        ins.then_inc(done[m][0], 1)
                    sum_squares(pe, LATENT, PS[:, 0, 0:LAT], hybrid_squares)

                @block.scalar
                def _(act):
                    for k in range(KT):
                        act.wait_ge(*at("residual_ready", k + 1))
                        square(act, k, LATENT, hybrid_squares)
                    root(act, PS[:, 0, 0:LAT], LATENT)

                @block.vector
                def _(dve):
                    for m in range(KT):
                        dve.wait_ge(*done[m])
                        nc.vector.scalar_tensor_tensor(XT[:, m, 0:LAT], PS[:, m, 0:LAT], modulation(4)[:, 2 * KT + m, :],
                                                       XT[:, m, 0:LAT], ALU.mult, ALU.add).then_inc(S["residual_ready"].sem, 1)
                    inverse(dve, LATENT)

            S["tile_ready"].passed(n_plain)
            S["residual_ready"].passed(KT)
            S["squares_ready"].passed(KT)
            for n in ("square_sum_ready", "rms_ready"):
                S[n].passed(1)

        hybrid_mixer()

        def routed_experts():
            E, K, SLOT, F = 32, 4, 64, 1024
            MAX_BLOCKS = LAT * K // SLOT + E
            W = expert_weights
            bias_landed = ctx.enter_context(nc.semaphore("expert_bias_landed"))
            rest = [12 * 2048]

            def take(buf, at, *shape):
                n = 1
                for x in shape:
                    n *= x
                v = buf[:, at[0]:at[0] + n]
                at[0] += n
                names = "abcd"[:len(shape)]
                return v if len(shape) == 1 else v.rearrange(f"p ({' '.join(names)}) -> p {' '.join(names)}",
                                                             **dict(zip(names, shape)))

            htok = take(BIG, rest, 2, D)
            bias1 = take(BIG, rest, 2 * F)
            bias2 = take(BIG, rest, D)
            w_router = take(BIG, rest, KT, E)
            scores_by = take(BIG, rest, LAT)
            onehot, placed = take(BIG, rest, 2, K, E), take(BIG, rest, 2, K, E)
            gates_of = take(BIG, rest, 2, E)
            gates_by = take(BIG, rest, LAT)
            gain_split = take(BIG, rest, 512)
            gain_rows = take(BIG, rest, D)
            xg = take(BIG, rest, 512)
            norm_rows = take(BIG, rest, D)
            pw = [0]
            gate_, up, sig, act_ = (take(PW, pw, 512) for _ in range(4))
            xt, at_, ys = take(PW, pw, 4, 2, SLOT), take(PW, pw, 4, 2, SLOT), take(PW, pw, 512)
            eq = take(PW, pw, 2, K, SLOT)
            hbuf, hat = HT[:].rearrange("p k t -> p (k t)"), [0]
            drow, grow, eq2 = (take(hbuf, hat, K, LAT) for _ in range(3))
            pick, spread = take(hbuf, hat, 2, SLOT), take(hbuf, hat, LAT)
            sm = [0]
            lg, sel = take(SM, sm, 2, E), take(SM, sm, 2, E)
            v8, gates, idx = take(SM, sm, 2, 8), take(SM, sm, 2, K), take(SM, sm, 2, K)
            gsum, count, blocks, pend, pos = take(SM, sm, 2), take(SM, sm, E), take(SM, sm, E), take(SM, sm, E), take(SM, sm, 2, E)
            dest, dest0, slot, tmp = take(SM, sm, 2, K), take(SM, sm, 2, K), take(SM, sm, 1), take(SM, sm, E)
            some, rank, scratch = take(SM, sm, E), take(SM, sm, E), take(SM, sm, E)
            plan_by = take(SM, sm, 5)
            plan = take(SM, sm, P).bitcast(I32)
            i8 = take(SM, sm, 2, 8).bitcast(U32)

            def flat(x):
                return x.rearrange("p a b -> p (a b)")

            with nc.Block() as block:

                @block.sync
                def _(sp):
                    sp.dma_start(w_router, t["w_router_2"].rearrange("(k p) e -> p k e", p=P)).then_inc(S["tokens_loaded"].sem, 16)
                    sp.dma_start(bias1[0:1, :], t["b1_2"][0:1, :]).then_inc(bias_landed, 16)
                    for c in range(12):
                        if c not in early_chunks:
                            load_expert_chunk(sp, 0, c)
                    sp.dma_start(bias2[0:E, :], t["b2_2"]).then_inc(S["late_loaded"].sem, 16)
                    sp.dma_start(norm_rows, t["final_norm_w_2"].partition_broadcast(P)).then_inc(S["late_loaded"].sem, 16)

                @block.scalar
                def _(act):
                    norm_scalar(act, 4, 1, part=1)
                    act.wait_ge(*at("scores_ready", 1))
                    nc.scalar.copy(scores_by[0:E, :], PS[0:E, 4, 0:LAT]).then_inc(S["e_ready"].sem, 1)
                    for n in range(4):
                        act.wait_ge(*at("transposed", n + 1))
                        nc.scalar.copy(htok[:, n // 2, n % 2 * 512:n % 2 * 512 + 512], PS[:, n, :]).then_inc(S["d_ready"].sem, 1)
                    act.wait_ge(*at("transposed", 5))
                    nc.scalar.copy(gain_split, PS[:, 4, :])
                    for g in range(2):
                        nc.scalar.copy(gain_rows[:, g * 512:g * 512 + 512], PS[:, 6 + g, :])

                @block.tensor
                def _(pe):
                    pe.wait_ge(*at("tokens_loaded", 16))
                    for k in range(KT):
                        pe.wait_ge(*at("h_ready", k + 1))
                        ins = nc.tensor.matmul(PS[0:E, 4, 0:LAT], w_router[:, k, :], HT[:, k, 0:LAT], start=(k == 0), stop=(k == KT - 1))
                    ins.then_inc(S["scores_ready"].sem, 1)
                    pe.wait_ge(*at("e_ready", 1))
                    for n in range(2):
                        ins = nc.tensor.transpose(PS[:, 5, n * E:(n + 1) * E], scores_by[0:E, n * P:(n + 1) * P], ident[0:E, 0:E])
                    ins.then_inc(S["c_ready"].sem, 1)
                    for n in range(4):
                        for j in range(4):
                            ins = nc.tensor.transpose(PS[:, n, j * P:(j + 1) * P], HT[:, n % 2 * 4 + j, n // 2 * P:(n // 2 + 1) * P], ident)
                        ins.then_inc(S["transposed"].sem, 1)
                    for k in range(KT):
                        column = modulation(4)[:, 5 * KT + k, :]
                        at_g = slice(k % 4 * P, k % 4 * P + P)
                        nc.tensor.matmul(PS[64 * (k // 4):64 * (k // 4) + 64, 4, at_g], column.to_broadcast([P, 64]), ident, start=True, stop=True)
                        ins = nc.tensor.matmul(PS[:, 6 + k // 4, at_g], column.to_broadcast([P, P]), ident, start=True, stop=True)
                    ins.then_inc(S["transposed"].sem, 1)
                    pe.wait_ge(*at("a_ready", 1))
                    nc.tensor.matmul(PS[:, 5, 0:E], ones, sel[:, 0, :], start=True, stop=False)
                    nc.tensor.matmul(PS[:, 5, 0:E], ones, sel[:, 1, :], start=False, stop=True)
                    nc.tensor.matmul(PS[:, 5, E:2 * E], const("before"), sel[:, 0, :], start=True, stop=True)
                    nc.tensor.matmul(PS[:, 5, 2 * E:3 * E], const("before"), sel[:, 1, :], start=True, stop=False)
                    nc.tensor.matmul(PS[:, 5, 2 * E:3 * E], ones, sel[:, 0, :], start=False, stop=True).then_inc(S["b_ready"].sem, 1)
                    for n in range(4):
                        pe.wait_ge(*at("d_ready", n + 1))
                        for j in range(4):
                            nc.tensor.matmul(PS[:, n, j * P:(j + 1) * P], XT[:, n % 2 * 4 + j, n // 2 * P:(n // 2 + 1) * P], ident,
                                             start=(j == 0), stop=False, skip_group_check=True)

                @block.vector
                def _(dve):
                    def link(ins):
                        dve_chain.link(dve, ins)

                    tt, ts = nc.vector.tensor_tensor, nc.vector.tensor_scalar
                    norm_vector(dve, 4, "norm2_w_2", 1, part=1)
                    dve.wait_ge(*at("c_ready", 1))
                    link(tt(lg, PS[:, 5, 0:2 * E].rearrange("p (n e) -> p n e", n=2),
                            bcast("b_router_2").unsqueeze(1).to_broadcast([P, 2, E]), ALU.add))
                    for n in range(2):
                        link(nc.vector.max(v8[:, n, :], lg[:, n, :]))
                        link(nc.vector.max_index(i8[:, n, :], v8[:, n, :], lg[:, n, :]))
                    link(nc.vector.tensor_copy(idx, i8[:, :, 0:K]))
                    for n in range(2):
                        link(tt(onehot[:, n, :, :], const("expert_row").unsqueeze(1).to_broadcast([P, K, E]),
                                idx[:, n, :].unsqueeze(2).to_broadcast([P, K, E]), ALU.is_equal))
                    for n in range(2):
                        link(nc.vector.tensor_reduce(sel[:, n, :], onehot[:, n, :, :].rearrange("p k e -> p e k"), AX, ALU.add))
                    link(tt(gates, v8[:, :, 0:K], v8[:, :, 0:1].to_broadcast([P, 2, K]), ALU.subtract))
                    ts(slot, const("slot_col"), 0.0, None, ALU.add).then_inc(S["a_ready"].sem, 1)
                    dve.wait_ge(*at("b_ready", 1))
                    link(nc.vector.tensor_copy(count, PS[:, 5, 0:E]))
                    link(ts(blocks, count, 0.0, None, ALU.is_gt))
                    link(nc.vector.memset(blocks[:, 0:1], 1.0))
                    for r in range(1, LAT // SLOT):
                        link(nc.vector.scalar_tensor_tensor(blocks, count, float(SLOT * r), blocks, ALU.is_gt, ALU.add))
                    link(nc.vector.tensor_tensor_scan(pend, ones[:, 0:E], blocks, 0.0, ALU.mult, ALU.add))
                    link(tt(tmp, pend, blocks, ALU.subtract))
                    link(nc.vector.scalar_tensor_tensor(pos, tmp.unsqueeze(1).to_broadcast([P, 2, E]), float(SLOT),
                                                        PS[:, 5, E:3 * E].rearrange("p (n e) -> p n e", n=2), ALU.mult, ALU.add))
                    for n in range(2):
                        link(tt(placed[:, n, :, :], onehot[:, n, :, :], pos[:, n, :].unsqueeze(1).to_broadcast([P, K, E]), ALU.mult))
                        link(nc.vector.tensor_reduce(dest[:, n, :], placed[:, n, :, :], AX, ALU.add))

            norm_passed(1)
            for n, k in (("transposed", 5), ("d_ready", 4), ("scores_ready", 1), ("a_ready", 1), ("b_ready", 1), ("c_ready", 1), ("e_ready", 1),
                         ("tokens_loaded", 16)):
                S[n].passed(k)

            used = ctx.enter_context(nc.semaphore("expert_chunk_used"))
            loop = {n: ctx.enter_context(nc.semaphore(n)) for n in (
                "pick_ready spread_ready gathered gathered_copied gate_clipped sigmoid_ready act_ready act_turned "
                "act_copied y_copied scattered bias_used plan_ready plan_turned plan_copied gate_exp_ready gates_ready gates_spread "
                "places_ready places_copied gates_turned gates_copied bias2_scaled gather_turned xt_copied".split())}

            with nc.Block() as block:

                def trips(eng):
                    eng.wait_ge(loop["plan_copied"], 1)
                    return eng.value_load(plan[3:4, 0:1], min_val=LAT * K // SLOT, max_val=MAX_BLOCKS)

                @block.sync
                def _(sp):
                    sp.wait_ge(loop["plan_copied"], 1)
                    loads = sp.value_load(plan[4:5, 0:1], min_val=1, max_val=E)
                    with sp.Fori(1, loads) as i:
                        e = sp.value_load(plan[1:2, bass.ds(i, 1)], min_val=0, max_val=E - 1)
                        last = sp.value_load(plan[2:3, bass.ds(i, 1)], min_val=0, max_val=MAX_BLOCKS)
                        sp.wait_ge(loop["bias_used"], last + 1)
                        sp.dma_start(bias1[0:1, :], t["b1_2"][bass.ds(e, 1), :]).then_inc(bias_landed, 16)
                        for c in range(12):
                            sp.wait_ge(used, last * 12 + (c + 1))
                            load_expert_chunk(sp, e, c)

                @block.tensor
                def _(pe):
                    def gather():
                        for a in range(2):
                            for g in range(2):
                                ins = nc.tensor.matmul(PS[64 * g:64 * g + 64, 6, :], pick[:, a, :], htok[:, a, g * 512:g * 512 + 512],
                                                       start=(a == 0), stop=(a == 1))
                        ins.then_inc(loop["gathered"], 1)

                    def turn_gathered(i):
                        pe.wait_ge(loop["gathered_copied"], i + 1)
                        for j in range(4):
                            ins = nc.tensor.transpose(PS[:, 6, j * P:(j + 1) * P], xg[:, j * P:(j + 1) * P], ident)
                        ins.then_inc(loop["gather_turned"], 1)

                    def scatter():
                        for a in range(2):
                            for g in range(2):
                                ins = nc.tensor.matmul(PS[:, 2 * a + g, :], spread[64 * g:64 * g + 64, a * P:(a + 1) * P],
                                                       ys[64 * g:64 * g + 64, :], start=False, stop=False, skip_group_check=True)
                        ins.then_inc(loop["scattered"], 1)

                    def first_products(i, load):
                        pe.wait_ge(bias_landed, load * 16 + 16)
                        for half in range(2):
                            for g in range(2):
                                ins = nc.tensor.matmul(PS[64 * g:64 * g + 64, 4 + half, :], ones[0:1, 0:SLOT],
                                                       bias1[0:1, half * F + g * 512:half * F + g * 512 + 512], start=True, stop=False)
                        ins.then_inc(loop["bias_used"], 1)
                        pe.wait_ge(loop["xt_copied"], i + 1)
                        for c in range(8):
                            pe.wait_ge(chunk_landed[c], load * 16 + 16)
                            for half in range(2):
                                for g in range(2):
                                    ins = nc.tensor.matmul(PS[64 * g:64 * g + 64, 4 + half, :], xt[:, c % 4, c // 4, :],
                                                           W[:, c, half * F + g * 512:half * F + g * 512 + 512], start=False, stop=(c == 7))
                            ins.then_inc(used, 1)

                    def gather_next(i):
                        pe.wait_ge(loop["pick_ready"], i + 2)
                        gather()

                    def scatter_last(i):
                        pe.wait_ge(loop["spread_ready"], i)
                        pe.wait_ge(loop["y_copied"], i)
                        scatter()

                    def second_products(i, load):
                        pe.wait_ge(loop["act_ready"], i + 1)
                        for j in range(4):
                            ins = nc.tensor.transpose(PS[:, 5, j * P:(j + 1) * P], act_[:, j * P:(j + 1) * P], ident)
                        ins.then_inc(loop["act_turned"], 1)
                        turn_gathered(i + 1)
                        pe.wait_ge(loop["act_copied"], i + 1)
                        for k in range(KT):
                            if k % 2 == 0:
                                pe.wait_ge(chunk_landed[8 + k // 2], load * 16 + 16)
                            for g in range(2):
                                ins = nc.tensor.matmul(PS[64 * g:64 * g + 64, 7, :], at_[:, k % 4, k // 4, :],
                                                       W[:, 8 + k // 2, k % 2 * D + g * 512:k % 2 * D + g * 512 + 512], start=(k == 0),
                                                       stop=(k == KT - 1))
                            if k % 2 == 1:
                                ins.then_inc(used, 1)

                    pe.wait_ge(loop["pick_ready"], 1)
                    gather()
                    turn_gathered(0)
                    pe.wait_ge(loop["plan_ready"], 1)
                    nc.tensor.transpose(PS[0:5, 7, 0:P], plan_by, ident).then_inc(loop["plan_turned"], 1)
                    first_products(0, 0)
                    pe.wait_ge(loop["gates_spread"], 2)
                    pe.wait_ge(loop["plan_copied"], 1)
                    for n in range(2):
                        ins = nc.tensor.transpose(PS[0:E, 7, n * P:(n + 1) * P], gates_of[:, n, :], ident)
                    ins.then_inc(loop["gates_turned"], 1)
                    gather_next(0)
                    pe.wait_ge(loop["gates_copied"], 1)
                    second_products(0, 0)
                    pe.wait_ge(loop["xt_copied"], 2)
                    for r, src in enumerate((dest0, gates)):
                        for n in range(2):
                            if r + n == 2:
                                pe.wait_ge(loop["y_copied"], 1)
                            for k in range(K):
                                ins = nc.tensor.matmul(PS[:, 4 + 2 * r + n, k * P:(k + 1) * P], src[:, n, k:k + 1].to_broadcast([P, P]), ident,
                                                       start=True, stop=True)
                            ins.then_inc(loop["places_ready"], 1)
                    pe.wait_ge(loop["places_copied"], 4)
                    load = pe.value_load(plan[0:1, 1:2], min_val=0, max_val=E - 1)
                    first_products(1, load)
                    pe.wait_ge(loop["bias2_scaled"], 1)
                    for a in range(2):
                        for g in range(2):
                            nc.tensor.matmul(PS[:, 2 * a + g, :], gates_by[0:E, a * P:(a + 1) * P], bias2[0:E, g * 512:g * 512 + 512],
                                             start=False, stop=False, skip_group_check=True)
                    gather_next(1)
                    scatter_last(1)
                    second_products(1, load)
                    n = trips(pe)
                    with pe.Fori(2, n) as i:
                        load = pe.value_load(plan[0:1, bass.ds(i, 1)], min_val=0, max_val=E - 1)
                        first_products(i, load)
                        gather_next(i)
                        scatter_last(i)
                        second_products(i, load)
                    scatter_last(n)

                @block.scalar
                def _(act):
                    nc.scalar.activation(gates, gates, ACT.Exp).then_inc(loop["gate_exp_ready"], 1)

                    def copy_gathered(i):
                        act.wait_ge(loop["gathered"], i + 1)
                        nc.scalar.copy(xg, PS[:, 6, :]).then_inc(loop["gathered_copied"], 1)

                    def copy_turned(i):
                        act.wait_ge(loop["gather_turned"], i + 1)
                        nc.scalar.copy(xt, PS[:, 6, :].rearrange("p (j g s) -> p j g s", j=4, g=2)).then_inc(loop["xt_copied"], 1)

                    copy_gathered(0)
                    copy_turned(0)

                    def one_block(i):
                        act.wait_ge(loop["gate_clipped"], i + 1)
                        nc.scalar.activation(sig, gate_, ACT.Sigmoid, scale=1.702).then_inc(loop["sigmoid_ready"], 1)
                        copy_gathered(i + 1)
                        act.wait_ge(loop["act_turned"], i + 1)
                        nc.scalar.copy(at_, PS[:, 5, :].rearrange("p (j g s) -> p j g s", j=4, g=2)).then_inc(loop["act_copied"], 1)
                        copy_turned(i + 1)

                    act.wait_ge(loop["gates_turned"], 1)
                    nc.scalar.copy(gates_by[0:E, :], PS[0:E, 7, 0:LAT]).then_inc(loop["gates_copied"], 1)
                    n = trips(act)
                    with act.Fori(0, n) as i:
                        one_block(i)

                @block.vector
                def _(dve):
                    steps = ctx.enter_context(nc.semaphore("block_steps"))

                    def tables(done):
                        for n in range(2):
                            nc.vector.tensor_tensor(eq[:, n, :, :], const("slot_row").unsqueeze(1).to_broadcast([P, K, SLOT]),
                                                    dest[:, n, :].unsqueeze(2).to_broadcast([P, K, SLOT]), ALU.is_equal).then_inc(steps, 1)
                        dve.wait_ge(steps, done(2))
                        nc.vector.tensor_scalar(dest, dest, -float(SLOT), None, ALU.add).then_inc(steps, 1)
                        nc.vector.tensor_reduce(pick[:, 0, :], eq[:, 0, :, :].rearrange("p k s -> p s k"), AX, ALU.add).then_inc(steps, 1)
                        nc.vector.tensor_reduce(pick[:, 1, :], eq[:, 1, :, :].rearrange("p k s -> p s k"), AX, ALU.add).then_inc(
                            loop["pick_ready"], 1)

                    def link(ins):
                        dve_chain.link(dve, ins)

                    ts = nc.vector.tensor_scalar
                    link(nc.vector.tensor_copy(dest0, dest))
                    tables(lambda x: x)
                    link(ts(some, blocks, 1.0, None, ALU.min))
                    link(nc.vector.tensor_tensor_scan(rank, ones[:, 0:E], some, 0.0, ALU.mult, ALU.add))
                    for n, (x, y) in enumerate(((pend, some), (rank, ones[:, 0:E]), (rank, blocks))):
                        link(nc.vector.scalar_tensor_tensor(scratch, x, const("partition"), y, ALU.is_le, ALU.mult,
                                                            accum_out=plan_by[:, n:n + 1]))
                    link(ts(plan_by[:, 1:2], plan_by[:, 1:2], float(E - 1), None, ALU.min))
                    link(ts(plan_by[:, 2:3], plan_by[:, 2:3], -1.0, 0.0, ALU.add, ALU.max))
                    link(nc.vector.tensor_copy(plan_by[:, 3:4], pend[:, E - 1:E]))
                    nc.vector.tensor_copy(plan_by[:, 4:5], rank[:, E - 1:E]).then_inc(loop["plan_ready"], 1)
                    dve.wait_ge(loop["plan_turned"], 1)
                    nc.vector.tensor_copy(plan[0:5, :], PS[0:5, 7, 0:P]).then_inc(loop["plan_copied"], 1)
                    dve.wait_ge(loop["gate_exp_ready"], 1)
                    link(nc.vector.tensor_reduce(gsum, gates, AX, ALU.add))
                    link(nc.vector.reciprocal(gsum, gsum))
                    nc.vector.tensor_tensor(gates, gates, gsum.unsqueeze(2).to_broadcast([P, 2, K]), ALU.mult).then_inc(loop["gates_ready"], 1)
                    dve.wait_ge(loop["gates_ready"], 1)
                    for n in range(2):
                        link(nc.vector.tensor_tensor(placed[:, n, :, :], onehot[:, n, :, :],
                                                     gates[:, n, :].unsqueeze(2).to_broadcast([P, K, E]), ALU.mult))
                        nc.vector.tensor_reduce(gates_of[:, n, :], placed[:, n, :, :].rearrange("p k e -> p e k"), AX,
                                                ALU.add).then_inc(loop["gates_spread"], 1)
                    dve.wait_ge(steps, 4)
                    dve.wait_ge(loop["gathered"], 1)
                    tables(lambda x: 4 + x)

                    def activation(i):
                        dve.wait_ge(used, i * 12 + 8)
                        nc.vector.tensor_scalar(gate_, PS[:, 4, :], 7.0, None, ALU.min).then_inc(loop["gate_clipped"], 1)
                        nc.vector.tensor_scalar(up, PS[:, 5, :], 7.0, -7.0, ALU.min, ALU.max).then_inc(steps, 1)
                        dve.wait_ge(steps, i * 8 + 9)
                        dve.wait_ge(loop["gate_clipped"], i + 1)
                        nc.vector.scalar_tensor_tensor(up, up, 1.0, gate_, ALU.add, ALU.mult).then_inc(steps, 1)
                        dve.wait_ge(steps, i * 8 + 10)
                        dve.wait_ge(loop["sigmoid_ready"], i + 1)
                        nc.vector.tensor_tensor(act_, up, sig, ALU.mult).then_inc(loop["act_ready"], 1)

                    def gates_of_slots(i):
                        nc.vector.scalar_tensor_tensor(eq2, drow, slot, grow, ALU.is_equal, ALU.mult).then_inc(steps, 1)
                        dve.wait_ge(steps, i * 8 + 11)
                        nc.vector.tensor_scalar(slot, slot, float(SLOT), None, ALU.add).then_inc(steps, 1)

                    def spread_slots():
                        nc.vector.tensor_reduce(spread, eq2.rearrange("p k t -> p t k"), AX, ALU.add).then_inc(loop["spread_ready"], 1)

                    def outputs(i):
                        dve.wait_ge(used, i * 12 + 12)
                        nc.vector.tensor_tensor(ys, PS[:, 7, :], gain_split, ALU.mult).then_inc(loop["y_copied"], 1)

                    dve.wait_ge(*at("late_loaded", 32))
                    nc.vector.tensor_tensor(bias2[0:E, :], bias2[0:E, :], gain_rows[0:E, :], ALU.mult).then_inc(loop["bias2_scaled"], 1)
                    activation(0)
                    outputs(0)
                    for r, dst in enumerate((drow, grow)):
                        for n in range(2):
                            dve.wait_ge(loop["places_ready"], 2 * r + n + 1)
                            nc.vector.tensor_copy(dst[:, :, n * P:(n + 1) * P],
                                                  PS[:, 4 + 2 * r + n, :].rearrange("p (k t) -> p k t", k=K)).then_inc(loop["places_copied"], 1)
                    dve.wait_ge(loop["places_copied"], 4)
                    gates_of_slots(0)
                    spread_slots()
                    dve.wait_ge(loop["gathered"], 2)
                    tables(lambda x: 12 + x)
                    n = trips(dve)
                    with dve.Fori(1, n) as i:
                        activation(i)
                        gates_of_slots(i)
                        dve.wait_ge(loop["scattered"], i)
                        spread_slots()
                        dve.wait_ge(loop["gathered"], i + 2)
                        tables(lambda x: i * 8 + (12 + x))
                        outputs(i)

            S["late_loaded"].passed(32)

            out_rows, squares = htok, take(PW, [0], 4, 512)
            square_sums, sums, rms, rstd = take(SM, sm, 4), take(SM, sm, 2), take(SM, sm, 2), take(SM, sm, 2)
            last = {n: ctx.enter_context(nc.semaphore(n)) for n in "half_summed tile_summed last_rms_ready tile_normed tile_stored".split()}
            with nc.Block() as block:

                @block.scalar
                def _(act):
                    for b in range(4):
                        nc.scalar.activation(squares[:, b, :], PS[:, b, :], ACT.Square, accum_out=square_sums[:, b:b + 1]).then_inc(last["half_summed"], 1)
                    for n in range(2):
                        act.wait_ge(last["tile_summed"], n + 1)
                        nc.scalar.activation(rms[:, n:n + 1], sums[:, n:n + 1], ACT.Sqrt, bias=const("eps"), scale=1.0 / D).then_inc(last["last_rms_ready"], 1)

                @block.vector
                def _(dve):
                    for n in range(2):
                        dve.wait_ge(last["half_summed"], 2 * n + 2)
                        nc.vector.tensor_tensor(sums[:, n:n + 1], square_sums[:, 2 * n:2 * n + 1], square_sums[:, 2 * n + 1:2 * n + 2],
                                                ALU.add).then_inc(last["tile_summed"], 1)
                    for n in range(2):
                        dve.wait_ge(last["last_rms_ready"], n + 1)
                        dve_chain.link(dve, nc.vector.reciprocal(rstd[:, n:n + 1], rms[:, n:n + 1]))
                        for g in range(2):
                            nc.vector.scalar_tensor_tensor(out_rows[:, n, g * 512:g * 512 + 512], PS[:, 2 * n + g, :], rstd[:, n:n + 1],
                                                           norm_rows[:, g * 512:g * 512 + 512], ALU.mult, ALU.mult).then_inc(last["tile_normed"], 1)

                @block.sync
                def _(sp):
                    for n in range(2):
                        sp.wait_ge(last["tile_normed"], 2 * n + 2)
                        sp.dma_start(out[0, n * P:(n + 1) * P, :], out_rows[:, n, :]).then_inc(last["tile_stored"], 16)
                    sp.wait_ge(last["tile_stored"], 32)

        routed_experts()


_OUTS = [((1, 256, 1024), "float32")]


def kernel(**inputs):
    import numpy as _np
    import concourse.bacc as _bacc
    from concourse import mybir as _mybir
    from concourse.bass_utils import run_bass_kernel_spmd as _run

    nc = _bacc.Bacc("TRN2", target_bir_lowering=False, num_devices=1)
    arrays, aps = {}, {}

    def give(name, a):
        arrays[f"in_{name}"] = a
        aps[name] = nc.dram_tensor(f"in_{name}", a.shape, _mybir.dt.from_np(a.dtype), kind="ExternalInput").ap()

    inputs = {name: _np.ascontiguousarray(a) for name, a in inputs.items()}
    packed = {name for r in VECTOR_ROWS for name, _ in r} | {name for name, _ in BROADCAST}
    rows = [_np.concatenate([inputs[name].reshape(k, P) for name, k in r]) for r in VECTOR_ROWS]
    give("vector_rows", _np.stack([_np.concatenate([r, _np.zeros((P - len(r), P), r.dtype)]) for r in rows]))
    give("broadcast_row", _np.concatenate([inputs[name].reshape(-1) for name, _ in BROADCAST]))
    for name, a in inputs.items():
        if name in packed:
            continue
        if name.endswith("_2") and a.ndim > 1:
            a = a.reshape(a.shape[1:])
        give(name, a)
    table, at = constant_tables()
    give("consts", table)
    shape, dtype = _OUTS[0]
    out = nc.dram_tensor("out_0", shape, _mybir.dt.from_np(_np.dtype(dtype)), kind="ExternalOutput").ap()
    layers_and_experts_kernel(nc, aps, at, out)
    r = _run(nc, [arrays], core_ids=[0])
    return r.results[0]["out_0"]
```
